# Optimizing a Trainium2 kernel written in Bass

```python
import math
import jax, jax.numpy as jnp
from jax import lax
import numpy as np
import jax
import jax.numpy as jnp

D_MODEL = 1024
BATCH = 1
SEQ = 512
DEPTH = 1

N_META = 16
SSM_WIDTH = 1024
SSM_GROUP = 16
SSM_GROUPS = SSM_WIDTH // SSM_GROUP
SSM_STATE = 64
DT_MIN = 1e-3
DT_MAX = 1e-1
HGRN_WIDTH = 1024
HGRN_HEAD_DIM = 128
HGRN_HEADS = HGRN_WIDTH // HGRN_HEAD_DIM
HGRN_CHUNK = 16
D_FF = 2816
CONV_WIDTH = 3
EPS = 1e-6
IN_COLS = SSM_WIDTH + 4 * HGRN_WIDTH + 2 * D_MODEL


def rmsnorm(x, g):
    xf = x.astype(jnp.float32)
    y = xf * lax.rsqrt(jnp.mean(xf * xf, axis=-1, keepdims=True) + EPS)
    return (y * g.astype(jnp.float32)).astype(x.dtype)

def _complex_affine_combine(e1, e2):
    a1r, a1i, b1r, b1i = e1
    a2r, a2i, b2r, b2i = e2
    ar = a1r * a2r - a1i * a2i
    ai = a1r * a2i + a1i * a2r
    br = a2r * b1r - a2i * b1i + b2r
    bi = a2r * b1i + a2i * b1r + b2i
    return ar, ai, br, bi

def s5_mixer(u, lam_re, lam_im, log_dt, b_re, b_im, c_re, c_im, d_skip, w_glu):
    bsz, L, _ = u.shape
    uf = u.astype(jnp.float32).reshape(bsz, L, SSM_GROUPS, SSM_GROUP)
    lr = lam_re.astype(jnp.float32)
    li = lam_im.astype(jnp.float32)
    dt = jnp.exp(log_dt.astype(jnp.float32))[:, None]
    mag = jnp.exp(lr * dt)
    ab_re = mag * jnp.cos(li * dt)
    ab_im = mag * jnp.sin(li * dt)
    den = lr * lr + li * li
    nr = ab_re - 1.0
    coef_re = (nr * lr + ab_im * li) / den
    coef_im = (ab_im * lr - nr * li) / den
    br = b_re.astype(jnp.float32)
    bi = b_im.astype(jnp.float32)
    bb_re = coef_re[..., None] * br - coef_im[..., None] * bi
    bb_im = coef_re[..., None] * bi + coef_im[..., None] * br
    v_re = jnp.einsum('blgh,gph->blgp', uf, bb_re)
    v_im = jnp.einsum('blgh,gph->blgp', uf, bb_im)
    a_re = jnp.broadcast_to(ab_re[None, None], (1, L, SSM_GROUPS, SSM_STATE))
    a_im = jnp.broadcast_to(ab_im[None, None], (1, L, SSM_GROUPS, SSM_STATE))
    _, _, s_re, s_im = lax.associative_scan(_complex_affine_combine, (a_re, a_im, v_re, v_im), axis=1)
    y = (jnp.einsum('blgp,ghp->blgh', s_re, c_re.astype(jnp.float32))
         - jnp.einsum('blgp,ghp->blgh', s_im, c_im.astype(jnp.float32))
         + d_skip.astype(jnp.float32).reshape(SSM_GROUPS, SSM_GROUP) * uf)
    y = jax.nn.gelu(y.reshape(bsz, L, SSM_WIDTH)).astype(u.dtype)
    return y * jax.nn.sigmoid(y @ w_glu)

def hgrn2_mixer(q, f_logit, i_in, og, lb, norm_g):
    bsz, L, _ = q.shape
    n_chunks = L // HGRN_CHUNK

    def heads(t):
        return t.reshape(bsz, n_chunks, HGRN_CHUNK, HGRN_HEADS, HGRN_HEAD_DIM).transpose(1, 0, 3, 2, 4)

    lbf = lb.astype(jnp.float32)
    f = lbf + (1.0 - lbf) * jax.nn.sigmoid(f_logit.astype(jnp.float32))
    log_f = jnp.log(f)
    qh = heads(q.astype(jnp.float32))
    kh = heads(1.0 - f)
    vh = heads(i_in.astype(jnp.float32))
    cum = jnp.cumsum(heads(log_f), axis=3)
    q_in = qh * jnp.exp(cum)
    k_in = kh * jnp.exp(-cum)
    k_out = kh * jnp.exp(cum[..., -1:, :] - cum)
    chunk_decay = jnp.exp(cum[..., -1, :])
    causal = jnp.tril(jnp.ones((HGRN_CHUNK, HGRN_CHUNK), dtype=bool))

    def chunk_step(state, xs):
        qi, ki, ko, v, dec = xs
        scores = jnp.where(causal, jnp.einsum('bhtd,bhsd->bhts', qi, ki), 0.0)
        o = jnp.einsum('bhts,bhsv->bhtv', scores, v) + jnp.einsum('bhtd,bhdv->bhtv', qi, state)
        state = dec[..., None] * state + jnp.einsum('bhsd,bhsv->bhdv', ko, v)
        return state, o

    init = jnp.zeros((bsz, HGRN_HEADS, HGRN_HEAD_DIM, HGRN_HEAD_DIM), jnp.float32)
    _, o = lax.scan(chunk_step, init, (q_in, k_in, k_out, vh, chunk_decay))
    o = o.transpose(1, 0, 3, 2, 4).reshape(bsz, L, HGRN_HEADS, HGRN_HEAD_DIM)
    o = o * lax.rsqrt(jnp.mean(o * o, axis=-1, keepdims=True) + EPS) * norm_g.astype(jnp.float32)
    o = o.reshape(bsz, L, HGRN_WIDTH).astype(q.dtype)
    return o * jax.nn.silu(og)

def causal_dwconv(u, w, b):
    L = u.shape[1]
    up = jnp.pad(u, ((0, 0), (CONV_WIDTH - 1, 0), (0, 0)))
    out = b
    for j in range(CONV_WIDTH):
        out = out + up[:, j:j + L, :] * w[j]
    return out

def first_inputs(seed: int = 0) -> dict:
    key = jax.random.key(seed)
    ks = jax.random.split(key, 24)
    f32 = jnp.float32

    def nrm(k, shape, scale):
        return jax.random.normal(k, shape, f32) * scale

    n_idx = jnp.arange(SSM_STATE, dtype=f32)
    return {
        'x': nrm(ks[0], (BATCH, SEQ, D_MODEL), 1.0),
        'meta_tokens': nrm(ks[1], (N_META, D_MODEL), 1.0),
        'mix_norm_g': 1.0 + nrm(ks[2], (DEPTH, D_MODEL), 0.02),
        'w_in': nrm(ks[3], (DEPTH, D_MODEL, IN_COLS), D_MODEL ** -0.5),
        'ssm_lambda_re': -0.5 + nrm(ks[4], (DEPTH, SSM_GROUPS, SSM_STATE), 0.01),
        'ssm_lambda_im': math.pi * n_idx + nrm(ks[5], (DEPTH, SSM_GROUPS, SSM_STATE), 0.01),
        'ssm_log_dt': jax.random.uniform(ks[6], (DEPTH, SSM_GROUPS), f32, math.log(DT_MIN), math.log(DT_MAX)),
        'ssm_b_re': nrm(ks[7], (DEPTH, SSM_GROUPS, SSM_STATE, SSM_GROUP), (2 * SSM_GROUP) ** -0.5),
        'ssm_b_im': nrm(ks[8], (DEPTH, SSM_GROUPS, SSM_STATE, SSM_GROUP), (2 * SSM_GROUP) ** -0.5),
        'ssm_c_re': nrm(ks[9], (DEPTH, SSM_GROUPS, SSM_GROUP, SSM_STATE), SSM_STATE ** -0.5),
        'ssm_c_im': nrm(ks[10], (DEPTH, SSM_GROUPS, SSM_GROUP, SSM_STATE), SSM_STATE ** -0.5),
        'ssm_d': nrm(ks[11], (DEPTH, SSM_WIDTH), 1.0),
        'ssm_w_glu': nrm(ks[12], (DEPTH, SSM_WIDTH, SSM_WIDTH), SSM_WIDTH ** -0.5),
        'w_ssm_proj': nrm(ks[13], (DEPTH, SSM_WIDTH, D_MODEL), SSM_WIDTH ** -0.5),
        'hgrn_lb_logits': nrm(ks[14], (DEPTH + 1, HGRN_WIDTH), 0.1),
        'hgrn_norm_g': 1.0 + nrm(ks[15], (DEPTH, HGRN_HEAD_DIM), 0.02),
        'w_hgrn_proj': nrm(ks[16], (DEPTH, HGRN_WIDTH, D_MODEL), HGRN_WIDTH ** -0.5),
        'w_out': nrm(ks[17], (DEPTH, D_MODEL, D_MODEL), D_MODEL ** -0.5),
        'ffn_norm_g': 1.0 + nrm(ks[18], (DEPTH, D_MODEL), 0.02),
        'w_up': nrm(ks[19], (DEPTH, D_MODEL, 2 * D_FF), D_MODEL ** -0.5),
        'conv_w': nrm(ks[20], (DEPTH, CONV_WIDTH, 2 * D_FF), CONV_WIDTH ** -0.5),
        'conv_b': nrm(ks[21], (DEPTH, 2 * D_FF), 0.01),
        'w_down': nrm(ks[22], (DEPTH, D_FF, D_MODEL), D_FF ** -0.5),
        'final_norm_g': 1.0 + nrm(ks[23], (D_MODEL,), 0.02),
    }

def first_block(x, meta_tokens, mix_norm_g, w_in, ssm_lambda_re, ssm_lambda_im, ssm_log_dt,
              ssm_b_re, ssm_b_im, ssm_c_re, ssm_c_im, ssm_d, ssm_w_glu, w_ssm_proj,
              hgrn_lb_logits, hgrn_norm_g, w_hgrn_proj, w_out, ffn_norm_g, w_up, conv_w,
              conv_b, w_down, final_norm_g):
    bsz = x.shape[0]
    meta = jnp.broadcast_to(meta_tokens.astype(x.dtype)[None], (bsz, N_META, D_MODEL))
    h = jnp.concatenate([meta, x], axis=1)
    lower_bounds = jnp.cumsum(jax.nn.softmax(hgrn_lb_logits.astype(jnp.float32), axis=0), axis=0)
    o1 = SSM_WIDTH
    o2 = o1 + HGRN_WIDTH
    o3 = o2 + HGRN_WIDTH
    o4 = o3 + HGRN_WIDTH
    o5 = o4 + HGRN_WIDTH
    o6 = o5 + D_MODEL
    for l in range(DEPTH):
        z = rmsnorm(h, mix_norm_g[l])
        p = z @ w_in[l]
        y_a = s5_mixer(p[..., :o1], ssm_lambda_re[l], ssm_lambda_im[l], ssm_log_dt[l],
                       ssm_b_re[l], ssm_b_im[l], ssm_c_re[l], ssm_c_im[l], ssm_d[l], ssm_w_glu[l])
        y_b = hgrn2_mixer(p[..., o1:o2], p[..., o2:o3], p[..., o3:o4], p[..., o4:o5],
                          lower_bounds[l], hgrn_norm_g[l])
        merged = (jax.nn.sigmoid(p[..., o5:o6]) * (y_a @ w_ssm_proj[l])
                  + jax.nn.sigmoid(p[..., o6:]) * (y_b @ w_hgrn_proj[l]))
        h = h + merged @ w_out[l]
        z = rmsnorm(h, ffn_norm_g[l])
        u = causal_dwconv(z @ w_up[l], conv_w[l], conv_b[l])
        h = h + (jax.nn.silu(u[..., :D_FF]) * u[..., D_FF:]) @ w_down[l]
    return rmsnorm(h[:, N_META:], final_norm_g)


GRID_W = 64
N_MEM = 256
HEAD_DIM = 64
NA_HEADS = 6
NA_WIDTH = NA_HEADS * HEAD_DIM
NA_WIN_ROWS = 8
NA_WIN_COLS = 16
RW_HEADS = 6
RW_WIDTH = RW_HEADS * HEAD_DIM
DECAY_LORA = 64
AAA_LORA = 64
GATE_LORA = 128
MEM_HEADS = 4
MEM_WIDTH = MEM_HEADS * HEAD_DIM
N_BRANCH = 3
N_EXPERTS = 16
EC_CAPACITY = 2
EXPERT_FF = 2 * D_MODEL
RMS_EPS = 1e-6
GN_EPS = 64e-5
IN_WIDTHS = (NA_WIDTH, NA_WIDTH, NA_WIDTH, RW_WIDTH, RW_WIDTH, RW_WIDTH, DECAY_LORA, AAA_LORA, GATE_LORA, MEM_WIDTH, D_MODEL, D_MODEL, D_MODEL)
D_IN = sum(IN_WIDTHS)


def rms_norm(x, g):
    xf = x.astype(jnp.float32)
    y = xf * lax.rsqrt(jnp.mean(xf * xf, axis=-1, keepdims=True) + RMS_EPS)
    return (y * g.astype(jnp.float32)).astype(x.dtype)

def split_columns(p):
    cuts = []
    acc = 0
    for w in IN_WIDTHS[:-1]:
        acc += w
        cuts.append(acc)
    return jnp.split(p, cuts, axis=-1)

def to_heads(t, n_heads):
    b, s, c = t.shape
    return t.reshape(b, s, n_heads, c // n_heads)

def neighborhood_attention(q, k, v, rpb):
    b, s, h, dh = q.shape
    rows = s // GRID_W
    kr = min(NA_WIN_ROWS, rows)
    kc = NA_WIN_COLS
    q = (q * (dh ** -0.5)).reshape(b, rows, GRID_W, h, dh).transpose(1, 0, 2, 3, 4)
    k = k.reshape(b, rows, GRID_W, h, dh)
    v = v.reshape(b, rows, GRID_W, h, dh)
    col = jnp.arange(GRID_W)
    col_start = jnp.clip(col - kc // 2, 0, GRID_W - kc)
    col_idx = col_start[:, None] + jnp.arange(kc)[None, :]
    col_off = col_idx - col[:, None] + (NA_WIN_COLS - 1)

    def row_block(args):
        r, q_r = args
        r_start = jnp.clip(r - kr // 2, 0, rows - kr)
        k_win = lax.dynamic_slice_in_dim(k, r_start, kr, axis=1)[:, :, col_idx]
        v_win = lax.dynamic_slice_in_dim(v, r_start, kr, axis=1)[:, :, col_idx]
        row_off = r_start + jnp.arange(kr) - r + (NA_WIN_ROWS - 1)
        bias = rpb[:, row_off[:, None, None], col_off[None, :, :]].transpose(0, 2, 1, 3)
        scores = jnp.einsum('bwhd,biwjhd->bhwij', q_r, k_win).astype(jnp.float32) + bias.astype(jnp.float32)[None]
        probs = jax.nn.softmax(scores.reshape(b, h, GRID_W, kr * kc), axis=-1).reshape(b, h, GRID_W, kr, kc)
        return jnp.einsum('bhwij,biwjhd->bwhd', probs.astype(v.dtype), v_win)

    out = lax.map(row_block, (jnp.arange(rows), q))
    return out.transpose(1, 0, 2, 3, 4).reshape(b, s, h * dh)

def token_shift(t, direction):
    if direction == 0:
        return jnp.pad(t[:, :-1], ((0, 0), (1, 0), (0, 0)))
    return jnp.pad(t[:, 1:], ((0, 0), (0, 1), (0, 0)))

def wkv7_scan(r, w, k, v, a, b, reverse):
    bsz, _, h, n = r.shape

    def step(state, inp):
        r_t, w_t, k_t, v_t, a_t, b_t = inp
        sa = jnp.einsum('bhvk,bhk->bhv', state, a_t)
        state = state * w_t[:, :, None, :] + sa[..., None] * b_t[:, :, None, :] + v_t[..., None] * k_t[:, :, None, :]
        return state, jnp.einsum('bhvk,bhk->bhv', state, r_t)

    xs = tuple(t.transpose(1, 0, 2, 3) for t in (r, w, k, v, a, b))
    _, y = lax.scan(step, jnp.zeros((bsz, h, n, n), jnp.float32), xs, reverse=reverse)
    return y.transpose(1, 0, 2, 3)

def rwkv7_bidirectional(p_r, p_k, p_v, lat_w, lat_a, lat_g, mu_rkv, mu_w, mu_a, w0, w2, a0, a2, k_k, k_a, r_k, g2, ln_g, ln_b):
    out_dtype = p_r.dtype
    f32 = lambda t: t.astype(jnp.float32)
    p_r, p_k, p_v, lat_w, lat_a, lat_g = (f32(t) for t in (p_r, p_k, p_v, lat_w, lat_a, lat_g))
    mu_rkv, mu_w, mu_a, w0, w2, a0, a2 = (f32(t) for t in (mu_rkv, mu_w, mu_a, w0, w2, a0, a2))
    k_k, k_a, r_k, g2, ln_g, ln_b = (f32(t) for t in (k_k, k_a, r_k, g2, ln_g, ln_b))
    bsz, s, c = p_r.shape
    y_sum = jnp.zeros((bsz, s, RW_HEADS, HEAD_DIM), jnp.float32)
    bonus_sum = jnp.zeros((bsz, s, RW_HEADS, HEAD_DIM), jnp.float32)
    for d in range(2):
        def mix(t, mu):
            return t + (token_shift(t, d) - t) * mu
        r = mix(p_r, mu_rkv[d, 0])
        k = mix(p_k, mu_rkv[d, 1])
        v = mix(p_v, mu_rkv[d, 2])
        w_log = -jax.nn.softplus(-(w0[d] + jnp.tanh(mix(lat_w, mu_w[d])) @ w2[d])) - 0.5
        decay = jnp.exp(-jnp.exp(w_log))
        a = jax.nn.sigmoid(a0[d] + mix(lat_a, mu_a[d]) @ a2[d])
        kk = to_heads(k * k_k, RW_HEADS)
        kk = kk / jnp.maximum(jnp.sqrt(jnp.sum(kk * kk, axis=-1, keepdims=True)), 1e-12)
        k = k * (1.0 + (a - 1.0) * k_a)
        rh, kh, vh, ah = (to_heads(t, RW_HEADS) for t in (r, k, v, a))
        y_sum = y_sum + wkv7_scan(rh, to_heads(decay, RW_HEADS), kh, vh, -kk, kk * ah, reverse=(d == 1))
        bonus_sum = bonus_sum + jnp.sum(rh * kh * r_k, axis=-1, keepdims=True) * vh
    mean = jnp.mean(y_sum, axis=-1, keepdims=True)
    var = jnp.mean(jnp.square(y_sum - mean), axis=-1, keepdims=True)
    y = ((y_sum - mean) * lax.rsqrt(var + GN_EPS)).reshape(bsz, s, c) * ln_g + ln_b
    y = y + bonus_sum.reshape(bsz, s, c)
    g = jax.nn.sigmoid(lat_g) @ g2
    return (y * g).astype(out_dtype)

def memory_attention(q, mem_h, w_mem_kv):
    b, s, _ = q.shape
    mk, mv = jnp.split(mem_h @ w_mem_kv, 2, axis=-1)
    qh = to_heads(q, MEM_HEADS) * (HEAD_DIM ** -0.5)
    kh = to_heads(mk, MEM_HEADS)
    vh = to_heads(mv, MEM_HEADS)
    scores = jnp.einsum('bshd,bmhd->bhsm', qh, kh).astype(jnp.float32)
    probs = jax.nn.softmax(scores, axis=-1)
    return jnp.einsum('bhsm,bmhd->bshd', probs.astype(vh.dtype), vh).reshape(b, s, MEM_WIDTH)

def expert_choice_ffn(h, w_router, w_gate, w_up, w_down):
    b, s, d = h.shape
    cap = EC_CAPACITY * s // N_EXPERTS
    affinity = jax.nn.softmax((h @ w_router).astype(jnp.float32), axis=-1)
    top_val, top_idx = lax.top_k(affinity.transpose(0, 2, 1), cap)
    xe = jax.vmap(lambda hb, ib: hb[ib])(h, top_idx)
    act = jax.nn.silu(jnp.einsum('becd,edf->becf', xe, w_gate)) * jnp.einsum('becd,edf->becf', xe, w_up)
    ye = jnp.einsum('becf,efd->becd', act, w_down) * top_val[..., None].astype(h.dtype)
    return jax.vmap(lambda yb, ib: jnp.zeros((s, d), yb.dtype).at[ib.reshape(-1)].add(yb.reshape(-1, d)))(ye, top_idx)

def second_inputs(seed: int = 0) -> dict:
    key = jax.random.key(seed)
    ks = iter(jax.random.split(key, 40))
    L = DEPTH

    def nrm(shape, scale):
        return scale * jax.random.normal(next(ks), shape, jnp.float32)

    def uni(shape):
        return jax.random.uniform(next(ks), shape, jnp.float32, 0.0, 1.0)

    decay_ramp = jnp.linspace(-6.5, -1.5, RW_WIDTH, dtype=jnp.float32)
    return {
        'x': nrm((BATCH, SEQ, D_MODEL), 1.0),
        'mem': nrm((BATCH, N_MEM, D_MODEL), 1.0),
        'norm_mix_g': 1.0 + nrm((L, D_MODEL), 0.02),
        'norm_mem_g': 1.0 + nrm((L, D_MODEL), 0.02),
        'w_in': nrm((L, D_MODEL, D_IN), D_MODEL ** -0.5),
        'na_rpb': nrm((L, NA_HEADS, 2 * NA_WIN_ROWS - 1, 2 * NA_WIN_COLS - 1), 0.05),
        'rw_mu_rkv': uni((L, 2, 3, RW_WIDTH)),
        'rw_mu_w': uni((L, 2, DECAY_LORA)),
        'rw_mu_a': uni((L, 2, AAA_LORA)),
        'rw_w0': decay_ramp + nrm((L, 2, RW_WIDTH), 0.1),
        'rw_w2': nrm((L, 2, DECAY_LORA, RW_WIDTH), 0.1),
        'rw_a0': nrm((L, 2, RW_WIDTH), 0.1),
        'rw_a2': nrm((L, 2, AAA_LORA, RW_WIDTH), 0.1),
        'rw_k_k': 0.85 + nrm((L, RW_WIDTH), 0.02),
        'rw_k_a': 1.0 + nrm((L, RW_WIDTH), 0.02),
        'rw_r_k': nrm((L, RW_HEADS, HEAD_DIM), 0.1),
        'rw_g2': nrm((L, GATE_LORA, RW_WIDTH), GATE_LORA ** -0.5),
        'rw_ln_g': 1.0 + nrm((L, RW_WIDTH), 0.02),
        'rw_ln_b': nrm((L, RW_WIDTH), 0.02),
        'w_mem_kv': nrm((L, D_MODEL, 2 * MEM_WIDTH), D_MODEL ** -0.5),
        'w_branch_na': nrm((L, NA_WIDTH, D_MODEL), NA_WIDTH ** -0.5),
        'w_branch_rw': nrm((L, RW_WIDTH, D_MODEL), RW_WIDTH ** -0.5),
        'w_branch_mem': nrm((L, MEM_WIDTH, D_MODEL), MEM_WIDTH ** -0.5),
        'w_out': nrm((L, D_MODEL, D_MODEL), D_MODEL ** -0.5),
        'norm_ffn_g': 1.0 + nrm((L, D_MODEL), 0.02),
        'w_router': nrm((L, D_MODEL, N_EXPERTS), D_MODEL ** -0.5),
        'w_exp_gate': nrm((L, N_EXPERTS, D_MODEL, EXPERT_FF), D_MODEL ** -0.5),
        'w_exp_up': nrm((L, N_EXPERTS, D_MODEL, EXPERT_FF), D_MODEL ** -0.5),
        'w_exp_down': nrm((L, N_EXPERTS, EXPERT_FF, D_MODEL), EXPERT_FF ** -0.5),
        'norm_final_g': 1.0 + nrm((D_MODEL,), 0.02),
    }

def second_block(x, mem, norm_mix_g, norm_mem_g, w_in, na_rpb, rw_mu_rkv, rw_mu_w, rw_mu_a, rw_w0, rw_w2, rw_a0, rw_a2, rw_k_k, rw_k_a, rw_r_k, rw_g2, rw_ln_g, rw_ln_b, w_mem_kv, w_branch_na, w_branch_rw, w_branch_mem, w_out, norm_ffn_g, w_router, w_exp_gate, w_exp_up, w_exp_down, norm_final_g):
    for l in range(DEPTH):
        h = rms_norm(x, norm_mix_g[l])
        (na_q, na_k, na_v, p_r, p_k, p_v, lat_w, lat_a, lat_g, mem_q,
         gate_na, gate_rw, gate_mem) = split_columns(h @ w_in[l])
        y_na = neighborhood_attention(to_heads(na_q, NA_HEADS), to_heads(na_k, NA_HEADS), to_heads(na_v, NA_HEADS), na_rpb[l])
        y_rw = rwkv7_bidirectional(p_r, p_k, p_v, lat_w, lat_a, lat_g, rw_mu_rkv[l], rw_mu_w[l], rw_mu_a[l], rw_w0[l], rw_w2[l], rw_a0[l], rw_a2[l], rw_k_k[l], rw_k_a[l], rw_r_k[l], rw_g2[l], rw_ln_g[l], rw_ln_b[l])
        y_mem = memory_attention(mem_q, rms_norm(mem, norm_mem_g[l]), w_mem_kv[l])
        merged = (jax.nn.sigmoid(gate_na) * (y_na @ w_branch_na[l])
                  + jax.nn.sigmoid(gate_rw) * (y_rw @ w_branch_rw[l])
                  + jax.nn.sigmoid(gate_mem) * (y_mem @ w_branch_mem[l]))
        x = x + merged @ w_out[l]
        x = x + expert_choice_ffn(rms_norm(x, norm_ffn_g[l]), w_router[l], w_exp_gate[l], w_exp_up[l], w_exp_down[l])
    return rms_norm(x, norm_final_g)


def setup_inputs(seed=0):
    out = dict(first_inputs(seed))
    for name, value in second_inputs(seed + 1).items():
        if name != "x":
            out[name + "_2"] = value
    return out


def reference(
    x, meta_tokens, mix_norm_g, w_in, ssm_lambda_re, ssm_lambda_im, ssm_log_dt, ssm_b_re,
    ssm_b_im, ssm_c_re, ssm_c_im, ssm_d, ssm_w_glu, w_ssm_proj, hgrn_lb_logits, hgrn_norm_g,
    w_hgrn_proj, w_out, ffn_norm_g, w_up, conv_w, conv_b, w_down, final_norm_g, mem_2,
    norm_mix_g_2, norm_mem_g_2, w_in_2, na_rpb_2, rw_mu_rkv_2, rw_mu_w_2, rw_mu_a_2, rw_w0_2,
    rw_w2_2, rw_a0_2, rw_a2_2, rw_k_k_2, rw_k_a_2, rw_r_k_2, rw_g2_2, rw_ln_g_2, rw_ln_b_2,
    w_mem_kv_2, w_branch_na_2, w_branch_rw_2, w_branch_mem_2, w_out_2, norm_ffn_g_2, w_router_2,
    w_exp_gate_2, w_exp_up_2, w_exp_down_2, norm_final_g_2,
):
    x = first_block(
        x, meta_tokens, mix_norm_g, w_in, ssm_lambda_re, ssm_lambda_im, ssm_log_dt, ssm_b_re,
        ssm_b_im, ssm_c_re, ssm_c_im, ssm_d, ssm_w_glu, w_ssm_proj, hgrn_lb_logits, hgrn_norm_g,
        w_hgrn_proj, w_out, ffn_norm_g, w_up, conv_w, conv_b, w_down, final_norm_g,
    )
    return second_block(
        x, mem_2, norm_mix_g_2, norm_mem_g_2, w_in_2, na_rpb_2, rw_mu_rkv_2, rw_mu_w_2,
        rw_mu_a_2, rw_w0_2, rw_w2_2, rw_a0_2, rw_a2_2, rw_k_k_2, rw_k_a_2, rw_r_k_2, rw_g2_2,
        rw_ln_g_2, rw_ln_b_2, w_mem_kv_2, w_branch_na_2, w_branch_rw_2, w_branch_mem_2, w_out_2,
        norm_ffn_g_2, w_router_2, w_exp_gate_2, w_exp_up_2, w_exp_down_2, norm_final_g_2,
    )


_drawn_inputs = setup_inputs


def setup_inputs(seed=0):
    import zlib

    import numpy as np

    out = dict(_drawn_inputs(seed))
    spreads = {}
    factors = {'ssm_lambda_re': 64.0,
     'ssm_b_re': 3.042,
     'ssm_b_im': 3.367,
     'ssm_c_re': 3.165,
     'ssm_c_im': 3.294,
     'hgrn_norm_g': 4.797,
     'ffn_norm_g': 2.764,
     'conv_b': 4.631,
     'norm_mix_g_2': 3.333,
     'norm_mem_g_2': 8.0,
     'na_rpb_2': 32.689,
     'rw_mu_w_2': 25.702,
     'rw_w2_2': 2.913,
     'rw_a0_2': 3.421,
     'rw_k_k_2': 55.52,
     'rw_k_a_2': 5.349,
     'rw_ln_g_2': 44.136,
     'rw_ln_b_2': 58.128,
     'norm_ffn_g_2': 11.905,
     'norm_final_g_2': 7.766}
    for name, (base, spread) in spreads.items():
        noise = np.random.default_rng([zlib.crc32(name.encode()), seed]).standard_normal(out[name].shape)
        drawn = base * np.exp(spread * noise) if base else spread * noise
        out[name] = jnp.asarray(drawn.astype(out[name].dtype))
    for name, factor in factors.items():
        out[name] = (out[name] * factor).astype(out[name].dtype)
    return out
```

```python
from contextlib import ExitStack

import numpy as np

import concourse.bass as bass
from concourse import mybir

P = 128
ALU = mybir.AluOpType
ACT = mybir.ActivationFunctionType
F32 = mybir.dt.float32
X = mybir.AxisListType.X

D_MODEL = 1024
KT = D_MODEL // P
SEQ = 512
N_META = 16
LEN = SEQ + N_META
EPS = 1e-6


STAGE_TURN = []


def opener(nc, ctx, stage):
    free = sorted(nc.free_semaphores)
    half = len(free) // 2
    STAGE_TURN.append(stage)
    own = free[:half] if len(STAGE_TURN) % 2 else free[half:2 * half]
    sems = []

    def close():
        nc.gpsimd.sem_clear(range(own[0], own[0] + len(sems)))
        for s in sems:
            nc.release_semaphore(s)

    ctx.callback(close)

    def sb(name, shape, dt=F32):
        return ctx.enter_context(nc.sbuf_tensor(f"{stage}_{name}", shape, dt))

    def ps(name, shape):
        return ctx.enter_context(nc.psum_tensor(f"{stage}_{name}", shape, F32))

    def sem(name):
        sems.append(nc.alloc_semaphore(f"{stage}_{name}", num=own[0] + len(sems)))
        return sems[-1]

    return sb, ps, sem


def rmsnorm(nc, stage, x_dram, gain_dram, out_dram):
    C, T = x_dram.shape
    kt = C // P
    halves = 1 if T <= 512 else 2
    w = T // halves
    with ExitStack() as ctx:
        sb, ps, sem = opener(nc, ctx, stage)
        x = sb("x", [P, kt, T])
        sq = sb("sq", [P, kt, T])
        gain = sb("gain", [P, kt])
        ones = sb("ones", [P, P])
        scale = sb("scale", [P, T])
        eps = sb("eps", [P, 1])
        total = ps("total", [P, halves, 512])
        x_loaded = [sem(f"x_loaded{k}") for k in range(kt)]
        gain_loaded = sem("gain_loaded")
        consts_ready = sem("consts_ready")
        squared = sem("squared")
        summed = sem("summed")
        meaned = sem("meaned")
        inverted = sem("inverted")
        rooted = sem("rooted")
        scaled = sem("scaled")
        stored = sem("stored")
        xv = x_dram.rearrange("(k p) t -> p k t", p=P)
        ov = out_dram.rearrange("(k p) t -> p k t", p=P)
        total_v = total[:, :, 0:w]

        with nc.Block() as block:

            @block.sync
            def _(sp):
                for k in range(kt):
                    sp.dma_start(x[:, k, :], xv[:, k, :]).then_inc(x_loaded[k], 16)
                sp.dma_start(gain[:], gain_dram).then_inc(gain_loaded, 16)
                for k in range(kt):
                    sp.wait_ge(scaled, k + 1)
                    sp.dma_start(ov[:, k, :], x[:, k, :]).then_inc(stored, 16)
                sp.wait_ge(stored, 16 * kt)

            @block.scalar
            def _(act):
                for k in range(kt):
                    act.wait_ge(x_loaded[k], 16)
                    nc.scalar.activation(sq[:, k, :], x[:, k, :], ACT.Square).then_inc(squared, 1)
                act.wait_ge(inverted, 1)
                nc.scalar.activation(scale[:], scale[:], ACT.Sqrt).then_inc(rooted, 1)

            @block.tensor
            def _(pe):
                pe.wait_ge(consts_ready, 2)
                for k in range(kt):
                    pe.wait_ge(squared, k + 1)
                    for h in range(halves):
                        last = nc.tensor.matmul(total[:, h, 0:w], ones[:], sq[:, k, h * w:(h + 1) * w],
                                                start=(k == 0), stop=(k == kt - 1))
                last.then_inc(summed, 1)

            @block.vector
            def _(dve):
                nc.vector.memset(ones[:], 1.0).then_inc(consts_ready, 1)
                nc.vector.memset(eps[:], EPS).then_inc(consts_ready, 1)
                dve.wait_ge(summed, 1)
                nc.vector.tensor_scalar(scale[:].rearrange("p (h t) -> p h t", h=halves), total_v,
                                        1.0 / C, EPS, ALU.mult, ALU.add).then_inc(meaned, 1)
                dve.wait_ge(meaned, 1)
                nc.vector.reciprocal(scale[:], scale[:]).then_inc(inverted, 1)
                dve.wait_ge(rooted, 1)
                dve.wait_ge(gain_loaded, 16)
                for k in range(kt):
                    dve.wait_ge(x_loaded[k], 16)
                    dve.wait_ge(squared, k + 1)
                    nc.vector.scalar_tensor_tensor(x[:, k, :], x[:, k, :], gain[:, k:k + 1], scale[:],
                                                   ALU.mult, ALU.mult).then_inc(scaled, 1)


def project(nc, stage, x_dram, w_dram, out_dram, epilogue="copy", extras=(), width=2 * P):
    K, T = x_dram.shape
    M = w_dram.shape[1]
    kt = K // P
    nm = width // P
    slots = M // width
    loops, tail = divmod(slots, 2)
    halves = 1 if T <= 512 else 2
    w_t = T // halves
    n_extra = len(extras)
    with ExitStack() as ctx:
        sb, ps, sem = opener(nc, ctx, stage)
        x = sb("x", [P, kt, T])
        w = sb("w", [P, 2, kt, width])
        out = sb("out", [P, 2, nm, T])
        e = sb("e", [P, 2, max(n_extra, 1), nm, T])
        gate = sb("gate", [P, 2, nm, T])
        y = ps("y", [P, 2, nm, halves, 512])
        x_loaded = [sem(f"x_loaded{k}") for k in range(kt)]
        w_loaded = [sem(f"w_loaded{s}") for s in range(2)]
        e_loaded = [sem(f"e_loaded{s}") for s in range(2)]
        y_ready = sem("y_ready")
        gate_ready = sem("gate_ready")
        mul_ready = sem("mul_ready")
        out_ready = sem("out_ready")
        stored = [sem(f"stored{s}") for s in range(2)]
        xv = x_dram.rearrange("(k p) t -> p k t", p=P)
        wv = w_dram.rearrange("(k p) m -> p k m", p=P)
        ov = out_dram.rearrange("(m p) t -> p m t", p=P)
        ev = [a.rearrange("(m p) t -> p m t", p=P) for a in extras]

        def y_of(s):
            return y[:, s, :, :, 0:w_t].rearrange("p m h t -> p (m h) t")

        def flat(a):
            return a.rearrange("p m (h t) -> p (m h) t", h=halves)

        def over_slots(eng, body, skip_first=False):
            first = 1 if skip_first else 0
            if skip_first:
                for s in range(min(2, slots)):
                    body(0, s, True)
            if loops > first:
                with eng.Fori(first, loops) as i:
                    for s in range(2):
                        body(i, s, False)
            if tail and loops >= first:
                body(loops, 0, loops == 0)

        with nc.Block() as block:

            @block.sync
            def _(sp):
                def load_w(i, s, first):
                    if not first:
                        sp.wait_ge(y_ready, 2 * i + s - 1)
                    sp.dma_start(w[:, s], wv[:, :, bass.ds((2 * i + s) * width, width)]).then_inc(w_loaded[s], 16)
                    for n in range(n_extra):
                        if not first and n == 0:
                            sp.wait_ge(out_ready, 2 * i + s - 1)
                        sp.dma_start(e[:, s, n], ev[n][:, bass.ds((2 * i + s) * nm, nm), :]).then_inc(e_loaded[s], 16)

                for k in range(kt):
                    sp.dma_start(x[:, k, :], xv[:, k, :]).then_inc(x_loaded[k], 16)
                over_slots(sp, load_w, skip_first=True)

            @block.tensor
            def _(pe):
                def products(i, s, first):
                    pe.wait_ge(w_loaded[s], (i + 1) * 16)
                    if not first:
                        pe.wait_ge(out_ready, 2 * i + s - 1)
                    for m in range(nm):
                        for h in range(halves):
                            for k in range(kt):
                                if first and s == 0 and m == 0 and h == 0:
                                    pe.wait_ge(x_loaded[k], 16)
                                last = nc.tensor.matmul(y[:, s, m, h, 0:w_t], w[:, s, k, m * P:(m + 1) * P],
                                                        x[:, k, h * w_t:(h + 1) * w_t],
                                                        start=(k == 0), stop=(k == kt - 1))
                    last.then_inc(y_ready, 1)

                over_slots(pe, products, skip_first=True)

            @block.scalar
            def _(act):
                def evacuate(i, s, first):
                    if epilogue == "copy":
                        act.wait_ge(y_ready, 2 * i + s + 1)
                        if not first:
                            act.wait_ge(stored[s], i * 16)
                        nc.scalar.copy(flat(out[:, s]), y_of(s)).then_inc(out_ready, 1)
                    elif epilogue == "glu":
                        act.wait_ge(y_ready, 2 * i + s + 1)
                        if not first:
                            act.wait_ge(out_ready, 2 * i + s - 1)
                        nc.scalar.activation(flat(gate[:, s]), y_of(s), ACT.Sigmoid).then_inc(gate_ready, 1)
                    elif epilogue in ("gate", "gate_add"):
                        act.wait_ge(e_loaded[s], (i + 1) * 16 * n_extra)
                        if not first:
                            act.wait_ge(out_ready, 2 * i + s - 1)
                        nc.scalar.activation(gate[:, s], e[:, s, 0], ACT.Sigmoid).then_inc(gate_ready, 1)
                    act.wait_ge(out_ready, 2 * i + s + 1)
                    act.dma_start(ov[:, bass.ds((2 * i + s) * nm, nm), :], out[:, s]).then_inc(stored[s], 16)

                over_slots(act, evacuate, skip_first=True)
                for s in range(2):
                    act.wait_ge(stored[s], 16 * ((slots + 1 - s) // 2))

            @block.vector
            def _(dve):
                def finish(i, s, first):
                    dve.wait_ge(y_ready, 2 * i + s + 1)
                    if n_extra:
                        dve.wait_ge(e_loaded[s], (i + 1) * 16 * n_extra)
                    if epilogue != "add":
                        dve.wait_ge(gate_ready, 2 * i + s + 1)
                    if not first:
                        dve.wait_ge(stored[s], i * 16)
                    if epilogue == "glu":
                        nc.vector.tensor_tensor(out[:, s], gate[:, s], e[:, s, 0], ALU.mult).then_inc(out_ready, 1)
                    elif epilogue == "gate":
                        nc.vector.tensor_tensor(flat(out[:, s]), y_of(s), flat(gate[:, s]), ALU.mult).then_inc(out_ready, 1)
                    elif epilogue == "gate_add":
                        nc.vector.tensor_tensor(flat(out[:, s]), y_of(s), flat(gate[:, s]), ALU.mult).then_inc(mul_ready, 1)
                        dve.wait_ge(mul_ready, 2 * i + s + 1)
                        nc.vector.tensor_tensor(out[:, s], out[:, s], e[:, s, 1], ALU.add).then_inc(out_ready, 1)
                    elif epilogue == "add":
                        nc.vector.tensor_tensor(flat(out[:, s]), y_of(s), flat(e[:, s, 0]), ALU.add).then_inc(out_ready, 1)

                if epilogue != "copy":
                    over_slots(dve, finish, skip_first=True)


def conv_gated_up(nc, stage, z_dram, w_dram, conv_w_dram, conv_b_dram, out_dram):
    T = z_dram.shape[1]
    kt = z_dram.shape[0] // P
    FT = w_dram.shape[1] // (2 * P)
    halves, hw = 2, T // 2
    with ExitStack() as ctx:
        sb, ps, sem = opener(nc, ctx, stage)
        z = sb("z", [P, kt, T])
        w = sb("w", [P, 2, 2, kt, P])
        conv_w = sb("conv_w", [P, 2 * FT, 3])
        conv_b = sb("conv_b", [P, 2 * FT])
        y = sb("y", [P, 2, 2, T + 2])
        u = sb("u", [P, 2, 2, T])
        gate = sb("gate", [P, 2, T])
        out = sb("out", [P, 2, T])
        prod = ps("prod", [P, 2, 2, halves, 512])
        z_loaded = [sem(f"z_loaded{k}") for k in range(kt)]
        conv_loaded = sem("conv_loaded")
        w_loaded = [sem(f"w_loaded{s}") for s in range(2)]
        prod_ready = sem("prod_ready")
        pads_ready = sem("pads_ready")
        y_ready = sem("y_ready")
        taps_done = sem("taps_done")
        gate_ready = sem("gate_ready")
        out_ready = sem("out_ready")
        stored = [sem(f"stored{s}") for s in range(2)]
        zv = z_dram.rearrange("(k p) t -> p k t", p=P)
        wv = w_dram.rearrange("(k p) m -> p k m", p=P)

        def over_tiles(eng, body):
            body(0, 0, True)
            body(0, 1, True)
            with eng.Fori(1, FT // 2) as i:
                body(i, 0, False)
                body(i, 1, False)

        with nc.Block() as block:

            @block.sync
            def _(sp):
                for k in range(kt):
                    sp.dma_start(z[:, k, :], zv[:, k, :]).then_inc(z_loaded[k], 16)
                sp.dma_start(conv_w[:], conv_w_dram).then_inc(conv_loaded, 16)
                sp.dma_start(conv_b[:], conv_b_dram).then_inc(conv_loaded, 16)

                def load(i, s, first):
                    if not first:
                        sp.wait_ge(prod_ready, 2 * i + s - 1)
                    for g in range(2):
                        sp.dma_start(w[:, s, g], wv[:, :, bass.ds(g * FT * P + (2 * i + s) * P, P)]).then_inc(w_loaded[s], 16)

                over_tiles(sp, load)

            @block.tensor
            def _(pe):
                def products(i, s, first):
                    pe.wait_ge(w_loaded[s], (i + 1) * 32)
                    if not first:
                        pe.wait_ge(y_ready, 2 * i + s - 1)
                    for g in range(2):
                        for h in range(halves):
                            for k in range(kt):
                                if first and s == 0 and g == 0 and h == 0:
                                    pe.wait_ge(z_loaded[k], 16)
                                last = nc.tensor.matmul(prod[:, s, g, h, 0:hw], w[:, s, g, k, :],
                                                        z[:, k, h * hw:(h + 1) * hw],
                                                        start=(k == 0), stop=(k == kt - 1))
                    last.then_inc(prod_ready, 1)

                over_tiles(pe, products)

            @block.scalar
            def _(act):
                act.wait_ge(pads_ready, 1)

                def tile_of(i, s, first):
                    act.wait_ge(prod_ready, 2 * i + s + 1)
                    if not first:
                        act.wait_ge(taps_done, (2 * i + s - 1) * 6)
                    nc.scalar.copy(y[:, s, :, 2:].rearrange("p g (h t) -> p g h t", h=halves),
                                   prod[:, s, :, :, 0:hw]).then_inc(y_ready, 1)
                    act.wait_ge(taps_done, (2 * i + s + 1) * 6)
                    if not first:
                        act.wait_ge(out_ready, 2 * i + s - 1)
                    nc.scalar.activation(gate[:, s], u[:, s, 0], ACT.Silu).then_inc(gate_ready, 1)
                    act.wait_ge(out_ready, 2 * i + s + 1)
                    act.dma_start(out_dram[bass.ds((2 * i + s) * P, P), :], out[:, s]).then_inc(stored[s], 16)

                over_tiles(act, tile_of)
                for s in range(2):
                    act.wait_ge(stored[s], 16 * (FT // 2))

            @block.vector
            def _(dve):
                nc.vector.memset(y[:], 0.0).then_inc(pads_ready, 1)
                dve.wait_ge(conv_loaded, 32)

                def tile_of(i, s, first):
                    t = 2 * i + s
                    dve.wait_ge(y_ready, t + 1)
                    if not first:
                        dve.wait_ge(out_ready, t - 1)
                    for j in range(3):
                        for g in range(2):
                            tap = conv_w[:, bass.ds(g * FT + t, 1), j]
                            if j == 0:
                                nc.vector.tensor_scalar(u[:, s, g], y[:, s, g, 0:T], tap,
                                                        conv_b[:, bass.ds(g * FT + t, 1)],
                                                        ALU.mult, ALU.add).then_inc(taps_done, 1)
                            else:
                                dve.wait_ge(taps_done, t * 6 + 2 * j + g - 1)
                                nc.vector.scalar_tensor_tensor(u[:, s, g], y[:, s, g, j:j + T], tap, u[:, s, g],
                                                               ALU.mult, ALU.add).then_inc(taps_done, 1)
                    dve.wait_ge(taps_done, t * 6 + 6)
                    dve.wait_ge(gate_ready, t + 1)
                    if not first:
                        dve.wait_ge(stored[s], i * 16)
                    nc.vector.tensor_tensor(out[:, s], gate[:, s], u[:, s, 1], ALU.mult).then_inc(out_ready, 1)

                over_tiles(dve, tile_of)


SSM_GROUP = 16
SSM_STATE = 64
SSM_GROUPS = D_MODEL // SSM_GROUP
CHUNK = 8
CHUNKS = LEN // CHUNK
PAIRS = SSM_GROUPS // 2
TWO_PI = 2.0 * float(np.pi)
TWO_PI_A = 6.28125
TWO_PI_B = float(np.float32(np.round((TWO_PI - TWO_PI_A) * 2.0 ** 20) / 2.0 ** 20))
TWO_PI_C = float(np.float32(TWO_PI - TWO_PI_A - TWO_PI_B))
ROUNDER = 1.5 * 2.0 ** 23
PI_BELOW = 3.1415925


def s5(nc, stage, u_dram, lam_dram, bc_dram, d_dram, ident_dram, out_dram):
    R_LEN = (CHUNKS - 1) * CHUNK + 1
    BATCH = 8
    BATCHES = SSM_GROUPS // BATCH
    RE, IM = 0, 1
    with ExitStack() as ctx:
        sb, ps, sem = opener(nc, ctx, stage)
        lam = sb("lam", [P, 3, PAIRS])
        bc = sb("bc", [P, 4, PAIRS, SSM_GROUP])
        d_skip = sb("d_skip", [P, KT])
        ident = sb("ident", [P, P])
        small = sb("small", [P, 24, PAIRS])
        tmp = sb("tmp", [P, 2, PAIRS, SSM_GROUP])
        bb = sb("bb", [P, 2, PAIRS, SSM_GROUP])
        wb = sb("wb", [P, 2, PAIRS, CHUNK, SSM_GROUP])
        ca = sb("ca", [P, 2, PAIRS, CHUNK + 1, SSM_GROUP])
        wbt = sb("wbt", [P, 2, 2, P])
        shifted = sb("shifted", [P, 2, BATCH, R_LEN])
        u = sb("u", [P, SSM_GROUPS, CHUNKS])
        toep = sb("toep", [P, SSM_GROUPS, CHUNK, SSM_GROUP])
        state = sb("state", [P, 2, PAIRS, CHUNKS + 1])
        prod = sb("prod", [P, 2, 2, PAIRS])
        wb_flat = wb[:].rearrange("p r q k h -> p (r q k h)")
        taps = wb_flat[0:SSM_GROUP, :].rearrange("h (g n) -> h g n", g=SSM_GROUPS)
        y_tok = wb_flat[0:CHUNKS, :].rearrange("c (t m) -> c t m", t=CHUNK)
        work = shifted[:].rearrange("p s g t -> p (s g t)")
        u_tile = work[:, 0:2 * LEN].rearrange("p (s t) -> p s t", s=2)
        y_tile = work[:, 2 * LEN:4 * LEN].rearrange("p (s t) -> p s t", s=2)
        o_tile = work[:, 4 * LEN:6 * LEN].rearrange("p (s t) -> p s t", s=2)
        bank = ps("bank", [P, 8, 512])

        params_loaded = sem("params_loaded")
        toep_zeroed = sem("toep_zeroed")
        u_loaded = [sem(f"u_loaded{s}") for s in range(2)]
        u_packed = sem("u_packed")
        dt_ready = sem("dt_ready")
        exponent_ready = sem("exponent_ready")
        mag_ready = sem("mag_ready")
        angle_ready = sem("angle_ready")
        sin_ready = sem("sin_ready")
        setup = sem("setup")
        wb_turned = sem("wb_turned")
        wbt_ready = sem("wbt_ready")
        input_ready = sem("input_ready")
        state_filled = sem("state_filled")
        scanned = sem("scanned")
        taps_made = sem("taps_made")
        taps_ready = sem("taps_ready")
        toep_ready = sem("toep_ready")
        y_made = sem("y_made")
        y_ready = sem("y_ready")
        y_turned = sem("y_turned")
        ut_loaded = [sem(f"ut_loaded{s}") for s in range(2)]
        skipped = sem("skipped")
        gelu_done = sem("gelu_done")
        stored = [sem(f"stored{s}") for s in range(2)]

        lr, li, ldt = lam[:, 0], lam[:, 1], lam[:, 2]
        (dt, expo, ang, cyc, red, half, mag, sn, snh, a_re, a_im, den, nr, co_re, co_im, t0, t1,
         s_re, s_im, s2_re, s2_im) = (small[:, n] for n in range(21))

        def over_h(a):
            return a.unsqueeze(2).broadcast_to([P, PAIRS, SSM_GROUP])

        def half_of(t, e):
            return t[64 * e:64 * e + 64]

        with nc.Block() as block:

            @block.sync
            def _(sp):
                sp.dma_start(lam[:], lam_dram).then_inc(params_loaded, 16)
                sp.dma_start(bc[:], bc_dram).then_inc(params_loaded, 16)
                sp.dma_start(d_skip[:], d_dram).then_inc(params_loaded, 16)
                sp.dma_start(ident[:], ident_dram).then_inc(params_loaded, 16)
                for b in range(BATCHES):
                    if b >= 2:
                        sp.wait_ge(u_packed, b - 1)
                    rows = u_dram[b * BATCH * SSM_GROUP:(b + 1) * BATCH * SSM_GROUP, :].rearrange(
                        "(g h) t -> h g t", h=SSM_GROUP)
                    for j in range(CHUNK):
                        sp.dma_start(shifted[16 * j:16 * j + 16, b % 2], rows[:, :, 7 - j:7 - j + R_LEN]).then_inc(
                            u_loaded[b % 2], 16)
                sp.wait_ge(taps_ready, PAIRS // 2)
                sp.wait_ge(toep_zeroed, 1)
                for j in range(CHUNK):
                    s = 7 - j
                    sp.dma_start(toep[16 * j:16 * j + 16, :, s:, :].rearrange("h g t m -> h g (t m)"),
                                 taps[:, :, 0:(CHUNK - s) * SSM_GROUP]).then_inc(toep_ready, 16)
                sp.wait_ge(toep_ready, 16 * CHUNK)
                sp.wait_ge(u_packed, BATCHES)
                for m in range(KT):
                    if m >= 2:
                        sp.wait_ge(skipped, m - 1)
                    sp.dma_start(u_tile[:, m % 2], u_dram[m * P:(m + 1) * P, :]).then_inc(ut_loaded[m % 2], 16)
                    if m >= 1:
                        sp.wait_ge(gelu_done, m)
                        sp.dma_start(out_dram[(m - 1) * P:m * P, :], o_tile[:, (m - 1) % 2]).then_inc(
                            stored[(m - 1) % 2], 16)
                sp.wait_ge(gelu_done, KT)
                sp.dma_start(out_dram[(KT - 1) * P:, :], o_tile[:, (KT - 1) % 2]).then_inc(stored[(KT - 1) % 2], 16)
                for s in range(2):
                    sp.wait_ge(stored[s], 16 * KT // 2)

            @block.gpsimd
            def _(pool):
                nc.gpsimd.memset(toep[:], 0.0).then_inc(toep_zeroed, 1)
                for b in range(BATCHES):
                    pool.wait_ge(u_loaded[b % 2], 16 * CHUNK * (b // 2 + 1))
                    nc.gpsimd.tensor_copy(u[:, b * BATCH:(b + 1) * BATCH, :],
                                          shifted[:, b % 2, :, 0:R_LEN:CHUNK]).then_inc(u_packed, 1)

            @block.vector
            def _(dve):
                done = [0]

                def count(n):
                    done[0] += n

                def step(ins):
                    ins.then_inc(setup, 1)
                    count(1)
                    dve.wait_ge(setup, done[0])

                def tt(out, a, b, op):
                    step(nc.vector.tensor_tensor(out, a, b, op))

                def mul_complex(o_re, o_im, x_re, x_im, w_re, w_im, w1, w2):
                    nc.vector.tensor_tensor(o_re, x_re, w_re, ALU.mult).then_inc(setup, 1)
                    nc.vector.tensor_tensor(w1, x_im, w_im, ALU.mult).then_inc(setup, 1)
                    nc.vector.tensor_tensor(o_im, x_re, w_im, ALU.mult).then_inc(setup, 1)
                    nc.vector.tensor_tensor(w2, x_im, w_re, ALU.mult).then_inc(setup, 1)
                    count(4)
                    dve.wait_ge(setup, done[0])
                    nc.vector.tensor_tensor(o_re, o_re, w1, ALU.subtract).then_inc(setup, 1)
                    nc.vector.tensor_tensor(o_im, o_im, w2, ALU.add).then_inc(setup, 1)
                    count(2)
                    dve.wait_ge(setup, done[0])

                step(nc.vector.memset(state[:, :, :, 0:1], 0.0))
                dve.wait_ge(params_loaded, 64)
                dve.wait_ge(dt_ready, 1)
                nc.vector.tensor_tensor(expo, lr, dt, ALU.mult).then_inc(exponent_ready, 1)
                tt(ang, li, dt, ALU.mult)
                step(nc.vector.tensor_scalar(cyc, ang, 1.0 / TWO_PI, ROUNDER, ALU.mult, ALU.add))
                step(nc.vector.tensor_scalar(cyc, cyc, -ROUNDER, None, ALU.add))
                step(nc.vector.scalar_tensor_tensor(red, cyc, -TWO_PI_A, ang, ALU.mult, ALU.add))
                step(nc.vector.scalar_tensor_tensor(red, cyc, -TWO_PI_B, red, ALU.mult, ALU.add))
                step(nc.vector.scalar_tensor_tensor(red, cyc, -TWO_PI_C, red, ALU.mult, ALU.add))
                step(nc.vector.tensor_scalar(red, red, PI_BELOW, -PI_BELOW, ALU.min, ALU.max))
                nc.vector.tensor_scalar(half, red, 0.5, None, ALU.mult).then_inc(angle_ready, 1)
                dve.wait_ge(sin_ready, 2)
                dve.wait_ge(mag_ready, 1)
                tt(t0, snh, snh, ALU.mult)
                step(nc.vector.tensor_scalar(t0, t0, -2.0, 1.0, ALU.mult, ALU.add))
                tt(a_re, mag, t0, ALU.mult)
                tt(a_im, mag, sn, ALU.mult)
                tt(den, lr, lr, ALU.mult)
                tt(t1, li, li, ALU.mult)
                tt(den, den, t1, ALU.add)
                step(nc.vector.reciprocal(den, den))
                step(nc.vector.tensor_scalar(nr, a_re, -1.0, None, ALU.add))
                tt(co_re, nr, lr, ALU.mult)
                tt(t0, a_im, li, ALU.mult)
                tt(co_re, co_re, t0, ALU.add)
                tt(co_re, co_re, den, ALU.mult)
                tt(co_im, a_im, lr, ALU.mult)
                tt(t0, nr, li, ALU.mult)
                tt(co_im, co_im, t0, ALU.subtract)
                tt(co_im, co_im, den, ALU.mult)
                w1, w2 = tmp[:, 0], tmp[:, 1]
                mul_complex(bb[:, RE], bb[:, IM], bc[:, 0], bc[:, 1], over_h(co_re), over_h(co_im), w1, w2)
                mul_complex(s_re, s_im, a_re, a_im, a_re, a_im, t0, t1)
                mul_complex(s2_re, s2_im, s_re, s_im, s_re, s_im, t0, t1)
                mul_complex(s_re, s_im, s2_re, s2_im, s2_re, s2_im, t0, t1)
                step(nc.vector.tensor_copy(wb[:, :, :, 0, :], bb[:]))
                for k in range(CHUNK - 1):
                    mul_complex(wb[:, RE, :, k + 1, :], wb[:, IM, :, k + 1, :], wb[:, RE, :, k, :], wb[:, IM, :, k, :],
                                over_h(a_re), over_h(a_im), w1, w2)
                wb_done = done[0]
                assert wb_done == S5_WB_DONE, wb_done
                step(nc.vector.tensor_copy(ca[:, RE, :, 0, :], bc[:, 2]))
                step(nc.vector.tensor_scalar(ca[:, IM, :, 0, :], bc[:, 3], -1.0, None, ALU.mult))
                step(nc.vector.tensor_scalar(t0, a_im, -1.0, None, ALU.mult))
                for k in range(CHUNK):
                    mul_complex(ca[:, RE, :, k + 1, :], ca[:, IM, :, k + 1, :], ca[:, RE, :, k, :], ca[:, IM, :, k, :],
                                over_h(a_re), over_h(t0), w1, w2)
                assert done[0] == S5_CA_DONE, done[0]
                for q in range(PAIRS):
                    dve.wait_ge(input_ready, q + 1)
                    nc.vector.tensor_copy(state[:, :, q, 1:], bank[:, 4 + q % 4, 0:2 * CHUNKS].rearrange(
                        "p (r c) -> p r c", r=2)).then_inc(state_filled, 1)
                dve.wait_ge(state_filled, PAIRS)
                wide = [P, 2, PAIRS]
                n = 0

                def with_step(*instructions):
                    nonlocal n
                    for ins in instructions:
                        ins.then_inc(scanned, 1)
                        n += 1
                    dve.wait_ge(scanned, n)

                for c in range(1, CHUNKS):
                    with_step(
                        nc.vector.tensor_tensor(prod[:, 0], state[:, :, :, c], s_re.unsqueeze(1).broadcast_to(wide), ALU.mult),
                        nc.vector.tensor_tensor(prod[:, 1], state[:, :, :, c], s_im.unsqueeze(1).broadcast_to(wide), ALU.mult))
                    with_step(nc.vector.tensor_tensor(state[:, :, :, c + 1], state[:, :, :, c + 1], prod[:, 0], ALU.add))
                    with_step(
                        nc.vector.tensor_tensor(state[:, RE, :, c + 1], state[:, RE, :, c + 1], prod[:, 1, IM], ALU.subtract),
                        nc.vector.tensor_tensor(state[:, IM, :, c + 1], state[:, IM, :, c + 1], prod[:, 1, RE], ALU.add))
                for m in range(KT):
                    dve.wait_ge(y_turned, m + 1)
                    dve.wait_ge(ut_loaded[m % 2], 16 * (m // 2 + 1))
                    if m >= 2:
                        dve.wait_ge(gelu_done, m - 1)
                    for b in range(2):
                        ins = nc.vector.scalar_tensor_tensor(
                            y_tile[:, m % 2].rearrange("p (c t) -> p t c", t=CHUNK)[:, 4 * b:4 * b + 4, :],
                            u_tile[:, m % 2].rearrange("p (c t) -> p t c", t=CHUNK)[:, 4 * b:4 * b + 4, :],
                            d_skip[:, m:m + 1],
                            bank[:, 2 * (m % 2) + b, 0:4 * CHUNKS].rearrange("p (t c) -> p t c", t=4),
                            ALU.mult, ALU.add)
                    ins.then_inc(skipped, 1)

            @block.scalar
            def _(act):
                act.wait_ge(params_loaded, 64)
                nc.scalar.activation(dt, ldt, ACT.Exp).then_inc(dt_ready, 1)
                act.wait_ge(exponent_ready, 1)
                nc.scalar.activation(mag, expo, ACT.Exp).then_inc(mag_ready, 1)
                act.wait_ge(angle_ready, 1)
                nc.scalar.activation(sn, red, ACT.Sin).then_inc(sin_ready, 1)
                nc.scalar.activation(snh, half, ACT.Sin).then_inc(sin_ready, 1)
                for q in range(PAIRS):
                    act.wait_ge(wb_turned, q + 1)
                    if q >= 2:
                        act.wait_ge(input_ready, q - 1)
                    nc.scalar.copy(wbt[:, q % 2], bank[:, q % 2, 0:2 * P].rearrange("p (r n) -> p r n", r=2)).then_inc(
                        wbt_ready, 1)
                for b in range(PAIRS // 2):
                    act.wait_ge(taps_made, b + 1)
                    e, q0 = b % 2, 4 * (b // 2)
                    g0 = 2 * q0 + e
                    nc.scalar.copy(taps[:, g0:g0 + 7:2, :], bank[0:SSM_GROUP, 2 + b % 2, :].rearrange(
                        "h (g n) -> h g n", g=4)).then_inc(taps_ready, 1)
                for b in range(SSM_GROUPS // 4):
                    act.wait_ge(y_made, b + 1)
                    if b == 0:
                        act.wait_ge(wb_turned, PAIRS)
                    for n in range(4):
                        g = 2 * (4 * (b // 2) + n) + b % 2
                        ins = nc.scalar.copy(y_tok[:, :, SSM_GROUP * g:SSM_GROUP * (g + 1)],
                                             bank[0:CHUNKS, 4 + b % 4, n * P:(n + 1) * P].rearrange(
                                                 "c (t h) -> c t h", t=CHUNK))
                    ins.then_inc(y_ready, 1)
                for m in range(KT):
                    act.wait_ge(skipped, m + 1)
                    if m >= 2:
                        act.wait_ge(stored[m % 2], 16 * (m // 2))
                    nc.scalar.activation(o_tile[:, m % 2], y_tile[:, m % 2], ACT.Gelu_apprx_tanh).then_inc(gelu_done, 1)

            @block.tensor
            def _(pe):
                pe.wait_ge(params_loaded, 64)
                pe.wait_ge(setup, S5_WB_DONE)

                def turn(q):
                    if q >= 2:
                        pe.wait_ge(wbt_ready, q - 1)
                    for r in (RE, IM):
                        last = nc.tensor.transpose(bank[:, q % 2, r * P:(r + 1) * P],
                                                   wb[:, r, q].rearrange("p k h -> p (k h)"), ident[:])
                    last.then_inc(wb_turned, 1)

                def chunk_inputs(q):
                    pe.wait_ge(wbt_ready, q + 1)
                    if q % (BATCH // 2) == 0:
                        pe.wait_ge(u_packed, 2 * q // BATCH + 1)
                    if q >= 4:
                        pe.wait_ge(state_filled, q - 3)
                    for e in range(2):
                        for r in (RE, IM):
                            last = nc.tensor.matmul(bank[64 * e:64 * e + 64, 4 + q % 4, r * CHUNKS:(r + 1) * CHUNKS],
                                                    wbt[:, q % 2, r, 64 * e:64 * e + 64], u[:, 2 * q + e, :],
                                                    start=True, stop=True)
                    last.then_inc(input_ready, 1)

                turn(0)
                for q in range(PAIRS):
                    if q + 1 < PAIRS:
                        turn(q + 1)
                    chunk_inputs(q)
                pe.wait_ge(setup, S5_CA_DONE)
                for b in range(PAIRS // 2):
                    e, q0 = b % 2, 4 * (b // 2)
                    if b >= 2:
                        pe.wait_ge(taps_ready, b - 1)
                    for n in range(4):
                        for r in (RE, IM):
                            last = nc.tensor.matmul(
                                bank[0:SSM_GROUP, 2 + b % 2, n * P:(n + 1) * P], half_of(bb, e)[:, r, q0 + n, :],
                                half_of(ca, e)[:, r, q0 + n, 0:CHUNK, :].rearrange("p k h -> p (k h)"),
                                start=(r == RE), stop=(r == IM))
                    last.then_inc(taps_made, 1)
                pe.wait_ge(toep_ready, 16 * CHUNK)
                pe.wait_ge(state_filled, PAIRS)
                pe.wait_ge(scanned, 5 * (CHUNKS - 1))
                for b in range(SSM_GROUPS // 4):
                    e, q0 = b % 2, 4 * (b // 2)
                    if b >= 4:
                        pe.wait_ge(y_ready, b - 3)
                    for n in range(4):
                        q = q0 + n
                        to = bank[0:CHUNKS, 4 + b % 4, n * P:(n + 1) * P]
                        nc.tensor.matmul(to, u[:, 2 * q + e, :], toep[:, 2 * q + e].rearrange("p t h -> p (t h)"),
                                         start=True, stop=False)
                        for r in (RE, IM):
                            last = nc.tensor.matmul(to, half_of(state, e)[:, r, q, 0:CHUNKS],
                                                    half_of(ca, e)[:, r, q, 1:, :].rearrange("p k h -> p (k h)"),
                                                    start=False, stop=(r == IM))
                    last.then_inc(y_made, 1)
                pe.wait_ge(y_ready, SSM_GROUPS // 4)
                for m in range(KT):
                    if m >= 2:
                        pe.wait_ge(skipped, m - 1)
                    for t in range(CHUNK):
                        last = nc.tensor.transpose(
                            bank[:, 2 * (m % 2) + t // 4, (t % 4) * CHUNKS:(t % 4 + 1) * CHUNKS],
                            y_tok[:, t, m * P:(m + 1) * P], ident[0:CHUNKS, 0:CHUNKS])
                    last.then_inc(y_turned, 1)


S5_WB_DONE = 1 + 24 + 6 * 4 + 1 + 6 * (CHUNK - 1)
S5_CA_DONE = S5_WB_DONE + 3 + 6 * CHUNK


HEADS = 8
HCHUNK = 16
HCHUNKS = LEN // HCHUNK


def hgrn2(nc, stage, p_dram, lb_dram, gain_dram, ident_dram, causal_dram, member_dram, out_dram):
    tiles = [P] * (LEN // P) + ([LEN % P] if LEN % P else [])
    nt = len(tiles)
    per_tile = P // HCHUNK
    RING = 3 * per_tile
    units = [(h, i) for h in range(HEADS) for i in range(nt)]
    with ExitStack() as ctx:
        sb, ps, sem = opener(nc, ctx, stage)
        q = sb("q", [P, HEADS, LEN])
        f = sb("f", [P, HEADS, LEN])
        v = sb("v", [P, HEADS, LEN])
        og = sb("og", [P, HEADS, LEN])
        og_sig = sb("og_sig", [P, HEADS, LEN])
        o = sb("o", [P, HEADS, LEN])
        cum = sb("cum", [P, 2, LEN])
        rest = sb("rest", [P, 2, LEN])
        e_up = sb("e_up", [P, 2, LEN])
        e_down = sb("e_down", [P, 2, LEN])
        e_rest = sb("e_rest", [P, 2, LEN])
        k_in = sb("k_in", [P, 2, LEN])
        k_out = sb("k_out", [P, 2, LEN])
        decay = sb("decay", [P, HEADS, HCHUNKS])
        resets = sb("resets", [P, LEN])
        lb = sb("lb", [P, 2, HEADS])
        low = sb("low", [P, 2, HEADS])
        gain = sb("gain", [P, 1])
        ident = sb("ident", [P, P])
        ones = sb("ones", [P, P])
        causal = sb("causal", [P, P])
        member = sb("member", [P, per_tile, P])
        turned = sb("turned", [P, 3, 2, P])
        v_by_chunk = sb("v_by_chunk", [P, 2, per_tile, P])
        scores = sb("scores", [P, 2, P])
        states = sb("states", [P, RING, P])
        scale = sb("scale", [P, 2, LEN])
        bank = ps("bank", [P, 8, 512])

        params_loaded = sem("params_loaded")
        loaded = [sem(f"loaded{h}") for h in range(HEADS)]
        consts_ready = sem("consts_ready")
        bound_diff = sem("bound_diff")
        bound_sig = sem("bound_sig")
        bound_ready = sem("bound_ready")
        sig_ready = sem("sig_ready")
        f_ready = sem("f_ready")
        log_ready = sem("log_ready")
        cum_ready = sem("cum_ready")
        rest_ready = sem("rest_ready")
        k_ready = sem("k_ready")
        exps_ready = sem("exps_ready")
        decay_ready = sem("decay_ready")
        qk_ready = sem("qk_ready")
        turn_made = sem("turn_made")
        turn_ready = sem("turn_ready")
        split_ready = sem("split_ready")
        scores_made = sem("scores_made")
        scores_ready = sem("scores_ready")
        kv_made = sem("kv_made")
        state_ready = sem("state_ready")
        o_made = sem("o_made")
        o_ready = sem("o_ready")
        squared = sem("squared")
        summed = sem("summed")
        meaned = sem("meaned")
        inverted = sem("inverted")
        rooted = sem("rooted")
        normed = sem("normed")
        gated = sem("gated")
        out_ready = sem("out_ready")
        stored = sem("stored")

        def rows(part, h):
            at = part * D_MODEL + h * P
            return p_dram[at:at + P, :]

        def span(i):
            return slice(i * P, i * P + tiles[i])

        def chunks_of(i):
            return tiles[i] // HCHUNK

        def states_before(n):
            return sum(chunks_of(i) for _, i in units[:n])

        def by_chunk(a):
            return a.rearrange("p (c t) -> p c t", t=HCHUNK)

        with nc.Block() as block:

            @block.sync
            def _(sp):
                for dst, src in ((lb, lb_dram), (gain, gain_dram), (ident, ident_dram), (causal, causal_dram),
                                 (member, member_dram)):
                    sp.dma_start(dst[:], src).then_inc(params_loaded, 16)
                for h in range(HEADS):
                    for part, dst in ((1, f), (0, q), (2, v), (3, og)):
                        sp.dma_start(dst[:, h], rows(part, h)).then_inc(loaded[h], 16)
                for h in range(HEADS):
                    sp.wait_ge(out_ready, h + 1)
                    sp.dma_start(out_dram[h * P:(h + 1) * P, :], o[:, h]).then_inc(stored, 16)
                sp.wait_ge(stored, 16 * HEADS)

            @block.scalar
            def _(act):
                act.wait_ge(bound_diff, 1)
                nc.scalar.activation(low[:, 0], low[:, 1], ACT.Sigmoid).then_inc(bound_sig, 1)
                for h in range(HEADS):
                    act.wait_ge(loaded[h], 64)
                    nc.scalar.activation(f[:, h], f[:, h], ACT.Sigmoid).then_inc(sig_ready, 1)
                    nc.scalar.activation(og_sig[:, h], og[:, h], ACT.Sigmoid).then_inc(sig_ready, 1)

                def prepare(h):
                    s = h % 2
                    act.wait_ge(f_ready, h + 1)
                    if h >= 2:
                        act.wait_ge(rest_ready, h - 1)
                        act.wait_ge(exps_ready, 3 * (h - 1))
                    nc.scalar.activation(rest[:, s], f[:, h], ACT.Ln).then_inc(log_ready, 1)
                    act.wait_ge(cum_ready, h + 1)
                    if h >= 2:
                        act.wait_ge(qk_ready, 3 * (h - 1))
                        act.wait_ge(decay_ready, h - 1)
                    nc.scalar.activation(e_up[:, s], cum[:, s], ACT.Exp).then_inc(exps_ready, 1)
                    nc.scalar.activation(e_down[:, s], cum[:, s], ACT.Exp, scale=-1.0).then_inc(exps_ready, 1)
                    act.wait_ge(rest_ready, h + 1)
                    nc.scalar.activation(e_rest[:, s], rest[:, s], ACT.Exp).then_inc(exps_ready, 1)

                prepare(0)
                prepare(1)
                for n, (h, i) in enumerate(units):
                    m = tiles[i]
                    act.wait_ge(turn_made, n + 1)
                    if n >= 3:
                        act.wait_ge(o_made, n - 2)
                    nc.scalar.copy(turned[0:m, n % 3], bank[0:m, n % 2, 0:2 * P].rearrange("p (a n) -> p a n", a=2)).then_inc(
                        turn_ready, 1)
                    if n >= 1:
                        hp, ip = units[n - 1]
                        act.wait_ge(o_made, n)
                        nc.scalar.copy(o[:, hp, span(ip)], bank[:, 3, 0:tiles[ip]]).then_inc(o_ready, 1)
                    if i == nt - 1 and h + 2 < HEADS:
                        prepare(h + 2)
                n = len(units)
                act.wait_ge(o_made, n)
                nc.scalar.copy(o[:, HEADS - 1, span(nt - 1)], bank[:, 3, 0:tiles[-1]]).then_inc(o_ready, 1)
                act.wait_ge(o_ready, n)
                act.wait_ge(scores_ready, n)
                for h in range(HEADS):
                    nc.scalar.activation(q[:, h], o[:, h], ACT.Square).then_inc(squared, 1)
                for h in range(HEADS):
                    act.wait_ge(inverted, h + 1)
                    nc.scalar.activation(scale[:, h % 2], scale[:, h % 2], ACT.Sqrt).then_inc(rooted, 1)

            @block.gpsimd
            def _(pool):
                def prepare(h):
                    s = h % 2
                    pool.wait_ge(k_ready, h + 1)
                    pool.wait_ge(exps_ready, 3 * (h + 1))
                    if h >= 2:
                        pool.wait_ge(turn_made, nt * (h - 1))
                        pool.wait_ge(scores_made, nt * (h - 1))
                    nc.gpsimd.tensor_tensor(q[:, h], q[:, h], e_up[:, s], ALU.mult).then_inc(qk_ready, 1)
                    nc.gpsimd.tensor_tensor(k_in[:, s], f[:, h], e_down[:, s], ALU.mult).then_inc(qk_ready, 1)
                    nc.gpsimd.tensor_tensor(k_out[:, s], f[:, h], e_rest[:, s], ALU.mult).then_inc(qk_ready, 1)

                pool.wait_ge(params_loaded, 80)
                prepare(0)
                prepare(1)
                for n, (h, i) in enumerate(units):
                    m, c = tiles[i], chunks_of(i)
                    pool.wait_ge(turn_ready, n + 1)
                    if n >= 2:
                        pool.wait_ge(kv_made, n - 1)
                    nc.gpsimd.tensor_tensor(v_by_chunk[0:m, n % 2, 0:c], member[0:m, 0:c],
                                            turned[0:m, n % 3, 1].unsqueeze(1).broadcast_to([m, c, P]),
                                            ALU.mult).then_inc(split_ready, 1)
                    if i == nt - 1 and h + 2 < HEADS:
                        prepare(h + 2)

            @block.vector
            def _(dve):
                nc.vector.memset(ones[:], 1.0).then_inc(consts_ready, 1)
                nc.vector.memset(resets[:], 1.0).then_inc(consts_ready, 1)
                dve.wait_ge(consts_ready, 2)
                nc.vector.memset(by_chunk(resets[:])[:, :, 0:1], 0.0).then_inc(consts_ready, 1)
                dve.wait_ge(params_loaded, 80)
                nc.vector.tensor_tensor(low[:, 1], lb[:, 0], lb[:, 1], ALU.subtract).then_inc(bound_diff, 1)
                dve.wait_ge(bound_sig, 1)
                nc.vector.tensor_scalar(low[:, 1], low[:, 0], -1.0, 1.0, ALU.mult, ALU.add).then_inc(bound_ready, 1)
                dve.wait_ge(bound_ready, 1)
                dve.wait_ge(consts_ready, 3)

                def prepare(h):
                    s = h % 2
                    dve.wait_ge(sig_ready, 2 * h + 1)
                    nc.vector.tensor_scalar(f[:, h], f[:, h], low[:, 1, h:h + 1], low[:, 0, h:h + 1],
                                            ALU.mult, ALU.add).then_inc(f_ready, 1)
                    dve.wait_ge(log_ready, h + 1)
                    if h >= 2:
                        dve.wait_ge(exps_ready, 3 * (h - 1))
                    nc.vector.tensor_tensor_scan(cum[:, s], resets[:], rest[:, s], 0.0, ALU.mult, ALU.add).then_inc(
                        cum_ready, 1)
                    nc.vector.tensor_scalar(f[:, h], f[:, h], -1.0, 1.0, ALU.mult, ALU.add).then_inc(k_ready, 1)
                    dve.wait_ge(cum_ready, h + 1)
                    nc.vector.tensor_tensor(by_chunk(rest[:, s]),
                                            by_chunk(cum[:, s])[:, :, HCHUNK - 1:].broadcast_to([P, HCHUNKS, HCHUNK]),
                                            by_chunk(cum[:, s]), ALU.subtract).then_inc(rest_ready, 1)
                    dve.wait_ge(exps_ready, 3 * h + 1)
                    nc.vector.tensor_copy(decay[:, h], e_up[:, s, HCHUNK - 1::HCHUNK]).then_inc(decay_ready, 1)
                    dve.wait_ge(decay_ready, h + 1)

                prepare(0)
                prepare(1)
                g = 0
                for n, (h, i) in enumerate(units):
                    m = tiles[i]
                    dve.wait_ge(scores_made, n + 1)
                    if n >= 2:
                        dve.wait_ge(o_made, n - 1)
                    nc.vector.tensor_tensor(scores[0:m, n % 2, 0:m], bank[0:m, 2, 0:m], causal[0:m, 0:m],
                                            ALU.mult).then_inc(scores_ready, 1)
                    dve.wait_ge(kv_made, n + 1)
                    for j in range(chunks_of(i)):
                        c = i * per_tile + j
                        kv = bank[:, 4 + 2 * (n % 2) + j // 4, (j % 4) * P:(j % 4 + 1) * P]
                        if c == 0:
                            nc.vector.tensor_copy(states[:, g % RING], kv).then_inc(state_ready, 1)
                        else:
                            nc.vector.scalar_tensor_tensor(states[:, g % RING], states[:, (g - 1) % RING],
                                                           decay[:, h, c:c + 1], kv, ALU.mult, ALU.add).then_inc(
                                state_ready, 1)
                        g += 1
                        dve.wait_ge(state_ready, g)
                    if i == nt - 1 and h + 2 < HEADS:
                        prepare(h + 2)
                for h in range(HEADS):
                    dve.wait_ge(summed, h + 1)
                    if h >= 2:
                        dve.wait_ge(normed, h - 1)
                    sc = scale[:, h % 2]
                    nc.vector.tensor_scalar(sc.rearrange("p (a t) -> p a t", a=2), bank[:, 2 * (h % 2):2 * (h % 2) + 2, 0:LEN // 2],
                                            1.0 / P, EPS, ALU.mult, ALU.add).then_inc(meaned, 1)
                    dve.wait_ge(meaned, h + 1)
                    nc.vector.reciprocal(sc, sc).then_inc(inverted, 1)
                    nc.vector.tensor_tensor(og[:, h], og[:, h], og_sig[:, h], ALU.mult).then_inc(gated, 1)
                    dve.wait_ge(rooted, h + 1)
                    nc.vector.scalar_tensor_tensor(o[:, h], o[:, h], gain[:, 0:1], sc, ALU.mult, ALU.mult).then_inc(
                        normed, 1)
                    dve.wait_ge(normed, h + 1)
                    dve.wait_ge(gated, h + 1)
                    nc.vector.tensor_tensor(o[:, h], o[:, h], og[:, h], ALU.mult).then_inc(out_ready, 1)

            @block.tensor
            def _(pe):
                pe.wait_ge(params_loaded, 80)

                def turn(n):
                    h, i = units[n]
                    m = tiles[i]
                    pe.wait_ge(qk_ready, 3 * (h + 1))
                    pe.wait_ge(loaded[h], 64)
                    if n >= 2:
                        pe.wait_ge(turn_ready, n - 1)
                    nc.tensor.transpose(bank[0:m, n % 2, 0:P], k_out[:, h % 2, span(i)], ident[:])
                    nc.tensor.transpose(bank[0:m, n % 2, P:2 * P], v[:, h, span(i)], ident[:]).then_inc(turn_made, 1)
                    if n >= 1:
                        pe.wait_ge(scores_ready, n)
                    nc.tensor.matmul(bank[0:m, 2, 0:m], k_in[:, h % 2, span(i)], q[:, h, span(i)],
                                     start=True, stop=True).then_inc(scores_made, 1)

                def key_values(n):
                    h, i = units[n]
                    m, c = tiles[i], chunks_of(i)
                    pe.wait_ge(split_ready, n + 1)
                    if n >= 2:
                        pe.wait_ge(state_ready, states_before(n - 1))
                    for b in range((c + 3) // 4):
                        w = min(4, c - 4 * b)
                        last = nc.tensor.matmul(bank[:, 4 + 2 * (n % 2) + b, 0:w * P], turned[0:m, n % 3, 0],
                                                v_by_chunk[0:m, n % 2, 4 * b:4 * b + w].rearrange("p c n -> p (c n)"),
                                                start=True, stop=True)
                    last.then_inc(kv_made, 1)

                def output(n):
                    h, i = units[n]
                    m = tiles[i]
                    pe.wait_ge(scores_ready, n + 1)
                    if n >= 1:
                        pe.wait_ge(o_ready, n)
                    last = nc.tensor.matmul(bank[:, 3, 0:m], turned[0:m, n % 3, 1], scores[0:m, n % 2, 0:m],
                                            start=True, stop=False)
                    before = states_before(n)
                    for j in range(chunks_of(i)):
                        if i * per_tile + j == 0:
                            continue
                        pe.wait_ge(state_ready, before + j)
                        last = nc.tensor.matmul(bank[:, 3, j * HCHUNK:(j + 1) * HCHUNK], states[:, (before + j - 1) % RING],
                                                q[:, h, i * P + j * HCHUNK:i * P + (j + 1) * HCHUNK],
                                                start=False, stop=(j == chunks_of(i) - 1))
                    last.then_inc(o_made, 1)

                turn(0)
                key_values(0)
                for n in range(len(units)):
                    if n + 1 < len(units):
                        turn(n + 1)
                        key_values(n + 1)
                    output(n)
                pe.wait_ge(turn_ready, len(units))
                pe.wait_ge(o_ready, len(units))
                for h in range(HEADS):
                    pe.wait_ge(squared, h + 1)
                    if h >= 2:
                        pe.wait_ge(meaned, h - 1)
                    for a in range(2):
                        last = nc.tensor.matmul(bank[:, 2 * (h % 2) + a, 0:LEN // 2], ones[:],
                                                q[:, h, a * LEN // 2:(a + 1) * LEN // 2], start=True, stop=True)
                    last.then_inc(summed, 1)


HEAD_DIM = 64
GRID_W = 64
GRID_ROWS = SEQ // GRID_W


def attention(nc, stage, q_dram, k_dram, v_dram, bias_dram, ident_dram, out_dram):
    C, T = q_dram.shape
    NK = k_dram.shape[1]
    heads, ct, kt, qt = C // HEAD_DIM, C // P, NK // P, T // P
    units = [(h, t) for h in range(heads) for t in range(qt)]
    with ExitStack() as ctx:
        sb, ps, sem = opener(nc, ctx, stage)
        q = sb("q", [P, ct, T])
        k = sb("k", [P, ct, NK])
        v = sb("v", [P, ct, NK])
        bias = sb("bias", [P, heads, 2 * GRID_ROWS, GRID_W]) if bias_dram is not None else None
        ident = sb("ident", [P, P])
        v_tok = sb("v_tok", [P, kt, C])
        s = sb("s", [P, 2, NK])
        low = sb("low", [P, len(units)])
        total = sb("total", [P, len(units)])
        inverse = sb("inverse", [P, len(units)])
        p_turned = sb("p_turned", [P, 2, kt, P])
        y_tok = sb("y_tok", [P, qt, C])
        y = sb("y", [P, ct, T])
        bank = ps("bank", [P, 8, 512])

        loaded = sem("loaded")
        v_turn_made = sem("v_turn_made")
        v_turn_ready = sem("v_turn_ready")
        scores_made = sem("scores_made")
        scores_ready = sem("scores_ready")
        low_ready = sem("low_ready")
        p_ready = sem("p_ready")
        p_turn_made = sem("p_turn_made")
        p_turn_ready = sem("p_turn_ready")
        inverse_ready = sem("inverse_ready")
        y_made = sem("y_made")
        y_ready = sem("y_ready")
        out_turned = sem("out_turned")
        out_ready = sem("out_ready")
        stored = sem("stored")
        n_loads = 5 if bias is not None else 4

        with nc.Block() as block:

            @block.sync
            def _(sp):
                for dst, src in ((ident[:], ident_dram), (v[:], v_dram.rearrange("(c p) t -> p c t", p=P)),
                                 (q[:], q_dram.rearrange("(c p) t -> p c t", p=P)),
                                 (k[:], k_dram.rearrange("(c p) t -> p c t", p=P))):
                    sp.dma_start(dst, src).then_inc(loaded, 16)
                if bias is not None:
                    sp.dma_start(bias[:], bias_dram).then_inc(loaded, 16)
                sp.wait_ge(out_ready, ct)
                sp.dma_start(out_dram.rearrange("(c p) t -> p c t", p=P), y[:]).then_inc(stored, 16)
                sp.wait_ge(stored, 16)

            @block.tensor
            def _(pe):
                pe.wait_ge(loaded, 16 * n_loads)
                for j in range(kt):
                    if j >= 2:
                        pe.wait_ge(v_turn_ready, j - 1)
                    for c in range(ct):
                        last = nc.tensor.transpose(bank[:, j % 2, c * P:(c + 1) * P], v[:, c, j * P:(j + 1) * P], ident[:])
                    last.then_inc(v_turn_made, 1)

                def scores(n):
                    h, t = units[n]
                    e = 64 * (h % 2)
                    if n >= 2:
                        pe.wait_ge(scores_ready, n - 1)
                    nc.tensor.matmul(bank[:, 2 + n % 2, 0:NK], q[e:e + 64, h // 2, t * P:(t + 1) * P],
                                     k[e:e + 64, h // 2, :], start=True, stop=True).then_inc(scores_made, 1)

                def turn(n):
                    pe.wait_ge(p_ready, n + 1)
                    if n >= 2:
                        pe.wait_ge(p_turn_ready, n - 1)
                    for j in range(kt):
                        last = nc.tensor.transpose(bank[:, 4 + n % 2, j * P:(j + 1) * P], s[:, n % 2, j * P:(j + 1) * P],
                                                   ident[:])
                    last.then_inc(p_turn_made, 1)

                def values(n):
                    h, t = units[n]
                    pe.wait_ge(p_turn_ready, n + 1)
                    if n >= 2:
                        pe.wait_ge(y_ready, n - 1)
                    for j in range(kt):
                        last = nc.tensor.matmul(bank[:, 6 + n % 2, 0:HEAD_DIM], p_turned[:, n % 2, j],
                                                v_tok[:, j, h * HEAD_DIM:(h + 1) * HEAD_DIM],
                                                start=(j == 0), stop=(j == kt - 1))
                    last.then_inc(y_made, 1)

                scores(0)
                pe.wait_ge(v_turn_ready, kt)
                for n in range(len(units)):
                    if n + 1 < len(units):
                        scores(n + 1)
                    turn(n)
                    values(n)
                for c in range(ct):
                    pe.wait_ge(y_ready, len(units))
                    if c >= 2:
                        pe.wait_ge(out_ready, c - 1)
                    for t in range(qt):
                        last = nc.tensor.transpose(bank[:, c % 2, t * P:(t + 1) * P], y_tok[:, t, c * P:(c + 1) * P], ident[:])
                    last.then_inc(out_turned, 1)

            @block.vector
            def _(dve):
                dve.wait_ge(loaded, 16 * n_loads)

                def soften(n):
                    h, t = units[n]
                    dve.wait_ge(scores_made, n + 1)
                    if n >= 2:
                        dve.wait_ge(p_turn_made, n - 1)
                    raw = bank[:, 2 + n % 2, 0:NK]
                    if bias is not None:
                        first = GRID_ROWS - 1 - 2 * t
                        nc.vector.scalar_tensor_tensor(
                            s[:, n % 2], raw, HEAD_DIM ** -0.5,
                            bias[:, h, first:first + GRID_ROWS, :].rearrange("p a j -> p (a j)"),
                            ALU.mult, ALU.add).then_inc(scores_ready, 1)
                    else:
                        nc.vector.tensor_scalar(s[:, n % 2], raw, HEAD_DIM ** -0.5, None, ALU.mult).then_inc(
                            scores_ready, 1)
                    dve.wait_ge(scores_ready, n + 1)
                    nc.vector.tensor_reduce(low[:, n:n + 1], s[:, n % 2], X, ALU.max, negate=True).then_inc(low_ready, 1)

                def finish(n):
                    h, t = units[n]
                    dve.wait_ge(p_ready, n + 1)
                    nc.vector.reciprocal(inverse[:, n:n + 1], total[:, n:n + 1]).then_inc(inverse_ready, 1)
                    dve.wait_ge(inverse_ready, n + 1)
                    dve.wait_ge(y_made, n + 1)
                    nc.vector.tensor_scalar(y_tok[:, t, h * HEAD_DIM:(h + 1) * HEAD_DIM], bank[:, 6 + n % 2, 0:HEAD_DIM],
                                            inverse[:, n:n + 1], None, ALU.mult).then_inc(y_ready, 1)

                soften(0)
                for n in range(len(units)):
                    if n + 1 < len(units):
                        soften(n + 1)
                    finish(n)

            @block.scalar
            def _(act):
                for j in range(kt):
                    act.wait_ge(v_turn_made, j + 1)
                    nc.scalar.copy(v_tok[:, j], bank[:, j % 2, 0:C]).then_inc(v_turn_ready, 1)
                for n in range(len(units)):
                    act.wait_ge(low_ready, n + 1)
                    nc.scalar.activation(s[:, n % 2], s[:, n % 2], ACT.Exp, bias=low[:, n:n + 1],
                                         accum_out=total[:, n:n + 1]).then_inc(p_ready, 1)
                    act.wait_ge(p_turn_made, n + 1)
                    if n >= 2:
                        act.wait_ge(y_made, n - 1)
                    nc.scalar.copy(p_turned[:, n % 2].rearrange("p j m -> p (j m)"), bank[:, 4 + n % 2, 0:NK]).then_inc(
                        p_turn_ready, 1)
                for c in range(ct):
                    act.wait_ge(out_turned, c + 1)
                    nc.scalar.copy(y[:, c], bank[:, c % 2, 0:T]).then_inc(out_ready, 1)


def window_bias(rpb):
    heads = rpb.shape[0]
    win = 16
    w = np.arange(GRID_W)[:, None]
    j = np.arange(GRID_W)[None, :]
    start = np.clip(w - win // 2, 0, GRID_W - win)
    inside = (j >= start) & (j < start + win)
    offset = np.clip(j - w + win - 1, 0, 2 * win - 2)
    rows = 2 * GRID_ROWS
    out = np.full((2, GRID_W, heads, rows, GRID_W), -1e30, np.float32)
    laid = np.where(inside[None, None], rpb[:, :, offset], np.float32(-1e30))
    laid = laid.transpose(2, 0, 1, 3)
    out[0, :, :, 0:rows - 1] = laid
    out[1, :, :, 1:rows] = laid
    return np.ascontiguousarray(out.reshape(P, heads, rows, GRID_W))


RW_WIDTH = 384
RW_X = RW_WIDTH // P
RCHUNK = 32
RSTEPS = SEQ // RCHUNK
LORA = 64
DECAY_SCALE = float(np.exp(-0.5))
GN_EPS = 64e-5
LEVELS = 5
MU_R, MU_K, MU_V, W0, A0, K_K, K_A, R_K, LN_G, LN_B = 0, 2, 4, 6, 8, 10, 11, 12, 13, 14
RW_COLS = 15


def rwkv7(nc, stage, p_dram, par_dram, mu_l_dram, lora_dram, g2_dram, ident_dram, masks_dram, member_dram,
          eye2_dram, out_dram):
    T = SEQ
    N = RW_X * T
    units = [(d, i, x) for d in range(2) for i in range(T // P) for x in range(RW_X)]
    with ExitStack() as ctx:
        sb, ps, sem = opener(nc, ctx, stage)
        par = sb("par", [P, RW_COLS, RW_X])
        mu_l = sb("mu_l", [P, 2])
        keep_k = sb("keep_k", [P, RW_X])
        lora = sb("lora", [P, 2, RW_WIDTH])
        g2 = sb("g2", [P, RW_WIDTH])
        ident = sb("ident", [P, P])
        blocks = sb("blocks", [P, P])
        masks = sb("masks", [P, 2, 4, P])
        member = sb("member", [P, 4, P])
        eye2 = sb("eye2", [P, HEAD_DIM])
        resets = sb("resets", [P, N])
        raw = sb("raw", [P, 3, RW_X, T + 2])
        raw_l = sb("raw_l", [P, T + 2])
        lat_g = sb("lat_g", [P, T])
        ar = sb("ar", [P, 2, RW_X, 2, T])
        bh = sb("bh", [P, 2, RW_X, T])
        kh = sb("kh", [P, 2, RW_X, T])
        v = sb("v", [P, 2, RW_X, T])
        qt = sb("qt", [P, 2, RW_X, T])
        y_loc = sb("y_loc", [P, 2, RW_X, T])
        bonus = sb("bonus", [P, RW_X, T])
        ends = sb("ends", [P, RSTEPS, 2 * RW_X])
        work = sb("work", [P, 11 * N])
        tmp = [work[:, n * N:(n + 1) * N].rearrange("p (x t) -> p x t", x=RW_X) for n in range(11)]
        dr, dk, dv, r, k, sw, sa, cum, e1, e2, sq = tmp
        e3, norm = dr, dk
        dl, lat = cum[:, 0], sq[:, 0]
        gate, y = e1, e2
        raw_flat = raw[:].rearrange("p j x t -> p (j x t)")
        per_step = RSTEPS * 2 * RW_X * HEAD_DIM
        ht = work[:, 0:per_step].rearrange("p (s n k) -> p s n k", s=RSTEPS, k=HEAD_DIM)
        nn = work[:, per_step:2 * per_step].rearrange("p (s n k) -> p s n k", s=RSTEPS, k=HEAD_DIM)
        states = sb("states", [P, 2, 2 * RW_X, HEAD_DIM])
        tok = sb("tok", [P, 2, 4, P])
        split = raw_flat[:, 0:16 * P].rearrange("p (s a c n) -> p s a c n", s=2, a=2, c=4)
        sm = raw_flat[:, 16 * P:32 * P].rearrange("p (s e a t) -> p s e a t", s=2, e=2, a=4)
        a_first = resets[:, 0:4 * P].rearrange("p (s e n) -> p s e n", s=2, e=2)
        z = resets[:, 4 * P:8 * P].rearrange("p (s e n) -> p s e n", s=2, e=2)
        power = sb("power", [P, 2, 2, 2, P])
        bank = ps("bank", [P, 8, 512])

        loaded = sem("loaded")
        raw_loaded = sem("raw_loaded")
        consts_ready = sem("consts_ready")
        diffed = sem("diffed")
        mixed = sem("mixed")
        tanhed = sem("tanhed")
        lora_made = sem("lora_made")
        sig_ready = sem("sig_ready")
        squared = sem("squared")
        norm_made = sem("norm_made")
        norm_rooted = sem("norm_rooted")
        chain = sem("chain")
        cum_ready = sem("cum_ready")
        cum_used = sem("cum_used")
        exps_ready = sem("exps_ready")
        prepared = sem("prepared")
        bonus_in = sem("bonus_in")
        bonus_made = sem("bonus_made")
        bonus_ready = sem("bonus_ready")
        turn_made = sem("turn_made")
        tok_ready = sem("tok_ready")
        split_ready = sem("split_ready")
        scores_made = sem("scores_made")
        scores_ready = sem("scores_ready")
        first_made = sem("first_made")
        first_ready = sem("first_ready")
        z_started = sem("z_started")
        level_made = sem("level_made")
        z_ready = sem("z_ready")
        power_ready = sem("power_ready")
        ends_made = sem("ends_made")
        ends_read = sem("ends_read")
        parts_read = sem("parts_read")
        step_made = sem("step_made")
        step_added = sem("step_added")
        state_ready = sem("state_ready")
        inter_made = sem("inter_made")
        gate_sig = sem("gate_sig")
        gate_made = sem("gate_made")
        gate_ready = sem("gate_ready")
        tail = sem("tail")
        mean_made = sem("mean_made")
        dev_squared = sem("dev_squared")
        var_made = sem("var_made")
        var_ready = sem("var_ready")
        var_rooted = sem("var_rooted")
        stored = sem("stored")

        def shifted(a, d):
            return a[..., 0:T] if d == 0 else a[..., 2:T + 2]

        def wide(a):
            return a.rearrange("p x t -> p (x t)")

        def steps_of_tile(d, i):
            if d == 0:
                return slice(4 * i, 4 * i + 4)
            last = RSTEPS - 1 - 4 * i
            return slice(last, last - 4 if last >= 4 else None, -1)

        with nc.Block() as block:

            @block.sync
            def _(sp):
                for dst, src in ((par, par_dram), (mu_l, mu_l_dram), (lora, lora_dram), (g2, g2_dram),
                                 (ident, ident_dram), (masks, masks_dram), (member, member_dram), (eye2, eye2_dram)):
                    sp.dma_start(dst[:], src).then_inc(loaded, 16)
                sp.wait_ge(consts_ready, 3)
                for j in range(3):
                    sp.dma_start(raw[:, j, :, 1:T + 1],
                                 p_dram[j * RW_WIDTH:(j + 1) * RW_WIDTH, :].rearrange("(x p) t -> p x t", p=P)).then_inc(
                        raw_loaded, 16)
                at = 3 * RW_WIDTH
                sp.dma_start(raw_l[:, 1:T + 1], p_dram[at:at + P, :]).then_inc(raw_loaded, 16)
                sp.dma_start(lat_g[:], p_dram[at + P:at + 2 * P, :]).then_inc(raw_loaded, 16)
                sp.wait_ge(tail, RW_TAIL)
                sp.dma_start(out_dram.rearrange("(x p) t -> p x t", p=P), y).then_inc(stored, 16)
                sp.wait_ge(stored, 16)

            @block.gpsimd
            def _(pool):
                for d in range(2):
                    pool.wait_ge(raw_loaded, 80)
                    if d == 1:
                        pool.wait_ge(prepared, RW_PREPARED)
                        pool.wait_ge(bonus_in, 1)
                        pool.wait_ge(chain, RW_CHAIN)
                        pool.wait_ge(mixed, 10)
                    for j, out in enumerate((dr, dk, dv)):
                        nc.gpsimd.tensor_tensor(out, shifted(raw[:, j], d), raw[:, j, :, 1:T + 1],
                                                ALU.subtract).then_inc(diffed, 1)
                    nc.gpsimd.tensor_tensor(dl, shifted(raw_l[:], d), raw_l[:, 1:T + 1], ALU.subtract).then_inc(diffed, 1)
                    pool.wait_ge(exps_ready, 3 * (d + 1))
                    pool.wait_ge(mixed, 10 * (d + 1))
                    nc.gpsimd.tensor_tensor(ar[:, d, :, 1, :], r, e1, ALU.mult).then_inc(prepared, 1)
                for n, (d, i, x) in enumerate(units):
                    pool.wait_ge(tok_ready, n + 1)
                    if n >= 2:
                        pool.wait_ge(ends_made, n - 1)
                    for j in range(2):
                        nc.gpsimd.tensor_tensor(split[:, n % 2, j], member[:],
                                                tok[:, n % 2, j].unsqueeze(1).broadcast_to([P, 4, P]),
                                                ALU.mult).then_inc(split_ready, 1)
                pool.wait_ge(parts_read, 2 * len(units))
                nc.gpsimd.tensor_tensor(y_loc[:, 0], y_loc[:, 0], y_loc[:, 1], ALU.add).then_inc(prepared, 1)

            @block.scalar
            def _(act):
                act.wait_ge(raw_loaded, 80)
                nc.scalar.activation(lat_g[:], lat_g[:], ACT.Sigmoid).then_inc(gate_sig, 1)
                act.wait_ge(loaded, 128)
                for d in range(2):
                    act.wait_ge(mixed, 10 * (d + 1))
                    nc.scalar.activation(lat[0:LORA], lat[0:LORA], ACT.Tanh).then_inc(tanhed, 1)
                    act.wait_ge(lora_made, d + 1)
                    for x in range(RW_X):
                        nc.scalar.activation(sw[:, x], bank[:, x], ACT.Sigmoid, bias=par[:, W0 + d, x:x + 1]).then_inc(
                            sig_ready, 1)
                    for x in range(RW_X):
                        nc.scalar.activation(sa[:, x], bank[:, 3 + x], ACT.Sigmoid, bias=par[:, A0 + d, x:x + 1]).then_inc(
                            sig_ready, 1)
                    for x in range(RW_X):
                        nc.scalar.activation(sq[:, x], k[:, x], ACT.Square, scale=par[:, K_K, x:x + 1]).then_inc(squared, 1)
                    act.wait_ge(norm_made, d + 1)
                    nc.scalar.activation(norm, bank[:, 0:3, :], ACT.Sqrt).then_inc(norm_rooted, 1)
                    act.wait_ge(cum_ready, 2 * d + 1)
                    nc.scalar.activation(e1, cum, ACT.Exp, scale=-DECAY_SCALE).then_inc(exps_ready, 1)
                    nc.scalar.activation(e2, cum, ACT.Exp, scale=DECAY_SCALE).then_inc(exps_ready, 1)
                    act.wait_ge(cum_ready, 2 * d + 2)
                    nc.scalar.activation(e3, sw, ACT.Exp, scale=-DECAY_SCALE).then_inc(exps_ready, 1)

                def front_a(n):
                    act.wait_ge(turn_made, n + 1)
                    if n >= 2:
                        act.wait_ge(ends_made, n - 1)
                    nc.scalar.copy(tok[:, n % 2].rearrange("p a c -> p (a c)"), bank[:, 0]).then_inc(tok_ready, 1)

                def front_b(n):
                    act.wait_ge(first_made, n + 1)
                    if n >= 2:
                        act.wait_ge(level_made, LEVELS * (n - 1))
                    nc.scalar.copy(a_first[:, n % 2], bank[:, 6, 0:2 * P].rearrange("p (e s) -> p e s", e=2)).then_inc(
                        first_ready, 1)

                def level(n, lv):
                    if lv < LEVELS - 1:
                        act.wait_ge(level_made, LEVELS * n + lv + 1)
                        first = 0 if lv < LEVELS - 2 else P
                        nc.scalar.copy(power[:, lv % 2, :, :, :].rearrange("p e a s -> p e (a s)")[:, :, first:],
                                       bank[:, 3:5, first:2 * P]).then_inc(power_ready, 1)

                def finish(n):
                    d, i, x = units[n]
                    act.wait_ge(ends_made, n + 1)
                    nc.scalar.copy(nn[:, steps_of_tile(d, i), 3 * d + x, :],
                                   bank[:, 6, 0:4 * HEAD_DIM].rearrange("p (c k) -> p c k", c=4)).then_inc(parts_read, 1)
                    nc.scalar.copy(y_loc[:, d, x, i * P:(i + 1) * P], bank[:, 6, 4 * HEAD_DIM:4 * HEAD_DIM + P]).then_inc(
                        parts_read, 1)

                act.wait_ge(prepared, 2 * RW_PREPARED)
                act.wait_ge(chain, 2 * RW_CHAIN)
                act.wait_ge(bonus_made, 2)
                front_a(0)
                front_b(0)
                for n in range(len(units)):
                    level(n, 0)
                    level(n, 1)
                    if n + 1 < len(units):
                        front_a(n + 1)
                    level(n, 2)
                    level(n, 3)
                    if n + 1 < len(units):
                        front_b(n + 1)
                    finish(n)
                act.wait_ge(gate_made, 1)
                nc.scalar.copy(gate, bank[:, 5:8, :]).then_inc(gate_ready, 1)
                act.wait_ge(tail, 2)
                nc.scalar.activation(sq, y, ACT.Square).then_inc(dev_squared, 1)
                act.wait_ge(var_ready, 1)
                nc.scalar.activation(sq, sq, ACT.Sqrt).then_inc(var_rooted, 1)

            @block.tensor
            def _(pe):
                pe.wait_ge(loaded, 128)
                pe.wait_ge(consts_ready, 5)
                for d in range(2):
                    pe.wait_ge(tanhed, d + 1)
                    pe.wait_ge(mixed, 10 * (d + 1))
                    if d == 1:
                        pe.wait_ge(bonus_ready, 1)
                        pe.wait_ge(sig_ready, 6)
                    for x in range(RW_X):
                        nc.tensor.matmul(bank[:, x], lora[0:LORA, d, x * P:(x + 1) * P], lat[0:LORA], start=True, stop=True)
                    for x in range(RW_X):
                        last = nc.tensor.matmul(bank[:, 3 + x], lora[LORA:, d, x * P:(x + 1) * P], lat[LORA:],
                                                start=True, stop=True)
                    last.then_inc(lora_made, 1)
                    pe.wait_ge(squared, 3 * (d + 1))
                    pe.wait_ge(sig_ready, 6 * d + 3)
                    for x in range(RW_X):
                        last = nc.tensor.matmul(bank[:, x], blocks[:], sq[:, x], start=True, stop=True)
                    last.then_inc(norm_made, 1)
                    pe.wait_ge(bonus_in, d + 1)
                    pe.wait_ge(norm_rooted, d + 1)
                    for x in range(RW_X):
                        last = nc.tensor.matmul(bank[:, x], blocks[:], sq[:, x], start=True, stop=True)
                    last.then_inc(bonus_made, 1)
                pe.wait_ge(bonus_ready, 2)
                pe.wait_ge(prepared, 2 * RW_PREPARED)
                pe.wait_ge(chain, 2 * RW_CHAIN)
                pe.wait_ge(sig_ready, 12)

                def heads(e):
                    return slice(64 * e, 64 * e + 64)

                def front_a(n):
                    d, i, x = units[n]
                    at = slice(i * P, (i + 1) * P)
                    if n >= 1:
                        pe.wait_ge(tok_ready, n)
                    for j, a in enumerate((bh[:, d, x, at], kh[:, d, x, at], ar[:, d, x, 0, at], v[:, d, x, at])):
                        last = nc.tensor.transpose(bank[:, 0, j * P:(j + 1) * P], a, ident[:])
                    last.then_inc(turn_made, 1)
                    if n >= 1:
                        pe.wait_ge(scores_ready, n)
                    for e in range(2):
                        for j, a in enumerate((bh, kh)):
                            last = nc.tensor.matmul(bank[:, 1 + e, 2 * j * P:2 * (j + 1) * P], a[heads(e), d, x, at],
                                                    ar[heads(e), d, x, :, at], start=True, stop=True)
                    last.then_inc(scores_made, 1)

                def front_b(n):
                    pe.wait_ge(scores_ready, n + 1)
                    pe.wait_ge(tok_ready, n + 1)
                    if n >= 2:
                        pe.wait_ge(ends_read, 2 * (n - 1))
                        pe.wait_ge(parts_read, 2 * (n - 1))
                    for e in range(2):
                        nc.tensor.transpose(bank[:, 6, e * P:(e + 1) * P], sm[:, n % 2, e, 0], ident[:])
                    for e in range(2):
                        last = nc.tensor.matmul(bank[:, 5, 64 * e:64 * e + 64], sm[:, n % 2, e, 2],
                                                tok[:, n % 2, 3, heads(e)], start=True, stop=True)
                    last.then_inc(first_made, 1)

                def level(n, lv):
                    if lv == 0:
                        pe.wait_ge(first_ready, n + 1)
                        pe.wait_ge(z_started, 2 * (n + 1))
                        if n >= 1:
                            pe.wait_ge(z_ready, LEVELS * n)
                    else:
                        pe.wait_ge(power_ready, (LEVELS - 1) * n + lv)
                        pe.wait_ge(z_ready, LEVELS * n + lv)
                    for e in range(2):
                        a_t = sm[:, n % 2, e, 0] if lv == 0 else power[:, (lv - 1) % 2, e, 1]
                        a = a_first[:, n % 2, e] if lv == 0 else power[:, (lv - 1) % 2, e, 0]
                        if lv < LEVELS - 1:
                            if lv < LEVELS - 2:
                                nc.tensor.matmul(bank[:, 3 + e, 0:P], a_t, a, start=True, stop=True)
                            nc.tensor.matmul(bank[:, 3 + e, P:2 * P], a, a_t, start=True, stop=True)
                        last = nc.tensor.matmul(bank[:, 7, e * P:(e + 1) * P], a_t, z[:, n % 2, e], start=True, stop=True)
                    last.then_inc(level_made, 1)

                def finish(n):
                    s = n % 2
                    pe.wait_ge(z_ready, LEVELS * (n + 1))
                    pe.wait_ge(split_ready, 2 * (n + 1))
                    m = min(n + 2, len(units))
                    pe.wait_ge(first_ready, m)
                    pe.wait_ge(z_started, 2 * m)
                    if n >= 1:
                        pe.wait_ge(ends_read, 2 * n)
                        pe.wait_ge(parts_read, 2 * n)
                    for e in range(2):
                        zz, ww, vv = z[:, s, e, 0:64], z[:, s, e, 64:P], tok[:, s, 3, heads(e)]
                        nc.tensor.matmul(bank[heads(e), 5, 0:256], ww, split[:, s, 0, :, heads(e)], start=True, stop=True)
                        nc.tensor.matmul(bank[heads(e), 5, 256:384], ww, sm[:, s, e, 1], start=True, stop=True)
                        for c in range(4):
                            to = bank[heads(e), 6, 64 * c:64 * c + 64]
                            nc.tensor.matmul(to, split[:, s, 0, c, heads(e)], zz, start=True, stop=False)
                            nc.tensor.matmul(to, split[:, s, 1, c, heads(e)], vv, start=False, stop=True)
                        to = bank[heads(e), 6, 256:384]
                        nc.tensor.matmul(to, zz, sm[:, s, e, 1], start=True, stop=False)
                        last = nc.tensor.matmul(to, vv, sm[:, s, e, 3], start=False, stop=True)
                    last.then_inc(ends_made, 1)

                front_a(0)
                front_b(0)
                for n in range(len(units)):
                    level(n, 0)
                    level(n, 1)
                    if n + 1 < len(units):
                        front_a(n + 1)
                    level(n, 2)
                    level(n, 3)
                    if n + 1 < len(units):
                        front_b(n + 1)
                    level(n, 4)
                    finish(n)

                pe.wait_ge(ends_read, 2 * len(units))
                pe.wait_ge(parts_read, 2 * len(units))
                pe.wait_ge(gate_sig, 1)
                for x in range(RW_X):
                    last = nc.tensor.matmul(bank[:, 5 + x], g2[:, x * P:(x + 1) * P], lat_g[:], start=True, stop=True)
                last.then_inc(gate_made, 1)
                pe.wait_ge(z_ready, LEVELS * len(units))
                for s in range(1, RSTEPS):
                    pe.wait_ge(state_ready, s)
                    if s < RSTEPS - 1:
                        for n in range(2 * RW_X):
                            for e in range(2):
                                last = nc.tensor.matmul(bank[heads(e), s % 2, 64 * n:64 * n + 64], ht[heads(e), s, n],
                                                        states[heads(e), s % 2, n], start=True, stop=True)
                        last.then_inc(step_made, 1)
                    for d in range(2):
                        c = s if d == 0 else RSTEPS - 1 - s
                        at = slice(c * RCHUNK, (c + 1) * RCHUNK)
                        for x in range(RW_X):
                            for e in range(2):
                                last = nc.tensor.matmul(bank[heads(e), 2 + x, at], states[heads(e), s % 2, 3 * d + x],
                                                        qt[heads(e), d, x, at], start=(s == 1 and d == 0),
                                                        stop=(s == RSTEPS - 1 and d == 1))
                    last.then_inc(inter_made, 1)
                pe.wait_ge(tail, 1)
                pe.wait_ge(gate_ready, 1)
                for x in range(RW_X):
                    last = nc.tensor.matmul(bank[:, 5 + x], blocks[:], y[:, x], start=True, stop=True)
                last.then_inc(mean_made, 1)
                pe.wait_ge(dev_squared, 1)
                pe.wait_ge(tail, 2)
                for x in range(RW_X):
                    last = nc.tensor.matmul(bank[:, 5 + x], blocks[:], sq[:, x], start=True, stop=True)
                last.then_inc(var_made, 1)

            @block.vector
            def _(dve):
                nc.vector.memset(raw[:], 0.0).then_inc(consts_ready, 1)
                nc.vector.memset(raw_l[:], 0.0).then_inc(consts_ready, 1)
                nc.vector.memset(blocks[:], 0.0).then_inc(consts_ready, 1)
                dve.wait_ge(consts_ready, 3)
                nc.vector.memset(blocks[0:64, 0:64], 1.0).then_inc(consts_ready, 1)
                nc.vector.memset(blocks[64:P, 64:P], 1.0).then_inc(consts_ready, 1)
                nc.vector.memset(resets[:], 1.0).then_inc(consts_ready, 1)
                dve.wait_ge(consts_ready, 6)
                nc.vector.memset(resets[:, 0:N:RCHUNK], 0.0).then_inc(consts_ready, 1)
                dve.wait_ge(loaded, 128)
                nc.vector.tensor_scalar(keep_k[:], par[:, K_A], -1.0, 1.0, ALU.mult, ALU.add).then_inc(consts_ready, 1)
                dve.wait_ge(consts_ready, 8)
                done = [0]

                def step(ins):
                    ins.then_inc(chain, 1)
                    done[0] += 1
                    dve.wait_ge(chain, done[0])

                for d in range(2):
                    for j, (diff, out, mu) in enumerate(((dr, r, MU_R), (dk, k, MU_K), (dv, v[:, d], MU_V))):
                        dve.wait_ge(diffed, 4 * d + j + 1)
                        if d == 1 and j == 0:
                            dve.wait_ge(prepared, RW_PREPARED)
                            dve.wait_ge(bonus_in, 1)
                        for x in range(RW_X):
                            nc.vector.scalar_tensor_tensor(out[:, x], diff[:, x], par[:, mu + d, x:x + 1],
                                                           raw[:, j, x, 1:T + 1], ALU.mult, ALU.add).then_inc(mixed, 1)
                    dve.wait_ge(diffed, 4 * d + 4)
                    if d == 1:
                        dve.wait_ge(lora_made, 1)
                    nc.vector.scalar_tensor_tensor(lat, dl, mu_l[:, d:d + 1], raw_l[:, 1:T + 1],
                                                   ALU.mult, ALU.add).then_inc(mixed, 1)
                    dve.wait_ge(sig_ready, 6 * d + 3)
                    if d == 0:
                        nc.vector.tensor_tensor_scan(wide(cum), resets[:], wide(sw), 0.0, ALU.mult, ALU.add).then_inc(
                            cum_ready, 1)
                    else:
                        nc.vector.tensor_tensor_scan(wide(cum)[:, ::-1], resets[:], wide(sw)[:, ::-1], 0.0,
                                                     ALU.mult, ALU.add).then_inc(cum_ready, 1)
                    dve.wait_ge(cum_ready, 2 * d + 1)
                    nc.vector.tensor_tensor(sw, cum, sw, ALU.subtract).then_inc(cum_ready, 1)
                    dve.wait_ge(norm_rooted, d + 1)
                    step(nc.vector.tensor_scalar(norm, norm, 1e-12, None, ALU.max))
                    step(nc.vector.reciprocal(norm, norm))
                    dve.wait_ge(mixed, 10 * (d + 1))
                    for x in range(RW_X):
                        nc.vector.scalar_tensor_tensor(norm[:, x], k[:, x], par[:, K_K, x:x + 1], norm[:, x],
                                                       ALU.mult, ALU.mult).then_inc(chain, 1)
                        done[0] += 1
                    dve.wait_ge(chain, done[0])
                    dve.wait_ge(exps_ready, 3 * (d + 1))
                    nc.vector.scalar_tensor_tensor(ar[:, d, :, 0, :], norm, -1.0, e3, ALU.mult, ALU.mult).then_inc(
                        prepared, 1)
                    dve.wait_ge(sig_ready, 6 * (d + 1))
                    step(nc.vector.tensor_tensor(norm, norm, sa, ALU.mult))
                    nc.vector.tensor_tensor(bh[:, d], norm, e2, ALU.mult).then_inc(prepared, 1)
                    for x in range(RW_X):
                        nc.vector.tensor_scalar(sa[:, x], sa[:, x], par[:, K_A, x:x + 1], keep_k[:, x:x + 1],
                                                ALU.mult, ALU.add).then_inc(chain, 1)
                        done[0] += 1
                    dve.wait_ge(chain, done[0])
                    step(nc.vector.tensor_tensor(k, k, sa, ALU.mult))
                    nc.vector.tensor_tensor(kh[:, d], k, e2, ALU.mult).then_inc(prepared, 1)
                    dve.wait_ge(norm_made, d + 1)
                    for x in range(RW_X):
                        ins = nc.vector.scalar_tensor_tensor(sq[:, x], r[:, x], par[:, R_K, x:x + 1], k[:, x],
                                                             ALU.mult, ALU.mult)
                    ins.then_inc(bonus_in, 1)
                    whole = e1[:, :, RCHUNK - 1::RCHUNK] if d == 0 else e1[:, :, T - RCHUNK::-RCHUNK]
                    nc.vector.tensor_copy(ends[:, :, 3 * d:3 * d + 3].rearrange("p s x -> p x s"), whole).then_inc(
                        prepared, 1)
                    dve.wait_ge(bonus_made, d + 1)
                    if d == 0:
                        nc.vector.tensor_tensor(bonus[:], bank[:, 0:3, :], v[:, 0], ALU.mult).then_inc(bonus_ready, 1)
                    else:
                        dve.wait_ge(prepared, 2 * RW_PREPARED)
                        step(nc.vector.tensor_tensor(e1, bank[:, 0:3, :], v[:, 1], ALU.mult))
                        dve.wait_ge(bonus_ready, 1)
                        nc.vector.tensor_tensor(bonus[:], bonus[:], e1, ALU.add).then_inc(bonus_ready, 1)
                    if d == 0:
                        assert done[0] == RW_CHAIN, done[0]

                def front_a(n):
                    d = units[n][0]
                    dve.wait_ge(scores_made, n + 1)
                    if n >= 2:
                        dve.wait_ge(ends_made, n - 1)
                    for e in range(2):
                        ins = nc.vector.tensor_tensor(sm[:, n % 2, e].rearrange("p a t -> p (a t)"), bank[:, 1 + e],
                                                      masks[:, d].rearrange("p a t -> p (a t)"), ALU.mult)
                    ins.then_inc(scores_ready, 1)

                def front_b(n):
                    dve.wait_ge(first_made, n + 1)
                    if n >= 2:
                        dve.wait_ge(ends_made, n - 1)
                    nc.vector.tensor_copy(z[:, n % 2, :, 0:64],
                                          bank[:, 5, 0:P].rearrange("p (e m) -> p e m", e=2)).then_inc(z_started, 1)
                    dve.wait_ge(tok_ready, n + 1)
                    nc.vector.tensor_copy(z[:, n % 2, :, 64:P],
                                          tok[:, n % 2, 2].rearrange("p (e m) -> p e m", e=2)).then_inc(z_started, 1)

                def level(n, lv):
                    dve.wait_ge(level_made, LEVELS * n + lv + 1)
                    if lv == 0:
                        dve.wait_ge(z_started, 2 * (n + 1))
                    else:
                        dve.wait_ge(z_ready, LEVELS * n + lv)
                    nc.vector.tensor_tensor(z[:, n % 2], z[:, n % 2], bank[:, 7, 0:2 * P].rearrange("p (e m) -> p e m", e=2),
                                            ALU.add).then_inc(z_ready, 1)

                def finish(n):
                    d, i, x = units[n]
                    at = slice(i * P, (i + 1) * P)
                    dve.wait_ge(ends_made, n + 1)
                    nc.vector.tensor_tensor(ht[:, steps_of_tile(d, i), 3 * d + x, :],
                                            bank[:, 5, 0:256].rearrange("p (c k) -> p c k", c=4),
                                            eye2[:].unsqueeze(1).broadcast_to([P, 4, HEAD_DIM]), ALU.add).then_inc(ends_read, 1)
                    nc.vector.tensor_tensor(qt[:, d, x, at], bank[:, 5, 256:384], ar[:, d, x, 1, at], ALU.add).then_inc(
                        ends_read, 1)

                dve.wait_ge(prepared, 2 * RW_PREPARED)
                dve.wait_ge(bonus_ready, 2)
                dve.wait_ge(exps_ready, 6)
                front_a(0)
                front_b(0)
                for n in range(len(units)):
                    level(n, 0)
                    level(n, 1)
                    if n + 1 < len(units):
                        front_a(n + 1)
                    level(n, 2)
                    level(n, 3)
                    if n + 1 < len(units):
                        front_b(n + 1)
                    level(n, 4)
                    finish(n)

                def over(a):
                    return a.unsqueeze(2).broadcast_to([P, 2 * RW_X, HEAD_DIM])

                dve.wait_ge(parts_read, 2 * len(units))
                nc.vector.tensor_tensor(states[:, 1], nn[:, 0], over(ends[:, 0]), ALU.mult).then_inc(state_ready, 1)
                for s in range(1, RSTEPS - 1):
                    dve.wait_ge(step_made, s)
                    if s >= 2:
                        dve.wait_ge(inter_made, s - 1)
                    dve.wait_ge(state_ready, s)
                    to = states[:, (s + 1) % 2]
                    nc.vector.tensor_tensor(to, nn[:, s], bank[:, s % 2, 0:2 * RW_X * HEAD_DIM].rearrange(
                        "p (n k) -> p n k", k=HEAD_DIM), ALU.add).then_inc(step_added, 1)
                    dve.wait_ge(step_added, s)
                    nc.vector.tensor_tensor(to, to, over(ends[:, s]), ALU.mult).then_inc(state_ready, 1)
                dve.wait_ge(inter_made, RSTEPS - 1)
                dve.wait_ge(prepared, 2 * RW_PREPARED + 1)
                count = [0]

                def tail_step(ins):
                    ins.then_inc(tail, 1)
                    count[0] += 1
                    dve.wait_ge(tail, count[0])

                tail_step(nc.vector.tensor_tensor(y, y_loc[:, 0], bank[:, 2:5, :], ALU.add))
                dve.wait_ge(mean_made, 1)
                tail_step(nc.vector.scalar_tensor_tensor(y, bank[:, 5:8, :], -1.0 / HEAD_DIM, y, ALU.mult, ALU.add))
                dve.wait_ge(var_made, 1)
                nc.vector.tensor_scalar(sq, bank[:, 5:8, :], 1.0 / HEAD_DIM, GN_EPS, ALU.mult, ALU.add).then_inc(tail, 1)
                count[0] += 1
                dve.wait_ge(tail, count[0])
                nc.vector.reciprocal(sq, sq).then_inc(var_ready, 1)
                dve.wait_ge(var_rooted, 1)
                tail_step(nc.vector.tensor_tensor(y, y, sq, ALU.mult))
                for x in range(RW_X):
                    tail_step(nc.vector.tensor_scalar(y[:, x], y[:, x], par[:, LN_G, x:x + 1], par[:, LN_B, x:x + 1],
                                                      ALU.mult, ALU.add))
                tail_step(nc.vector.tensor_tensor(y, y, bonus[:], ALU.add))
                dve.wait_ge(gate_ready, 1)
                tail_step(nc.vector.tensor_tensor(y, y, gate, ALU.mult))
                assert count[0] == RW_TAIL, count[0]


RW_PREPARED = 5
RW_CHAIN = 2 + 3 + 1 + 3 + 1
RW_TAIL = 4 + RW_X + 2


EXPERTS = 16
CAPACITY = 2 * SEQ // EXPERTS
EXPERT_FF = 2 * D_MODEL


def expert_ffn(nc, stage, z_dram, x_dram, router_dram, gate_dram, up_dram, down_dram, ident_dram, slots_dram,
               out_dram):
    T = SEQ
    TT = T // P
    HALF = 512
    FC = EXPERT_FF // HALF
    FT = HALF // P
    with ExitStack() as ctx:
        sb, ps, sem = opener(nc, ctx, stage)
        z = sb("z", [P, KT, T])
        z_tok = sb("z_tok", [P, TT, D_MODEL])
        acc = z_tok[:].rearrange("p a b -> p (a b)").rearrange("p (m t) -> p m t", t=T)
        hot = sb("hot", [P, TT, EXPERTS, CAPACITY])
        xe = sb("xe", [P, KT, EXPERTS * CAPACITY])
        scatter = sb("scatter", [P, EXPERTS // 2, T])
        router = sb("router", [P, KT, EXPERTS])
        ident = sb("ident", [P, P])
        slots = sb("slots", [P, CAPACITY])
        logits = sb("logits", [P, TT, EXPERTS])
        high = sb("high", [P, TT])
        affinity = sb("affinity", [P, TT, EXPERTS])
        place_tok = sb("place_tok", [P, TT, EXPERTS])
        left = sb("left", [EXPERTS, T])
        best = sb("best", [EXPERTS, 8])
        chosen = sb("chosen", [EXPERTS, T])
        ones = sb("ones", [EXPERTS, T])
        w_in = sb("w_in", [P, 2, 2, KT, HALF])
        w_out = sb("w_out", [P, 2, FT, D_MODEL])
        xs = sb("xs", [P, 2, KT, CAPACITY])
        hot_flat = hot[:].rearrange("p t e s -> p (t e s)")
        sg = hot_flat[0:CAPACITY, 0:2 * HALF].rearrange("n (s f) -> n s f", s=2)
        act_t = hot_flat[:, 2 * HALF:3 * HALF].rearrange("p (s j n) -> p s j n", s=2, j=FT)
        ye = hot_flat[:, 3 * HALF:3 * HALF + D_MODEL]
        bank = ps("bank", [P, 8, 512])

        loaded = sem("loaded")
        z_loaded = sem("z_loaded")
        x_loaded = sem("x_loaded")
        logits_made = sem("logits_made")
        route = sem("route")
        exp_ready = sem("exp_ready")
        aff_turned = sem("aff_turned")
        place_turned = sem("place_turned")
        hot_ready = sem("hot_ready")
        z_turned = sem("z_turned")
        z_tok_ready = sem("z_tok_ready")
        xe_made = sem("xe_made")
        xe_ready = sem("xe_ready")
        weighted = sem("weighted")
        hot_turned = sem("hot_turned")
        scatter_ready = sem("scatter_ready")
        in_loaded = [sem(f"in_loaded{s}") for s in range(2)]
        out_loaded = [sem(f"out_loaded{s}") for s in range(2)]
        in_used = [sem(f"in_used{s}") for s in range(2)]
        out_used = [sem(f"out_used{s}") for s in range(2)]
        xs_ready = [sem(f"xs_ready{s}") for s in range(2)]
        silu_ready = sem("silu_ready")
        act_ready = sem("act_ready")
        act_turned = sem("act_turned")
        act_t_ready = sem("act_t_ready")
        y_made = sem("y_made")
        y_ready = sem("y_ready")
        part_made = sem("part_made")
        part_added = sem("part_added")
        stored = sem("stored")

        in_v = [w.rearrange("e (k p) f -> e p k f", p=P) for w in (gate_dram, up_dram)]
        out_v = down_dram.rearrange("e (c p) d -> e p c d", p=P)

        def pairs(eng, body):
            with eng.Fori(0, EXPERTS // 2) as i:
                body(i)

        with nc.Block() as block:

            @block.sync
            def _(sp):
                sp.dma_start(z[:], z_dram.rearrange("(k p) t -> p k t", p=P)).then_inc(z_loaded, 16)
                for dst, src in ((router[:], router_dram.rearrange("(k p) e -> p k e", p=P)), (ident[:], ident_dram),
                                 (slots[:], slots_dram)):
                    sp.dma_start(dst, src).then_inc(loaded, 16)

                def stream(i):
                    for m in range(2 * FC):
                        s, e, c = m % 2, m // FC, m % FC
                        sp.wait_ge(in_used[s], FC * i + m // 2)
                        for g in range(2):
                            sp.dma_start(w_in[:, s, g], in_v[g][bass.ds(2 * i + e, 1), :, :, c * HALF:(c + 1) * HALF]
                                         .rearrange("e p k f -> p (e k) f")).then_inc(in_loaded[s], 16)
                        sp.wait_ge(out_used[s], FC * i + m // 2)
                        sp.dma_start(w_out[:, s], out_v[bass.ds(2 * i + e, 1), :, c * FT:(c + 1) * FT, :]
                                     .rearrange("e p c d -> p (e c) d")).then_inc(out_loaded[s], 16)

                pairs(sp, stream)
                sp.wait_ge(part_added, KT * EXPERTS // 2)
                sp.dma_start(out_dram.rearrange("(m p) t -> p m t", p=P), acc).then_inc(stored, 16)
                sp.wait_ge(stored, 16)

            @block.gpsimd
            def _(pool):
                pool.wait_ge(xe_ready, 2 * KT)

                def stage_tokens(i):
                    for e in range(2):
                        pool.wait_ge(in_used[1], (2 * i + e) * FC // 2)
                        nc.gpsimd.tensor_copy(xs[:, e], xe[:, :, bass.ds((2 * i + e) * CAPACITY, CAPACITY)]).then_inc(
                            xs_ready[e], 1)

                pairs(pool, stage_tokens)

            @block.tensor
            def _(pe):
                pe.wait_ge(z_loaded, 16)
                pe.wait_ge(loaded, 48)
                for t in range(TT):
                    for k in range(KT):
                        last = nc.tensor.matmul(bank[:, 0, t * EXPERTS:(t + 1) * EXPERTS], z[:, k, t * P:(t + 1) * P],
                                                router[:, k, :], start=(k == 0), stop=(k == KT - 1))
                last.then_inc(logits_made, 1)
                for n in range(2 * TT):
                    t, h = n // 2, n % 2
                    if n >= 2:
                        pe.wait_ge(z_tok_ready, n - 1)
                    for j in range(4):
                        last = nc.tensor.transpose(bank[:, 2 + n % 2, j * P:(j + 1) * P],
                                                   z[:, 4 * h + j, t * P:(t + 1) * P], ident[:])
                    last.then_inc(z_turned, 1)
                pe.wait_ge(route, MOE_AFFINITY)
                for t in range(TT):
                    last = nc.tensor.transpose(bank[0:EXPERTS, 1, t * P:(t + 1) * P], affinity[:, t], ident[:])
                last.then_inc(aff_turned, 1)
                pe.wait_ge(route, MOE_PLACES)
                for t in range(TT):
                    last = nc.tensor.transpose(bank[:, 0, t * EXPERTS:(t + 1) * EXPERTS], chosen[:, t * P:(t + 1) * P],
                                               ident[0:EXPERTS, 0:EXPERTS])
                last.then_inc(place_turned, 1)
                pe.wait_ge(hot_ready, TT)
                pe.wait_ge(z_tok_ready, 2 * TT)
                for n in range(2 * KT):
                    h, m = n // KT, n % KT
                    if n >= 2:
                        pe.wait_ge(xe_ready, n - 1)
                    for t in range(TT):
                        last = nc.tensor.matmul(bank[:, 4 + n % 2], z_tok[:, t, m * P:(m + 1) * P],
                                                hot[:, t, 8 * h:8 * h + 8].rearrange("p e s -> p (e s)"),
                                                start=(t == 0), stop=(t == TT - 1))
                    last.then_inc(xe_made, 1)
                for j in range(EXPERTS // 2):
                    pe.wait_ge(weighted, TT)
                    if j >= 2:
                        pe.wait_ge(scatter_ready, j - 1)
                    for t in range(TT):
                        last = nc.tensor.transpose(bank[:, 6 + j % 2, t * P:(t + 1) * P],
                                                   hot[:, t, 2 * j:2 * j + 2].rearrange("p e s -> p (e s)"), ident[:])
                    last.then_inc(hot_turned, 1)
                pe.wait_ge(xe_ready, 2 * KT)
                pe.wait_ge(scatter_ready, EXPERTS // 2)

                def experts(i):
                    def hidden(m):
                        s, e = m % 2, m // FC
                        pe.wait_ge(in_loaded[s], 32 * (FC * i + m // 2 + 1))
                        pe.wait_ge(xs_ready[e], i + 1)
                        if m >= 2:
                            pe.wait_ge(act_ready, 2 * FC * i + m - 1)
                        for k in range(KT):
                            for g in range(2):
                                last = nc.tensor.matmul(bank[64 * g:64 * g + 64, s], xs[:, e, k], w_in[:, s, g, k],
                                                        start=(k == 0), stop=(k == KT - 1))
                        last.then_inc(in_used[s], 1)

                    def output(m):
                        s, e, c = m % 2, m // FC, m % FC
                        pe.wait_ge(act_ready, 2 * FC * i + m + 1)
                        if m >= 2:
                            pe.wait_ge(act_t_ready, 2 * FC * i + m - 1)
                        for j in range(FT):
                            last = nc.tensor.transpose(bank[:, 2 + s, j * P:(j + 1) * P],
                                                       hot_flat[:, s * HALF + j * P:s * HALF + (j + 1) * P], ident[:])
                        last.then_inc(act_turned, 1)
                        pe.wait_ge(act_t_ready, 2 * FC * i + m + 1)
                        pe.wait_ge(out_loaded[s], 16 * (FC * i + m // 2 + 1))
                        if c == 0:
                            pe.wait_ge(y_ready, 2 * i + e)
                        for j in range(FT):
                            for h in range(2):
                                last = nc.tensor.matmul(bank[64 * e:64 * e + 64, 4 + h], act_t[:, s, j],
                                                        w_out[:, s, j, h * 512:(h + 1) * 512],
                                                        start=(c == 0 and j == 0), stop=(c == FC - 1 and j == FT - 1))
                        last.then_inc(out_used[s], 1)

                    for m in range(2 * FC):
                        hidden(m)
                        if m >= 1:
                            output(m - 1)
                    output(2 * FC - 1)
                    pe.wait_ge(y_ready, 2 * i + 2)
                    for m in range(KT):
                        if m >= 2:
                            pe.wait_ge(part_added, KT * i + m - 1)
                        nc.tensor.matmul(bank[:, 6 + m % 2], ye[:, m * P:(m + 1) * P],
                                         scatter[:, bass.ds(i, 1), :].rearrange("p a t -> p (a t)"),
                                         start=True, stop=True).then_inc(part_made, 1)

                pairs(pe, experts)

            @block.scalar
            def _(act):
                act.wait_ge(route, 3)
                nc.scalar.activation(logits[:], logits[:], ACT.Exp).then_inc(exp_ready, 1)
                for n in range(2 * TT):
                    act.wait_ge(z_turned, n + 1)
                    nc.scalar.copy(z_tok[:, n // 2, 512 * (n % 2):512 * (n % 2) + 512], bank[:, 2 + n % 2]).then_inc(
                        z_tok_ready, 1)
                for n in range(2 * KT):
                    act.wait_ge(xe_made, n + 1)
                    nc.scalar.copy(xe[:, n % KT, 512 * (n // KT):512 * (n // KT) + 512], bank[:, 4 + n % 2]).then_inc(
                        xe_ready, 1)
                for j in range(EXPERTS // 2):
                    act.wait_ge(hot_turned, j + 1)
                    nc.scalar.copy(scatter[:, j], bank[:, 6 + j % 2]).then_inc(scatter_ready, 1)

                act.wait_ge(xe_ready, 2 * KT)
                act.dma_start(acc, x_dram.rearrange("(m p) t -> p m t", p=P)).then_inc(x_loaded, 16)

                def experts(i):
                    for m in range(2 * FC):
                        s = m % 2
                        act.wait_ge(in_used[s], FC * i + m // 2 + 1)
                        if m >= 2:
                            act.wait_ge(act_turned, 2 * FC * i + m - 1)
                        nc.scalar.activation(sg[:, s], bank[0:CAPACITY, s], ACT.Silu).then_inc(silu_ready, 1)
                        act.wait_ge(act_turned, 2 * FC * i + m + 1)
                        if m >= 2:
                            act.wait_ge(out_used[s], FC * i + m // 2)
                        nc.scalar.copy(act_t[:, s], bank[:, 2 + s].rearrange("p (j n) -> p j n", j=FT)[:, :, 0:CAPACITY]).then_inc(
                            act_t_ready, 1)

                pairs(act, experts)

            @block.vector
            def _(dve):
                nc.vector.memset(ones[:], 1.0).then_inc(route, 1)
                done = [1]

                def step(ins):
                    ins.then_inc(route, 1)
                    done[0] += 1
                    dve.wait_ge(route, done[0])

                wide = [P, TT, EXPERTS]
                dve.wait_ge(logits_made, 1)
                raw = bank[:, 0, 0:TT * EXPERTS].rearrange("p (t e) -> p t e", t=TT)
                step(nc.vector.tensor_reduce(high[:], raw, X, ALU.max))
                step(nc.vector.tensor_tensor(logits[:], raw, high[:].unsqueeze(2).broadcast_to(wide), ALU.subtract))
                dve.wait_ge(exp_ready, 1)
                step(nc.vector.tensor_reduce(high[:], logits[:], X, ALU.add))
                step(nc.vector.reciprocal(high[:], high[:]))
                step(nc.vector.tensor_tensor(affinity[:], logits[:], high[:].unsqueeze(2).broadcast_to(wide), ALU.mult))
                assert done[0] == MOE_AFFINITY, done[0]
                dve.wait_ge(aff_turned, 1)
                step(nc.vector.tensor_copy(left[:], bank[0:EXPERTS, 1]))
                for _ in range(CAPACITY // 8):
                    step(nc.vector.max(best[:], left[:]))
                    step(nc.vector.match_replace(left[:], best[:], left[:], -1.0))
                step(nc.vector.tensor_scalar(chosen[:], left[:], 0.0, None, ALU.is_lt))
                step(nc.vector.tensor_tensor_scan(left[:], ones[:], chosen[:], 0.0, ALU.mult, ALU.add))
                step(nc.vector.tensor_tensor(chosen[:], chosen[:], left[:], ALU.mult))
                assert done[0] == MOE_PLACES, done[0]
                dve.wait_ge(place_turned, 1)
                step(nc.vector.tensor_copy(place_tok[:], raw))
                grid = [P, EXPERTS, CAPACITY]
                for t in range(TT):
                    nc.vector.tensor_tensor(hot[:, t], slots[:].unsqueeze(1).broadcast_to(grid),
                                            place_tok[:, t].unsqueeze(2).broadcast_to(grid), ALU.is_equal).then_inc(
                        hot_ready, 1)
                dve.wait_ge(xe_made, 2 * KT)
                dve.wait_ge(hot_ready, TT)
                for t in range(TT):
                    nc.vector.tensor_tensor(hot[:, t], hot[:, t], affinity[:, t].unsqueeze(2).broadcast_to(grid),
                                            ALU.mult).then_inc(weighted, 1)
                dve.wait_ge(x_loaded, 16)

                def experts(i):
                    for e in range(2):
                        for c in range(FC):
                            m = FC * e + c
                            s = m % 2
                            dve.wait_ge(silu_ready, 2 * FC * i + m + 1)
                            nc.vector.tensor_tensor(sg[:, s], sg[:, s], bank[64:64 + CAPACITY, s], ALU.mult).then_inc(
                                act_ready, 1)
                        dve.wait_ge(out_used[1], FC * i + FC // 2 * (e + 1))
                        dve.wait_ge(part_made, KT * i)
                        nc.vector.tensor_copy(ye[64 * e:64 * e + 64, :].rearrange("p (h d) -> p h d", h=2),
                                              bank[64 * e:64 * e + 64, 4:6, :]).then_inc(y_ready, 1)
                    for m in range(KT):
                        dve.wait_ge(part_made, KT * i + m + 1)
                        dve.wait_ge(part_added, KT * i)
                        nc.vector.tensor_tensor(acc[:, m], acc[:, m], bank[:, 6 + m % 2], ALU.add).then_inc(part_added, 1)

                pairs(dve, experts)


MOE_AFFINITY = 6
MOE_PLACES = MOE_AFFINITY + 1 + 2 * (CAPACITY // 8) + 3


D_FF = 2816
N_MEM = 256
NA_WIDTH = 384
MEM_WIDTH = 256


def two_blocks(nc, d, out_dram):
    STAGE_TURN.clear()

    def scratch(name, rows, cols):
        return nc.dram_tensor(name, (rows, cols), F32, kind="Internal").ap()

    z = scratch("z", D_MODEL, LEN)
    p = scratch("p", 5 * D_MODEL + 2 * D_MODEL, LEN)
    ya_raw = scratch("ya_raw", D_MODEL, LEN)
    ya = scratch("ya", D_MODEL, LEN)
    yb = scratch("yb", D_MODEL, LEN)
    gated_a = scratch("gated_a", D_MODEL, LEN)
    merged = scratch("merged", D_MODEL, LEN)
    h1 = scratch("h1", D_MODEL, LEN)
    z1 = scratch("z1", D_MODEL, LEN)
    a1 = scratch("a1", D_FF, LEN)
    h2 = scratch("h2", D_MODEL, LEN)
    rmsnorm(nc, "norm_mix", d["h"], d["mix_norm_g"], z)
    project(nc, "in", z, d["w_in"], p)
    s5(nc, "s5", p[0:D_MODEL], d["ssm_lam"], d["ssm_bc"], d["ssm_d"], d["ident"], ya_raw)
    project(nc, "glu", ya_raw, d["ssm_w_glu"], ya, "glu", [ya_raw])
    hgrn2(nc, "hgrn", p[D_MODEL:5 * D_MODEL], d["hgrn_lb"], d["hgrn_norm_g"], d["ident"], d["hgrn_causal"],
          d["hgrn_member"], yb)
    project(nc, "ssm_proj", ya, d["w_ssm_proj"], gated_a, "gate", [p[5 * D_MODEL:6 * D_MODEL]])
    project(nc, "hgrn_proj", yb, d["w_hgrn_proj"], merged, "gate_add", [p[6 * D_MODEL:7 * D_MODEL], gated_a])
    project(nc, "mix_out", merged, d["w_out"], h1, "add", [d["h"]])
    rmsnorm(nc, "norm_ffn", h1, d["ffn_norm_g"], z1)
    conv_gated_up(nc, "up", z1, d["w_up"], d["conv_w"], d["conv_b"], a1)
    project(nc, "down", a1, d["w_down"], h2, "add", [h1])

    x = scratch("x", D_MODEL, SEQ)
    z2 = scratch("z2", D_MODEL, SEQ)
    mem_z = scratch("mem_z", D_MODEL, N_MEM)
    widths = [3 * NA_WIDTH, 3 * RW_WIDTH + 2 * P, MEM_WIDTH, D_MODEL, D_MODEL, D_MODEL]
    starts = [sum(widths[:n]) for n in range(len(widths) + 1)]
    p2 = scratch("p2", starts[-1], SEQ)
    p_na, p_rw, q_mem, g_na, g_rw, g_mem = (p2[starts[n]:starts[n + 1]] for n in range(len(widths)))
    kv = scratch("kv", 2 * MEM_WIDTH, N_MEM)
    y_na = scratch("y_na", NA_WIDTH, SEQ)
    y_rw = scratch("y_rw", RW_WIDTH, SEQ)
    y_mem = scratch("y_mem", MEM_WIDTH, SEQ)
    m_na = scratch("m_na", D_MODEL, SEQ)
    m_rw = scratch("m_rw", D_MODEL, SEQ)
    m_all = scratch("m_all", D_MODEL, SEQ)
    x3 = scratch("x3", D_MODEL, SEQ)
    z3 = scratch("z3", D_MODEL, SEQ)
    x4 = scratch("x4", D_MODEL, SEQ)
    rmsnorm(nc, "norm_final", h2[:, N_META:], d["final_norm_g"], x)
    rmsnorm(nc, "norm_mix_2", x, d["norm_mix_g_2"], z2)
    rmsnorm(nc, "norm_mem_2", d["mem"], d["norm_mem_g_2"], mem_z)
    project(nc, "in_2", z2, d["w_in_2"], p2)
    project(nc, "mem_kv", mem_z, d["w_mem_kv_2"], kv)
    attention(nc, "na", p_na[0:NA_WIDTH], p_na[NA_WIDTH:2 * NA_WIDTH], p_na[2 * NA_WIDTH:], d["na_bias"],
              d["ident"], y_na)
    attention(nc, "mem", q_mem, kv[0:MEM_WIDTH], kv[MEM_WIDTH:], None, d["ident"], y_mem)
    rwkv7(nc, "rw", p_rw, d["rw_par"], d["rw_mu_l"], d["rw_lora"], d["rw_g2_2"], d["ident"], d["rw_masks"],
          d["rw_member"], d["eye2"], y_rw)
    project(nc, "na_proj", y_na, d["w_branch_na_2"], m_na, "gate", [g_na])
    project(nc, "rw_proj", y_rw, d["w_branch_rw_2"], m_rw, "gate_add", [g_rw, m_na])
    project(nc, "mem_proj", y_mem, d["w_branch_mem_2"], m_all, "gate_add", [g_mem, m_rw])
    project(nc, "mix_out_2", m_all, d["w_out_2"], x3, "add", [x])
    rmsnorm(nc, "norm_ffn_2", x3, d["norm_ffn_g_2"], z3)
    expert_ffn(nc, "moe", z3, x3, d["w_router_2"], d["w_exp_gate_2"], d["w_exp_up_2"], d["w_exp_down_2"],
               d["ident"], d["slots"], x4)
    rmsnorm(nc, "norm_final_2", x4, d["norm_final_g_2"], out_dram)


def by_partition(a):
    return np.ascontiguousarray(a.reshape(-1, P).T)


def by_state(a):
    a = a.reshape(PAIRS, 2, SSM_STATE, *a.shape[2:])
    return np.moveaxis(a, 0, 2).reshape(P, PAIRS, *a.shape[3:])


def laid_out(v):
    d = {}
    d["h"] = np.concatenate([v["meta_tokens"], v["x"][0]], axis=0).T
    d["mem"] = v["mem_2"][0].T
    for name in ("mix_norm_g", "ffn_norm_g", "final_norm_g", "norm_mix_g_2", "norm_mem_g_2", "norm_ffn_g_2",
                 "norm_final_g_2"):
        d[name] = by_partition(v[name].reshape(-1))
    for name in ("w_in", "ssm_w_glu", "w_ssm_proj", "w_hgrn_proj", "w_out", "w_up", "w_down", "w_in_2", "w_mem_kv_2",
                 "w_branch_na_2", "w_branch_rw_2", "w_branch_mem_2", "w_out_2", "w_router_2", "w_exp_gate_2",
                 "w_exp_up_2", "w_exp_down_2", "rw_g2_2"):
        d[name] = v[name][0]
    log_dt = np.broadcast_to(v["ssm_log_dt"][0][:, None], (SSM_GROUPS, SSM_STATE))
    d["ssm_lam"] = np.stack([by_state(a) for a in (v["ssm_lambda_re"][0], v["ssm_lambda_im"][0], log_dt)], 1)
    d["ssm_bc"] = np.stack([by_state(a) for a in (
        v["ssm_b_re"][0], v["ssm_b_im"][0], v["ssm_c_re"][0].transpose(0, 2, 1), v["ssm_c_im"][0].transpose(0, 2, 1))], 1)
    d["ssm_d"] = by_partition(v["ssm_d"][0])
    d["hgrn_lb"] = v["hgrn_lb_logits"].reshape(2, HEADS, P).transpose(2, 0, 1)
    d["hgrn_norm_g"] = v["hgrn_norm_g"][0].reshape(P, 1)
    d["conv_w"] = v["conv_w"][0].reshape(3, 2 * D_FF // P, P).transpose(2, 1, 0)
    d["conv_b"] = by_partition(v["conv_b"][0])
    d["na_bias"] = window_bias(v["na_rpb_2"][0])
    rw = {name: v[f"rw_{name}_2"][0] for name in ("mu_rkv", "mu_w", "mu_a", "w0", "w2", "a0", "a2", "k_k", "k_a", "r_k",
                                                 "ln_g", "ln_b")}
    columns = [rw["mu_rkv"][dd, j] for j in range(3) for dd in range(2)] + [rw["w0"][dd] for dd in range(2)] + [
        rw["a0"][dd] for dd in range(2)] + [rw["k_k"], rw["k_a"], rw["r_k"].reshape(-1), rw["ln_g"], rw["ln_b"]]
    d["rw_par"] = np.stack([c.reshape(RW_X, P) for c in columns]).transpose(2, 0, 1)
    d["rw_mu_l"] = np.concatenate([rw["mu_w"], rw["mu_a"]], 1).T
    d["rw_lora"] = np.concatenate([rw["w2"], rw["a2"]], 1).transpose(1, 0, 2)
    n = np.arange(P)
    f32 = np.float32
    d["ident"] = np.eye(P, dtype=f32)
    d["eye2"] = np.concatenate([np.eye(HEAD_DIM, dtype=f32)] * 2)
    d["slots"] = np.broadcast_to(np.arange(1, CAPACITY + 1, dtype=f32), (P, CAPACITY))
    s, t = n[:, None], n[None, :]
    d["hgrn_causal"] = ((s // HCHUNK == t // HCHUNK) & (s <= t)).astype(f32)
    d["hgrn_member"] = np.broadcast_to((s // HCHUNK == np.arange(P // HCHUNK))[:, :, None],
                                       (P, P // HCHUNK, P)).astype(f32)
    same = s // RCHUNK == t // RCHUNK
    d["rw_masks"] = np.stack([np.stack([same & (s < t), same & (s <= t)] * 2, 1),
                              np.stack([same & (s > t), same & (s >= t)] * 2, 1)], 1).astype(f32)
    d["rw_member"] = np.broadcast_to((s // RCHUNK == np.arange(P // RCHUNK))[:, :, None],
                                     (P, P // RCHUNK, P)).astype(f32)
    return {name: np.ascontiguousarray(a) for name, a in d.items()}


def kernel(**inputs):
    import concourse.bacc as bacc
    from concourse.bass_utils import run_bass_kernel_spmd

    arrays = laid_out({name: np.asarray(a) for name, a in inputs.items()})
    nc = bacc.Bacc("TRN2", target_bir_lowering=False, num_devices=1)
    ins = {name: nc.dram_tensor(f"in_{name}", a.shape, mybir.dt.from_np(a.dtype), kind="ExternalInput").ap()
           for name, a in arrays.items()}
    out = nc.dram_tensor("out", (D_MODEL, SEQ), F32, kind="ExternalOutput").ap()
    two_blocks(nc, ins, out)
    r = run_bass_kernel_spmd(nc, [{f"in_{name}": a for name, a in arrays.items()}], core_ids=[0])
    return np.ascontiguousarray(r.results[0]["out"].T).reshape(1, SEQ, D_MODEL)
```

```python
from contextlib import ExitStack

import numpy as np

import concourse.bass as bass
from concourse import mybir

P = 128
ALU = mybir.AluOpType
ACT = mybir.ActivationFunctionType
F32 = mybir.dt.float32
X = mybir.AxisListType.X

D_MODEL = 1024
KT = D_MODEL // P
SEQ = 512
N_META = 16
LEN = SEQ + N_META
EPS = 1e-6


STAGE_TURN = []


def opener(nc, ctx, stage):
    free = sorted(nc.free_semaphores)
    half = len(free) // 2
    STAGE_TURN.append(stage)
    own = free[:half] if len(STAGE_TURN) % 2 else free[half:2 * half]
    sems = []

    def close():
        nc.gpsimd.sem_clear(range(own[0], own[0] + len(sems)))
        for s in sems:
            nc.release_semaphore(s)

    ctx.callback(close)

    def sb(name, shape, dt=F32):
        return ctx.enter_context(nc.sbuf_tensor(f"{stage}_{name}", shape, dt))

    def ps(name, shape):
        return ctx.enter_context(nc.psum_tensor(f"{stage}_{name}", shape, F32))

    def sem(name):
        sems.append(nc.alloc_semaphore(f"{stage}_{name}", num=own[0] + len(sems)))
        return sems[-1]

    return sb, ps, sem


def rmsnorm(nc, stage, x_dram, gain_dram, out_dram):
    C, T = x_dram.shape
    kt = C // P
    halves = 1 if T <= 512 else 2
    w = T // halves
    with ExitStack() as ctx:
        sb, ps, sem = opener(nc, ctx, stage)
        x = sb("x", [P, kt, T])
        sq = sb("sq", [P, kt, T])
        gain = sb("gain", [P, kt])
        ones = sb("ones", [P, P])
        scale = sb("scale", [P, T])
        eps = sb("eps", [P, 1])
        total = ps("total", [P, halves, 512])
        x_loaded = [sem(f"x_loaded{k}") for k in range(kt)]
        gain_loaded = sem("gain_loaded")
        consts_ready = sem("consts_ready")
        squared = sem("squared")
        summed = sem("summed")
        meaned = sem("meaned")
        inverted = sem("inverted")
        rooted = sem("rooted")
        scaled = sem("scaled")
        stored = sem("stored")
        xv = x_dram.rearrange("(k p) t -> p k t", p=P)
        ov = out_dram.rearrange("(k p) t -> p k t", p=P)
        total_v = total[:, :, 0:w]

        with nc.Block() as block:

            @block.sync
            def _(sp):
                for k in range(kt):
                    sp.dma_start(x[:, k, :], xv[:, k, :]).then_inc(x_loaded[k], 16)
                sp.dma_start(gain[:], gain_dram).then_inc(gain_loaded, 16)
                for k in range(kt):
                    sp.wait_ge(scaled, k + 1)
                    sp.dma_start(ov[:, k, :], x[:, k, :]).then_inc(stored, 16)
                sp.wait_ge(stored, 16 * kt)

            @block.scalar
            def _(act):
                for k in range(kt):
                    act.wait_ge(x_loaded[k], 16)
                    nc.scalar.activation(sq[:, k, :], x[:, k, :], ACT.Square).then_inc(squared, 1)
                act.wait_ge(inverted, 1)
                nc.scalar.activation(scale[:], scale[:], ACT.Sqrt).then_inc(rooted, 1)

            @block.tensor
            def _(pe):
                pe.wait_ge(consts_ready, 2)
                for k in range(kt):
                    pe.wait_ge(squared, k + 1)
                    for h in range(halves):
                        last = nc.tensor.matmul(total[:, h, 0:w], ones[:], sq[:, k, h * w:(h + 1) * w],
                                                start=(k == 0), stop=(k == kt - 1))
                last.then_inc(summed, 1)

            @block.vector
            def _(dve):
                nc.vector.memset(ones[:], 1.0).then_inc(consts_ready, 1)
                nc.vector.memset(eps[:], EPS).then_inc(consts_ready, 1)
                dve.wait_ge(summed, 1)
                nc.vector.tensor_scalar(scale[:].rearrange("p (h t) -> p h t", h=halves), total_v,
                                        1.0 / C, EPS, ALU.mult, ALU.add).then_inc(meaned, 1)
                dve.wait_ge(meaned, 1)
                nc.vector.reciprocal(scale[:], scale[:]).then_inc(inverted, 1)
                dve.wait_ge(rooted, 1)
                dve.wait_ge(gain_loaded, 16)
                for k in range(kt):
                    dve.wait_ge(x_loaded[k], 16)
                    dve.wait_ge(squared, k + 1)
                    nc.vector.scalar_tensor_tensor(x[:, k, :], x[:, k, :], gain[:, k:k + 1], scale[:],
                                                   ALU.mult, ALU.mult).then_inc(scaled, 1)


F32R = mybir.dt.float32r


def three_passes(nc, to, w_high, w_low, x_high, x_low, start, stop):
    nc.tensor.matmul(to, w_high, x_low, start=start, stop=False)
    nc.tensor.matmul(to, w_low, x_high, start=False, stop=False)
    return nc.tensor.matmul(to, w_high, x_high, start=False, stop=stop)


def project(nc, stage, x_dram, w_dram, out_dram, epilogue="copy", extras=(), width=2 * P, gain_dram=None):
    K, T = x_dram.shape
    M = w_dram.shape[1]
    kt = K // P
    nm = width // P
    slots = M // width
    halves = 1 if T <= 512 else 2
    w_t = T // halves
    n_extra = len(extras)
    norm = gain_dram is not None
    assert not norm or epilogue == "copy"
    RAW = min(kt, 8)
    with ExitStack() as ctx:
        sb, ps, sem = opener(nc, ctx, stage)
        x_raw = sb("x_raw", [P, RAW, T])
        x_high = sb("x_high", [P, kt, T], F32R)
        x_low = sb("x_low", [P, kt, T], F32R)
        w = sb("w", [P, 2, kt, width])
        w_high = sb("w_high", [P, 2, kt, width], F32R)
        w_low = sb("w_low", [P, 2, kt, width], F32R)
        out = sb("out", [P, 2, nm, T])
        if n_extra:
            e = sb("e", [P, 2, n_extra, nm, T])
        if epilogue in ("glu", "gate", "gate_add"):
            gate = sb("gate", [P, 2, nm, T])
        if norm:
            gain = sb("gain", [P, kt])
            sq = sb("sq", [P, 2, T])
            ones = sb("ones", [P, P])
            scale = sb("scale", [P, halves, w_t])
            gain_loaded = sem("gain_loaded")
            ones_ready = sem("ones_ready")
            squared = sem("squared")
            summed = sem("summed")
            meaned = sem("meaned")
            inverted = sem("inverted")
            rooted = sem("rooted")
        y = ps("y", [P, 2, nm, halves, 512])
        x_loaded = [sem(f"x_loaded{k}") for k in range(kt)]
        x_high_ready = sem("x_high_ready")
        x_ready = sem("x_ready")
        w_loaded = [sem(f"w_loaded{s}") for s in range(2)]
        w_high_ready = sem("w_high_ready")
        w_ready = sem("w_ready")
        e_loaded = [sem(f"e_loaded{s}") for s in range(2)]
        y_ready = sem("y_ready")
        gate_ready = sem("gate_ready")
        mul_ready = sem("mul_ready")
        out_ready = sem("out_ready")
        stored = [sem(f"stored{s}") for s in range(2)]
        xv = x_dram.rearrange("(k p) t -> p k t", p=P)
        wv = w_dram.rearrange("(k p) m -> p k m", p=P)
        ov = out_dram.rearrange("(m p) t -> p m t", p=P)
        ev = [a.rearrange("(m p) t -> p m t", p=P) for a in extras]

        def y_of(s):
            return y[:, s, :, :, 0:w_t].rearrange("p m h t -> p (m h) t")

        def flat(a):
            return a.rearrange("p m (h t) -> p (m h) t", h=halves)

        def over_slots(eng, body):
            loops = slots // 2
            for s in range(min(2, slots)):
                body(0, s, True, s == slots - 1)
            end = loops - 1 if slots % 2 == 0 else loops
            if end > 1:
                with eng.Fori(1, end) as i:
                    for s in range(2):
                        body(i, s, False, False)
            for n in range(2 * max(end, 1), slots):
                body(n // 2, n % 2, False, n == slots - 1)

        with nc.Block() as block:

            @block.sync
            def _(sp):
                def load_w(i, s, first, last):
                    if not first:
                        sp.wait_ge(w_ready, 2 * i + s - 1)
                    sp.dma_start(w[:, s], wv[:, :, bass.ds((2 * i + s) * width, width)]).then_inc(w_loaded[s], 16)
                    for n in range(n_extra):
                        if not first and n == 0:
                            sp.wait_ge(out_ready, 2 * i + s - 1)
                        sp.dma_start(e[:, s, n], ev[n][:, bass.ds((2 * i + s) * nm, nm), :]).then_inc(e_loaded[s], 16)
                    if first and s == 1:
                        for k in range(RAW, kt):
                            sp.wait_ge(x_ready, k - RAW + 1)
                            sp.dma_start(x_raw[:, k % RAW, :], xv[:, k, :]).then_inc(x_loaded[k], 16)

                if norm:
                    sp.dma_start(gain[:], gain_dram).then_inc(gain_loaded, 16)
                over_slots(sp, load_w)

            @block.tensor
            def _(pe):
                if norm:
                    pe.wait_ge(ones_ready, 1)

                def products(i, s, first, last):
                    pe.wait_ge(w_ready, 2 * i + s + 1)
                    if not first:
                        pe.wait_ge(out_ready, 2 * i + s - 1)
                    if norm and first and s == 1:
                        pe.wait_ge(meaned, 1)
                    for m in range(nm):
                        for h in range(halves):
                            for k in range(kt):
                                if first and s == 0 and m == 0 and h == 0:
                                    pe.wait_ge(x_ready, k + 1)
                                    if norm:
                                        pe.wait_ge(squared, k + 1)
                                        for b in range(halves):
                                            one = nc.tensor.matmul(y[:, 1, 0, b, 0:w_t], ones[:],
                                                                   sq[:, k % 2, b * w_t:(b + 1) * w_t],
                                                                   start=(k == 0), stop=(k == kt - 1))
                                        one.then_inc(summed, 1)
                                tokens = slice(h * w_t, (h + 1) * w_t)
                                columns = slice(m * P, (m + 1) * P)
                                done = three_passes(nc, y[:, s, m, h, 0:w_t], w_high[:, s, k, columns],
                                                    w_low[:, s, k, columns], x_high[:, k, tokens],
                                                    x_low[:, k, tokens], k == 0, k == kt - 1)
                    done.then_inc(y_ready, 1)

                over_slots(pe, products)

            @block.scalar
            def _(act):
                def split_x_high(k):
                    act.wait_ge(x_loaded[k], 16)
                    if norm:
                        if k >= 2:
                            act.wait_ge(summed, k - 1)
                        nc.scalar.activation(sq[:, k % 2, :], x_raw[:, k], ACT.Square).then_inc(squared, 1)
                        act.wait_ge(gain_loaded, 16)
                        nc.scalar.activation(x_high[:, k], x_raw[:, k], ACT.Copy, scale=gain[:, k:k + 1]).then_inc(
                            x_high_ready, 1)
                    else:
                        nc.scalar.copy(x_high[:, k], x_raw[:, k % RAW]).then_inc(x_high_ready, 1)

                def split_w_high(i, s, fresh):
                    act.wait_ge(w_loaded[s], (i + 1) * 16)
                    if not fresh:
                        act.wait_ge(y_ready, 2 * i + s - 1)
                    nc.scalar.copy(w_high[:, s], w[:, s]).then_inc(w_high_ready, 1)

                for k in range(RAW):
                    act.dma_start(x_raw[:, k, :], xv[:, k, :]).then_inc(x_loaded[k], 16)
                split_x_high(0)
                split_w_high(0, 0, True)
                for k in range(1, kt):
                    split_x_high(k)

                def evacuate(i, s, first, last):
                    if not last:
                        split_w_high(i + (s + 1) // 2, (s + 1) % 2, first and s == 0)
                    if epilogue == "copy" and not norm:
                        act.wait_ge(y_ready, 2 * i + s + 1)
                        if not first:
                            act.wait_ge(stored[s], i * 16)
                        nc.scalar.copy(flat(out[:, s]), y_of(s)).then_inc(out_ready, 1)
                    elif epilogue == "glu":
                        act.wait_ge(y_ready, 2 * i + s + 1)
                        if not first:
                            act.wait_ge(out_ready, 2 * i + s - 1)
                        nc.scalar.activation(flat(gate[:, s]), y_of(s), ACT.Sigmoid).then_inc(gate_ready, 1)
                    elif epilogue in ("gate", "gate_add"):
                        act.wait_ge(e_loaded[s], (i + 1) * 16 * n_extra)
                        if not first:
                            act.wait_ge(out_ready, 2 * i + s - 1)
                        nc.scalar.activation(gate[:, s], e[:, s, 0], ACT.Sigmoid).then_inc(gate_ready, 1)
                    act.wait_ge(out_ready, 2 * i + s + 1)
                    act.dma_start(ov[:, bass.ds((2 * i + s) * nm, nm), :], out[:, s]).then_inc(stored[s], 16)

                if norm:
                    act.wait_ge(inverted, 1)
                    nc.scalar.activation(scale[:], scale[:], ACT.Sqrt).then_inc(rooted, 1)
                over_slots(act, evacuate)
                for s in range(2):
                    if (slots + 1 - s) // 2:
                        act.wait_ge(stored[s], 16 * ((slots + 1 - s) // 2))

            @block.vector
            def _(dve):
                if norm:
                    nc.vector.memset(ones[:], 1.0).then_inc(ones_ready, 1)
                    dve.wait_ge(gain_loaded, 16)

                def split_w_low(i, s, fresh):
                    dve.wait_ge(w_high_ready, 2 * i + s + 1)
                    if not fresh:
                        dve.wait_ge(y_ready, 2 * i + s - 1)
                    nc.vector.tensor_tensor(w_low[:, s], w[:, s], w_high[:, s].bitcast(F32), ALU.subtract).then_inc(
                        w_ready, 1)

                for k in range(kt):
                    if k == 1:
                        split_w_low(0, 0, True)
                    dve.wait_ge(x_high_ready, k + 1)
                    high = x_high[:, k].bitcast(F32)
                    if norm:
                        nc.vector.scalar_tensor_tensor(x_low[:, k], x_raw[:, k], gain[:, k:k + 1], high, ALU.mult,
                                                       ALU.subtract).then_inc(x_ready, 1)
                    else:
                        nc.vector.tensor_tensor(x_low[:, k], x_raw[:, k % RAW], high, ALU.subtract).then_inc(x_ready, 1)
                if norm:
                    dve.wait_ge(summed, kt)
                    nc.vector.tensor_scalar(scale[:], y[:, 1, 0, :, 0:w_t], 1.0 / K, EPS, ALU.mult, ALU.add).then_inc(
                        meaned, 1)
                    dve.wait_ge(meaned, 1)
                    nc.vector.reciprocal(scale[:], scale[:]).then_inc(inverted, 1)

                def finish(i, s, first, last):
                    if not last:
                        split_w_low(i + (s + 1) // 2, (s + 1) % 2, first and s == 0)
                    if epilogue == "copy" and not norm:
                        return
                    dve.wait_ge(y_ready, 2 * i + s + 1)
                    if n_extra:
                        dve.wait_ge(e_loaded[s], (i + 1) * 16 * n_extra)
                    if epilogue in ("glu", "gate", "gate_add"):
                        dve.wait_ge(gate_ready, 2 * i + s + 1)
                    if not first:
                        dve.wait_ge(stored[s], i * 16)
                    if norm:
                        if first and s == 0:
                            dve.wait_ge(rooted, 1)
                        for m in range(nm):
                            done = nc.vector.tensor_tensor(
                                out[:, s, m].rearrange("p (h t) -> p h t", h=halves), y[:, s, m, :, 0:w_t], scale[:],
                                ALU.mult)
                        done.then_inc(out_ready, 1)
                    elif epilogue == "glu":
                        nc.vector.tensor_tensor(out[:, s], gate[:, s], e[:, s, 0], ALU.mult).then_inc(out_ready, 1)
                    elif epilogue == "gate":
                        nc.vector.tensor_tensor(flat(out[:, s]), y_of(s), flat(gate[:, s]), ALU.mult).then_inc(out_ready, 1)
                    elif epilogue == "gate_add":
                        nc.vector.tensor_tensor(flat(out[:, s]), y_of(s), flat(gate[:, s]), ALU.mult).then_inc(mul_ready, 1)
                        dve.wait_ge(mul_ready, 2 * i + s + 1)
                        nc.vector.tensor_tensor(out[:, s], out[:, s], e[:, s, 1], ALU.add).then_inc(out_ready, 1)
                    elif epilogue == "add":
                        nc.vector.tensor_tensor(flat(out[:, s]), y_of(s), flat(e[:, s, 0]), ALU.add).then_inc(out_ready, 1)

                over_slots(dve, finish)


def conv_gated_up(nc, stage, x_dram, gain_dram, w_dram, conv_w_dram, conv_b_dram, out_dram):
    K, T = x_dram.shape
    kt = K // P
    FT = w_dram.shape[1] // (2 * P)
    halves, hw = 2, T // 2
    with ExitStack() as ctx:
        sb, ps, sem = opener(nc, ctx, stage)
        x = sb("x", [P, kt, T])
        x_high = sb("x_high", [P, kt, T], F32R)
        x_low = sb("x_low", [P, kt, T], F32R)
        gain = sb("gain", [P, kt])
        sq = sb("sq", [P, 2, T])
        ones = sb("ones", [P, P])
        scale = sb("scale", [P, halves, hw])
        w = sb("w", [P, 2, 2, kt, P])
        w_high = sb("w_high", [P, 2, 2, kt, P], F32R)
        w_low = sb("w_low", [P, 2, 2, kt, P], F32R)
        conv_w = sb("conv_w", [P, 2 * FT, 3])
        conv_b = sb("conv_b", [P, 2 * FT])
        y = sb("y", [P, 2, 2, T + 2])
        u = sb("u", [P, 2, 2, T])
        gate = sb("gate", [P, 2, T])
        out = sb("out", [P, 2, T])
        prod = ps("prod", [P, 2, 2, halves, 512])
        x_loaded = [sem(f"x_loaded{k}") for k in range(kt)]
        gain_loaded = sem("gain_loaded")
        squared = sem("squared")
        summed = sem("summed")
        meaned = sem("meaned")
        inverted = sem("inverted")
        rooted = sem("rooted")
        x_high_ready = sem("x_high_ready")
        x_ready = sem("x_ready")
        w_high_ready = sem("w_high_ready")
        w_ready = sem("w_ready")
        conv_loaded = sem("conv_loaded")
        w_loaded = [sem(f"w_loaded{s}") for s in range(2)]
        prod_ready = sem("prod_ready")
        consts_ready = sem("consts_ready")
        y_ready = sem("y_ready")
        first_tap = sem("first_tap")
        taps_done = sem("taps_done")
        gate_ready = sem("gate_ready")
        out_ready = sem("out_ready")
        stored = [sem(f"stored{s}") for s in range(2)]
        xv = x_dram.rearrange("(k p) t -> p k t", p=P)
        wv = w_dram.rearrange("(k p) m -> p k m", p=P)

        def over_tiles(eng, body):
            body(0, 0, True, False)
            body(0, 1, True, False)
            with eng.Fori(1, FT // 2 - 1) as i:
                body(i, 0, False, False)
                body(i, 1, False, False)
            body(FT // 2 - 1, 0, False, False)
            body(FT // 2 - 1, 1, False, True)

        with nc.Block() as block:

            @block.sync
            def _(sp):
                def load(i, s, first, last):
                    if not first:
                        sp.wait_ge(w_ready, 2 * i + s - 1)
                    for g in range(2):
                        sp.dma_start(w[:, s, g], wv[:, :, bass.ds(g * FT * P + (2 * i + s) * P, P)]).then_inc(w_loaded[s], 16)

                sp.dma_start(gain[:], gain_dram).then_inc(gain_loaded, 16)
                over_tiles(sp, load)

            @block.tensor
            def _(pe):
                pe.wait_ge(consts_ready, 2)

                def products(i, s, first, last):
                    pe.wait_ge(w_ready, 2 * i + s + 1)
                    if not first:
                        pe.wait_ge(y_ready, 2 * i + s - 1)
                    if first and s == 1:
                        pe.wait_ge(meaned, 1)
                    for g in range(2):
                        for h in range(halves):
                            for k in range(kt):
                                if first and s == 0 and g == 0 and h == 0:
                                    pe.wait_ge(x_ready, k + 1)
                                    pe.wait_ge(squared, k + 1)
                                    for b in range(halves):
                                        one = nc.tensor.matmul(prod[:, 1, 0, b, 0:hw], ones[:],
                                                               sq[:, k % 2, b * hw:(b + 1) * hw],
                                                               start=(k == 0), stop=(k == kt - 1))
                                    one.then_inc(summed, 1)
                                tokens = slice(h * hw, (h + 1) * hw)
                                done = three_passes(nc, prod[:, s, g, h, 0:hw], w_high[:, s, g, k], w_low[:, s, g, k],
                                                    x_high[:, k, tokens], x_low[:, k, tokens], k == 0, k == kt - 1)
                    done.then_inc(prod_ready, 1)

                over_tiles(pe, products)

            @block.scalar
            def _(act):
                for k in range(kt):
                    act.dma_start(x[:, k, :], xv[:, k, :]).then_inc(x_loaded[k], 16)
                act.dma_start(conv_w[:], conv_w_dram).then_inc(conv_loaded, 16)
                act.dma_start(conv_b[:], conv_b_dram).then_inc(conv_loaded, 16)

                def split_w_high(i, s, fresh):
                    act.wait_ge(w_loaded[s], (i + 1) * 32)
                    if not fresh:
                        act.wait_ge(prod_ready, 2 * i + s - 1)
                    nc.scalar.copy(w_high[:, s], w[:, s]).then_inc(w_high_ready, 1)

                act.wait_ge(gain_loaded, 16)
                for k in range(kt):
                    if k == 1:
                        split_w_high(0, 0, True)
                    act.wait_ge(x_loaded[k], 16)
                    if k >= 2:
                        act.wait_ge(summed, k - 1)
                    nc.scalar.activation(sq[:, k % 2, :], x[:, k], ACT.Square).then_inc(squared, 1)
                    nc.scalar.activation(x_high[:, k], x[:, k], ACT.Copy, scale=gain[:, k:k + 1]).then_inc(
                        x_high_ready, 1)
                act.wait_ge(inverted, 1)
                nc.scalar.activation(scale[:], scale[:], ACT.Sqrt).then_inc(rooted, 1)
                act.wait_ge(conv_loaded, 32)

                def tile_of(i, s, first, last):
                    t = 2 * i + s
                    if not last:
                        split_w_high(i + (s + 1) // 2, (s + 1) % 2, first and s == 0)
                    act.wait_ge(y_ready, t + 1)
                    if not first:
                        act.wait_ge(out_ready, t - 1)
                    for g in range(2):
                        nc.scalar.activation(u[:, s, g], y[:, s, g, 0:T], ACT.Identity,
                                             bias=conv_b[:, bass.ds(g * FT + t, 1)],
                                             scale=conv_w[:, bass.ds(g * FT + t, 1), 0]).then_inc(first_tap, 1)
                    act.wait_ge(taps_done, 4 * t + 4)
                    nc.scalar.activation(gate[:, s], u[:, s, 0], ACT.Silu).then_inc(gate_ready, 1)
                    act.wait_ge(out_ready, t + 1)
                    act.dma_start(out_dram[bass.ds(t * P, P), :], out[:, s]).then_inc(stored[s], 16)

                over_tiles(act, tile_of)
                for s in range(2):
                    act.wait_ge(stored[s], 16 * (FT // 2))

            @block.vector
            def _(dve):
                nc.vector.memset(y[:], 0.0).then_inc(consts_ready, 1)
                nc.vector.memset(ones[:], 1.0).then_inc(consts_ready, 1)
                dve.wait_ge(consts_ready, 2)
                dve.wait_ge(gain_loaded, 16)

                def split_w_low(i, s, fresh):
                    dve.wait_ge(w_high_ready, 2 * i + s + 1)
                    if not fresh:
                        dve.wait_ge(prod_ready, 2 * i + s - 1)
                    nc.vector.tensor_tensor(w_low[:, s], w[:, s], w_high[:, s].bitcast(F32), ALU.subtract).then_inc(
                        w_ready, 1)

                for k in range(kt):
                    if k == 1:
                        split_w_low(0, 0, True)
                    dve.wait_ge(x_high_ready, k + 1)
                    nc.vector.scalar_tensor_tensor(x_low[:, k], x[:, k], gain[:, k:k + 1], x_high[:, k].bitcast(F32),
                                                   ALU.mult, ALU.subtract).then_inc(x_ready, 1)
                dve.wait_ge(summed, kt)
                nc.vector.tensor_scalar(scale[:], prod[:, 1, 0, :, 0:hw], 1.0 / K, EPS, ALU.mult, ALU.add).then_inc(
                    meaned, 1)
                dve.wait_ge(meaned, 1)
                nc.vector.reciprocal(scale[:], scale[:]).then_inc(inverted, 1)

                def tile_of(i, s, first, last):
                    t = 2 * i + s
                    if not last:
                        split_w_low(i + (s + 1) // 2, (s + 1) % 2, first and s == 0)
                    dve.wait_ge(prod_ready, t + 1)
                    if first and s == 0:
                        dve.wait_ge(rooted, 1)
                    if not first:
                        dve.wait_ge(first_tap, 2 * t - 2)
                        dve.wait_ge(taps_done, 4 * t - 4)
                    for g in range(2):
                        done = nc.vector.tensor_tensor(y[:, s, g, 2:].rearrange("p (h t) -> p h t", h=halves),
                                                       prod[:, s, g, :, 0:hw], scale[:], ALU.mult)
                    done.then_inc(y_ready, 1)
                    dve.wait_ge(y_ready, t + 1)
                    for j in (1, 2):
                        for g in range(2):
                            if j == 1:
                                dve.wait_ge(first_tap, 2 * t + g + 1)
                            else:
                                dve.wait_ge(taps_done, 4 * t + g + 1)
                            nc.vector.scalar_tensor_tensor(u[:, s, g], y[:, s, g, j:j + T],
                                                           conv_w[:, bass.ds(g * FT + t, 1), j], u[:, s, g],
                                                           ALU.mult, ALU.add).then_inc(taps_done, 1)
                    dve.wait_ge(taps_done, 4 * t + 4)
                    dve.wait_ge(gate_ready, t + 1)
                    if not first:
                        dve.wait_ge(stored[s], i * 16)
                    nc.vector.tensor_tensor(out[:, s], gate[:, s], u[:, s, 1], ALU.mult).then_inc(out_ready, 1)

                over_tiles(dve, tile_of)


SSM_GROUP = 16
SSM_STATE = 64
SSM_GROUPS = D_MODEL // SSM_GROUP
CHUNK = 8
CHUNKS = LEN // CHUNK
PAIRS = SSM_GROUPS // 2
TWO_PI = 2.0 * float(np.pi)
TWO_PI_A = 6.28125
TWO_PI_B = float(np.float32(np.round((TWO_PI - TWO_PI_A) * 2.0 ** 20) / 2.0 ** 20))
TWO_PI_C = float(np.float32(TWO_PI - TWO_PI_A - TWO_PI_B))
ROUNDER = 1.5 * 2.0 ** 23
PI_BELOW = 3.1415925


def s5(nc, stage, u_dram, lam_dram, bc_dram, d_dram, ident_dram, out_dram):
    R_LEN = (CHUNKS - 1) * CHUNK + 1
    BATCH = 8
    BATCHES = SSM_GROUPS // BATCH
    RE, IM = 0, 1
    with ExitStack() as ctx:
        sb, ps, sem = opener(nc, ctx, stage)
        lam = sb("lam", [P, 3, PAIRS])
        bc = sb("bc", [P, 4, PAIRS, SSM_GROUP])
        d_skip = sb("d_skip", [P, KT])
        ident = sb("ident", [P, P])
        small = sb("small", [P, 24, PAIRS])
        tmp = sb("tmp", [P, 2, PAIRS, SSM_GROUP])
        bb = sb("bb", [P, 2, PAIRS, SSM_GROUP])
        wb = sb("wb", [P, 2, PAIRS, CHUNK, SSM_GROUP])
        ca = sb("ca", [P, 2, PAIRS, CHUNK + 1, SSM_GROUP])
        wbt = sb("wbt", [P, 2, 2, P])
        shifted = sb("shifted", [P, 2, BATCH, R_LEN])
        u = sb("u", [P, SSM_GROUPS, CHUNKS])
        toep = sb("toep", [P, SSM_GROUPS, CHUNK, SSM_GROUP])
        state = sb("state", [P, 2, PAIRS, CHUNKS + 1])
        prod = sb("prod", [P, 2, 2, PAIRS])
        wb_flat = wb[:].rearrange("p r q k h -> p (r q k h)")
        taps = wb_flat[0:SSM_GROUP, :].rearrange("h (g n) -> h g n", g=SSM_GROUPS)
        y_tok = wb_flat[0:CHUNKS, :].rearrange("c (t m) -> c t m", t=CHUNK)
        work = shifted[:].rearrange("p s g t -> p (s g t)")
        u_tile = work[:, 0:2 * LEN].rearrange("p (s t) -> p s t", s=2)
        y_tile = work[:, 2 * LEN:4 * LEN].rearrange("p (s t) -> p s t", s=2)
        o_tile = work[:, 4 * LEN:6 * LEN].rearrange("p (s t) -> p s t", s=2)
        bank = ps("bank", [P, 8, 512])

        params_loaded = sem("params_loaded")
        toep_zeroed = sem("toep_zeroed")
        u_loaded = [sem(f"u_loaded{s}") for s in range(2)]
        u_packed = sem("u_packed")
        dt_ready = sem("dt_ready")
        exponent_ready = sem("exponent_ready")
        mag_ready = sem("mag_ready")
        angle_ready = sem("angle_ready")
        sin_ready = sem("sin_ready")
        setup = sem("setup")
        wb_turned = sem("wb_turned")
        wbt_ready = sem("wbt_ready")
        input_ready = sem("input_ready")
        state_filled = sem("state_filled")
        scanned = sem("scanned")
        taps_made = sem("taps_made")
        taps_ready = sem("taps_ready")
        toep_ready = sem("toep_ready")
        y_made = sem("y_made")
        y_ready = sem("y_ready")
        y_turned = sem("y_turned")
        ut_loaded = [sem(f"ut_loaded{s}") for s in range(2)]
        skipped = sem("skipped")
        gelu_done = sem("gelu_done")
        stored = [sem(f"stored{s}") for s in range(2)]

        lr, li, ldt = lam[:, 0], lam[:, 1], lam[:, 2]
        (dt, expo, ang, cyc, red, half, mag, sn, snh, a_re, a_im, den, nr, co_re, co_im, t0, t1,
         s_re, s_im, s2_re, s2_im) = (small[:, n] for n in range(21))

        def over_h(a):
            return a.unsqueeze(2).broadcast_to([P, PAIRS, SSM_GROUP])

        def half_of(t, e):
            return t[64 * e:64 * e + 64]

        with nc.Block() as block:

            @block.sync
            def _(sp):
                sp.dma_start(lam[:], lam_dram).then_inc(params_loaded, 16)
                sp.dma_start(bc[:], bc_dram).then_inc(params_loaded, 16)
                sp.dma_start(d_skip[:], d_dram).then_inc(params_loaded, 16)
                sp.dma_start(ident[:], ident_dram).then_inc(params_loaded, 16)
                for b in range(BATCHES):
                    if b >= 2:
                        sp.wait_ge(u_packed, b - 1)
                    rows = u_dram[b * BATCH * SSM_GROUP:(b + 1) * BATCH * SSM_GROUP, :].rearrange(
                        "(g h) t -> h g t", h=SSM_GROUP)
                    for j in range(CHUNK):
                        sp.dma_start(shifted[16 * j:16 * j + 16, b % 2], rows[:, :, 7 - j:7 - j + R_LEN]).then_inc(
                            u_loaded[b % 2], 16)
                sp.wait_ge(taps_ready, PAIRS // 2)
                sp.wait_ge(toep_zeroed, 1)
                for j in range(CHUNK):
                    s = 7 - j
                    sp.dma_start(toep[16 * j:16 * j + 16, :, s:, :].rearrange("h g t m -> h g (t m)"),
                                 taps[:, :, 0:(CHUNK - s) * SSM_GROUP]).then_inc(toep_ready, 16)
                sp.wait_ge(toep_ready, 16 * CHUNK)
                sp.wait_ge(u_packed, BATCHES)
                for m in range(KT):
                    if m >= 2:
                        sp.wait_ge(skipped, m - 1)
                    sp.dma_start(u_tile[:, m % 2], u_dram[m * P:(m + 1) * P, :]).then_inc(ut_loaded[m % 2], 16)
                    if m >= 1:
                        sp.wait_ge(gelu_done, m)
                        sp.dma_start(out_dram[(m - 1) * P:m * P, :], o_tile[:, (m - 1) % 2]).then_inc(
                            stored[(m - 1) % 2], 16)
                sp.wait_ge(gelu_done, KT)
                sp.dma_start(out_dram[(KT - 1) * P:, :], o_tile[:, (KT - 1) % 2]).then_inc(stored[(KT - 1) % 2], 16)
                for s in range(2):
                    sp.wait_ge(stored[s], 16 * KT // 2)

            @block.gpsimd
            def _(pool):
                nc.gpsimd.memset(toep[:], 0.0).then_inc(toep_zeroed, 1)
                for b in range(BATCHES):
                    pool.wait_ge(u_loaded[b % 2], 16 * CHUNK * (b // 2 + 1))
                    nc.gpsimd.tensor_copy(u[:, b * BATCH:(b + 1) * BATCH, :],
                                          shifted[:, b % 2, :, 0:R_LEN:CHUNK]).then_inc(u_packed, 1)

            @block.vector
            def _(dve):
                done = [0]

                def count(n):
                    done[0] += n

                def step(ins):
                    ins.then_inc(setup, 1)
                    count(1)
                    dve.wait_ge(setup, done[0])

                def tt(out, a, b, op):
                    step(nc.vector.tensor_tensor(out, a, b, op))

                def mul_complex(o_re, o_im, x_re, x_im, w_re, w_im, w1, w2):
                    nc.vector.tensor_tensor(o_re, x_re, w_re, ALU.mult).then_inc(setup, 1)
                    nc.vector.tensor_tensor(w1, x_im, w_im, ALU.mult).then_inc(setup, 1)
                    nc.vector.tensor_tensor(o_im, x_re, w_im, ALU.mult).then_inc(setup, 1)
                    nc.vector.tensor_tensor(w2, x_im, w_re, ALU.mult).then_inc(setup, 1)
                    count(4)
                    dve.wait_ge(setup, done[0])
                    nc.vector.tensor_tensor(o_re, o_re, w1, ALU.subtract).then_inc(setup, 1)
                    nc.vector.tensor_tensor(o_im, o_im, w2, ALU.add).then_inc(setup, 1)
                    count(2)
                    dve.wait_ge(setup, done[0])

                step(nc.vector.memset(state[:, :, :, 0:1], 0.0))
                dve.wait_ge(params_loaded, 64)
                dve.wait_ge(dt_ready, 1)
                nc.vector.tensor_tensor(expo, lr, dt, ALU.mult).then_inc(exponent_ready, 1)
                tt(ang, li, dt, ALU.mult)
                step(nc.vector.tensor_scalar(cyc, ang, 1.0 / TWO_PI, ROUNDER, ALU.mult, ALU.add))
                step(nc.vector.tensor_scalar(cyc, cyc, -ROUNDER, None, ALU.add))
                step(nc.vector.scalar_tensor_tensor(red, cyc, -TWO_PI_A, ang, ALU.mult, ALU.add))
                step(nc.vector.scalar_tensor_tensor(red, cyc, -TWO_PI_B, red, ALU.mult, ALU.add))
                step(nc.vector.scalar_tensor_tensor(red, cyc, -TWO_PI_C, red, ALU.mult, ALU.add))
                step(nc.vector.tensor_scalar(red, red, PI_BELOW, -PI_BELOW, ALU.min, ALU.max))
                nc.vector.tensor_scalar(half, red, 0.5, None, ALU.mult).then_inc(angle_ready, 1)
                dve.wait_ge(sin_ready, 2)
                dve.wait_ge(mag_ready, 1)
                tt(t0, snh, snh, ALU.mult)
                step(nc.vector.tensor_scalar(t0, t0, -2.0, 1.0, ALU.mult, ALU.add))
                tt(a_re, mag, t0, ALU.mult)
                tt(a_im, mag, sn, ALU.mult)
                tt(den, lr, lr, ALU.mult)
                tt(t1, li, li, ALU.mult)
                tt(den, den, t1, ALU.add)
                step(nc.vector.reciprocal(den, den))
                step(nc.vector.tensor_scalar(nr, a_re, -1.0, None, ALU.add))
                tt(co_re, nr, lr, ALU.mult)
                tt(t0, a_im, li, ALU.mult)
                tt(co_re, co_re, t0, ALU.add)
                tt(co_re, co_re, den, ALU.mult)
                tt(co_im, a_im, lr, ALU.mult)
                tt(t0, nr, li, ALU.mult)
                tt(co_im, co_im, t0, ALU.subtract)
                tt(co_im, co_im, den, ALU.mult)
                w1, w2 = tmp[:, 0], tmp[:, 1]
                mul_complex(bb[:, RE], bb[:, IM], bc[:, 0], bc[:, 1], over_h(co_re), over_h(co_im), w1, w2)
                mul_complex(s_re, s_im, a_re, a_im, a_re, a_im, t0, t1)
                mul_complex(s2_re, s2_im, s_re, s_im, s_re, s_im, t0, t1)
                mul_complex(s_re, s_im, s2_re, s2_im, s2_re, s2_im, t0, t1)
                step(nc.vector.tensor_copy(wb[:, :, :, 0, :], bb[:]))
                for k in range(CHUNK - 1):
                    mul_complex(wb[:, RE, :, k + 1, :], wb[:, IM, :, k + 1, :], wb[:, RE, :, k, :], wb[:, IM, :, k, :],
                                over_h(a_re), over_h(a_im), w1, w2)
                wb_done = done[0]
                assert wb_done == S5_WB_DONE, wb_done
                step(nc.vector.tensor_copy(ca[:, RE, :, 0, :], bc[:, 2]))
                step(nc.vector.tensor_scalar(ca[:, IM, :, 0, :], bc[:, 3], -1.0, None, ALU.mult))
                step(nc.vector.tensor_scalar(t0, a_im, -1.0, None, ALU.mult))
                for k in range(CHUNK):
                    mul_complex(ca[:, RE, :, k + 1, :], ca[:, IM, :, k + 1, :], ca[:, RE, :, k, :], ca[:, IM, :, k, :],
                                over_h(a_re), over_h(t0), w1, w2)
                assert done[0] == S5_CA_DONE, done[0]
                for q in range(PAIRS):
                    dve.wait_ge(input_ready, q + 1)
                    nc.vector.tensor_copy(state[:, :, q, 1:], bank[:, 4 + q % 4, 0:2 * CHUNKS].rearrange(
                        "p (r c) -> p r c", r=2)).then_inc(state_filled, 1)
                dve.wait_ge(state_filled, PAIRS)
                wide = [P, 2, PAIRS]
                n = 0

                def with_step(*instructions):
                    nonlocal n
                    for ins in instructions:
                        ins.then_inc(scanned, 1)
                        n += 1
                    dve.wait_ge(scanned, n)

                for c in range(1, CHUNKS):
                    with_step(
                        nc.vector.tensor_tensor(prod[:, 0], state[:, :, :, c], s_re.unsqueeze(1).broadcast_to(wide), ALU.mult),
                        nc.vector.tensor_tensor(prod[:, 1], state[:, :, :, c], s_im.unsqueeze(1).broadcast_to(wide), ALU.mult))
                    with_step(nc.vector.tensor_tensor(state[:, :, :, c + 1], state[:, :, :, c + 1], prod[:, 0], ALU.add))
                    with_step(
                        nc.vector.tensor_tensor(state[:, RE, :, c + 1], state[:, RE, :, c + 1], prod[:, 1, IM], ALU.subtract),
                        nc.vector.tensor_tensor(state[:, IM, :, c + 1], state[:, IM, :, c + 1], prod[:, 1, RE], ALU.add))
                for m in range(KT):
                    dve.wait_ge(y_turned, m + 1)
                    dve.wait_ge(ut_loaded[m % 2], 16 * (m // 2 + 1))
                    if m >= 2:
                        dve.wait_ge(gelu_done, m - 1)
                    for b in range(2):
                        ins = nc.vector.scalar_tensor_tensor(
                            y_tile[:, m % 2].rearrange("p (c t) -> p t c", t=CHUNK)[:, 4 * b:4 * b + 4, :],
                            u_tile[:, m % 2].rearrange("p (c t) -> p t c", t=CHUNK)[:, 4 * b:4 * b + 4, :],
                            d_skip[:, m:m + 1],
                            bank[:, 2 * (m % 2) + b, 0:4 * CHUNKS].rearrange("p (t c) -> p t c", t=4),
                            ALU.mult, ALU.add)
                    ins.then_inc(skipped, 1)

            @block.scalar
            def _(act):
                act.wait_ge(params_loaded, 64)
                nc.scalar.activation(dt, ldt, ACT.Exp).then_inc(dt_ready, 1)
                act.wait_ge(exponent_ready, 1)
                nc.scalar.activation(mag, expo, ACT.Exp).then_inc(mag_ready, 1)
                act.wait_ge(angle_ready, 1)
                nc.scalar.activation(sn, red, ACT.Sin).then_inc(sin_ready, 1)
                nc.scalar.activation(snh, half, ACT.Sin).then_inc(sin_ready, 1)
                for q in range(PAIRS):
                    act.wait_ge(wb_turned, q + 1)
                    if q >= 2:
                        act.wait_ge(input_ready, q - 1)
                    nc.scalar.copy(wbt[:, q % 2], bank[:, q % 2, 0:2 * P].rearrange("p (r n) -> p r n", r=2)).then_inc(
                        wbt_ready, 1)
                for b in range(PAIRS // 2):
                    act.wait_ge(taps_made, b + 1)
                    e, q0 = b % 2, 4 * (b // 2)
                    g0 = 2 * q0 + e
                    nc.scalar.copy(taps[:, g0:g0 + 7:2, :], bank[0:SSM_GROUP, 2 + b % 2, :].rearrange(
                        "h (g n) -> h g n", g=4)).then_inc(taps_ready, 1)
                for b in range(SSM_GROUPS // 4):
                    act.wait_ge(y_made, b + 1)
                    if b == 0:
                        act.wait_ge(wb_turned, PAIRS)
                    for n in range(4):
                        g = 2 * (4 * (b // 2) + n) + b % 2
                        ins = nc.scalar.copy(y_tok[:, :, SSM_GROUP * g:SSM_GROUP * (g + 1)],
                                             bank[0:CHUNKS, 4 + b % 4, n * P:(n + 1) * P].rearrange(
                                                 "c (t h) -> c t h", t=CHUNK))
                    ins.then_inc(y_ready, 1)
                for m in range(KT):
                    act.wait_ge(skipped, m + 1)
                    if m >= 2:
                        act.wait_ge(stored[m % 2], 16 * (m // 2))
                    nc.scalar.activation(o_tile[:, m % 2], y_tile[:, m % 2], ACT.Gelu_apprx_tanh).then_inc(gelu_done, 1)

            @block.tensor
            def _(pe):
                pe.wait_ge(params_loaded, 64)
                pe.wait_ge(setup, S5_WB_DONE)

                def turn(q):
                    if q >= 2:
                        pe.wait_ge(wbt_ready, q - 1)
                    for r in (RE, IM):
                        last = nc.tensor.transpose(bank[:, q % 2, r * P:(r + 1) * P],
                                                   wb[:, r, q].rearrange("p k h -> p (k h)"), ident[:])
                    last.then_inc(wb_turned, 1)

                def chunk_inputs(q):
                    pe.wait_ge(wbt_ready, q + 1)
                    if q % (BATCH // 2) == 0:
                        pe.wait_ge(u_packed, 2 * q // BATCH + 1)
                    if q >= 4:
                        pe.wait_ge(state_filled, q - 3)
                    for e in range(2):
                        for r in (RE, IM):
                            last = nc.tensor.matmul(bank[64 * e:64 * e + 64, 4 + q % 4, r * CHUNKS:(r + 1) * CHUNKS],
                                                    wbt[:, q % 2, r, 64 * e:64 * e + 64], u[:, 2 * q + e, :],
                                                    start=True, stop=True)
                    last.then_inc(input_ready, 1)

                turn(0)
                for q in range(PAIRS):
                    if q + 1 < PAIRS:
                        turn(q + 1)
                    chunk_inputs(q)
                pe.wait_ge(setup, S5_CA_DONE)
                for b in range(PAIRS // 2):
                    e, q0 = b % 2, 4 * (b // 2)
                    if b >= 2:
                        pe.wait_ge(taps_ready, b - 1)
                    for n in range(4):
                        for r in (RE, IM):
                            last = nc.tensor.matmul(
                                bank[0:SSM_GROUP, 2 + b % 2, n * P:(n + 1) * P], half_of(bb, e)[:, r, q0 + n, :],
                                half_of(ca, e)[:, r, q0 + n, 0:CHUNK, :].rearrange("p k h -> p (k h)"),
                                start=(r == RE), stop=(r == IM))
                    last.then_inc(taps_made, 1)
                pe.wait_ge(toep_ready, 16 * CHUNK)
                pe.wait_ge(state_filled, PAIRS)
                pe.wait_ge(scanned, 5 * (CHUNKS - 1))
                for b in range(SSM_GROUPS // 4):
                    e, q0 = b % 2, 4 * (b // 2)
                    if b >= 4:
                        pe.wait_ge(y_ready, b - 3)
                    for n in range(4):
                        q = q0 + n
                        to = bank[0:CHUNKS, 4 + b % 4, n * P:(n + 1) * P]
                        nc.tensor.matmul(to, u[:, 2 * q + e, :], toep[:, 2 * q + e].rearrange("p t h -> p (t h)"),
                                         start=True, stop=False)
                        for r in (RE, IM):
                            last = nc.tensor.matmul(to, half_of(state, e)[:, r, q, 0:CHUNKS],
                                                    half_of(ca, e)[:, r, q, 1:, :].rearrange("p k h -> p (k h)"),
                                                    start=False, stop=(r == IM))
                    last.then_inc(y_made, 1)
                pe.wait_ge(y_ready, SSM_GROUPS // 4)
                for m in range(KT):
                    if m >= 2:
                        pe.wait_ge(skipped, m - 1)
                    for t in range(CHUNK):
                        last = nc.tensor.transpose(
                            bank[:, 2 * (m % 2) + t // 4, (t % 4) * CHUNKS:(t % 4 + 1) * CHUNKS],
                            y_tok[:, t, m * P:(m + 1) * P], ident[0:CHUNKS, 0:CHUNKS])
                    last.then_inc(y_turned, 1)


S5_WB_DONE = 1 + 24 + 6 * 4 + 1 + 6 * (CHUNK - 1)
S5_CA_DONE = S5_WB_DONE + 3 + 6 * CHUNK


HEADS = 8
HCHUNK = 16
HCHUNKS = LEN // HCHUNK


def hgrn2(nc, stage, p_dram, lb_dram, gain_dram, ident_dram, causal_dram, member_dram, out_dram):
    tiles = [P] * (LEN // P) + ([LEN % P] if LEN % P else [])
    nt = len(tiles)
    per_tile = P // HCHUNK
    RING = 3 * per_tile
    units = [(h, i) for h in range(HEADS) for i in range(nt)]
    U = len(units)
    with ExitStack() as ctx:
        sb, ps, sem = opener(nc, ctx, stage)
        q = sb("q", [P, HEADS, LEN])
        f = sb("f", [P, HEADS, LEN])
        v = sb("v", [P, HEADS, LEN])
        og = sb("og", [P, HEADS, LEN])
        o = sb("o", [P, HEADS, LEN])
        cum = sb("cum", [P, 2, LEN])
        rest = sb("rest", [P, 2, LEN])
        e_up = sb("e_up", [P, 2, LEN])
        e_down = sb("e_down", [P, 2, LEN])
        e_rest = sb("e_rest", [P, 2, LEN])
        k_in = sb("k_in", [P, 2, LEN])
        k_out = sb("k_out", [P, 2, LEN])
        decay = sb("decay", [P, HEADS, HCHUNKS])
        resets = sb("resets", [P, LEN])
        lb = sb("lb", [P, 2, HEADS])
        low = sb("low", [P, 2, HEADS])
        gain = sb("gain", [P, 1])
        ident = sb("ident", [P, P])
        ones = sb("ones", [P, P])
        causal = sb("causal", [P, P])
        member = sb("member", [P, per_tile, P])
        turned = sb("turned", [P, 3, 2, P])
        v_by_chunk = sb("v_by_chunk", [P, 2, per_tile, P])
        scores = sb("scores", [P, 3, P])
        states = sb("states", [P, RING, P])
        sq = sb("sq", [P, 2, P])
        root = sb("root", [P, 2, P])
        eps = sb("eps", [P, 1])
        bank = ps("bank", [P, 8, 512])

        params_loaded = sem("params_loaded")
        loaded = [sem(f"loaded{h}") for h in range(HEADS)]
        consts_ready = sem("consts_ready")
        eps_ready = sem("eps_ready")
        bound_diff = sem("bound_diff")
        bound_sig = sem("bound_sig")
        bound_ready = sem("bound_ready")
        sig_ready = sem("sig_ready")
        f_ready = sem("f_ready")
        log_ready = sem("log_ready")
        cum_ready = sem("cum_ready")
        rest_ready = sem("rest_ready")
        k_ready = sem("k_ready")
        exps_ready = sem("exps_ready")
        decay_ready = sem("decay_ready")
        qk_ready = sem("qk_ready")
        turn_made = sem("turn_made")
        turn_ready = sem("turn_ready")
        split_ready = sem("split_ready")
        scores_made = sem("scores_made")
        scores_ready = sem("scores_ready")
        kv_made = sem("kv_made")
        state_ready = sem("state_ready")
        o_made = sem("o_made")
        o_ready = sem("o_ready")
        gate_ready = sem("gate_ready")
        summed = sem("summed")
        rooted = sem("rooted")
        inverted = sem("inverted")
        normed = sem("normed")
        out_ready = sem("out_ready")
        stored = sem("stored")

        def rows(part, h):
            at = part * D_MODEL + h * P
            return p_dram[at:at + P, :]

        def span(i):
            return slice(i * P, i * P + tiles[i])

        def chunks_of(i):
            return tiles[i] // HCHUNK

        def states_before(n):
            return sum(chunks_of(i) for _, i in units[:n])

        def by_chunk(a):
            return a.rearrange("p (c t) -> p c t", t=HCHUNK)

        with nc.Block() as block:

            @block.sync
            def _(sp):
                for dst, src in ((lb, lb_dram), (gain, gain_dram), (ident, ident_dram), (causal, causal_dram),
                                 (member, member_dram)):
                    sp.dma_start(dst[:], src).then_inc(params_loaded, 16)
                for h in range(HEADS):
                    for part, dst in ((1, f), (0, q), (2, v), (3, og)):
                        sp.dma_start(dst[:, h], rows(part, h)).then_inc(loaded[h], 16)
                for h in range(HEADS):
                    sp.wait_ge(out_ready, nt * (h + 1))
                    sp.dma_start(out_dram[h * P:(h + 1) * P, :], o[:, h]).then_inc(stored, 16)
                sp.wait_ge(stored, 16 * HEADS)

            @block.scalar
            def _(act):
                act.wait_ge(bound_diff, 1)
                nc.scalar.activation(low[:, 0], low[:, 1], ACT.Sigmoid).then_inc(bound_sig, 1)

                def sigmoid(h):
                    act.wait_ge(loaded[h], 64)
                    nc.scalar.activation(f[:, h], f[:, h], ACT.Sigmoid).then_inc(sig_ready, 1)

                def output_gate(h):
                    nc.scalar.activation(og[:, h], og[:, h], ACT.Silu).then_inc(gate_ready, 1)

                def log(h):
                    act.wait_ge(f_ready, h + 1)
                    if h >= 2:
                        act.wait_ge(exps_ready, 3 * (h - 1))
                    nc.scalar.activation(rest[:, h % 2], f[:, h], ACT.Ln).then_inc(log_ready, 1)

                def exponentials(h):
                    s = h % 2
                    act.wait_ge(cum_ready, h + 1)
                    if h >= 2:
                        act.wait_ge(qk_ready, 3 * (h - 1))
                        act.wait_ge(decay_ready, h - 1)
                    nc.scalar.activation(e_up[:, s], cum[:, s], ACT.Exp).then_inc(exps_ready, 1)
                    nc.scalar.activation(e_down[:, s], cum[:, s], ACT.Exp, scale=-1.0).then_inc(exps_ready, 1)
                    act.wait_ge(rest_ready, h + 1)
                    nc.scalar.activation(e_rest[:, s], rest[:, s], ACT.Exp).then_inc(exps_ready, 1)

                sigmoid(0)
                sigmoid(1)
                log(0)
                log(1)
                exponentials(0)
                exponentials(1)
                for n in range(U + 3):
                    if n < U:
                        h, i = units[n]
                        m = tiles[i]
                        act.wait_ge(turn_made, n + 1)
                        if n >= 3:
                            act.wait_ge(o_made, n - 2)
                        nc.scalar.copy(turned[0:m, n % 3], bank[0:m, n % 2, 0:2 * P].rearrange("p (a n) -> p a n", a=2)).then_inc(
                            turn_ready, 1)
                    if n >= 3:
                        m = tiles[units[n - 3][1]]
                        act.wait_ge(summed, n - 2)
                        act.wait_ge(eps_ready, 1)
                        if n >= 5:
                            act.wait_ge(normed, n - 4)
                        nc.scalar.activation(root[:, (n - 3) % 2, 0:m], bank[:, 3, P:P + m], ACT.Sqrt,
                                             bias=eps[:, 0:1], scale=1.0 / P).then_inc(rooted, 1)
                    if 2 <= n < U + 2:
                        h, i = units[n - 2]
                        act.wait_ge(o_made, n - 1)
                        nc.scalar.copy(o[:, h, span(i)], bank[:, 3, 0:tiles[i]])
                        nc.scalar.activation(sq[:, n % 2, 0:tiles[i]], bank[:, 3, 0:tiles[i]], ACT.Square).then_inc(
                            o_ready, 1)
                    if n < U:
                        h, i = units[n]
                        if i == 0 and 1 <= h < HEADS - 1:
                            log(h + 1)
                        if i == 1 and h == 0:
                            sigmoid(2)
                            for a in range(3):
                                output_gate(a)
                        if i == 2 and 1 <= h < HEADS - 1:
                            exponentials(h + 1)
                        if i == 3 and h + 3 < HEADS:
                            sigmoid(h + 3)
                            output_gate(h + 3)

            @block.gpsimd
            def _(pool):
                def prepare(h):
                    s = h % 2
                    pool.wait_ge(k_ready, h + 1)
                    pool.wait_ge(exps_ready, 3 * (h + 1))
                    if h >= 2:
                        pool.wait_ge(turn_made, nt * (h - 1))
                        pool.wait_ge(scores_made, nt * (h - 1))
                    nc.gpsimd.tensor_tensor(q[:, h], q[:, h], e_up[:, s], ALU.mult).then_inc(qk_ready, 1)
                    nc.gpsimd.tensor_tensor(k_in[:, s], f[:, h], e_down[:, s], ALU.mult).then_inc(qk_ready, 1)
                    nc.gpsimd.tensor_tensor(k_out[:, s], f[:, h], e_rest[:, s], ALU.mult).then_inc(qk_ready, 1)

                pool.wait_ge(params_loaded, 80)
                prepare(0)
                prepare(1)
                for n, (h, i) in enumerate(units):
                    m, c = tiles[i], chunks_of(i)
                    pool.wait_ge(turn_ready, n + 1)
                    if n >= 2:
                        pool.wait_ge(kv_made, n - 1)
                    nc.gpsimd.tensor_tensor(v_by_chunk[0:m, n % 2, 0:c], member[0:m, 0:c],
                                            turned[0:m, n % 3, 1].unsqueeze(1).broadcast_to([m, c, P]),
                                            ALU.mult).then_inc(split_ready, 1)
                    if i == 3 and 1 <= h < HEADS - 1:
                        prepare(h + 1)

            @block.vector
            def _(dve):
                nc.vector.memset(ones[:], 1.0).then_inc(consts_ready, 1)
                nc.vector.memset(resets[:], 1.0).then_inc(consts_ready, 1)
                nc.vector.memset(eps[:], EPS).then_inc(eps_ready, 1)
                dve.wait_ge(consts_ready, 2)
                nc.vector.memset(by_chunk(resets[:])[:, :, 0:1], 0.0).then_inc(consts_ready, 1)
                dve.wait_ge(params_loaded, 80)
                nc.vector.tensor_tensor(low[:, 1], lb[:, 0], lb[:, 1], ALU.subtract).then_inc(bound_diff, 1)
                dve.wait_ge(bound_sig, 1)
                nc.vector.tensor_scalar(low[:, 1], low[:, 0], -1.0, 1.0, ALU.mult, ALU.add).then_inc(bound_ready, 1)
                dve.wait_ge(bound_ready, 1)
                dve.wait_ge(consts_ready, 3)

                def bounded(h):
                    dve.wait_ge(sig_ready, h + 1)
                    nc.vector.tensor_scalar(f[:, h], f[:, h], low[:, 1, h:h + 1], low[:, 0, h:h + 1],
                                            ALU.mult, ALU.add).then_inc(f_ready, 1)

                def sums(h):
                    s = h % 2
                    dve.wait_ge(log_ready, h + 1)
                    if h >= 2:
                        dve.wait_ge(exps_ready, 3 * (h - 1))
                    nc.vector.tensor_tensor_scan(cum[:, s], resets[:], rest[:, s], 0.0, ALU.mult, ALU.add).then_inc(
                        cum_ready, 1)
                    nc.vector.tensor_scalar(f[:, h], f[:, h], -1.0, 1.0, ALU.mult, ALU.add).then_inc(k_ready, 1)
                    dve.wait_ge(cum_ready, h + 1)
                    nc.vector.tensor_tensor(by_chunk(rest[:, s]),
                                            by_chunk(cum[:, s])[:, :, HCHUNK - 1:].broadcast_to([P, HCHUNKS, HCHUNK]),
                                            by_chunk(cum[:, s]), ALU.subtract).then_inc(rest_ready, 1)

                def chunk_decay(h):
                    dve.wait_ge(exps_ready, 3 * h + 1)
                    nc.vector.tensor_copy(decay[:, h], e_up[:, h % 2, HCHUNK - 1::HCHUNK]).then_inc(decay_ready, 1)

                def masked_scores(n):
                    m = tiles[units[n][1]]
                    dve.wait_ge(scores_made, n + 1)
                    nc.vector.tensor_tensor(scores[0:m, n % 3, 0:m], bank[0:m, 2, 0:m], causal[0:m, 0:m],
                                            ALU.mult).then_inc(scores_ready, 1)

                def finish(n):
                    h, i = units[n]
                    m = tiles[i]
                    dve.wait_ge(rooted, n + 1)
                    nc.vector.reciprocal(root[:, n % 2, 0:m], root[:, n % 2, 0:m]).then_inc(inverted, 1)
                    dve.wait_ge(inverted, n + 1)
                    nc.vector.scalar_tensor_tensor(o[:, h, span(i)], o[:, h, span(i)], gain[:, 0:1],
                                                   root[:, n % 2, 0:m], ALU.mult, ALU.mult).then_inc(normed, 1)
                    dve.wait_ge(normed, n + 1)
                    dve.wait_ge(gate_ready, h + 1)
                    nc.vector.tensor_tensor(o[:, h, span(i)], o[:, h, span(i)], og[:, h, span(i)], ALU.mult).then_inc(
                        out_ready, 1)

                bounded(0)
                bounded(1)
                sums(0)
                sums(1)
                chunk_decay(0)
                chunk_decay(1)
                masked_scores(0)
                g = 0
                for n, (h, i) in enumerate(units):
                    if n >= 2:
                        dve.wait_ge(o_made, n - 1)
                    if n + 1 < U:
                        masked_scores(n + 1)
                    dve.wait_ge(kv_made, n + 1)
                    if i == 0:
                        dve.wait_ge(decay_ready, h + 1)
                    for j in range(chunks_of(i)):
                        c = i * per_tile + j
                        kv = bank[:, 4 + 2 * (n % 2) + j // 4, (j % 4) * P:(j % 4 + 1) * P]
                        if c == 0:
                            nc.vector.tensor_copy(states[:, g % RING], kv).then_inc(state_ready, 1)
                        else:
                            nc.vector.scalar_tensor_tensor(states[:, g % RING], states[:, (g - 1) % RING],
                                                           decay[:, h, c:c + 1], kv, ALU.mult, ALU.add).then_inc(
                                state_ready, 1)
                        g += 1
                        dve.wait_ge(state_ready, g)
                    if n >= 2:
                        finish(n - 2)
                    if i == 0 and h + 2 < HEADS:
                        bounded(h + 2)
                    if i == 0 and 1 <= h < HEADS - 1:
                        sums(h + 1)
                    if i == 2 and 1 <= h < HEADS - 1:
                        chunk_decay(h + 1)
                finish(U - 2)
                finish(U - 1)

            @block.tensor
            def _(pe):
                pe.wait_ge(params_loaded, 80)

                def turn(n):
                    h, i = units[n]
                    m = tiles[i]
                    pe.wait_ge(qk_ready, 3 * (h + 1))
                    pe.wait_ge(loaded[h], 64)
                    if n >= 2:
                        pe.wait_ge(turn_ready, n - 1)
                    nc.tensor.transpose(bank[0:m, n % 2, 0:P], k_out[:, h % 2, span(i)], ident[:])
                    nc.tensor.transpose(bank[0:m, n % 2, P:2 * P], v[:, h, span(i)], ident[:]).then_inc(turn_made, 1)
                    if n >= 1:
                        pe.wait_ge(scores_ready, n)
                    nc.tensor.matmul(bank[0:m, 2, 0:m], k_in[:, h % 2, span(i)], q[:, h, span(i)],
                                     start=True, stop=True).then_inc(scores_made, 1)

                def key_values(n, b):
                    m, c = tiles[units[n][1]], chunks_of(units[n][1])
                    pe.wait_ge(split_ready, n + 1)
                    if n >= 2:
                        pe.wait_ge(state_ready, states_before(n - 1))
                    w = min(4, c - 4 * b)
                    if w > 0:
                        last = nc.tensor.matmul(bank[:, 4 + 2 * (n % 2) + b, 0:w * P], turned[0:m, n % 3, 0],
                                                v_by_chunk[0:m, n % 2, 4 * b:4 * b + w].rearrange("p c n -> p (c n)"),
                                                start=True, stop=True)
                        if 4 * b + w == c:
                            last.then_inc(kv_made, 1)

                def sum_squares(n):
                    m = tiles[units[n][1]]
                    pe.wait_ge(consts_ready, 1)
                    pe.wait_ge(o_ready, n + 1)
                    if n >= 1:
                        pe.wait_ge(rooted, n)
                    nc.tensor.matmul(bank[:, 3, P:P + m], ones[:], sq[:, n % 2, 0:m], start=True, stop=True).then_inc(
                        summed, 1)

                def output(n):
                    h, i = units[n]
                    m = tiles[i]
                    pe.wait_ge(scores_ready, n + 1)
                    if n >= 1:
                        pe.wait_ge(o_ready, n)
                        pe.wait_ge(rooted, n)
                    last = nc.tensor.matmul(bank[:, 3, 0:m], turned[0:m, n % 3, 1], scores[0:m, n % 3, 0:m],
                                            start=True, stop=False)
                    before = states_before(n)
                    for j in range(chunks_of(i)):
                        if i * per_tile + j == 0:
                            continue
                        pe.wait_ge(state_ready, before + j)
                        last = nc.tensor.matmul(bank[:, 3, j * HCHUNK:(j + 1) * HCHUNK], states[:, (before + j - 1) % RING],
                                                q[:, h, i * P + j * HCHUNK:i * P + (j + 1) * HCHUNK],
                                                start=False, stop=(j == chunks_of(i) - 1))
                    last.then_inc(o_made, 1)

                turn(0)
                turn(1)
                key_values(0, 0)
                key_values(0, 1)
                for n in range(U):
                    if n + 2 < U:
                        turn(n + 2)
                    if n + 1 < U:
                        key_values(n + 1, 0)
                    if n >= 1:
                        sum_squares(n - 1)
                    if n + 1 < U:
                        key_values(n + 1, 1)
                    output(n)
                sum_squares(U - 1)


HEAD_DIM = 64
GRID_W = 64
GRID_ROWS = SEQ // GRID_W


def attention(nc, stage, q_dram, k_dram, v_dram, bias_dram, ident_dram, out_dram):
    C, T = q_dram.shape
    NK = k_dram.shape[1]
    heads, ct, kt, qt = C // HEAD_DIM, C // P, NK // P, T // P
    units = [(h, t) for h in range(heads) for t in range(qt)]
    with ExitStack() as ctx:
        sb, ps, sem = opener(nc, ctx, stage)
        q = sb("q", [P, ct, T])
        k = sb("k", [P, ct, NK])
        v = sb("v", [P, ct, NK])
        bias = sb("bias", [P, heads, 2 * GRID_ROWS, GRID_W]) if bias_dram is not None else None
        ident = sb("ident", [P, P])
        v_tok = sb("v_tok", [P, kt, C])
        s = sb("s", [P, 2, NK])
        low = sb("low", [P, len(units)])
        total = sb("total", [P, len(units)])
        inverse = sb("inverse", [P, len(units)])
        p_turned = sb("p_turned", [P, 2, kt, P])
        y_tok = sb("y_tok", [P, qt, C])
        y = sb("y", [P, ct, T])
        bank = ps("bank", [P, 8, 512])

        loaded = sem("loaded")
        v_turn_made = sem("v_turn_made")
        v_turn_ready = sem("v_turn_ready")
        scores_made = sem("scores_made")
        scores_ready = sem("scores_ready")
        low_ready = sem("low_ready")
        p_ready = sem("p_ready")
        p_turn_made = sem("p_turn_made")
        p_turn_ready = sem("p_turn_ready")
        inverse_ready = sem("inverse_ready")
        y_made = sem("y_made")
        y_ready = sem("y_ready")
        out_turned = sem("out_turned")
        out_ready = sem("out_ready")
        stored = sem("stored")
        n_loads = 5 if bias is not None else 4

        with nc.Block() as block:

            @block.sync
            def _(sp):
                for dst, src in ((ident[:], ident_dram), (v[:], v_dram.rearrange("(c p) t -> p c t", p=P)),
                                 (q[:], q_dram.rearrange("(c p) t -> p c t", p=P)),
                                 (k[:], k_dram.rearrange("(c p) t -> p c t", p=P))):
                    sp.dma_start(dst, src).then_inc(loaded, 16)
                if bias is not None:
                    sp.dma_start(bias[:], bias_dram).then_inc(loaded, 16)
                sp.wait_ge(out_ready, ct)
                sp.dma_start(out_dram.rearrange("(c p) t -> p c t", p=P), y[:]).then_inc(stored, 16)
                sp.wait_ge(stored, 16)

            @block.tensor
            def _(pe):
                pe.wait_ge(loaded, 16 * n_loads)
                for j in range(kt):
                    if j >= 2:
                        pe.wait_ge(v_turn_ready, j - 1)
                    for c in range(ct):
                        last = nc.tensor.transpose(bank[:, j % 2, c * P:(c + 1) * P], v[:, c, j * P:(j + 1) * P], ident[:])
                    last.then_inc(v_turn_made, 1)

                def scores(n):
                    h, t = units[n]
                    e = 64 * (h % 2)
                    if n >= 2:
                        pe.wait_ge(scores_ready, n - 1)
                    nc.tensor.matmul(bank[:, 2 + n % 2, 0:NK], q[e:e + 64, h // 2, t * P:(t + 1) * P],
                                     k[e:e + 64, h // 2, :], start=True, stop=True).then_inc(scores_made, 1)

                def turn(n):
                    pe.wait_ge(p_ready, n + 1)
                    if n >= 2:
                        pe.wait_ge(p_turn_ready, n - 1)
                    for j in range(kt):
                        last = nc.tensor.transpose(bank[:, 4 + n % 2, j * P:(j + 1) * P], s[:, n % 2, j * P:(j + 1) * P],
                                                   ident[:])
                    last.then_inc(p_turn_made, 1)

                def values(n):
                    h, t = units[n]
                    pe.wait_ge(p_turn_ready, n + 1)
                    if n >= 2:
                        pe.wait_ge(y_ready, n - 1)
                    for j in range(kt):
                        last = nc.tensor.matmul(bank[:, 6 + n % 2, 0:HEAD_DIM], p_turned[:, n % 2, j],
                                                v_tok[:, j, h * HEAD_DIM:(h + 1) * HEAD_DIM],
                                                start=(j == 0), stop=(j == kt - 1))
                    last.then_inc(y_made, 1)

                scores(0)
                pe.wait_ge(v_turn_ready, kt)
                for n in range(len(units)):
                    if n + 1 < len(units):
                        scores(n + 1)
                    turn(n)
                    values(n)
                for c in range(ct):
                    pe.wait_ge(y_ready, len(units))
                    if c >= 2:
                        pe.wait_ge(out_ready, c - 1)
                    for t in range(qt):
                        last = nc.tensor.transpose(bank[:, c % 2, t * P:(t + 1) * P], y_tok[:, t, c * P:(c + 1) * P], ident[:])
                    last.then_inc(out_turned, 1)

            @block.vector
            def _(dve):
                dve.wait_ge(loaded, 16 * n_loads)

                def soften(n):
                    h, t = units[n]
                    dve.wait_ge(scores_made, n + 1)
                    if n >= 2:
                        dve.wait_ge(p_turn_made, n - 1)
                    raw = bank[:, 2 + n % 2, 0:NK]
                    if bias is not None:
                        first = GRID_ROWS - 1 - 2 * t
                        nc.vector.scalar_tensor_tensor(
                            s[:, n % 2], raw, HEAD_DIM ** -0.5,
                            bias[:, h, first:first + GRID_ROWS, :].rearrange("p a j -> p (a j)"),
                            ALU.mult, ALU.add).then_inc(scores_ready, 1)
                    else:
                        nc.vector.tensor_scalar(s[:, n % 2], raw, HEAD_DIM ** -0.5, None, ALU.mult).then_inc(
                            scores_ready, 1)
                    dve.wait_ge(scores_ready, n + 1)
                    nc.vector.tensor_reduce(low[:, n:n + 1], s[:, n % 2], X, ALU.max, negate=True).then_inc(low_ready, 1)

                def finish(n):
                    h, t = units[n]
                    dve.wait_ge(p_ready, n + 1)
                    nc.vector.reciprocal(inverse[:, n:n + 1], total[:, n:n + 1]).then_inc(inverse_ready, 1)
                    dve.wait_ge(inverse_ready, n + 1)
                    dve.wait_ge(y_made, n + 1)
                    nc.vector.tensor_scalar(y_tok[:, t, h * HEAD_DIM:(h + 1) * HEAD_DIM], bank[:, 6 + n % 2, 0:HEAD_DIM],
                                            inverse[:, n:n + 1], None, ALU.mult).then_inc(y_ready, 1)

                soften(0)
                for n in range(len(units)):
                    if n + 1 < len(units):
                        soften(n + 1)
                    finish(n)

            @block.scalar
            def _(act):
                for j in range(kt):
                    act.wait_ge(v_turn_made, j + 1)
                    nc.scalar.copy(v_tok[:, j], bank[:, j % 2, 0:C]).then_inc(v_turn_ready, 1)
                for n in range(len(units)):
                    act.wait_ge(low_ready, n + 1)
                    nc.scalar.activation(s[:, n % 2], s[:, n % 2], ACT.Exp, bias=low[:, n:n + 1],
                                         accum_out=total[:, n:n + 1]).then_inc(p_ready, 1)
                    act.wait_ge(p_turn_made, n + 1)
                    if n >= 2:
                        act.wait_ge(y_made, n - 1)
                    nc.scalar.copy(p_turned[:, n % 2].rearrange("p j m -> p (j m)"), bank[:, 4 + n % 2, 0:NK]).then_inc(
                        p_turn_ready, 1)
                for c in range(ct):
                    act.wait_ge(out_turned, c + 1)
                    nc.scalar.copy(y[:, c], bank[:, c % 2, 0:T]).then_inc(out_ready, 1)


def window_bias(rpb):
    heads = rpb.shape[0]
    win = 16
    w = np.arange(GRID_W)[:, None]
    j = np.arange(GRID_W)[None, :]
    start = np.clip(w - win // 2, 0, GRID_W - win)
    inside = (j >= start) & (j < start + win)
    offset = np.clip(j - w + win - 1, 0, 2 * win - 2)
    rows = 2 * GRID_ROWS
    out = np.full((2, GRID_W, heads, rows, GRID_W), -1e30, np.float32)
    laid = np.where(inside[None, None], rpb[:, :, offset], np.float32(-1e30))
    laid = laid.transpose(2, 0, 1, 3)
    out[0, :, :, 0:rows - 1] = laid
    out[1, :, :, 1:rows] = laid
    return np.ascontiguousarray(out.reshape(P, heads, rows, GRID_W))


RW_WIDTH = 384
RW_X = RW_WIDTH // P
RCHUNK = 32
RSTEPS = SEQ // RCHUNK
LORA = 64
DECAY_SCALE = float(np.exp(-0.5))
GN_EPS = 64e-5
LEVELS = 5
MU_R, MU_K, MU_V, W0, A0, K_K, K_A, R_K, LN_G, LN_B = 0, 2, 4, 6, 8, 10, 11, 12, 13, 14
RW_COLS = 15


def rwkv7(nc, stage, p_dram, par_dram, mu_l_dram, lora_dram, g2_dram, ident_dram, masks_dram, member_dram,
          eye2_dram, out_dram):
    T = SEQ
    N = RW_X * T
    units = [(d, i, x) for d in range(2) for i in range(T // P) for x in range(RW_X)]
    with ExitStack() as ctx:
        sb, ps, sem = opener(nc, ctx, stage)
        par = sb("par", [P, RW_COLS, RW_X])
        mu_l = sb("mu_l", [P, 2])
        keep_k = sb("keep_k", [P, RW_X])
        lora = sb("lora", [P, 2, RW_WIDTH])
        g2 = sb("g2", [P, RW_WIDTH])
        ident = sb("ident", [P, P])
        blocks = sb("blocks", [P, P])
        masks = sb("masks", [P, 2, 4, P])
        member = sb("member", [P, 4, P])
        eye2 = sb("eye2", [P, HEAD_DIM])
        resets = sb("resets", [P, N])
        raw = sb("raw", [P, 3, RW_X, T + 2])
        raw_l = sb("raw_l", [P, T + 2])
        lat_g = sb("lat_g", [P, T])
        ar = sb("ar", [P, 2, RW_X, 2, T])
        bh = sb("bh", [P, 2, RW_X, T])
        kh = sb("kh", [P, 2, RW_X, T])
        v = sb("v", [P, 2, RW_X, T])
        qt = sb("qt", [P, 2, RW_X, T])
        y_loc = sb("y_loc", [P, 2, RW_X, T])
        bonus = sb("bonus", [P, RW_X, T])
        ends = sb("ends", [P, RSTEPS, 2 * RW_X])
        work = sb("work", [P, 11 * N])
        tmp = [work[:, n * N:(n + 1) * N].rearrange("p (x t) -> p x t", x=RW_X) for n in range(11)]
        dr, dk, dv, r, k, sw, sa, cum, e1, e2, sq = tmp
        e3, norm = dr, dk
        dl, lat = cum[:, 0], sq[:, 0]
        gate, y = e1, e2
        raw_flat = raw[:].rearrange("p j x t -> p (j x t)")
        per_step = RSTEPS * 2 * RW_X * HEAD_DIM
        ht = work[:, 0:per_step].rearrange("p (s n k) -> p s n k", s=RSTEPS, k=HEAD_DIM)
        nn = work[:, per_step:2 * per_step].rearrange("p (s n k) -> p s n k", s=RSTEPS, k=HEAD_DIM)
        states = sb("states", [P, 2, 2 * RW_X, HEAD_DIM])
        tok = sb("tok", [P, 2, 4, P])
        split = raw_flat[:, 0:16 * P].rearrange("p (s a c n) -> p s a c n", s=2, a=2, c=4)
        sm = raw_flat[:, 16 * P:32 * P].rearrange("p (s e a t) -> p s e a t", s=2, e=2, a=4)
        a_first = resets[:, 0:4 * P].rearrange("p (s e n) -> p s e n", s=2, e=2)
        z = resets[:, 4 * P:8 * P].rearrange("p (s e n) -> p s e n", s=2, e=2)
        power = sb("power", [P, 2, 2, 2, P])
        bank = ps("bank", [P, 8, 512])

        loaded = sem("loaded")
        raw_loaded = sem("raw_loaded")
        consts_ready = sem("consts_ready")
        diffed = sem("diffed")
        mixed = sem("mixed")
        tanhed = sem("tanhed")
        lora_made = sem("lora_made")
        sig_ready = sem("sig_ready")
        squared = sem("squared")
        norm_made = sem("norm_made")
        norm_rooted = sem("norm_rooted")
        chain = sem("chain")
        cum_ready = sem("cum_ready")
        cum_used = sem("cum_used")
        exps_ready = sem("exps_ready")
        prepared = sem("prepared")
        bonus_in = sem("bonus_in")
        bonus_made = sem("bonus_made")
        bonus_ready = sem("bonus_ready")
        turn_made = sem("turn_made")
        tok_ready = sem("tok_ready")
        split_ready = sem("split_ready")
        scores_made = sem("scores_made")
        scores_ready = sem("scores_ready")
        first_made = sem("first_made")
        first_ready = sem("first_ready")
        z_started = sem("z_started")
        level_made = sem("level_made")
        z_ready = sem("z_ready")
        power_ready = sem("power_ready")
        ends_made = sem("ends_made")
        ends_read = sem("ends_read")
        parts_read = sem("parts_read")
        step_made = sem("step_made")
        step_added = sem("step_added")
        state_ready = sem("state_ready")
        inter_made = sem("inter_made")
        gate_sig = sem("gate_sig")
        gate_made = sem("gate_made")
        gate_ready = sem("gate_ready")
        tail = sem("tail")
        mean_made = sem("mean_made")
        dev_squared = sem("dev_squared")
        var_made = sem("var_made")
        var_ready = sem("var_ready")
        var_rooted = sem("var_rooted")
        stored = sem("stored")

        def shifted(a, d):
            return a[..., 0:T] if d == 0 else a[..., 2:T + 2]

        def wide(a):
            return a.rearrange("p x t -> p (x t)")

        def steps_of_tile(d, i):
            if d == 0:
                return slice(4 * i, 4 * i + 4)
            last = RSTEPS - 1 - 4 * i
            return slice(last, last - 4 if last >= 4 else None, -1)

        with nc.Block() as block:

            @block.sync
            def _(sp):
                for dst, src in ((par, par_dram), (mu_l, mu_l_dram), (lora, lora_dram), (g2, g2_dram),
                                 (ident, ident_dram), (masks, masks_dram), (member, member_dram), (eye2, eye2_dram)):
                    sp.dma_start(dst[:], src).then_inc(loaded, 16)
                sp.wait_ge(consts_ready, 3)
                for j in range(3):
                    sp.dma_start(raw[:, j, :, 1:T + 1],
                                 p_dram[j * RW_WIDTH:(j + 1) * RW_WIDTH, :].rearrange("(x p) t -> p x t", p=P)).then_inc(
                        raw_loaded, 16)
                at = 3 * RW_WIDTH
                sp.dma_start(raw_l[:, 1:T + 1], p_dram[at:at + P, :]).then_inc(raw_loaded, 16)
                sp.dma_start(lat_g[:], p_dram[at + P:at + 2 * P, :]).then_inc(raw_loaded, 16)
                sp.wait_ge(tail, RW_TAIL)
                sp.dma_start(out_dram.rearrange("(x p) t -> p x t", p=P), y).then_inc(stored, 16)
                sp.wait_ge(stored, 16)

            @block.gpsimd
            def _(pool):
                for d in range(2):
                    pool.wait_ge(raw_loaded, 80)
                    if d == 1:
                        pool.wait_ge(prepared, RW_PREPARED)
                        pool.wait_ge(bonus_in, 1)
                        pool.wait_ge(chain, RW_CHAIN)
                        pool.wait_ge(mixed, 10)
                    for j, out in enumerate((dr, dk, dv)):
                        nc.gpsimd.tensor_tensor(out, shifted(raw[:, j], d), raw[:, j, :, 1:T + 1],
                                                ALU.subtract).then_inc(diffed, 1)
                    nc.gpsimd.tensor_tensor(dl, shifted(raw_l[:], d), raw_l[:, 1:T + 1], ALU.subtract).then_inc(diffed, 1)
                    pool.wait_ge(exps_ready, 3 * (d + 1))
                    pool.wait_ge(mixed, 10 * (d + 1))
                    nc.gpsimd.tensor_tensor(ar[:, d, :, 1, :], r, e1, ALU.mult).then_inc(prepared, 1)
                for n, (d, i, x) in enumerate(units):
                    pool.wait_ge(tok_ready, n + 1)
                    if n >= 2:
                        pool.wait_ge(ends_made, n - 1)
                    for j in range(2):
                        nc.gpsimd.tensor_tensor(split[:, n % 2, j], member[:],
                                                tok[:, n % 2, j].unsqueeze(1).broadcast_to([P, 4, P]),
                                                ALU.mult).then_inc(split_ready, 1)
                pool.wait_ge(parts_read, 2 * len(units))
                nc.gpsimd.tensor_tensor(y_loc[:, 0], y_loc[:, 0], y_loc[:, 1], ALU.add).then_inc(prepared, 1)

            @block.scalar
            def _(act):
                act.wait_ge(raw_loaded, 80)
                nc.scalar.activation(lat_g[:], lat_g[:], ACT.Sigmoid).then_inc(gate_sig, 1)
                act.wait_ge(loaded, 128)
                for d in range(2):
                    act.wait_ge(mixed, 10 * (d + 1))
                    nc.scalar.activation(lat[0:LORA], lat[0:LORA], ACT.Tanh).then_inc(tanhed, 1)
                    act.wait_ge(lora_made, d + 1)
                    for x in range(RW_X):
                        nc.scalar.activation(sw[:, x], bank[:, x], ACT.Sigmoid, bias=par[:, W0 + d, x:x + 1]).then_inc(
                            sig_ready, 1)
                    for x in range(RW_X):
                        nc.scalar.activation(sa[:, x], bank[:, 3 + x], ACT.Sigmoid, bias=par[:, A0 + d, x:x + 1]).then_inc(
                            sig_ready, 1)
                    for x in range(RW_X):
                        nc.scalar.activation(sq[:, x], k[:, x], ACT.Square, scale=par[:, K_K, x:x + 1]).then_inc(squared, 1)
                    act.wait_ge(norm_made, d + 1)
                    nc.scalar.activation(norm, bank[:, 0:3, :], ACT.Sqrt).then_inc(norm_rooted, 1)
                    act.wait_ge(cum_ready, 2 * d + 1)
                    nc.scalar.activation(e1, cum, ACT.Exp, scale=-DECAY_SCALE).then_inc(exps_ready, 1)
                    nc.scalar.activation(e2, cum, ACT.Exp, scale=DECAY_SCALE).then_inc(exps_ready, 1)
                    act.wait_ge(cum_ready, 2 * d + 2)
                    nc.scalar.activation(e3, sw, ACT.Exp, scale=-DECAY_SCALE).then_inc(exps_ready, 1)

                def front_a(n):
                    act.wait_ge(turn_made, n + 1)
                    if n >= 2:
                        act.wait_ge(ends_made, n - 1)
                    nc.scalar.copy(tok[:, n % 2].rearrange("p a c -> p (a c)"), bank[:, 0]).then_inc(tok_ready, 1)

                def front_b(n):
                    act.wait_ge(first_made, n + 1)
                    if n >= 2:
                        act.wait_ge(level_made, LEVELS * (n - 1))
                    nc.scalar.copy(a_first[:, n % 2], bank[:, 6, 0:2 * P].rearrange("p (e s) -> p e s", e=2)).then_inc(
                        first_ready, 1)

                def level(n, lv):
                    if lv < LEVELS - 1:
                        act.wait_ge(level_made, LEVELS * n + lv + 1)
                        first = 0 if lv < LEVELS - 2 else P
                        nc.scalar.copy(power[:, lv % 2, :, :, :].rearrange("p e a s -> p e (a s)")[:, :, first:],
                                       bank[:, 3:5, first:2 * P]).then_inc(power_ready, 1)

                def finish(n):
                    d, i, x = units[n]
                    act.wait_ge(ends_made, n + 1)
                    nc.scalar.copy(nn[:, steps_of_tile(d, i), 3 * d + x, :],
                                   bank[:, 6, 0:4 * HEAD_DIM].rearrange("p (c k) -> p c k", c=4)).then_inc(parts_read, 1)
                    nc.scalar.copy(y_loc[:, d, x, i * P:(i + 1) * P], bank[:, 6, 4 * HEAD_DIM:4 * HEAD_DIM + P]).then_inc(
                        parts_read, 1)

                act.wait_ge(prepared, 2 * RW_PREPARED)
                act.wait_ge(chain, 2 * RW_CHAIN)
                act.wait_ge(bonus_made, 2)
                front_a(0)
                front_b(0)
                for n in range(len(units)):
                    level(n, 0)
                    level(n, 1)
                    if n + 1 < len(units):
                        front_a(n + 1)
                    level(n, 2)
                    level(n, 3)
                    if n + 1 < len(units):
                        front_b(n + 1)
                    finish(n)
                act.wait_ge(gate_made, 1)
                nc.scalar.copy(gate, bank[:, 5:8, :]).then_inc(gate_ready, 1)
                act.wait_ge(tail, 2)
                nc.scalar.activation(sq, y, ACT.Square).then_inc(dev_squared, 1)
                act.wait_ge(var_ready, 1)
                nc.scalar.activation(sq, sq, ACT.Sqrt).then_inc(var_rooted, 1)

            @block.tensor
            def _(pe):
                pe.wait_ge(loaded, 128)
                pe.wait_ge(consts_ready, 5)
                for d in range(2):
                    pe.wait_ge(tanhed, d + 1)
                    pe.wait_ge(mixed, 10 * (d + 1))
                    if d == 1:
                        pe.wait_ge(bonus_ready, 1)
                        pe.wait_ge(sig_ready, 6)
                    for x in range(RW_X):
                        nc.tensor.matmul(bank[:, x], lora[0:LORA, d, x * P:(x + 1) * P], lat[0:LORA], start=True, stop=True)
                    for x in range(RW_X):
                        last = nc.tensor.matmul(bank[:, 3 + x], lora[LORA:, d, x * P:(x + 1) * P], lat[LORA:],
                                                start=True, stop=True)
                    last.then_inc(lora_made, 1)
                    pe.wait_ge(squared, 3 * (d + 1))
                    pe.wait_ge(sig_ready, 6 * d + 3)
                    for x in range(RW_X):
                        last = nc.tensor.matmul(bank[:, x], blocks[:], sq[:, x], start=True, stop=True)
                    last.then_inc(norm_made, 1)
                    pe.wait_ge(bonus_in, d + 1)
                    pe.wait_ge(norm_rooted, d + 1)
                    for x in range(RW_X):
                        last = nc.tensor.matmul(bank[:, x], blocks[:], sq[:, x], start=True, stop=True)
                    last.then_inc(bonus_made, 1)
                pe.wait_ge(bonus_ready, 2)
                pe.wait_ge(prepared, 2 * RW_PREPARED)
                pe.wait_ge(chain, 2 * RW_CHAIN)
                pe.wait_ge(sig_ready, 12)

                def heads(e):
                    return slice(64 * e, 64 * e + 64)

                def front_a(n):
                    d, i, x = units[n]
                    at = slice(i * P, (i + 1) * P)
                    if n >= 1:
                        pe.wait_ge(tok_ready, n)
                    for j, a in enumerate((bh[:, d, x, at], kh[:, d, x, at], ar[:, d, x, 0, at], v[:, d, x, at])):
                        last = nc.tensor.transpose(bank[:, 0, j * P:(j + 1) * P], a, ident[:])
                    last.then_inc(turn_made, 1)
                    if n >= 1:
                        pe.wait_ge(scores_ready, n)
                    for e in range(2):
                        for j, a in enumerate((bh, kh)):
                            last = nc.tensor.matmul(bank[:, 1 + e, 2 * j * P:2 * (j + 1) * P], a[heads(e), d, x, at],
                                                    ar[heads(e), d, x, :, at], start=True, stop=True)
                    last.then_inc(scores_made, 1)

                def front_b(n):
                    pe.wait_ge(scores_ready, n + 1)
                    pe.wait_ge(tok_ready, n + 1)
                    if n >= 2:
                        pe.wait_ge(ends_read, 2 * (n - 1))
                        pe.wait_ge(parts_read, 2 * (n - 1))
                    for e in range(2):
                        nc.tensor.transpose(bank[:, 6, e * P:(e + 1) * P], sm[:, n % 2, e, 0], ident[:])
                    for e in range(2):
                        last = nc.tensor.matmul(bank[:, 5, 64 * e:64 * e + 64], sm[:, n % 2, e, 2],
                                                tok[:, n % 2, 3, heads(e)], start=True, stop=True)
                    last.then_inc(first_made, 1)

                def level(n, lv):
                    if lv == 0:
                        pe.wait_ge(first_ready, n + 1)
                        pe.wait_ge(z_started, 2 * (n + 1))
                        if n >= 1:
                            pe.wait_ge(z_ready, LEVELS * n)
                    else:
                        pe.wait_ge(power_ready, (LEVELS - 1) * n + lv)
                        pe.wait_ge(z_ready, LEVELS * n + lv)
                    for e in range(2):
                        a_t = sm[:, n % 2, e, 0] if lv == 0 else power[:, (lv - 1) % 2, e, 1]
                        a = a_first[:, n % 2, e] if lv == 0 else power[:, (lv - 1) % 2, e, 0]
                        if lv < LEVELS - 1:
                            if lv < LEVELS - 2:
                                nc.tensor.matmul(bank[:, 3 + e, 0:P], a_t, a, start=True, stop=True)
                            nc.tensor.matmul(bank[:, 3 + e, P:2 * P], a, a_t, start=True, stop=True)
                        last = nc.tensor.matmul(bank[:, 7, e * P:(e + 1) * P], a_t, z[:, n % 2, e], start=True, stop=True)
                    last.then_inc(level_made, 1)

                def finish(n):
                    s = n % 2
                    pe.wait_ge(z_ready, LEVELS * (n + 1))
                    pe.wait_ge(split_ready, 2 * (n + 1))
                    m = min(n + 2, len(units))
                    pe.wait_ge(first_ready, m)
                    pe.wait_ge(z_started, 2 * m)
                    if n >= 1:
                        pe.wait_ge(ends_read, 2 * n)
                        pe.wait_ge(parts_read, 2 * n)
                    for e in range(2):
                        zz, ww, vv = z[:, s, e, 0:64], z[:, s, e, 64:P], tok[:, s, 3, heads(e)]
                        nc.tensor.matmul(bank[heads(e), 5, 0:256], ww, split[:, s, 0, :, heads(e)], start=True, stop=True)
                        nc.tensor.matmul(bank[heads(e), 5, 256:384], ww, sm[:, s, e, 1], start=True, stop=True)
                        for c in range(4):
                            to = bank[heads(e), 6, 64 * c:64 * c + 64]
                            nc.tensor.matmul(to, split[:, s, 0, c, heads(e)], zz, start=True, stop=False)
                            nc.tensor.matmul(to, split[:, s, 1, c, heads(e)], vv, start=False, stop=True)
                        to = bank[heads(e), 6, 256:384]
                        nc.tensor.matmul(to, zz, sm[:, s, e, 1], start=True, stop=False)
                        last = nc.tensor.matmul(to, vv, sm[:, s, e, 3], start=False, stop=True)
                    last.then_inc(ends_made, 1)

                front_a(0)
                front_b(0)
                for n in range(len(units)):
                    level(n, 0)
                    level(n, 1)
                    if n + 1 < len(units):
                        front_a(n + 1)
                    level(n, 2)
                    level(n, 3)
                    if n + 1 < len(units):
                        front_b(n + 1)
                    level(n, 4)
                    finish(n)

                pe.wait_ge(ends_read, 2 * len(units))
                pe.wait_ge(parts_read, 2 * len(units))
                pe.wait_ge(gate_sig, 1)
                for x in range(RW_X):
                    last = nc.tensor.matmul(bank[:, 5 + x], g2[:, x * P:(x + 1) * P], lat_g[:], start=True, stop=True)
                last.then_inc(gate_made, 1)
                pe.wait_ge(z_ready, LEVELS * len(units))
                for s in range(1, RSTEPS):
                    pe.wait_ge(state_ready, s)
                    if s < RSTEPS - 1:
                        for n in range(2 * RW_X):
                            for e in range(2):
                                last = nc.tensor.matmul(bank[heads(e), s % 2, 64 * n:64 * n + 64], ht[heads(e), s, n],
                                                        states[heads(e), s % 2, n], start=True, stop=True)
                        last.then_inc(step_made, 1)
                    for d in range(2):
                        c = s if d == 0 else RSTEPS - 1 - s
                        at = slice(c * RCHUNK, (c + 1) * RCHUNK)
                        for x in range(RW_X):
                            for e in range(2):
                                last = nc.tensor.matmul(bank[heads(e), 2 + x, at], states[heads(e), s % 2, 3 * d + x],
                                                        qt[heads(e), d, x, at], start=(s == 1 and d == 0),
                                                        stop=(s == RSTEPS - 1 and d == 1))
                    last.then_inc(inter_made, 1)
                pe.wait_ge(tail, 1)
                pe.wait_ge(gate_ready, 1)
                for x in range(RW_X):
                    last = nc.tensor.matmul(bank[:, 5 + x], blocks[:], y[:, x], start=True, stop=True)
                last.then_inc(mean_made, 1)
                pe.wait_ge(dev_squared, 1)
                pe.wait_ge(tail, 2)
                for x in range(RW_X):
                    last = nc.tensor.matmul(bank[:, 5 + x], blocks[:], sq[:, x], start=True, stop=True)
                last.then_inc(var_made, 1)

            @block.vector
            def _(dve):
                nc.vector.memset(raw[:], 0.0).then_inc(consts_ready, 1)
                nc.vector.memset(raw_l[:], 0.0).then_inc(consts_ready, 1)
                nc.vector.memset(blocks[:], 0.0).then_inc(consts_ready, 1)
                dve.wait_ge(consts_ready, 3)
                nc.vector.memset(blocks[0:64, 0:64], 1.0).then_inc(consts_ready, 1)
                nc.vector.memset(blocks[64:P, 64:P], 1.0).then_inc(consts_ready, 1)
                nc.vector.memset(resets[:], 1.0).then_inc(consts_ready, 1)
                dve.wait_ge(consts_ready, 6)
                nc.vector.memset(resets[:, 0:N:RCHUNK], 0.0).then_inc(consts_ready, 1)
                dve.wait_ge(loaded, 128)
                nc.vector.tensor_scalar(keep_k[:], par[:, K_A], -1.0, 1.0, ALU.mult, ALU.add).then_inc(consts_ready, 1)
                dve.wait_ge(consts_ready, 8)
                done = [0]

                def step(ins):
                    ins.then_inc(chain, 1)
                    done[0] += 1
                    dve.wait_ge(chain, done[0])

                for d in range(2):
                    for j, (diff, out, mu) in enumerate(((dr, r, MU_R), (dk, k, MU_K), (dv, v[:, d], MU_V))):
                        dve.wait_ge(diffed, 4 * d + j + 1)
                        if d == 1 and j == 0:
                            dve.wait_ge(prepared, RW_PREPARED)
                            dve.wait_ge(bonus_in, 1)
                        for x in range(RW_X):
                            nc.vector.scalar_tensor_tensor(out[:, x], diff[:, x], par[:, mu + d, x:x + 1],
                                                           raw[:, j, x, 1:T + 1], ALU.mult, ALU.add).then_inc(mixed, 1)
                    dve.wait_ge(diffed, 4 * d + 4)
                    if d == 1:
                        dve.wait_ge(lora_made, 1)
                    nc.vector.scalar_tensor_tensor(lat, dl, mu_l[:, d:d + 1], raw_l[:, 1:T + 1],
                                                   ALU.mult, ALU.add).then_inc(mixed, 1)
                    dve.wait_ge(sig_ready, 6 * d + 3)
                    if d == 0:
                        nc.vector.tensor_tensor_scan(wide(cum), resets[:], wide(sw), 0.0, ALU.mult, ALU.add).then_inc(
                            cum_ready, 1)
                    else:
                        nc.vector.tensor_tensor_scan(wide(cum)[:, ::-1], resets[:], wide(sw)[:, ::-1], 0.0,
                                                     ALU.mult, ALU.add).then_inc(cum_ready, 1)
                    dve.wait_ge(cum_ready, 2 * d + 1)
                    nc.vector.tensor_tensor(sw, cum, sw, ALU.subtract).then_inc(cum_ready, 1)
                    dve.wait_ge(norm_rooted, d + 1)
                    step(nc.vector.tensor_scalar(norm, norm, 1e-12, None, ALU.max))
                    step(nc.vector.reciprocal(norm, norm))
                    dve.wait_ge(mixed, 10 * (d + 1))
                    for x in range(RW_X):
                        nc.vector.scalar_tensor_tensor(norm[:, x], k[:, x], par[:, K_K, x:x + 1], norm[:, x],
                                                       ALU.mult, ALU.mult).then_inc(chain, 1)
                        done[0] += 1
                    dve.wait_ge(chain, done[0])
                    dve.wait_ge(exps_ready, 3 * (d + 1))
                    nc.vector.scalar_tensor_tensor(ar[:, d, :, 0, :], norm, -1.0, e3, ALU.mult, ALU.mult).then_inc(
                        prepared, 1)
                    dve.wait_ge(sig_ready, 6 * (d + 1))
                    step(nc.vector.tensor_tensor(norm, norm, sa, ALU.mult))
                    nc.vector.tensor_tensor(bh[:, d], norm, e2, ALU.mult).then_inc(prepared, 1)
                    for x in range(RW_X):
                        nc.vector.tensor_scalar(sa[:, x], sa[:, x], par[:, K_A, x:x + 1], keep_k[:, x:x + 1],
                                                ALU.mult, ALU.add).then_inc(chain, 1)
                        done[0] += 1
                    dve.wait_ge(chain, done[0])
                    step(nc.vector.tensor_tensor(k, k, sa, ALU.mult))
                    nc.vector.tensor_tensor(kh[:, d], k, e2, ALU.mult).then_inc(prepared, 1)
                    dve.wait_ge(norm_made, d + 1)
                    for x in range(RW_X):
                        ins = nc.vector.scalar_tensor_tensor(sq[:, x], r[:, x], par[:, R_K, x:x + 1], k[:, x],
                                                             ALU.mult, ALU.mult)
                    ins.then_inc(bonus_in, 1)
                    whole = e1[:, :, RCHUNK - 1::RCHUNK] if d == 0 else e1[:, :, T - RCHUNK::-RCHUNK]
                    nc.vector.tensor_copy(ends[:, :, 3 * d:3 * d + 3].rearrange("p s x -> p x s"), whole).then_inc(
                        prepared, 1)
                    dve.wait_ge(bonus_made, d + 1)
                    if d == 0:
                        nc.vector.tensor_tensor(bonus[:], bank[:, 0:3, :], v[:, 0], ALU.mult).then_inc(bonus_ready, 1)
                    else:
                        dve.wait_ge(prepared, 2 * RW_PREPARED)
                        step(nc.vector.tensor_tensor(e1, bank[:, 0:3, :], v[:, 1], ALU.mult))
                        dve.wait_ge(bonus_ready, 1)
                        nc.vector.tensor_tensor(bonus[:], bonus[:], e1, ALU.add).then_inc(bonus_ready, 1)
                    if d == 0:
                        assert done[0] == RW_CHAIN, done[0]

                def front_a(n):
                    d = units[n][0]
                    dve.wait_ge(scores_made, n + 1)
                    if n >= 2:
                        dve.wait_ge(ends_made, n - 1)
                    for e in range(2):
                        ins = nc.vector.tensor_tensor(sm[:, n % 2, e].rearrange("p a t -> p (a t)"), bank[:, 1 + e],
                                                      masks[:, d].rearrange("p a t -> p (a t)"), ALU.mult)
                    ins.then_inc(scores_ready, 1)

                def front_b(n):
                    dve.wait_ge(first_made, n + 1)
                    if n >= 2:
                        dve.wait_ge(ends_made, n - 1)
                    nc.vector.tensor_copy(z[:, n % 2, :, 0:64],
                                          bank[:, 5, 0:P].rearrange("p (e m) -> p e m", e=2)).then_inc(z_started, 1)
                    dve.wait_ge(tok_ready, n + 1)
                    nc.vector.tensor_copy(z[:, n % 2, :, 64:P],
                                          tok[:, n % 2, 2].rearrange("p (e m) -> p e m", e=2)).then_inc(z_started, 1)

                def level(n, lv):
                    dve.wait_ge(level_made, LEVELS * n + lv + 1)
                    if lv == 0:
                        dve.wait_ge(z_started, 2 * (n + 1))
                    else:
                        dve.wait_ge(z_ready, LEVELS * n + lv)
                    nc.vector.tensor_tensor(z[:, n % 2], z[:, n % 2], bank[:, 7, 0:2 * P].rearrange("p (e m) -> p e m", e=2),
                                            ALU.add).then_inc(z_ready, 1)

                def finish(n):
                    d, i, x = units[n]
                    at = slice(i * P, (i + 1) * P)
                    dve.wait_ge(ends_made, n + 1)
                    nc.vector.tensor_tensor(ht[:, steps_of_tile(d, i), 3 * d + x, :],
                                            bank[:, 5, 0:256].rearrange("p (c k) -> p c k", c=4),
                                            eye2[:].unsqueeze(1).broadcast_to([P, 4, HEAD_DIM]), ALU.add).then_inc(ends_read, 1)
                    nc.vector.tensor_tensor(qt[:, d, x, at], bank[:, 5, 256:384], ar[:, d, x, 1, at], ALU.add).then_inc(
                        ends_read, 1)

                dve.wait_ge(prepared, 2 * RW_PREPARED)
                dve.wait_ge(bonus_ready, 2)
                dve.wait_ge(exps_ready, 6)
                front_a(0)
                front_b(0)
                for n in range(len(units)):
                    level(n, 0)
                    level(n, 1)
                    if n + 1 < len(units):
                        front_a(n + 1)
                    level(n, 2)
                    level(n, 3)
                    if n + 1 < len(units):
                        front_b(n + 1)
                    level(n, 4)
                    finish(n)

                def over(a):
                    return a.unsqueeze(2).broadcast_to([P, 2 * RW_X, HEAD_DIM])

                dve.wait_ge(parts_read, 2 * len(units))
                nc.vector.tensor_tensor(states[:, 1], nn[:, 0], over(ends[:, 0]), ALU.mult).then_inc(state_ready, 1)
                for s in range(1, RSTEPS - 1):
                    dve.wait_ge(step_made, s)
                    if s >= 2:
                        dve.wait_ge(inter_made, s - 1)
                    dve.wait_ge(state_ready, s)
                    to = states[:, (s + 1) % 2]
                    nc.vector.tensor_tensor(to, nn[:, s], bank[:, s % 2, 0:2 * RW_X * HEAD_DIM].rearrange(
                        "p (n k) -> p n k", k=HEAD_DIM), ALU.add).then_inc(step_added, 1)
                    dve.wait_ge(step_added, s)
                    nc.vector.tensor_tensor(to, to, over(ends[:, s]), ALU.mult).then_inc(state_ready, 1)
                dve.wait_ge(inter_made, RSTEPS - 1)
                dve.wait_ge(prepared, 2 * RW_PREPARED + 1)
                count = [0]

                def tail_step(ins):
                    ins.then_inc(tail, 1)
                    count[0] += 1
                    dve.wait_ge(tail, count[0])

                tail_step(nc.vector.tensor_tensor(y, y_loc[:, 0], bank[:, 2:5, :], ALU.add))
                dve.wait_ge(mean_made, 1)
                tail_step(nc.vector.scalar_tensor_tensor(y, bank[:, 5:8, :], -1.0 / HEAD_DIM, y, ALU.mult, ALU.add))
                dve.wait_ge(var_made, 1)
                nc.vector.tensor_scalar(sq, bank[:, 5:8, :], 1.0 / HEAD_DIM, GN_EPS, ALU.mult, ALU.add).then_inc(tail, 1)
                count[0] += 1
                dve.wait_ge(tail, count[0])
                nc.vector.reciprocal(sq, sq).then_inc(var_ready, 1)
                dve.wait_ge(var_rooted, 1)
                tail_step(nc.vector.tensor_tensor(y, y, sq, ALU.mult))
                for x in range(RW_X):
                    tail_step(nc.vector.tensor_scalar(y[:, x], y[:, x], par[:, LN_G, x:x + 1], par[:, LN_B, x:x + 1],
                                                      ALU.mult, ALU.add))
                tail_step(nc.vector.tensor_tensor(y, y, bonus[:], ALU.add))
                dve.wait_ge(gate_ready, 1)
                tail_step(nc.vector.tensor_tensor(y, y, gate, ALU.mult))
                assert count[0] == RW_TAIL, count[0]


RW_PREPARED = 5
RW_CHAIN = 2 + 3 + 1 + 3 + 1
RW_TAIL = 4 + RW_X + 2


EXPERTS = 16
CAPACITY = 2 * SEQ // EXPERTS
EXPERT_FF = 2 * D_MODEL


def expert_ffn(nc, stage, z_dram, x_dram, router_dram, gate_dram, up_dram, down_dram, ident_dram, slots_dram,
               out_dram):
    T = SEQ
    TT = T // P
    HALF = 512
    FC = EXPERT_FF // HALF
    FT = HALF // P
    with ExitStack() as ctx:
        sb, ps, sem = opener(nc, ctx, stage)
        z = sb("z", [P, KT, T])
        z_tok = sb("z_tok", [P, TT, D_MODEL])
        acc = z_tok[:].rearrange("p a b -> p (a b)").rearrange("p (m t) -> p m t", t=T)
        hot = sb("hot", [P, TT, EXPERTS, CAPACITY])
        xe = sb("xe", [P, KT, EXPERTS * CAPACITY])
        scatter = sb("scatter", [P, EXPERTS // 2, T])
        router = sb("router", [P, KT, EXPERTS])
        ident = sb("ident", [P, P])
        slots = sb("slots", [P, CAPACITY])
        logits = sb("logits", [P, TT, EXPERTS])
        high = sb("high", [P, TT])
        affinity = sb("affinity", [P, TT, EXPERTS])
        place_tok = sb("place_tok", [P, TT, EXPERTS])
        left = sb("left", [EXPERTS, T])
        best = sb("best", [EXPERTS, 8])
        chosen = sb("chosen", [EXPERTS, T])
        ones = sb("ones", [EXPERTS, T])
        w_in = sb("w_in", [P, 2, 2, KT, HALF])
        w_out = sb("w_out", [P, 2, FT, D_MODEL])
        xs = sb("xs", [P, 2, KT, CAPACITY])
        hot_flat = hot[:].rearrange("p t e s -> p (t e s)")
        sg = hot_flat[0:CAPACITY, 0:2 * HALF].rearrange("n (s f) -> n s f", s=2)
        act_t = hot_flat[:, 2 * HALF:3 * HALF].rearrange("p (s j n) -> p s j n", s=2, j=FT)
        ye = hot_flat[:, 3 * HALF:3 * HALF + D_MODEL]
        bank = ps("bank", [P, 8, 512])

        loaded = sem("loaded")
        z_loaded = sem("z_loaded")
        x_loaded = sem("x_loaded")
        logits_made = sem("logits_made")
        route = sem("route")
        exp_ready = sem("exp_ready")
        aff_turned = sem("aff_turned")
        place_turned = sem("place_turned")
        hot_ready = sem("hot_ready")
        z_turned = sem("z_turned")
        z_tok_ready = sem("z_tok_ready")
        xe_made = sem("xe_made")
        xe_ready = sem("xe_ready")
        weighted = sem("weighted")
        hot_turned = sem("hot_turned")
        scatter_ready = sem("scatter_ready")
        in_loaded = [sem(f"in_loaded{s}") for s in range(2)]
        out_loaded = [sem(f"out_loaded{s}") for s in range(2)]
        in_used = [sem(f"in_used{s}") for s in range(2)]
        out_used = [sem(f"out_used{s}") for s in range(2)]
        xs_ready = [sem(f"xs_ready{s}") for s in range(2)]
        silu_ready = sem("silu_ready")
        act_ready = sem("act_ready")
        act_turned = sem("act_turned")
        act_t_ready = sem("act_t_ready")
        y_made = sem("y_made")
        y_ready = sem("y_ready")
        part_made = sem("part_made")
        part_added = sem("part_added")
        stored = sem("stored")

        in_v = [w.rearrange("e (k p) f -> e p k f", p=P) for w in (gate_dram, up_dram)]
        out_v = down_dram.rearrange("e (c p) d -> e p c d", p=P)

        def pairs(eng, body):
            with eng.Fori(0, EXPERTS // 2) as i:
                body(i)

        with nc.Block() as block:

            @block.sync
            def _(sp):
                sp.dma_start(z[:], z_dram.rearrange("(k p) t -> p k t", p=P)).then_inc(z_loaded, 16)
                for dst, src in ((router[:], router_dram.rearrange("(k p) e -> p k e", p=P)), (ident[:], ident_dram),
                                 (slots[:], slots_dram)):
                    sp.dma_start(dst, src).then_inc(loaded, 16)

                def stream(i):
                    for m in range(2 * FC):
                        s, e, c = m % 2, m // FC, m % FC
                        sp.wait_ge(in_used[s], FC * i + m // 2)
                        for g in range(2):
                            sp.dma_start(w_in[:, s, g], in_v[g][bass.ds(2 * i + e, 1), :, :, c * HALF:(c + 1) * HALF]
                                         .rearrange("e p k f -> p (e k) f")).then_inc(in_loaded[s], 16)
                        sp.wait_ge(out_used[s], FC * i + m // 2)
                        sp.dma_start(w_out[:, s], out_v[bass.ds(2 * i + e, 1), :, c * FT:(c + 1) * FT, :]
                                     .rearrange("e p c d -> p (e c) d")).then_inc(out_loaded[s], 16)

                pairs(sp, stream)
                sp.wait_ge(part_added, KT * EXPERTS // 2)
                sp.dma_start(out_dram.rearrange("(m p) t -> p m t", p=P), acc).then_inc(stored, 16)
                sp.wait_ge(stored, 16)

            @block.gpsimd
            def _(pool):
                pool.wait_ge(xe_ready, 2 * KT)

                def stage_tokens(i):
                    for e in range(2):
                        pool.wait_ge(in_used[1], (2 * i + e) * FC // 2)
                        nc.gpsimd.tensor_copy(xs[:, e], xe[:, :, bass.ds((2 * i + e) * CAPACITY, CAPACITY)]).then_inc(
                            xs_ready[e], 1)

                pairs(pool, stage_tokens)

            @block.tensor
            def _(pe):
                pe.wait_ge(z_loaded, 16)
                pe.wait_ge(loaded, 48)
                for t in range(TT):
                    for k in range(KT):
                        last = nc.tensor.matmul(bank[:, 0, t * EXPERTS:(t + 1) * EXPERTS], z[:, k, t * P:(t + 1) * P],
                                                router[:, k, :], start=(k == 0), stop=(k == KT - 1))
                last.then_inc(logits_made, 1)
                for n in range(2 * TT):
                    t, h = n // 2, n % 2
                    if n >= 2:
                        pe.wait_ge(z_tok_ready, n - 1)
                    for j in range(4):
                        last = nc.tensor.transpose(bank[:, 2 + n % 2, j * P:(j + 1) * P],
                                                   z[:, 4 * h + j, t * P:(t + 1) * P], ident[:])
                    last.then_inc(z_turned, 1)
                pe.wait_ge(route, MOE_AFFINITY)
                for t in range(TT):
                    last = nc.tensor.transpose(bank[0:EXPERTS, 1, t * P:(t + 1) * P], affinity[:, t], ident[:])
                last.then_inc(aff_turned, 1)
                pe.wait_ge(route, MOE_PLACES)
                for t in range(TT):
                    last = nc.tensor.transpose(bank[:, 0, t * EXPERTS:(t + 1) * EXPERTS], chosen[:, t * P:(t + 1) * P],
                                               ident[0:EXPERTS, 0:EXPERTS])
                last.then_inc(place_turned, 1)
                pe.wait_ge(hot_ready, TT)
                pe.wait_ge(z_tok_ready, 2 * TT)
                for n in range(2 * KT):
                    h, m = n // KT, n % KT
                    if n >= 2:
                        pe.wait_ge(xe_ready, n - 1)
                    for t in range(TT):
                        last = nc.tensor.matmul(bank[:, 4 + n % 2], z_tok[:, t, m * P:(m + 1) * P],
                                                hot[:, t, 8 * h:8 * h + 8].rearrange("p e s -> p (e s)"),
                                                start=(t == 0), stop=(t == TT - 1))
                    last.then_inc(xe_made, 1)
                for j in range(EXPERTS // 2):
                    pe.wait_ge(weighted, TT)
                    if j >= 2:
                        pe.wait_ge(scatter_ready, j - 1)
                    for t in range(TT):
                        last = nc.tensor.transpose(bank[:, 6 + j % 2, t * P:(t + 1) * P],
                                                   hot[:, t, 2 * j:2 * j + 2].rearrange("p e s -> p (e s)"), ident[:])
                    last.then_inc(hot_turned, 1)
                pe.wait_ge(xe_ready, 2 * KT)
                pe.wait_ge(scatter_ready, EXPERTS // 2)

                def experts(i):
                    def hidden(m):
                        s, e = m % 2, m // FC
                        pe.wait_ge(in_loaded[s], 32 * (FC * i + m // 2 + 1))
                        pe.wait_ge(xs_ready[e], i + 1)
                        if m >= 2:
                            pe.wait_ge(act_ready, 2 * FC * i + m - 1)
                        for k in range(KT):
                            for g in range(2):
                                last = nc.tensor.matmul(bank[64 * g:64 * g + 64, s], xs[:, e, k], w_in[:, s, g, k],
                                                        start=(k == 0), stop=(k == KT - 1))
                        last.then_inc(in_used[s], 1)

                    def output(m):
                        s, e, c = m % 2, m // FC, m % FC
                        pe.wait_ge(act_ready, 2 * FC * i + m + 1)
                        if m >= 2:
                            pe.wait_ge(act_t_ready, 2 * FC * i + m - 1)
                        for j in range(FT):
                            last = nc.tensor.transpose(bank[:, 2 + s, j * P:(j + 1) * P],
                                                       hot_flat[:, s * HALF + j * P:s * HALF + (j + 1) * P], ident[:])
                        last.then_inc(act_turned, 1)
                        pe.wait_ge(act_t_ready, 2 * FC * i + m + 1)
                        pe.wait_ge(out_loaded[s], 16 * (FC * i + m // 2 + 1))
                        if c == 0:
                            pe.wait_ge(y_ready, 2 * i + e)
                        for j in range(FT):
                            for h in range(2):
                                last = nc.tensor.matmul(bank[64 * e:64 * e + 64, 4 + h], act_t[:, s, j],
                                                        w_out[:, s, j, h * 512:(h + 1) * 512],
                                                        start=(c == 0 and j == 0), stop=(c == FC - 1 and j == FT - 1))
                        last.then_inc(out_used[s], 1)

                    for m in range(2 * FC):
                        hidden(m)
                        if m >= 1:
                            output(m - 1)
                    output(2 * FC - 1)
                    pe.wait_ge(y_ready, 2 * i + 2)
                    for m in range(KT):
                        if m >= 2:
                            pe.wait_ge(part_added, KT * i + m - 1)
                        nc.tensor.matmul(bank[:, 6 + m % 2], ye[:, m * P:(m + 1) * P],
                                         scatter[:, bass.ds(i, 1), :].rearrange("p a t -> p (a t)"),
                                         start=True, stop=True).then_inc(part_made, 1)

                pairs(pe, experts)

            @block.scalar
            def _(act):
                act.wait_ge(route, 3)
                nc.scalar.activation(logits[:], logits[:], ACT.Exp).then_inc(exp_ready, 1)
                for n in range(2 * TT):
                    act.wait_ge(z_turned, n + 1)
                    nc.scalar.copy(z_tok[:, n // 2, 512 * (n % 2):512 * (n % 2) + 512], bank[:, 2 + n % 2]).then_inc(
                        z_tok_ready, 1)
                for n in range(2 * KT):
                    act.wait_ge(xe_made, n + 1)
                    nc.scalar.copy(xe[:, n % KT, 512 * (n // KT):512 * (n // KT) + 512], bank[:, 4 + n % 2]).then_inc(
                        xe_ready, 1)
                for j in range(EXPERTS // 2):
                    act.wait_ge(hot_turned, j + 1)
                    nc.scalar.copy(scatter[:, j], bank[:, 6 + j % 2]).then_inc(scatter_ready, 1)

                act.wait_ge(xe_ready, 2 * KT)
                act.dma_start(acc, x_dram.rearrange("(m p) t -> p m t", p=P)).then_inc(x_loaded, 16)

                def experts(i):
                    for m in range(2 * FC):
                        s = m % 2
                        act.wait_ge(in_used[s], FC * i + m // 2 + 1)
                        if m >= 2:
                            act.wait_ge(act_turned, 2 * FC * i + m - 1)
                        nc.scalar.activation(sg[:, s], bank[0:CAPACITY, s], ACT.Silu).then_inc(silu_ready, 1)
                        act.wait_ge(act_turned, 2 * FC * i + m + 1)
                        if m >= 2:
                            act.wait_ge(out_used[s], FC * i + m // 2)
                        nc.scalar.copy(act_t[:, s], bank[:, 2 + s].rearrange("p (j n) -> p j n", j=FT)[:, :, 0:CAPACITY]).then_inc(
                            act_t_ready, 1)

                pairs(act, experts)

            @block.vector
            def _(dve):
                nc.vector.memset(ones[:], 1.0).then_inc(route, 1)
                done = [1]

                def step(ins):
                    ins.then_inc(route, 1)
                    done[0] += 1
                    dve.wait_ge(route, done[0])

                wide = [P, TT, EXPERTS]
                dve.wait_ge(logits_made, 1)
                raw = bank[:, 0, 0:TT * EXPERTS].rearrange("p (t e) -> p t e", t=TT)
                step(nc.vector.tensor_reduce(high[:], raw, X, ALU.max))
                step(nc.vector.tensor_tensor(logits[:], raw, high[:].unsqueeze(2).broadcast_to(wide), ALU.subtract))
                dve.wait_ge(exp_ready, 1)
                step(nc.vector.tensor_reduce(high[:], logits[:], X, ALU.add))
                step(nc.vector.reciprocal(high[:], high[:]))
                step(nc.vector.tensor_tensor(affinity[:], logits[:], high[:].unsqueeze(2).broadcast_to(wide), ALU.mult))
                assert done[0] == MOE_AFFINITY, done[0]
                dve.wait_ge(aff_turned, 1)
                step(nc.vector.tensor_copy(left[:], bank[0:EXPERTS, 1]))
                for _ in range(CAPACITY // 8):
                    step(nc.vector.max(best[:], left[:]))
                    step(nc.vector.match_replace(left[:], best[:], left[:], -1.0))
                step(nc.vector.tensor_scalar(chosen[:], left[:], 0.0, None, ALU.is_lt))
                step(nc.vector.tensor_tensor_scan(left[:], ones[:], chosen[:], 0.0, ALU.mult, ALU.add))
                step(nc.vector.tensor_tensor(chosen[:], chosen[:], left[:], ALU.mult))
                assert done[0] == MOE_PLACES, done[0]
                dve.wait_ge(place_turned, 1)
                step(nc.vector.tensor_copy(place_tok[:], raw))
                grid = [P, EXPERTS, CAPACITY]
                for t in range(TT):
                    nc.vector.tensor_tensor(hot[:, t], slots[:].unsqueeze(1).broadcast_to(grid),
                                            place_tok[:, t].unsqueeze(2).broadcast_to(grid), ALU.is_equal).then_inc(
                        hot_ready, 1)
                dve.wait_ge(xe_made, 2 * KT)
                dve.wait_ge(hot_ready, TT)
                for t in range(TT):
                    nc.vector.tensor_tensor(hot[:, t], hot[:, t], affinity[:, t].unsqueeze(2).broadcast_to(grid),
                                            ALU.mult).then_inc(weighted, 1)
                dve.wait_ge(x_loaded, 16)

                def experts(i):
                    for e in range(2):
                        for c in range(FC):
                            m = FC * e + c
                            s = m % 2
                            dve.wait_ge(silu_ready, 2 * FC * i + m + 1)
                            nc.vector.tensor_tensor(sg[:, s], sg[:, s], bank[64:64 + CAPACITY, s], ALU.mult).then_inc(
                                act_ready, 1)
                        dve.wait_ge(out_used[1], FC * i + FC // 2 * (e + 1))
                        dve.wait_ge(part_made, KT * i)
                        nc.vector.tensor_copy(ye[64 * e:64 * e + 64, :].rearrange("p (h d) -> p h d", h=2),
                                              bank[64 * e:64 * e + 64, 4:6, :]).then_inc(y_ready, 1)
                    for m in range(KT):
                        dve.wait_ge(part_made, KT * i + m + 1)
                        dve.wait_ge(part_added, KT * i)
                        nc.vector.tensor_tensor(acc[:, m], acc[:, m], bank[:, 6 + m % 2], ALU.add).then_inc(part_added, 1)

                pairs(dve, experts)


MOE_AFFINITY = 6
MOE_PLACES = MOE_AFFINITY + 1 + 2 * (CAPACITY // 8) + 3


D_FF = 2816
N_MEM = 256
NA_WIDTH = 384
MEM_WIDTH = 256


def two_blocks(nc, d, out_dram):
    STAGE_TURN.clear()

    def scratch(name, rows, cols):
        return nc.dram_tensor(name, (rows, cols), F32, kind="Internal").ap()

    p = scratch("p", 5 * D_MODEL + 2 * D_MODEL, LEN)
    ya_raw = scratch("ya_raw", D_MODEL, LEN)
    ya = scratch("ya", D_MODEL, LEN)
    yb = scratch("yb", D_MODEL, LEN)
    gated_a = scratch("gated_a", D_MODEL, LEN)
    merged = scratch("merged", D_MODEL, LEN)
    h1 = scratch("h1", D_MODEL, LEN)
    a1 = scratch("a1", D_FF, LEN)
    h2 = scratch("h2", D_MODEL, LEN)
    project(nc, "in", d["h"], d["w_in"], p, gain_dram=d["mix_norm_g"])
    s5(nc, "s5", p[0:D_MODEL], d["ssm_lam"], d["ssm_bc"], d["ssm_d"], d["ident"], ya_raw)
    project(nc, "glu", ya_raw, d["ssm_w_glu"], ya, "glu", [ya_raw])
    hgrn2(nc, "hgrn", p[D_MODEL:5 * D_MODEL], d["hgrn_lb"], d["hgrn_norm_g"], d["ident"], d["hgrn_causal"],
          d["hgrn_member"], yb)
    project(nc, "ssm_proj", ya, d["w_ssm_proj"], gated_a, "gate", [p[5 * D_MODEL:6 * D_MODEL]])
    project(nc, "hgrn_proj", yb, d["w_hgrn_proj"], merged, "gate_add", [p[6 * D_MODEL:7 * D_MODEL], gated_a])
    project(nc, "mix_out", merged, d["w_out"], h1, "add", [d["h"]])
    conv_gated_up(nc, "up", h1, d["ffn_norm_g"], d["w_up"], d["conv_w"], d["conv_b"], a1)
    project(nc, "down", a1, d["w_down"], h2, "add", [h1], width=P)

    x = scratch("x", D_MODEL, SEQ)
    widths = [3 * NA_WIDTH, 3 * RW_WIDTH + 2 * P, MEM_WIDTH, D_MODEL, D_MODEL, D_MODEL]
    starts = [sum(widths[:n]) for n in range(len(widths) + 1)]
    p2 = scratch("p2", starts[-1], SEQ)
    p_na, p_rw, q_mem, g_na, g_rw, g_mem = (p2[starts[n]:starts[n + 1]] for n in range(len(widths)))
    kv = scratch("kv", 2 * MEM_WIDTH, N_MEM)
    y_na = scratch("y_na", NA_WIDTH, SEQ)
    y_rw = scratch("y_rw", RW_WIDTH, SEQ)
    y_mem = scratch("y_mem", MEM_WIDTH, SEQ)
    m_na = scratch("m_na", D_MODEL, SEQ)
    m_rw = scratch("m_rw", D_MODEL, SEQ)
    m_all = scratch("m_all", D_MODEL, SEQ)
    x3 = scratch("x3", D_MODEL, SEQ)
    z3 = scratch("z3", D_MODEL, SEQ)
    x4 = scratch("x4", D_MODEL, SEQ)
    rmsnorm(nc, "norm_final", h2[:, N_META:], d["final_norm_g"], x)
    project(nc, "in_2", x, d["w_in_2"], p2, gain_dram=d["norm_mix_g_2"])
    project(nc, "mem_kv", d["mem"], d["w_mem_kv_2"], kv, gain_dram=d["norm_mem_g_2"])
    attention(nc, "na", p_na[0:NA_WIDTH], p_na[NA_WIDTH:2 * NA_WIDTH], p_na[2 * NA_WIDTH:], d["na_bias"],
              d["ident"], y_na)
    attention(nc, "mem", q_mem, kv[0:MEM_WIDTH], kv[MEM_WIDTH:], None, d["ident"], y_mem)
    rwkv7(nc, "rw", p_rw, d["rw_par"], d["rw_mu_l"], d["rw_lora"], d["rw_g2_2"], d["ident"], d["rw_masks"],
          d["rw_member"], d["eye2"], y_rw)
    project(nc, "na_proj", y_na, d["w_branch_na_2"], m_na, "gate", [g_na])
    project(nc, "rw_proj", y_rw, d["w_branch_rw_2"], m_rw, "gate_add", [g_rw, m_na])
    project(nc, "mem_proj", y_mem, d["w_branch_mem_2"], m_all, "gate_add", [g_mem, m_rw])
    project(nc, "mix_out_2", m_all, d["w_out_2"], x3, "add", [x])
    rmsnorm(nc, "norm_ffn_2", x3, d["norm_ffn_g_2"], z3)
    expert_ffn(nc, "moe", z3, x3, d["w_router_2"], d["w_exp_gate_2"], d["w_exp_up_2"], d["w_exp_down_2"],
               d["ident"], d["slots"], x4)
    rmsnorm(nc, "norm_final_2", x4, d["norm_final_g_2"], out_dram)


def by_partition(a):
    return np.ascontiguousarray(a.reshape(-1, P).T)


def by_state(a):
    a = a.reshape(PAIRS, 2, SSM_STATE, *a.shape[2:])
    return np.moveaxis(a, 0, 2).reshape(P, PAIRS, *a.shape[3:])


def laid_out(v):
    d = {}
    d["h"] = np.concatenate([v["meta_tokens"], v["x"][0]], axis=0).T
    d["mem"] = v["mem_2"][0].T
    for name in ("mix_norm_g", "ffn_norm_g", "final_norm_g", "norm_mix_g_2", "norm_mem_g_2", "norm_ffn_g_2",
                 "norm_final_g_2"):
        d[name] = by_partition(v[name].reshape(-1))
    for name in ("w_in", "ssm_w_glu", "w_ssm_proj", "w_hgrn_proj", "w_out", "w_up", "w_down", "w_in_2", "w_mem_kv_2",
                 "w_branch_na_2", "w_branch_rw_2", "w_branch_mem_2", "w_out_2", "w_router_2", "w_exp_gate_2",
                 "w_exp_up_2", "w_exp_down_2", "rw_g2_2"):
        d[name] = v[name][0]
    log_dt = np.broadcast_to(v["ssm_log_dt"][0][:, None], (SSM_GROUPS, SSM_STATE))
    d["ssm_lam"] = np.stack([by_state(a) for a in (v["ssm_lambda_re"][0], v["ssm_lambda_im"][0], log_dt)], 1)
    d["ssm_bc"] = np.stack([by_state(a) for a in (
        v["ssm_b_re"][0], v["ssm_b_im"][0], v["ssm_c_re"][0].transpose(0, 2, 1), v["ssm_c_im"][0].transpose(0, 2, 1))], 1)
    d["ssm_d"] = by_partition(v["ssm_d"][0])
    d["hgrn_lb"] = v["hgrn_lb_logits"].reshape(2, HEADS, P).transpose(2, 0, 1)
    d["hgrn_norm_g"] = v["hgrn_norm_g"][0].reshape(P, 1)
    d["conv_w"] = v["conv_w"][0].reshape(3, 2 * D_FF // P, P).transpose(2, 1, 0)
    d["conv_b"] = by_partition(v["conv_b"][0])
    d["na_bias"] = window_bias(v["na_rpb_2"][0])
    rw = {name: v[f"rw_{name}_2"][0] for name in ("mu_rkv", "mu_w", "mu_a", "w0", "w2", "a0", "a2", "k_k", "k_a", "r_k",
                                                 "ln_g", "ln_b")}
    columns = [rw["mu_rkv"][dd, j] for j in range(3) for dd in range(2)] + [rw["w0"][dd] for dd in range(2)] + [
        rw["a0"][dd] for dd in range(2)] + [rw["k_k"], rw["k_a"], rw["r_k"].reshape(-1), rw["ln_g"], rw["ln_b"]]
    d["rw_par"] = np.stack([c.reshape(RW_X, P) for c in columns]).transpose(2, 0, 1)
    d["rw_mu_l"] = np.concatenate([rw["mu_w"], rw["mu_a"]], 1).T
    d["rw_lora"] = np.concatenate([rw["w2"], rw["a2"]], 1).transpose(1, 0, 2)
    n = np.arange(P)
    f32 = np.float32
    d["ident"] = np.eye(P, dtype=f32)
    d["eye2"] = np.concatenate([np.eye(HEAD_DIM, dtype=f32)] * 2)
    d["slots"] = np.broadcast_to(np.arange(1, CAPACITY + 1, dtype=f32), (P, CAPACITY))
    s, t = n[:, None], n[None, :]
    d["hgrn_causal"] = ((s // HCHUNK == t // HCHUNK) & (s <= t)).astype(f32)
    d["hgrn_member"] = np.broadcast_to((s // HCHUNK == np.arange(P // HCHUNK))[:, :, None],
                                       (P, P // HCHUNK, P)).astype(f32)
    same = s // RCHUNK == t // RCHUNK
    d["rw_masks"] = np.stack([np.stack([same & (s < t), same & (s <= t)] * 2, 1),
                              np.stack([same & (s > t), same & (s >= t)] * 2, 1)], 1).astype(f32)
    d["rw_member"] = np.broadcast_to((s // RCHUNK == np.arange(P // RCHUNK))[:, :, None],
                                     (P, P // RCHUNK, P)).astype(f32)
    return {name: np.ascontiguousarray(a) for name, a in d.items()}


def kernel(**inputs):
    import concourse.bacc as bacc
    from concourse.bass_utils import run_bass_kernel_spmd

    arrays = laid_out({name: np.asarray(a) for name, a in inputs.items()})
    nc = bacc.Bacc("TRN2", target_bir_lowering=False, num_devices=1)
    ins = {name: nc.dram_tensor(f"in_{name}", a.shape, mybir.dt.from_np(a.dtype), kind="ExternalInput").ap()
           for name, a in arrays.items()}
    out = nc.dram_tensor("out", (D_MODEL, SEQ), F32, kind="ExternalOutput").ap()
    two_blocks(nc, ins, out)
    r = run_bass_kernel_spmd(nc, [{f"in_{name}": a for name, a in arrays.items()}], core_ids=[0])
    return np.ascontiguousarray(r.results[0]["out"].T).reshape(1, SEQ, D_MODEL)
```

```python
from contextlib import ExitStack

import numpy as np

import concourse.bass as bass
from concourse import mybir

P = 128
ALU = mybir.AluOpType
ACT = mybir.ActivationFunctionType
F32 = mybir.dt.float32
X = mybir.AxisListType.X

D_MODEL = 1024
KT = D_MODEL // P
SEQ = 512
N_META = 16
LEN = SEQ + N_META
EPS = 1e-6


STAGE_TURN = []


def opener(nc, ctx, stage):
    free = sorted(nc.free_semaphores)
    half = len(free) // 2
    STAGE_TURN.append(stage)
    own = free[:half] if len(STAGE_TURN) % 2 else free[half:2 * half]
    sems = []

    def close():
        nc.gpsimd.sem_clear(range(own[0], own[0] + len(sems)))
        for s in sems:
            nc.release_semaphore(s)

    ctx.callback(close)

    def sb(name, shape, dt=F32):
        return ctx.enter_context(nc.sbuf_tensor(f"{stage}_{name}", shape, dt))

    def ps(name, shape):
        return ctx.enter_context(nc.psum_tensor(f"{stage}_{name}", shape, F32))

    def sem(name):
        sems.append(nc.alloc_semaphore(f"{stage}_{name}", num=own[0] + len(sems)))
        return sems[-1]

    return sb, ps, sem


def rmsnorm(nc, stage, x_dram, gain_dram, out_dram):
    C, T = x_dram.shape
    kt = C // P
    halves = 1 if T <= 512 else 2
    w = T // halves
    with ExitStack() as ctx:
        sb, ps, sem = opener(nc, ctx, stage)
        x = sb("x", [P, kt, T])
        sq = sb("sq", [P, kt, T])
        gain = sb("gain", [P, kt])
        ones = sb("ones", [P, P])
        scale = sb("scale", [P, T])
        total = ps("total", [P, halves, 512])
        x_loaded = [sem(f"x_loaded{k}") for k in range(kt)]
        gain_loaded = sem("gain_loaded")
        consts_ready = sem("consts_ready")
        squared = sem("squared")
        summed = sem("summed")
        meaned = sem("meaned")
        inverted = sem("inverted")
        rooted = sem("rooted")
        scaled = sem("scaled")
        stored = sem("stored")
        xv = x_dram.rearrange("(k p) t -> p k t", p=P)
        ov = out_dram.rearrange("(k p) t -> p k t", p=P)
        total_v = total[:, :, 0:w]

        with nc.Block() as block:

            @block.sync
            def _(sp):
                for k in range(kt):
                    sp.dma_start(x[:, k, :], xv[:, k, :]).then_inc(x_loaded[k], 16)
                sp.dma_start(gain[:], gain_dram).then_inc(gain_loaded, 16)
                for k in range(kt):
                    sp.wait_ge(scaled, k + 1)
                    sp.dma_start(ov[:, k, :], x[:, k, :]).then_inc(stored, 16)
                sp.wait_ge(stored, 16 * kt)

            @block.scalar
            def _(act):
                for k in range(kt):
                    act.wait_ge(x_loaded[k], 16)
                    nc.scalar.activation(sq[:, k, :], x[:, k, :], ACT.Square).then_inc(squared, 1)
                act.wait_ge(inverted, 1)
                nc.scalar.activation(scale[:], scale[:], ACT.Sqrt).then_inc(rooted, 1)

            @block.tensor
            def _(pe):
                pe.wait_ge(consts_ready, 1)
                for k in range(kt):
                    pe.wait_ge(squared, k + 1)
                    for h in range(halves):
                        last = nc.tensor.matmul(total[:, h, 0:w], ones[:], sq[:, k, h * w:(h + 1) * w],
                                                start=(k == 0), stop=(k == kt - 1))
                last.then_inc(summed, 1)

            @block.vector
            def _(dve):
                nc.vector.memset(ones[:], 1.0).then_inc(consts_ready, 1)
                dve.wait_ge(summed, 1)
                nc.vector.tensor_scalar(scale[:].rearrange("p (h t) -> p h t", h=halves), total_v,
                                        1.0 / C, EPS, ALU.mult, ALU.add).then_inc(meaned, 1)
                dve.wait_ge(meaned, 1)
                nc.vector.reciprocal(scale[:], scale[:]).then_inc(inverted, 1)
                dve.wait_ge(rooted, 1)
                dve.wait_ge(gain_loaded, 16)
                for k in range(kt):
                    dve.wait_ge(x_loaded[k], 16)
                    dve.wait_ge(squared, k + 1)
                    nc.vector.scalar_tensor_tensor(x[:, k, :], x[:, k, :], gain[:, k:k + 1], scale[:],
                                                   ALU.mult, ALU.mult).then_inc(scaled, 1)


F32R = mybir.dt.float32r


def three_passes(nc, to, w_high, w_low, x_high, x_low, start, stop):
    nc.tensor.matmul(to, w_high, x_low, start=start, stop=False)
    nc.tensor.matmul(to, w_low, x_high, start=False, stop=False)
    return nc.tensor.matmul(to, w_high, x_high, start=False, stop=stop)


def project(nc, stage, x_dram, w_dram, out_dram, epilogue="copy", extras=(), width=2 * P, gain_dram=None):
    K, T = x_dram.shape
    M = w_dram.shape[1]
    kt = K // P
    nm = width // P
    slots = M // width
    halves = 1 if T <= 512 else 2
    w_t = T // halves
    n_extra = len(extras)
    norm = gain_dram is not None
    assert not norm or epilogue == "copy"
    RAW = min(kt, 8)
    with ExitStack() as ctx:
        sb, ps, sem = opener(nc, ctx, stage)
        x_raw = sb("x_raw", [P, RAW, T])
        x_high = sb("x_high", [P, kt, T], F32R)
        x_low = sb("x_low", [P, kt, T], F32R)
        w = sb("w", [P, 2, kt, width])
        w_high = sb("w_high", [P, 2, kt, width], F32R)
        w_low = sb("w_low", [P, 2, kt, width], F32R)
        out = sb("out", [P, 2, nm, T])
        if n_extra:
            e = sb("e", [P, 2, n_extra, nm, T])
        if epilogue in ("glu", "gate", "gate_add"):
            gate = sb("gate", [P, 2, nm, T])
        if norm:
            gain = sb("gain", [P, kt])
            sq = sb("sq", [P, 2, T])
            ones = sb("ones", [P, P])
            scale = sb("scale", [P, halves, w_t])
            gain_loaded = sem("gain_loaded")
            ones_ready = sem("ones_ready")
            squared = sem("squared")
            summed = sem("summed")
            meaned = sem("meaned")
            inverted = sem("inverted")
            rooted = sem("rooted")
        y = ps("y", [P, 2, nm, halves, 512])
        x_loaded = [sem(f"x_loaded{k}") for k in range(kt)]
        x_high_ready = sem("x_high_ready")
        x_ready = sem("x_ready")
        w_loaded = [sem(f"w_loaded{s}") for s in range(2)]
        w_high_ready = sem("w_high_ready")
        w_ready = sem("w_ready")
        e_loaded = [sem(f"e_loaded{s}") for s in range(2)]
        y_ready = sem("y_ready")
        gate_ready = sem("gate_ready")
        mul_ready = sem("mul_ready")
        out_ready = sem("out_ready")
        stored = [sem(f"stored{s}") for s in range(2)]
        xv = x_dram.rearrange("(k p) t -> p k t", p=P)
        wv = w_dram.rearrange("(k p) m -> p k m", p=P)
        ov = out_dram.rearrange("(m p) t -> p m t", p=P)
        ev = [a.rearrange("(m p) t -> p m t", p=P) for a in extras]

        def y_of(s):
            return y[:, s, :, :, 0:w_t].rearrange("p m h t -> p (m h) t")

        def flat(a):
            return a.rearrange("p m (h t) -> p (m h) t", h=halves)

        def over_slots(eng, body):
            loops = slots // 2
            for s in range(min(2, slots)):
                body(0, s, True, s == slots - 1)
            end = loops - 1 if slots % 2 == 0 else loops
            if end > 1:
                with eng.Fori(1, end) as i:
                    for s in range(2):
                        body(i, s, False, False)
            for n in range(2 * max(end, 1), slots):
                body(n // 2, n % 2, False, n == slots - 1)

        with nc.Block() as block:

            @block.sync
            def _(sp):
                def load_w(i, s, first, last):
                    if not first:
                        sp.wait_ge(w_ready, 2 * i + s - 1)
                    sp.dma_start(w[:, s], wv[:, :, bass.ds((2 * i + s) * width, width)]).then_inc(w_loaded[s], 16)
                    for n in range(n_extra):
                        if not first and n == 0:
                            sp.wait_ge(out_ready, 2 * i + s - 1)
                        sp.dma_start(e[:, s, n], ev[n][:, bass.ds((2 * i + s) * nm, nm), :]).then_inc(e_loaded[s], 16)
                    if first and s == 1:
                        for k in range(RAW, kt):
                            sp.wait_ge(x_ready, k - RAW + 1)
                            sp.dma_start(x_raw[:, k % RAW, :], xv[:, k, :]).then_inc(x_loaded[k], 16)

                if norm:
                    sp.dma_start(gain[:], gain_dram).then_inc(gain_loaded, 16)
                over_slots(sp, load_w)

            @block.tensor
            def _(pe):
                if norm:
                    pe.wait_ge(ones_ready, 1)

                def products(i, s, first, last):
                    pe.wait_ge(w_ready, 2 * i + s + 1)
                    if not first:
                        pe.wait_ge(out_ready, 2 * i + s - 1)
                    if norm and first and s == 1:
                        pe.wait_ge(meaned, 1)
                    for m in range(nm):
                        for h in range(halves):
                            for k in range(kt):
                                if first and s == 0 and m == 0 and h == 0:
                                    pe.wait_ge(x_ready, k + 1)
                                    if norm:
                                        pe.wait_ge(squared, k + 1)
                                        for b in range(halves):
                                            one = nc.tensor.matmul(y[:, 1, 0, b, 0:w_t], ones[:],
                                                                   sq[:, k % 2, b * w_t:(b + 1) * w_t],
                                                                   start=(k == 0), stop=(k == kt - 1))
                                        one.then_inc(summed, 1)
                                tokens = slice(h * w_t, (h + 1) * w_t)
                                columns = slice(m * P, (m + 1) * P)
                                done = three_passes(nc, y[:, s, m, h, 0:w_t], w_high[:, s, k, columns],
                                                    w_low[:, s, k, columns], x_high[:, k, tokens],
                                                    x_low[:, k, tokens], k == 0, k == kt - 1)
                    done.then_inc(y_ready, 1)

                over_slots(pe, products)

            @block.scalar
            def _(act):
                def split_x_high(k):
                    act.wait_ge(x_loaded[k], 16)
                    if norm:
                        if k >= 2:
                            act.wait_ge(summed, k - 1)
                        nc.scalar.activation(sq[:, k % 2, :], x_raw[:, k], ACT.Square).then_inc(squared, 1)
                        act.wait_ge(gain_loaded, 16)
                        nc.scalar.activation(x_high[:, k], x_raw[:, k], ACT.Copy, scale=gain[:, k:k + 1]).then_inc(
                            x_high_ready, 1)
                    else:
                        nc.scalar.copy(x_high[:, k], x_raw[:, k % RAW]).then_inc(x_high_ready, 1)

                def split_w_high(i, s, fresh):
                    act.wait_ge(w_loaded[s], (i + 1) * 16)
                    if not fresh:
                        act.wait_ge(y_ready, 2 * i + s - 1)
                    nc.scalar.copy(w_high[:, s], w[:, s]).then_inc(w_high_ready, 1)

                for k in range(RAW):
                    act.dma_start(x_raw[:, k, :], xv[:, k, :]).then_inc(x_loaded[k], 16)
                split_x_high(0)
                split_w_high(0, 0, True)
                for k in range(1, kt):
                    split_x_high(k)

                def evacuate(i, s, first, last):
                    if not last:
                        split_w_high(i + (s + 1) // 2, (s + 1) % 2, first and s == 0)
                    if epilogue == "copy" and not norm:
                        act.wait_ge(y_ready, 2 * i + s + 1)
                        if not first:
                            act.wait_ge(stored[s], i * 16)
                        nc.scalar.copy(flat(out[:, s]), y_of(s)).then_inc(out_ready, 1)
                    elif epilogue == "glu":
                        act.wait_ge(y_ready, 2 * i + s + 1)
                        if not first:
                            act.wait_ge(out_ready, 2 * i + s - 1)
                        nc.scalar.activation(flat(gate[:, s]), y_of(s), ACT.Sigmoid).then_inc(gate_ready, 1)
                    elif epilogue in ("gate", "gate_add"):
                        act.wait_ge(e_loaded[s], (i + 1) * 16 * n_extra)
                        if not first:
                            act.wait_ge(out_ready, 2 * i + s - 1)
                        nc.scalar.activation(gate[:, s], e[:, s, 0], ACT.Sigmoid).then_inc(gate_ready, 1)
                    act.wait_ge(out_ready, 2 * i + s + 1)
                    act.dma_start(ov[:, bass.ds((2 * i + s) * nm, nm), :], out[:, s]).then_inc(stored[s], 16)

                if norm:
                    act.wait_ge(inverted, 1)
                    nc.scalar.activation(scale[:], scale[:], ACT.Sqrt).then_inc(rooted, 1)
                over_slots(act, evacuate)
                for s in range(2):
                    if (slots + 1 - s) // 2:
                        act.wait_ge(stored[s], 16 * ((slots + 1 - s) // 2))

            @block.vector
            def _(dve):
                if norm:
                    nc.vector.memset(ones[:], 1.0).then_inc(ones_ready, 1)
                    dve.wait_ge(gain_loaded, 16)

                def split_w_low(i, s, fresh):
                    dve.wait_ge(w_high_ready, 2 * i + s + 1)
                    if not fresh:
                        dve.wait_ge(y_ready, 2 * i + s - 1)
                    nc.vector.tensor_tensor(w_low[:, s], w[:, s], w_high[:, s].bitcast(F32), ALU.subtract).then_inc(
                        w_ready, 1)

                for k in range(kt):
                    if k == 1:
                        split_w_low(0, 0, True)
                    dve.wait_ge(x_high_ready, k + 1)
                    high = x_high[:, k].bitcast(F32)
                    if norm:
                        nc.vector.scalar_tensor_tensor(x_low[:, k], x_raw[:, k], gain[:, k:k + 1], high, ALU.mult,
                                                       ALU.subtract).then_inc(x_ready, 1)
                    else:
                        nc.vector.tensor_tensor(x_low[:, k], x_raw[:, k % RAW], high, ALU.subtract).then_inc(x_ready, 1)
                if norm:
                    dve.wait_ge(summed, kt)
                    nc.vector.tensor_scalar(scale[:], y[:, 1, 0, :, 0:w_t], 1.0 / K, EPS, ALU.mult, ALU.add).then_inc(
                        meaned, 1)
                    dve.wait_ge(meaned, 1)
                    nc.vector.reciprocal(scale[:], scale[:]).then_inc(inverted, 1)

                def finish(i, s, first, last):
                    if not last:
                        split_w_low(i + (s + 1) // 2, (s + 1) % 2, first and s == 0)
                    if epilogue == "copy" and not norm:
                        return
                    dve.wait_ge(y_ready, 2 * i + s + 1)
                    if n_extra:
                        dve.wait_ge(e_loaded[s], (i + 1) * 16 * n_extra)
                    if epilogue in ("glu", "gate", "gate_add"):
                        dve.wait_ge(gate_ready, 2 * i + s + 1)
                    if not first:
                        dve.wait_ge(stored[s], i * 16)
                    if norm:
                        if first and s == 0:
                            dve.wait_ge(rooted, 1)
                        for m in range(nm):
                            done = nc.vector.tensor_tensor(
                                out[:, s, m].rearrange("p (h t) -> p h t", h=halves), y[:, s, m, :, 0:w_t], scale[:],
                                ALU.mult)
                        done.then_inc(out_ready, 1)
                    elif epilogue == "glu":
                        nc.vector.tensor_tensor(out[:, s], gate[:, s], e[:, s, 0], ALU.mult).then_inc(out_ready, 1)
                    elif epilogue == "gate":
                        nc.vector.tensor_tensor(flat(out[:, s]), y_of(s), flat(gate[:, s]), ALU.mult).then_inc(out_ready, 1)
                    elif epilogue == "gate_add":
                        nc.vector.tensor_tensor(flat(out[:, s]), y_of(s), flat(gate[:, s]), ALU.mult).then_inc(mul_ready, 1)
                        dve.wait_ge(mul_ready, 2 * i + s + 1)
                        nc.vector.tensor_tensor(out[:, s], out[:, s], e[:, s, 1], ALU.add).then_inc(out_ready, 1)
                    elif epilogue == "add":
                        nc.vector.tensor_tensor(flat(out[:, s]), y_of(s), flat(e[:, s, 0]), ALU.add).then_inc(out_ready, 1)

                over_slots(dve, finish)


def project_chain(nc, stage, steps, out_dram, gain_dram=None, z_dram=None):
    T = steps[0][3].shape[1]
    nm = 2
    width = nm * P
    per_step = D_MODEL // width
    halves = 1 if T <= 512 else 2
    w_t = T // halves
    slots = [(n, j) for n in range(len(steps)) for j in range(per_step)]
    kts = [w.shape[0] // P for _, w, *_ in steps]
    x_before = [sum(kts[:n]) for n in range(len(steps))]
    rounds = [sum(x is not None for x, *_ in steps[:n]) for n in range(len(steps))]
    assert all(steps[n][0] is not None or steps[n - 1][4] == "x" for n in range(len(steps)))
    with ExitStack() as ctx:
        sb, ps, sem = opener(nc, ctx, stage)
        x_raw = sb("x_raw", [P, KT, T])
        x_high = sb("x_high", [P, 2, KT, T], F32R)
        x_low = sb("x_low", [P, 2, KT, T], F32R)
        w = sb("w", [P, 2, KT, width])
        w_high = sb("w_high", [P, 2, KT, width], F32R)
        w_low = sb("w_low", [P, 2, KT, width], F32R)
        e = sb("e", [P, 2, nm, T])
        gate = sb("gate", [P, 2, nm, T])
        res = sb("res", [P, KT, T])
        y = ps("y", [P, 2, nm, halves, 512])
        norm = gain_dram is not None
        if norm:
            total = ps("total", [P, 512])
            gain = sb("gain", [P, KT])
            ones = sb("ones", [P, P])
            scale = sb("scale", [P, T])
            consts_ready = sem("consts_ready")
            gain_loaded = sem("gain_loaded")
            squared = sem("squared")
            summed = sem("summed")
            meaned = sem("meaned")
            inverted = sem("inverted")
            rooted = sem("rooted")
            scaled = sem("scaled")
            z_stored = sem("z_stored")
        x_loaded = [sem(f"x_loaded{k}") for k in range(KT)]
        x_high_ready = sem("x_high_ready")
        x_ready = sem("x_ready")
        w_loaded = [sem(f"w_loaded{s}") for s in range(2)]
        w_high_ready = sem("w_high_ready")
        w_ready = sem("w_ready")
        e_loaded = [sem(f"e_loaded{s}") for s in range(2)]
        y_ready = sem("y_ready")
        gate_ready = sem("gate_ready")
        gated = sem("gated")
        res_ready = sem("res_ready")
        stored = sem("stored")

        def flat(a):
            return a.rearrange("p m (h t) -> p (m h) t", h=halves)

        def y_of(s):
            return y[:, s, :, :, 0:w_t].rearrange("p m h t -> p (m h) t")

        def tiles(j):
            return slice(nm * j, nm * j + nm)

        def rounds_of(n, k):
            return sum(steps[i][0] is not None and k < kts[i] for i in range(n))

        def load_x(eng, n):
            if rounds[n]:
                before = max(i for i in range(n) if steps[i][0] is not None)
                eng.wait_ge(x_ready, x_before[before] + kts[before])
            xv = steps[n][0].rearrange("(k p) t -> p k t", p=P)
            for k in range(kts[n]):
                eng.dma_start(x_raw[:, k], xv[:, k]).then_inc(x_loaded[k], 16)

        with nc.Block() as block:

            @block.sync
            def _(sp):
                for g, (n, j) in enumerate(slots):
                    s = g % 2
                    if g >= 2:
                        sp.wait_ge(w_ready, g - 1)
                    sp.dma_start(w[:, s, 0:kts[n]], steps[n][1].rearrange("(k p) m -> p k m", p=P)[
                        :, :, j * width:(j + 1) * width]).then_inc(w_loaded[s], 16)
                    if g >= 2:
                        sp.wait_ge(res_ready, g - 1)
                    sp.dma_start(e[:, s], steps[n][3].rearrange("(m p) t -> p m t", p=P)[:, tiles(j)]).then_inc(
                        e_loaded[s], 16)
                    if j == 0 and n + 1 < len(steps) and steps[n + 1][0] is not None:
                        load_x(sp, n + 1)
                if norm:
                    sp.dma_start(gain[:], gain_dram).then_inc(gain_loaded, 16)
                    for k in range(KT):
                        sp.wait_ge(scaled, k + 1)
                        sp.dma_start(z_dram[k * P:(k + 1) * P, :], x_raw[:, k]).then_inc(z_stored, 16)
                    sp.wait_ge(z_stored, 16 * KT)

            @block.tensor
            def _(pe):
                def sum_squares(j):
                    pe.wait_ge(consts_ready, 1)
                    pe.wait_ge(squared, j + 1)
                    for m in range(nm):
                        last = nc.tensor.matmul(total[:, 0:T], ones[:], gate[:, j % 2, m], start=(j == 0 and m == 0),
                                                stop=(j == per_step - 1 and m == nm - 1))
                    last.then_inc(summed, 1)

                for g, (n, j) in enumerate(slots):
                    s = g % 2
                    pe.wait_ge(w_ready, g + 1)
                    if g >= 2:
                        pe.wait_ge(res_ready, g - 1)
                    for m in range(nm):
                        for h in range(halves):
                            for k in range(kts[n]):
                                if j == 0 and m == 0 and h == 0:
                                    pe.wait_ge(x_ready, x_before[n] + k + 1)
                                tokens = slice(h * w_t, (h + 1) * w_t)
                                columns = slice(m * P, (m + 1) * P)
                                done = three_passes(nc, y[:, s, m, h, 0:w_t], w_high[:, s, k, columns],
                                                    w_low[:, s, k, columns], x_high[:, n % 2, k, tokens],
                                                    x_low[:, n % 2, k, tokens], k == 0, k == kts[n] - 1)
                    done.then_inc(y_ready, 1)
                    if norm and n == len(steps) - 1 and j >= 1:
                        sum_squares(j - 1)
                if norm:
                    sum_squares(per_step - 1)

            @block.scalar
            def _(act):
                def split_w_high(g):
                    kt = kts[slots[g][0]]
                    act.wait_ge(w_loaded[g % 2], 16 * (g // 2 + 1))
                    if g >= 2:
                        act.wait_ge(y_ready, g - 1)
                    nc.scalar.copy(w_high[:, g % 2, 0:kt], w[:, g % 2, 0:kt]).then_inc(w_high_ready, 1)

                def split_x_high(n, k):
                    act.wait_ge(x_loaded[k], 16 * (rounds_of(n, k) + 1))
                    if n >= 2:
                        act.wait_ge(y_ready, per_step * (n - 1))
                    nc.scalar.copy(x_high[:, n % 2, k], x_raw[:, k]).then_inc(x_high_ready, 1)

                load_x(act, 0)
                for k in range(kts[0]):
                    split_x_high(0, k)
                    if k == 0:
                        split_w_high(0)
                for g, (n, j) in enumerate(slots):
                    s = g % 2
                    _, _, epilogue, _, goes_to = steps[n]
                    if g + 1 < len(slots):
                        split_w_high(g + 1)
                    if j == 1 and n + 1 < len(steps) and steps[n + 1][0] is not None:
                        for k in range(kts[n + 1]):
                            split_x_high(n + 1, k)
                    if epilogue != "add":
                        if g >= 2:
                            act.wait_ge(res_ready, g - 1)
                        if epilogue == "glu":
                            act.wait_ge(y_ready, g + 1)
                            nc.scalar.activation(flat(gate[:, s]), y_of(s), ACT.Sigmoid).then_inc(gate_ready, 1)
                        else:
                            act.wait_ge(e_loaded[s], 16 * (g // 2 + 1))
                            nc.scalar.activation(gate[:, s], e[:, s], ACT.Sigmoid).then_inc(gate_ready, 1)
                    if goes_to != "merged":
                        act.wait_ge(res_ready, g + 1)
                    if goes_to == "x":
                        if n >= 1:
                            act.wait_ge(y_ready, per_step * n)
                        nc.scalar.copy(x_high[:, (n + 1) % 2, tiles(j)], res[:, tiles(j)]).then_inc(x_high_ready, nm)
                    if goes_to == "out":
                        act.dma_start(out_dram.rearrange("(m p) t -> p m t", p=P)[:, tiles(j)],
                                      res[:, tiles(j)]).then_inc(stored, 16)
                        if norm:
                            if j >= 2:
                                act.wait_ge(summed, j - 1)
                            nc.scalar.activation(gate[:, s], res[:, tiles(j)], ACT.Square).then_inc(squared, 1)
                if norm:
                    act.wait_ge(inverted, 1)
                    nc.scalar.activation(scale[:], scale[:], ACT.Sqrt).then_inc(rooted, 1)
                act.wait_ge(stored, 16 * per_step)

            @block.vector
            def _(dve):
                def split_w_low(g):
                    kt = kts[slots[g][0]]
                    dve.wait_ge(w_high_ready, g + 1)
                    if g >= 2:
                        dve.wait_ge(y_ready, g - 1)
                    nc.vector.tensor_tensor(w_low[:, g % 2, 0:kt], w[:, g % 2, 0:kt], w_high[:, g % 2, 0:kt].bitcast(F32),
                                            ALU.subtract).then_inc(w_ready, 1)

                def split_x_low(n, k):
                    dve.wait_ge(x_high_ready, x_before[n] + k + 1)
                    nc.vector.tensor_tensor(x_low[:, n % 2, k], x_raw[:, k], x_high[:, n % 2, k].bitcast(F32),
                                            ALU.subtract).then_inc(x_ready, 1)

                if norm:
                    nc.vector.memset(ones[:], 1.0).then_inc(consts_ready, 1)
                for k in range(kts[0]):
                    split_x_low(0, k)
                    if k == 0:
                        split_w_low(0)
                for g, (n, j) in enumerate(slots):
                    s = g % 2
                    _, _, epilogue, _, goes_to = steps[n]
                    to = res[:, tiles(j)]
                    if g + 1 < len(slots):
                        split_w_low(g + 1)
                    if j == 1 and n + 1 < len(steps) and steps[n + 1][0] is not None:
                        for k in range(kts[n + 1]):
                            split_x_low(n + 1, k)
                    dve.wait_ge(y_ready, g + 1)
                    dve.wait_ge(e_loaded[s], 16 * (g // 2 + 1))
                    if epilogue != "add":
                        dve.wait_ge(gate_ready, g + 1)
                    if n >= 1 and steps[n - 1][4] == "x":
                        dve.wait_ge(x_ready, x_before[n] + kts[n])
                    if epilogue == "glu":
                        nc.vector.tensor_tensor(to, gate[:, s], e[:, s], ALU.mult).then_inc(res_ready, 1)
                    elif epilogue == "gate":
                        nc.vector.tensor_tensor(flat(to), y_of(s), flat(gate[:, s]), ALU.mult).then_inc(res_ready, 1)
                    elif epilogue == "gate_add":
                        nc.vector.tensor_tensor(flat(gate[:, s]), y_of(s), flat(gate[:, s]), ALU.mult).then_inc(gated, 1)
                        dve.wait_ge(gated, sum(steps[i][2] == "gate_add" for i, _ in slots[:g + 1]))
                        dve.wait_ge(res_ready, g)
                        nc.vector.tensor_tensor(to, gate[:, s], to, ALU.add).then_inc(res_ready, 1)
                    else:
                        nc.vector.tensor_tensor(flat(to), y_of(s), flat(e[:, s]), ALU.add).then_inc(res_ready, 1)
                    if goes_to == "x":
                        dve.wait_ge(x_high_ready, x_before[n + 1] + nm * (j + 1))
                        nc.vector.tensor_tensor(x_low[:, (n + 1) % 2, tiles(j)], to,
                                                x_high[:, (n + 1) % 2, tiles(j)].bitcast(F32),
                                                ALU.subtract).then_inc(x_ready, nm)
                if norm:
                    dve.wait_ge(summed, per_step)
                    nc.vector.tensor_scalar(scale[:], total[:, 0:T], 1.0 / D_MODEL, EPS, ALU.mult, ALU.add).then_inc(
                        meaned, 1)
                    dve.wait_ge(meaned, 1)
                    nc.vector.reciprocal(scale[:], scale[:]).then_inc(inverted, 1)
                    dve.wait_ge(rooted, 1)
                    dve.wait_ge(gain_loaded, 16)
                    for k in range(KT):
                        nc.vector.scalar_tensor_tensor(x_raw[:, k], res[:, k], gain[:, k:k + 1], scale[:],
                                                       ALU.mult, ALU.mult).then_inc(scaled, 1)


def conv_gated_up(nc, stage, x_dram, gain_dram, w_dram, conv_w_dram, conv_b_dram, out_dram):
    K, T = x_dram.shape
    kt = K // P
    FT = w_dram.shape[1] // (2 * P)
    halves, hw = 2, T // 2
    with ExitStack() as ctx:
        sb, ps, sem = opener(nc, ctx, stage)
        x = sb("x", [P, kt, T])
        x_high = sb("x_high", [P, kt, T], F32R)
        x_low = sb("x_low", [P, kt, T], F32R)
        gain = sb("gain", [P, kt])
        sq = sb("sq", [P, 2, T])
        ones = sb("ones", [P, P])
        scale = sb("scale", [P, halves, hw])
        w = sb("w", [P, 2, 2, kt, P])
        w_high = sb("w_high", [P, 2, 2, kt, P], F32R)
        w_low = sb("w_low", [P, 2, 2, kt, P], F32R)
        conv_w = sb("conv_w", [P, 2 * FT, 3])
        conv_b = sb("conv_b", [P, 2 * FT])
        y = sb("y", [P, 2, 2, T + 2])
        u = sb("u", [P, 2, 2, T])
        gate = sb("gate", [P, 2, T])
        out = sb("out", [P, 2, T])
        prod = ps("prod", [P, 2, 2, halves, 512])
        x_loaded = [sem(f"x_loaded{k}") for k in range(kt)]
        gain_loaded = sem("gain_loaded")
        squared = sem("squared")
        summed = sem("summed")
        meaned = sem("meaned")
        inverted = sem("inverted")
        rooted = sem("rooted")
        x_high_ready = sem("x_high_ready")
        x_ready = sem("x_ready")
        w_high_ready = sem("w_high_ready")
        w_ready = sem("w_ready")
        conv_loaded = sem("conv_loaded")
        w_loaded = [sem(f"w_loaded{s}") for s in range(2)]
        prod_ready = sem("prod_ready")
        consts_ready = sem("consts_ready")
        y_ready = sem("y_ready")
        first_tap = sem("first_tap")
        taps_done = sem("taps_done")
        gate_ready = sem("gate_ready")
        out_ready = sem("out_ready")
        stored = [sem(f"stored{s}") for s in range(2)]
        xv = x_dram.rearrange("(k p) t -> p k t", p=P)
        wv = w_dram.rearrange("(k p) m -> p k m", p=P)

        def over_tiles(eng, body):
            body(0, 0, True, False)
            body(0, 1, True, False)
            with eng.Fori(1, FT // 2 - 1) as i:
                body(i, 0, False, False)
                body(i, 1, False, False)
            body(FT // 2 - 1, 0, False, True)
            body(FT // 2 - 1, 1, False, True)

        with nc.Block() as block:

            @block.sync
            def _(sp):
                def load(i, s, first, last):
                    if not first:
                        sp.wait_ge(w_ready, 2 * i + s - 1)
                    for g in range(2):
                        sp.dma_start(w[:, s, g], wv[:, :, bass.ds(g * FT * P + (2 * i + s) * P, P)]).then_inc(w_loaded[s], 16)

                sp.dma_start(gain[:], gain_dram).then_inc(gain_loaded, 16)
                over_tiles(sp, load)

            @block.tensor
            def _(pe):
                pe.wait_ge(consts_ready, 2)

                def products(i, s, first, last):
                    pe.wait_ge(w_ready, 2 * i + s + 1)
                    if not first:
                        pe.wait_ge(y_ready, 2 * i + s - 1)
                    if first and s == 1:
                        pe.wait_ge(meaned, 1)
                    for g in range(2):
                        for h in range(halves):
                            for k in range(kt):
                                if first and s == 0 and g == 0 and h == 0:
                                    pe.wait_ge(x_ready, k + 1)
                                    pe.wait_ge(squared, k + 1)
                                    for b in range(halves):
                                        one = nc.tensor.matmul(prod[:, 1, 0, b, 0:hw], ones[:],
                                                               sq[:, k % 2, b * hw:(b + 1) * hw],
                                                               start=(k == 0), stop=(k == kt - 1))
                                    one.then_inc(summed, 1)
                                tokens = slice(h * hw, (h + 1) * hw)
                                done = three_passes(nc, prod[:, s, g, h, 0:hw], w_high[:, s, g, k], w_low[:, s, g, k],
                                                    x_high[:, k, tokens], x_low[:, k, tokens], k == 0, k == kt - 1)
                    done.then_inc(prod_ready, 1)

                over_tiles(pe, products)

            @block.scalar
            def _(act):
                for k in range(kt):
                    act.dma_start(x[:, k, :], xv[:, k, :]).then_inc(x_loaded[k], 16)
                act.dma_start(conv_w[:], conv_w_dram).then_inc(conv_loaded, 16)
                act.dma_start(conv_b[:], conv_b_dram).then_inc(conv_loaded, 16)

                def split_w_high(i, s, fresh):
                    act.wait_ge(w_loaded[s], (i + 1) * 32)
                    if not fresh:
                        act.wait_ge(prod_ready, 2 * i + s - 1)
                    nc.scalar.copy(w_high[:, s], w[:, s]).then_inc(w_high_ready, 1)

                act.wait_ge(gain_loaded, 16)
                for k in range(kt):
                    if k == 1:
                        split_w_high(0, 0, True)
                    act.wait_ge(x_loaded[k], 16)
                    if k >= 2:
                        act.wait_ge(summed, k - 1)
                    nc.scalar.activation(sq[:, k % 2, :], x[:, k], ACT.Square).then_inc(squared, 1)
                    nc.scalar.activation(x_high[:, k], x[:, k], ACT.Copy, scale=gain[:, k:k + 1]).then_inc(
                        x_high_ready, 1)
                split_w_high(0, 1, True)
                act.wait_ge(inverted, 1)
                nc.scalar.activation(scale[:], scale[:], ACT.Sqrt).then_inc(rooted, 1)
                act.wait_ge(conv_loaded, 32)

                def tile_of(i, s, first, last):
                    t = 2 * i + s
                    if not last:
                        split_w_high(i + 1, s, False)
                    act.wait_ge(y_ready, t + 1)
                    if not first:
                        act.wait_ge(out_ready, t - 1)
                    for g in range(2):
                        nc.scalar.activation(u[:, s, g], y[:, s, g, 0:T], ACT.Identity,
                                             bias=conv_b[:, bass.ds(g * FT + t, 1)],
                                             scale=conv_w[:, bass.ds(g * FT + t, 1), 0]).then_inc(first_tap, 1)
                    act.wait_ge(taps_done, 4 * t + 4)
                    nc.scalar.activation(gate[:, s], u[:, s, 0], ACT.Silu).then_inc(gate_ready, 1)
                    act.wait_ge(out_ready, t + 1)
                    act.dma_start(out_dram[bass.ds(t * P, P), :], out[:, s]).then_inc(stored[s], 16)

                over_tiles(act, tile_of)
                for s in range(2):
                    act.wait_ge(stored[s], 16 * (FT // 2))

            @block.vector
            def _(dve):
                nc.vector.memset(y[:], 0.0).then_inc(consts_ready, 1)
                nc.vector.memset(ones[:], 1.0).then_inc(consts_ready, 1)
                dve.wait_ge(consts_ready, 2)
                dve.wait_ge(gain_loaded, 16)

                def split_w_low(i, s, fresh):
                    dve.wait_ge(w_high_ready, 2 * i + s + 1)
                    if not fresh:
                        dve.wait_ge(prod_ready, 2 * i + s - 1)
                    nc.vector.tensor_tensor(w_low[:, s], w[:, s], w_high[:, s].bitcast(F32), ALU.subtract).then_inc(
                        w_ready, 1)

                for k in range(kt):
                    if k == 1:
                        split_w_low(0, 0, True)
                    dve.wait_ge(x_high_ready, k + 1)
                    nc.vector.scalar_tensor_tensor(x_low[:, k], x[:, k], gain[:, k:k + 1], x_high[:, k].bitcast(F32),
                                                   ALU.mult, ALU.subtract).then_inc(x_ready, 1)
                split_w_low(0, 1, True)
                dve.wait_ge(summed, kt)
                nc.vector.tensor_scalar(scale[:], prod[:, 1, 0, :, 0:hw], 1.0 / K, EPS, ALU.mult, ALU.add).then_inc(
                    meaned, 1)
                dve.wait_ge(meaned, 1)
                nc.vector.reciprocal(scale[:], scale[:]).then_inc(inverted, 1)

                def tile_of(i, s, first, last):
                    t = 2 * i + s
                    if not last:
                        split_w_low(i + 1, s, False)
                    dve.wait_ge(prod_ready, t + 1)
                    if first and s == 0:
                        dve.wait_ge(rooted, 1)
                    if not first:
                        dve.wait_ge(first_tap, 2 * t - 2)
                        dve.wait_ge(taps_done, 4 * t - 4)
                    for g in range(2):
                        done = nc.vector.tensor_tensor(y[:, s, g, 2:].rearrange("p (h t) -> p h t", h=halves),
                                                       prod[:, s, g, :, 0:hw], scale[:], ALU.mult)
                    done.then_inc(y_ready, 1)
                    dve.wait_ge(y_ready, t + 1)
                    for j in (1, 2):
                        for g in range(2):
                            if j == 1:
                                dve.wait_ge(first_tap, 2 * t + g + 1)
                            else:
                                dve.wait_ge(taps_done, 4 * t + g + 1)
                            nc.vector.scalar_tensor_tensor(u[:, s, g], y[:, s, g, j:j + T],
                                                           conv_w[:, bass.ds(g * FT + t, 1), j], u[:, s, g],
                                                           ALU.mult, ALU.add).then_inc(taps_done, 1)
                    dve.wait_ge(taps_done, 4 * t + 4)
                    dve.wait_ge(gate_ready, t + 1)
                    if not first:
                        dve.wait_ge(stored[s], i * 16)
                    nc.vector.tensor_tensor(out[:, s], gate[:, s], u[:, s, 1], ALU.mult).then_inc(out_ready, 1)

                over_tiles(dve, tile_of)


SSM_GROUP = 16
SSM_STATE = 64
SSM_GROUPS = D_MODEL // SSM_GROUP
CHUNK = 8
CHUNKS = LEN // CHUNK
PAIRS = SSM_GROUPS // 2
TWO_PI = 2.0 * float(np.pi)
TWO_PI_A = 6.28125
TWO_PI_B = float(np.float32(np.round((TWO_PI - TWO_PI_A) * 2.0 ** 20) / 2.0 ** 20))
TWO_PI_C = float(np.float32(TWO_PI - TWO_PI_A - TWO_PI_B))
ROUNDER = 1.5 * 2.0 ** 23
PI_BELOW = 3.1415925


def s5(nc, stage, u_dram, lam_dram, bc_dram, d_dram, ident_dram, out_dram):
    R_LEN = (CHUNKS - 1) * CHUNK + 1
    BATCH = 8
    BATCHES = SSM_GROUPS // BATCH
    RE, IM = 0, 1
    with ExitStack() as ctx:
        sb, ps, sem = opener(nc, ctx, stage)
        lam = sb("lam", [P, 3, PAIRS])
        bc = sb("bc", [P, 4, PAIRS, SSM_GROUP])
        d_skip = sb("d_skip", [P, KT])
        ident = sb("ident", [P, P])
        small = sb("small", [P, 24, PAIRS])
        tmp = sb("tmp", [P, 2, PAIRS, SSM_GROUP])
        bb = sb("bb", [P, 2, PAIRS, SSM_GROUP])
        wb = sb("wb", [P, 2, PAIRS, CHUNK, SSM_GROUP])
        ca = sb("ca", [P, 2, PAIRS, CHUNK + 1, SSM_GROUP])
        wbt = sb("wbt", [P, 2, 2, P])
        shifted = sb("shifted", [P, 2, BATCH, R_LEN])
        u = sb("u", [P, SSM_GROUPS, CHUNKS])
        toep = sb("toep", [P, SSM_GROUPS, CHUNK, SSM_GROUP])
        state = sb("state", [P, 2, PAIRS, CHUNKS + 1])
        prod = sb("prod", [P, 2, 2, PAIRS])
        both = sb("both", [P, PAIRS, 2, CHUNKS])
        wb_flat = wb[:].rearrange("p r q k h -> p (r q k h)")
        taps = wb_flat[0:SSM_GROUP, :].rearrange("h (g n) -> h g n", g=SSM_GROUPS)
        y_tok = wb_flat[0:CHUNKS, :].rearrange("c (t m) -> c t m", t=CHUNK)
        work = shifted[:].rearrange("p s g t -> p (s g t)")
        ca_both = work[:, 0:PAIRS * 2 * CHUNK * SSM_GROUP].rearrange("p (q e n) -> p q e n", q=PAIRS, e=2)
        u_tile = work[:, 0:2 * LEN].rearrange("p (s t) -> p s t", s=2)
        y_tile = work[:, 2 * LEN:4 * LEN].rearrange("p (s t) -> p s t", s=2)
        o_tile = work[:, 4 * LEN:6 * LEN].rearrange("p (s t) -> p s t", s=2)
        bank = ps("bank", [P, 8, 512])

        params_loaded = sem("params_loaded")
        toep_zeroed = sem("toep_zeroed")
        u_loaded = [sem(f"u_loaded{s}") for s in range(2)]
        u_packed = sem("u_packed")
        dt_ready = sem("dt_ready")
        exponent_ready = sem("exponent_ready")
        mag_ready = sem("mag_ready")
        angle_ready = sem("angle_ready")
        sin_ready = sem("sin_ready")
        setup = sem("setup")
        wb_turned = sem("wb_turned")
        wbt_ready = sem("wbt_ready")
        input_ready = sem("input_ready")
        state_filled = sem("state_filled")
        scanned = sem("scanned")
        ca_step = sem("ca_step")
        ca_moved = sem("ca_moved")
        both_ready = sem("both_ready")
        taps_made = sem("taps_made")
        taps_ready = sem("taps_ready")
        toep_ready = sem("toep_ready")
        y_made = sem("y_made")
        y_ready = sem("y_ready")
        y_turned = sem("y_turned")
        ut_loaded = [sem(f"ut_loaded{s}") for s in range(2)]
        skipped = sem("skipped")
        gelu_done = sem("gelu_done")
        stored = [sem(f"stored{s}") for s in range(2)]

        lr, li, ldt = lam[:, 0], lam[:, 1], lam[:, 2]
        (dt, expo, ang, cyc, red, half, mag, sn, snh, a_re, a_im, den, nr, co_re, co_im, t0, t1,
         s_re, s_im, s2_re, s2_im, neg_im) = (small[:, n] for n in range(22))

        def over_h(a):
            return a.unsqueeze(2).broadcast_to([P, PAIRS, SSM_GROUP])

        def half_of(t, e):
            return t[64 * e:64 * e + 64]

        with nc.Block() as block:

            @block.sync
            def _(sp):
                sp.dma_start(lam[:], lam_dram).then_inc(params_loaded, 16)
                sp.dma_start(bc[:], bc_dram).then_inc(params_loaded, 16)
                sp.dma_start(d_skip[:], d_dram).then_inc(params_loaded, 16)
                sp.dma_start(ident[:], ident_dram).then_inc(params_loaded, 16)
                for b in range(BATCHES):
                    if b >= 2:
                        sp.wait_ge(u_packed, b - 1)
                    rows = u_dram[b * BATCH * SSM_GROUP:(b + 1) * BATCH * SSM_GROUP, :].rearrange(
                        "(g h) t -> h g t", h=SSM_GROUP)
                    for j in range(CHUNK):
                        sp.dma_start(shifted[16 * j:16 * j + 16, b % 2], rows[:, :, 7 - j:7 - j + R_LEN]).then_inc(
                            u_loaded[b % 2], 16)
                sp.wait_ge(ca_step, S5_CA_STEPS)
                sp.wait_ge(u_packed, BATCHES)
                for r in (RE, IM):
                    for e in range(2):
                        sp.dma_start(half_of(ca_both, r)[:, :, e], half_of(ca, e)[:, r, :, 1:, :].rearrange(
                            "p q k h -> p q (k h)")).then_inc(ca_moved, 16)
                sp.wait_ge(taps_ready, PAIRS // 2)
                sp.wait_ge(toep_zeroed, 1)
                for j in range(CHUNK):
                    s = 7 - j
                    sp.dma_start(toep[16 * j:16 * j + 16, :, s:, :].rearrange("h g t m -> h g (t m)"),
                                 taps[:, :, 0:(CHUNK - s) * SSM_GROUP]).then_inc(toep_ready, 16)
                sp.wait_ge(toep_ready, 16 * CHUNK)
                sp.wait_ge(y_made, SSM_GROUPS // 4)
                for m in range(KT):
                    if m >= 2:
                        sp.wait_ge(skipped, m - 1)
                    sp.dma_start(u_tile[:, m % 2], u_dram[m * P:(m + 1) * P, :]).then_inc(ut_loaded[m % 2], 16)
                    if m >= 1:
                        sp.wait_ge(gelu_done, m)
                        sp.dma_start(out_dram[(m - 1) * P:m * P, :], o_tile[:, (m - 1) % 2]).then_inc(
                            stored[(m - 1) % 2], 16)
                sp.wait_ge(gelu_done, KT)
                sp.dma_start(out_dram[(KT - 1) * P:, :], o_tile[:, (KT - 1) % 2]).then_inc(stored[(KT - 1) % 2], 16)
                for s in range(2):
                    sp.wait_ge(stored[s], 16 * KT // 2)

            @block.gpsimd
            def _(pool):
                nc.gpsimd.memset(toep[:], 0.0).then_inc(toep_zeroed, 1)
                steps = [0]

                def together(*instructions):
                    for ins in instructions:
                        ins.then_inc(ca_step, 1)
                        steps[0] += 1
                    pool.wait_ge(ca_step, steps[0])

                def times_a(k):
                    re, im, re_next, im_next = ca[:, RE, :, k, :], ca[:, IM, :, k, :], ca[:, RE, :, k + 1, :], ca[:, IM, :, k + 1, :]
                    together(nc.gpsimd.tensor_tensor(re_next, re, over_h(a_re), ALU.mult),
                             nc.gpsimd.tensor_tensor(bc[:, 0], im, over_h(neg_im), ALU.mult),
                             nc.gpsimd.tensor_tensor(im_next, re, over_h(neg_im), ALU.mult),
                             nc.gpsimd.tensor_tensor(bc[:, 1], im, over_h(a_re), ALU.mult))
                    together(nc.gpsimd.tensor_tensor(re_next, re_next, bc[:, 0], ALU.subtract),
                             nc.gpsimd.tensor_tensor(im_next, im_next, bc[:, 1], ALU.add))

                pool.wait_ge(setup, S5_BB_DONE)
                together(nc.gpsimd.tensor_copy(ca[:, RE, :, 0, :], bc[:, 2]),
                         nc.gpsimd.tensor_scalar(ca[:, IM, :, 0, :], bc[:, 3], -1.0, None, ALU.mult),
                         nc.gpsimd.tensor_scalar(neg_im, a_im, -1.0, None, ALU.mult))
                for k in range(CHUNK):
                    times_a(k)

            @block.vector
            def _(dve):
                done = [0]

                def count(n):
                    done[0] += n

                def step(ins):
                    ins.then_inc(setup, 1)
                    count(1)
                    dve.wait_ge(setup, done[0])

                def tt(out, a, b, op):
                    step(nc.vector.tensor_tensor(out, a, b, op))

                def mul_complex(o_re, o_im, x_re, x_im, w_re, w_im, w1, w2):
                    nc.vector.tensor_tensor(o_re, x_re, w_re, ALU.mult).then_inc(setup, 1)
                    nc.vector.tensor_tensor(w1, x_im, w_im, ALU.mult).then_inc(setup, 1)
                    nc.vector.tensor_tensor(o_im, x_re, w_im, ALU.mult).then_inc(setup, 1)
                    nc.vector.tensor_tensor(w2, x_im, w_re, ALU.mult).then_inc(setup, 1)
                    count(4)
                    dve.wait_ge(setup, done[0])
                    nc.vector.tensor_tensor(o_re, o_re, w1, ALU.subtract).then_inc(setup, 1)
                    nc.vector.tensor_tensor(o_im, o_im, w2, ALU.add).then_inc(setup, 1)
                    count(2)
                    dve.wait_ge(setup, done[0])

                step(nc.vector.memset(state[:, :, :, 0:1], 0.0))
                dve.wait_ge(params_loaded, 64)
                dve.wait_ge(dt_ready, 1)
                nc.vector.tensor_tensor(expo, lr, dt, ALU.mult).then_inc(exponent_ready, 1)
                tt(ang, li, dt, ALU.mult)
                step(nc.vector.tensor_scalar(cyc, ang, 1.0 / TWO_PI, ROUNDER, ALU.mult, ALU.add))
                step(nc.vector.tensor_scalar(cyc, cyc, -ROUNDER, None, ALU.add))
                step(nc.vector.scalar_tensor_tensor(red, cyc, -TWO_PI_A, ang, ALU.mult, ALU.add))
                step(nc.vector.scalar_tensor_tensor(red, cyc, -TWO_PI_B, red, ALU.mult, ALU.add))
                step(nc.vector.scalar_tensor_tensor(red, cyc, -TWO_PI_C, red, ALU.mult, ALU.add))
                step(nc.vector.tensor_scalar(red, red, PI_BELOW, -PI_BELOW, ALU.min, ALU.max))
                nc.vector.tensor_scalar(half, red, 0.5, None, ALU.mult).then_inc(angle_ready, 1)
                dve.wait_ge(sin_ready, 2)
                dve.wait_ge(mag_ready, 1)
                tt(t0, snh, snh, ALU.mult)
                step(nc.vector.tensor_scalar(t0, t0, -2.0, 1.0, ALU.mult, ALU.add))
                tt(a_re, mag, t0, ALU.mult)
                tt(a_im, mag, sn, ALU.mult)
                tt(den, lr, lr, ALU.mult)
                tt(t1, li, li, ALU.mult)
                tt(den, den, t1, ALU.add)
                step(nc.vector.reciprocal(den, den))
                step(nc.vector.tensor_scalar(nr, a_re, -1.0, None, ALU.add))
                tt(co_re, nr, lr, ALU.mult)
                tt(t0, a_im, li, ALU.mult)
                tt(co_re, co_re, t0, ALU.add)
                tt(co_re, co_re, den, ALU.mult)
                tt(co_im, a_im, lr, ALU.mult)
                tt(t0, nr, li, ALU.mult)
                tt(co_im, co_im, t0, ALU.subtract)
                tt(co_im, co_im, den, ALU.mult)
                w1, w2 = tmp[:, 0], tmp[:, 1]
                mul_complex(bb[:, RE], bb[:, IM], bc[:, 0], bc[:, 1], over_h(co_re), over_h(co_im), w1, w2)
                mul_complex(s_re, s_im, a_re, a_im, a_re, a_im, t0, t1)
                mul_complex(s2_re, s2_im, s_re, s_im, s_re, s_im, t0, t1)
                mul_complex(s_re, s_im, s2_re, s2_im, s2_re, s2_im, t0, t1)
                step(nc.vector.tensor_copy(wb[:, :, :, 0, :], bb[:]))
                for k in range(CHUNK - 1):
                    mul_complex(wb[:, RE, :, k + 1, :], wb[:, IM, :, k + 1, :], wb[:, RE, :, k, :], wb[:, IM, :, k, :],
                                over_h(a_re), over_h(a_im), w1, w2)
                wb_done = done[0]
                assert wb_done == S5_WB_DONE, wb_done
                for q in range(PAIRS):
                    dve.wait_ge(input_ready, q + 1)
                    nc.vector.tensor_copy(state[:, :, q, 1:], bank[:, 4 + q % 4, 0:2 * CHUNKS].rearrange(
                        "p (r c) -> p r c", r=2)).then_inc(state_filled, 1)
                dve.wait_ge(state_filled, PAIRS)
                wide = [P, 2, PAIRS]
                n = 0

                def with_step(*instructions):
                    nonlocal n
                    for ins in instructions:
                        ins.then_inc(scanned, 1)
                        n += 1
                    dve.wait_ge(scanned, n)

                for c in range(1, CHUNKS - 1):
                    with_step(
                        nc.vector.tensor_tensor(prod[:, 0], state[:, :, :, c], s_re.unsqueeze(1).broadcast_to(wide), ALU.mult),
                        nc.vector.tensor_tensor(prod[:, 1], state[:, :, :, c], s_im.unsqueeze(1).broadcast_to(wide), ALU.mult))
                    with_step(nc.vector.tensor_tensor(state[:, :, :, c + 1], state[:, :, :, c + 1], prod[:, 0], ALU.add))
                    with_step(
                        nc.vector.tensor_tensor(state[:, RE, :, c + 1], state[:, RE, :, c + 1], prod[:, 1, IM], ALU.subtract),
                        nc.vector.tensor_tensor(state[:, IM, :, c + 1], state[:, IM, :, c + 1], prod[:, 1, RE], ALU.add))
                for r in (RE, IM):
                    nc.vector.tensor_copy(half_of(both, r)[:, :, 0, BOTH_EARLY:], half_of(state, 0)[:, r, :, BOTH_EARLY:CHUNKS]).then_inc(
                        both_ready, 1)
                for m in range(KT):
                    dve.wait_ge(y_turned, m + 1)
                    dve.wait_ge(ut_loaded[m % 2], 16 * (m // 2 + 1))
                    if m >= 2:
                        dve.wait_ge(gelu_done, m - 1)
                    for b in range(2):
                        ins = nc.vector.scalar_tensor_tensor(
                            y_tile[:, m % 2].rearrange("p (c t) -> p t c", t=CHUNK)[:, 4 * b:4 * b + 4, :],
                            u_tile[:, m % 2].rearrange("p (c t) -> p t c", t=CHUNK)[:, 4 * b:4 * b + 4, :],
                            d_skip[:, m:m + 1],
                            bank[:, 2 * (m % 2) + b, 0:4 * CHUNKS].rearrange("p (t c) -> p t c", t=4),
                            ALU.mult, ALU.add)
                    ins.then_inc(skipped, 1)

            @block.scalar
            def _(act):
                act.wait_ge(params_loaded, 64)
                nc.scalar.activation(dt, ldt, ACT.Exp).then_inc(dt_ready, 1)
                act.wait_ge(exponent_ready, 1)
                nc.scalar.activation(mag, expo, ACT.Exp).then_inc(mag_ready, 1)
                act.wait_ge(angle_ready, 1)
                nc.scalar.activation(sn, red, ACT.Sin).then_inc(sin_ready, 1)
                nc.scalar.activation(snh, half, ACT.Sin).then_inc(sin_ready, 1)

                def pack(b):
                    act.wait_ge(u_loaded[b % 2], 16 * CHUNK * (b // 2 + 1))
                    nc.scalar.copy(u[:, b * BATCH:(b + 1) * BATCH, :], shifted[:, b % 2, :, 0:R_LEN:CHUNK]).then_inc(
                        u_packed, 1)

                for b in range(BATCHES - 2):
                    pack(b)
                for q in range(PAIRS):
                    if q in (2, 6):
                        pack(BATCHES - 2 + q // 4)
                    act.wait_ge(wb_turned, q + 1)
                    if q >= 2:
                        act.wait_ge(input_ready, q - 1)
                    nc.scalar.copy(wbt[:, q % 2], bank[:, q % 2, 0:2 * P].rearrange("p (r n) -> p r n", r=2)).then_inc(
                        wbt_ready, 1)
                for b in range(PAIRS // 2):
                    act.wait_ge(taps_made, b + 1)
                    e, q0 = b % 2, 4 * (b // 2)
                    g0 = 2 * q0 + e
                    nc.scalar.copy(taps[:, g0:g0 + 7:2, :], bank[0:SSM_GROUP, 2 + b % 2, :].rearrange(
                        "h (g n) -> h g n", g=4)).then_inc(taps_ready, 1)
                for cols, engines_part in ((slice(0, BOTH_EARLY), (0, 1)), (slice(BOTH_EARLY, CHUNKS), (1,))):
                    act.wait_ge(scanned, 5 * (cols.stop - 2))
                    for r in (RE, IM):
                        for e in engines_part:
                            nc.scalar.copy(half_of(both, r)[:, :, e, cols], half_of(state, e)[:, r, :, cols]).then_inc(
                                both_ready, 1)
                for b in range(SSM_GROUPS // 4):
                    act.wait_ge(y_made, b + 1)
                    if b == 0:
                        act.wait_ge(wb_turned, PAIRS)
                    for n in range(4):
                        g = 2 * (4 * (b // 2) + n) + b % 2
                        ins = nc.scalar.copy(y_tok[:, :, SSM_GROUP * g:SSM_GROUP * (g + 1)],
                                             bank[0:CHUNKS, 4 + b % 4, n * P:(n + 1) * P].rearrange(
                                                 "c (t h) -> c t h", t=CHUNK))
                    ins.then_inc(y_ready, 1)
                for m in range(KT):
                    act.wait_ge(skipped, m + 1)
                    if m >= 2:
                        act.wait_ge(stored[m % 2], 16 * (m // 2))
                    nc.scalar.activation(o_tile[:, m % 2], y_tile[:, m % 2], ACT.Gelu_apprx_tanh).then_inc(gelu_done, 1)

            @block.tensor
            def _(pe):
                pe.wait_ge(params_loaded, 64)
                pe.wait_ge(setup, S5_WB_DONE)

                def turn(q):
                    if q >= 2:
                        pe.wait_ge(wbt_ready, q - 1)
                    for r in (RE, IM):
                        last = nc.tensor.transpose(bank[:, q % 2, r * P:(r + 1) * P],
                                                   wb[:, r, q].rearrange("p k h -> p (k h)"), ident[:])
                    last.then_inc(wb_turned, 1)

                def chunk_inputs(q):
                    pe.wait_ge(wbt_ready, q + 1)
                    if q % (BATCH // 2) == 0:
                        pe.wait_ge(u_packed, 2 * q // BATCH + 1)
                    if q >= 4:
                        pe.wait_ge(state_filled, q - 3)
                    for e in range(2):
                        for r in (RE, IM):
                            last = nc.tensor.matmul(bank[64 * e:64 * e + 64, 4 + q % 4, r * CHUNKS:(r + 1) * CHUNKS],
                                                    wbt[:, q % 2, r, 64 * e:64 * e + 64], u[:, 2 * q + e, :],
                                                    start=True, stop=True)
                    last.then_inc(input_ready, 1)

                turn(0)
                for q in range(PAIRS):
                    if q + 1 < PAIRS:
                        turn(q + 1)
                    chunk_inputs(q)
                pe.wait_ge(ca_step, S5_CA_STEPS)
                for b in range(PAIRS // 2):
                    e, q0 = b % 2, 4 * (b // 2)
                    if b >= 2:
                        pe.wait_ge(taps_ready, b - 1)
                    for n in range(4):
                        for r in (RE, IM):
                            last = nc.tensor.matmul(
                                bank[0:SSM_GROUP, 2 + b % 2, n * P:(n + 1) * P], half_of(bb, e)[:, r, q0 + n, :],
                                half_of(ca, e)[:, r, q0 + n, 0:CHUNK, :].rearrange("p k h -> p (k h)"),
                                start=(r == RE), stop=(r == IM))
                    last.then_inc(taps_made, 1)
                pe.wait_ge(toep_ready, 16 * CHUNK)
                pe.wait_ge(state_filled, PAIRS)
                pe.wait_ge(ca_moved, 16 * 4)
                pe.wait_ge(both_ready, 8)
                for b in range(SSM_GROUPS // 4):
                    e, q0 = b % 2, 4 * (b // 2)
                    if b >= 4:
                        pe.wait_ge(y_ready, b - 3)
                    for n in range(4):
                        q = q0 + n
                        to = bank[0:CHUNKS, 4 + b % 4, n * P:(n + 1) * P]
                        nc.tensor.matmul(to, u[:, 2 * q + e, :], toep[:, 2 * q + e].rearrange("p t h -> p (t h)"),
                                         start=True, stop=False)
                        last = nc.tensor.matmul(to, both[:, q, e, :], ca_both[:, q, e], start=False, stop=True)
                    last.then_inc(y_made, 1)
                pe.wait_ge(y_ready, SSM_GROUPS // 4)
                for m in range(KT):
                    if m >= 2:
                        pe.wait_ge(skipped, m - 1)
                    for t in range(CHUNK):
                        last = nc.tensor.transpose(
                            bank[:, 2 * (m % 2) + t // 4, (t % 4) * CHUNKS:(t % 4 + 1) * CHUNKS],
                            y_tok[:, t, m * P:(m + 1) * P], ident[0:CHUNKS, 0:CHUNKS])
                    last.then_inc(y_turned, 1)


S5_BB_DONE = 1 + 24 + 6
S5_WB_DONE = S5_BB_DONE + 6 * 3 + 1 + 6 * (CHUNK - 1)
S5_CA_STEPS = 3 + 6 * CHUNK
BOTH_EARLY = 48


HEADS = 8
HCHUNK = 16
HCHUNKS = LEN // HCHUNK


def hgrn2(nc, stage, p_dram, lb_dram, gain_dram, ident_dram, causal_dram, member_dram, out_dram):
    tiles = [P] * (LEN // P) + ([LEN % P] if LEN % P else [])
    nt = len(tiles)
    per_tile = P // HCHUNK
    RING = 3 * per_tile
    units = [(h, i) for h in range(HEADS) for i in range(nt)]
    U = len(units)
    with ExitStack() as ctx:
        sb, ps, sem = opener(nc, ctx, stage)
        q = sb("q", [P, HEADS, LEN])
        f = sb("f", [P, HEADS, LEN])
        v = sb("v", [P, HEADS, LEN])
        og = sb("og", [P, HEADS, LEN])
        o = sb("o", [P, HEADS, LEN])
        cum = sb("cum", [P, 2, LEN])
        rest = sb("rest", [P, 2, LEN])
        e_up = sb("e_up", [P, 2, LEN])
        e_down = sb("e_down", [P, 2, LEN])
        e_rest = sb("e_rest", [P, 2, LEN])
        k_in = sb("k_in", [P, 2, LEN])
        k_out = sb("k_out", [P, 2, LEN])
        decay = sb("decay", [P, HEADS, HCHUNKS])
        resets = sb("resets", [P, LEN])
        lb = sb("lb", [P, 2, HEADS])
        low = sb("low", [P, 2, HEADS])
        gain = sb("gain", [P, 1])
        ident = sb("ident", [P, P])
        ones = sb("ones", [P, P])
        causal = sb("causal", [P, P])
        member = sb("member", [P, per_tile, P])
        turned = sb("turned", [P, 3, 2, P])
        v_by_chunk = sb("v_by_chunk", [P, 2, per_tile, P])
        scores = sb("scores", [P, 3, P])
        states = sb("states", [P, RING, P])
        sq = sb("sq", [P, 2, P])
        root = sb("root", [P, 2, P])
        eps = sb("eps", [P, 1])
        bank = ps("bank", [P, 8, 512])

        params_loaded = sem("params_loaded")
        loaded = [sem(f"loaded{h}") for h in range(HEADS)]
        consts_ready = sem("consts_ready")
        eps_ready = sem("eps_ready")
        bound_diff = sem("bound_diff")
        bound_sig = sem("bound_sig")
        bound_ready = sem("bound_ready")
        sig_ready = sem("sig_ready")
        f_ready = sem("f_ready")
        log_ready = sem("log_ready")
        cum_ready = sem("cum_ready")
        rest_ready = sem("rest_ready")
        k_ready = sem("k_ready")
        exps_ready = sem("exps_ready")
        decay_ready = sem("decay_ready")
        qk_ready = sem("qk_ready")
        turn_made = sem("turn_made")
        turn_ready = sem("turn_ready")
        split_ready = sem("split_ready")
        scores_made = sem("scores_made")
        scores_ready = sem("scores_ready")
        kv_made = sem("kv_made")
        state_ready = sem("state_ready")
        o_made = sem("o_made")
        o_ready = sem("o_ready")
        gate_ready = sem("gate_ready")
        summed = sem("summed")
        rooted = sem("rooted")
        inverted = sem("inverted")
        normed = sem("normed")
        out_ready = sem("out_ready")
        stored = sem("stored")

        def rows(part, h):
            at = part * D_MODEL + h * P
            return p_dram[at:at + P, :]

        def span(i):
            return slice(i * P, i * P + tiles[i])

        def chunks_of(i):
            return tiles[i] // HCHUNK

        def states_before(n):
            return sum(chunks_of(i) for _, i in units[:n])

        def by_chunk(a):
            return a.rearrange("p (c t) -> p c t", t=HCHUNK)

        with nc.Block() as block:

            @block.sync
            def _(sp):
                for dst, src in ((lb, lb_dram), (gain, gain_dram), (ident, ident_dram), (causal, causal_dram),
                                 (member, member_dram)):
                    sp.dma_start(dst[:], src).then_inc(params_loaded, 16)
                for h in range(HEADS):
                    for part, dst in ((1, f), (0, q), (2, v), (3, og)):
                        sp.dma_start(dst[:, h], rows(part, h)).then_inc(loaded[h], 16)
                for h in range(HEADS):
                    sp.wait_ge(out_ready, nt * (h + 1))
                    sp.dma_start(out_dram[h * P:(h + 1) * P, :], o[:, h]).then_inc(stored, 16)
                sp.wait_ge(stored, 16 * HEADS)

            @block.scalar
            def _(act):
                act.wait_ge(bound_diff, 1)
                nc.scalar.activation(low[:, 0], low[:, 1], ACT.Sigmoid).then_inc(bound_sig, 1)

                def sigmoid(h):
                    act.wait_ge(loaded[h], 64)
                    nc.scalar.activation(f[:, h], f[:, h], ACT.Sigmoid).then_inc(sig_ready, 1)

                def output_gate(h):
                    nc.scalar.activation(og[:, h], og[:, h], ACT.Silu).then_inc(gate_ready, 1)

                def log(h):
                    act.wait_ge(f_ready, h + 1)
                    if h >= 2:
                        act.wait_ge(exps_ready, 3 * (h - 1))
                    nc.scalar.activation(rest[:, h % 2], f[:, h], ACT.Ln).then_inc(log_ready, 1)

                def exponentials(h):
                    s = h % 2
                    act.wait_ge(cum_ready, h + 1)
                    if h >= 2:
                        act.wait_ge(qk_ready, 3 * (h - 1))
                        act.wait_ge(decay_ready, h - 1)
                    nc.scalar.activation(e_up[:, s], cum[:, s], ACT.Exp).then_inc(exps_ready, 1)
                    nc.scalar.activation(e_down[:, s], cum[:, s], ACT.Exp, scale=-1.0).then_inc(exps_ready, 1)
                    act.wait_ge(rest_ready, h + 1)
                    nc.scalar.activation(e_rest[:, s], rest[:, s], ACT.Exp).then_inc(exps_ready, 1)

                sigmoid(0)
                sigmoid(1)
                log(0)
                log(1)
                exponentials(0)
                exponentials(1)
                for n in range(U + 3):
                    if n < U:
                        h, i = units[n]
                        m = tiles[i]
                        act.wait_ge(turn_made, n + 1)
                        if n >= 3:
                            act.wait_ge(o_made, n - 2)
                        nc.scalar.copy(turned[0:m, n % 3], bank[0:m, n % 2, 0:2 * P].rearrange("p (a n) -> p a n", a=2)).then_inc(
                            turn_ready, 1)
                    if n >= 3:
                        m = tiles[units[n - 3][1]]
                        act.wait_ge(summed, n - 2)
                        act.wait_ge(eps_ready, 1)
                        if n >= 5:
                            act.wait_ge(normed, n - 4)
                        nc.scalar.activation(root[:, (n - 3) % 2, 0:m], bank[:, 3, P:P + m], ACT.Sqrt,
                                             bias=eps[:, 0:1], scale=1.0 / P).then_inc(rooted, 1)
                    if 2 <= n < U + 2:
                        h, i = units[n - 2]
                        act.wait_ge(o_made, n - 1)
                        nc.scalar.copy(o[:, h, span(i)], bank[:, 3, 0:tiles[i]])
                        nc.scalar.activation(sq[:, n % 2, 0:tiles[i]], bank[:, 3, 0:tiles[i]], ACT.Square).then_inc(
                            o_ready, 1)
                    if n < U:
                        h, i = units[n]
                        if i == 0 and 1 <= h < HEADS - 1:
                            log(h + 1)
                        if i == 1 and h == 0:
                            sigmoid(2)
                            for a in range(3):
                                output_gate(a)
                        if i == 2 and 1 <= h < HEADS - 1:
                            exponentials(h + 1)
                        if i == 3 and h + 3 < HEADS:
                            sigmoid(h + 3)
                            output_gate(h + 3)

            @block.gpsimd
            def _(pool):
                def prepare(h):
                    s = h % 2
                    pool.wait_ge(k_ready, h + 1)
                    pool.wait_ge(exps_ready, 3 * (h + 1))
                    if h >= 2:
                        pool.wait_ge(turn_made, nt * (h - 1))
                        pool.wait_ge(scores_made, nt * (h - 1))
                    nc.gpsimd.tensor_tensor(q[:, h], q[:, h], e_up[:, s], ALU.mult).then_inc(qk_ready, 1)
                    nc.gpsimd.tensor_tensor(k_in[:, s], f[:, h], e_down[:, s], ALU.mult).then_inc(qk_ready, 1)
                    nc.gpsimd.tensor_tensor(k_out[:, s], f[:, h], e_rest[:, s], ALU.mult).then_inc(qk_ready, 1)

                pool.wait_ge(params_loaded, 80)
                prepare(0)
                prepare(1)
                for n, (h, i) in enumerate(units):
                    m, c = tiles[i], chunks_of(i)
                    pool.wait_ge(turn_ready, n + 1)
                    if n >= 2:
                        pool.wait_ge(kv_made, n - 1)
                    nc.gpsimd.tensor_tensor(v_by_chunk[0:m, n % 2, 0:c], member[0:m, 0:c],
                                            turned[0:m, n % 3, 1].unsqueeze(1).broadcast_to([m, c, P]),
                                            ALU.mult).then_inc(split_ready, 1)
                    if i == 3 and 1 <= h < HEADS - 1:
                        prepare(h + 1)

            @block.vector
            def _(dve):
                nc.vector.memset(ones[:], 1.0).then_inc(consts_ready, 1)
                nc.vector.memset(resets[:], 1.0).then_inc(consts_ready, 1)
                nc.vector.memset(eps[:], EPS).then_inc(eps_ready, 1)
                dve.wait_ge(consts_ready, 2)
                nc.vector.memset(by_chunk(resets[:])[:, :, 0:1], 0.0).then_inc(consts_ready, 1)
                dve.wait_ge(params_loaded, 80)
                nc.vector.tensor_tensor(low[:, 1], lb[:, 0], lb[:, 1], ALU.subtract).then_inc(bound_diff, 1)
                dve.wait_ge(bound_sig, 1)
                nc.vector.tensor_scalar(low[:, 1], low[:, 0], -1.0, 1.0, ALU.mult, ALU.add).then_inc(bound_ready, 1)
                dve.wait_ge(bound_ready, 1)
                dve.wait_ge(consts_ready, 3)

                def bounded(h):
                    dve.wait_ge(sig_ready, h + 1)
                    nc.vector.tensor_scalar(f[:, h], f[:, h], low[:, 1, h:h + 1], low[:, 0, h:h + 1],
                                            ALU.mult, ALU.add).then_inc(f_ready, 1)

                def sums(h):
                    s = h % 2
                    dve.wait_ge(log_ready, h + 1)
                    if h >= 2:
                        dve.wait_ge(exps_ready, 3 * (h - 1))
                    nc.vector.tensor_tensor_scan(cum[:, s], resets[:], rest[:, s], 0.0, ALU.mult, ALU.add).then_inc(
                        cum_ready, 1)
                    nc.vector.tensor_scalar(f[:, h], f[:, h], -1.0, 1.0, ALU.mult, ALU.add).then_inc(k_ready, 1)
                    dve.wait_ge(cum_ready, h + 1)
                    nc.vector.tensor_tensor(by_chunk(rest[:, s]),
                                            by_chunk(cum[:, s])[:, :, HCHUNK - 1:].broadcast_to([P, HCHUNKS, HCHUNK]),
                                            by_chunk(cum[:, s]), ALU.subtract).then_inc(rest_ready, 1)

                def chunk_decay(h):
                    dve.wait_ge(exps_ready, 3 * h + 1)
                    nc.vector.tensor_copy(decay[:, h], e_up[:, h % 2, HCHUNK - 1::HCHUNK]).then_inc(decay_ready, 1)

                def masked_scores(n):
                    m = tiles[units[n][1]]
                    dve.wait_ge(scores_made, n + 1)
                    nc.vector.tensor_tensor(scores[0:m, n % 3, 0:m], bank[0:m, 2, 0:m], causal[0:m, 0:m],
                                            ALU.mult).then_inc(scores_ready, 1)

                def finish(n):
                    h, i = units[n]
                    m = tiles[i]
                    dve.wait_ge(rooted, n + 1)
                    nc.vector.reciprocal(root[:, n % 2, 0:m], root[:, n % 2, 0:m]).then_inc(inverted, 1)
                    dve.wait_ge(inverted, n + 1)
                    nc.vector.scalar_tensor_tensor(o[:, h, span(i)], o[:, h, span(i)], gain[:, 0:1],
                                                   root[:, n % 2, 0:m], ALU.mult, ALU.mult).then_inc(normed, 1)
                    dve.wait_ge(normed, n + 1)
                    dve.wait_ge(gate_ready, h + 1)
                    nc.vector.tensor_tensor(o[:, h, span(i)], o[:, h, span(i)], og[:, h, span(i)], ALU.mult).then_inc(
                        out_ready, 1)

                bounded(0)
                bounded(1)
                sums(0)
                sums(1)
                chunk_decay(0)
                chunk_decay(1)
                masked_scores(0)
                g = 0
                for n, (h, i) in enumerate(units):
                    if n >= 2:
                        dve.wait_ge(o_made, n - 1)
                    if n + 1 < U:
                        masked_scores(n + 1)
                    dve.wait_ge(kv_made, n + 1)
                    if i == 0:
                        dve.wait_ge(decay_ready, h + 1)
                    for j in range(chunks_of(i)):
                        c = i * per_tile + j
                        kv = bank[:, 4 + 2 * (n % 2) + j // 4, (j % 4) * P:(j % 4 + 1) * P]
                        if c == 0:
                            nc.vector.tensor_copy(states[:, g % RING], kv).then_inc(state_ready, 1)
                        else:
                            nc.vector.scalar_tensor_tensor(states[:, g % RING], states[:, (g - 1) % RING],
                                                           decay[:, h, c:c + 1], kv, ALU.mult, ALU.add).then_inc(
                                state_ready, 1)
                        g += 1
                        dve.wait_ge(state_ready, g)
                    if n >= 2:
                        finish(n - 2)
                    if i == 0 and h + 2 < HEADS:
                        bounded(h + 2)
                    if i == 0 and 1 <= h < HEADS - 1:
                        sums(h + 1)
                    if i == 2 and 1 <= h < HEADS - 1:
                        chunk_decay(h + 1)
                finish(U - 2)
                finish(U - 1)

            @block.tensor
            def _(pe):
                pe.wait_ge(params_loaded, 80)

                def turn(n):
                    h, i = units[n]
                    m = tiles[i]
                    pe.wait_ge(qk_ready, 3 * (h + 1))
                    pe.wait_ge(loaded[h], 64)
                    if n >= 2:
                        pe.wait_ge(turn_ready, n - 1)
                    nc.tensor.transpose(bank[0:m, n % 2, 0:P], k_out[:, h % 2, span(i)], ident[:])
                    nc.tensor.transpose(bank[0:m, n % 2, P:2 * P], v[:, h, span(i)], ident[:]).then_inc(turn_made, 1)
                    if n >= 1:
                        pe.wait_ge(scores_ready, n)
                    nc.tensor.matmul(bank[0:m, 2, 0:m], k_in[:, h % 2, span(i)], q[:, h, span(i)],
                                     start=True, stop=True).then_inc(scores_made, 1)

                def key_values(n, b):
                    m, c = tiles[units[n][1]], chunks_of(units[n][1])
                    pe.wait_ge(split_ready, n + 1)
                    if n >= 2:
                        pe.wait_ge(state_ready, states_before(n - 1))
                    w = min(4, c - 4 * b)
                    if w > 0:
                        last = nc.tensor.matmul(bank[:, 4 + 2 * (n % 2) + b, 0:w * P], turned[0:m, n % 3, 0],
                                                v_by_chunk[0:m, n % 2, 4 * b:4 * b + w].rearrange("p c n -> p (c n)"),
                                                start=True, stop=True)
                        if 4 * b + w == c:
                            last.then_inc(kv_made, 1)

                def sum_squares(n):
                    m = tiles[units[n][1]]
                    pe.wait_ge(consts_ready, 1)
                    pe.wait_ge(o_ready, n + 1)
                    if n >= 1:
                        pe.wait_ge(rooted, n)
                    nc.tensor.matmul(bank[:, 3, P:P + m], ones[:], sq[:, n % 2, 0:m], start=True, stop=True).then_inc(
                        summed, 1)

                def output(n):
                    h, i = units[n]
                    m = tiles[i]
                    pe.wait_ge(scores_ready, n + 1)
                    if n >= 1:
                        pe.wait_ge(o_ready, n)
                        pe.wait_ge(rooted, n)
                    last = nc.tensor.matmul(bank[:, 3, 0:m], turned[0:m, n % 3, 1], scores[0:m, n % 3, 0:m],
                                            start=True, stop=False)
                    before = states_before(n)
                    for j in range(chunks_of(i)):
                        if i * per_tile + j == 0:
                            continue
                        pe.wait_ge(state_ready, before + j)
                        last = nc.tensor.matmul(bank[:, 3, j * HCHUNK:(j + 1) * HCHUNK], states[:, (before + j - 1) % RING],
                                                q[:, h, i * P + j * HCHUNK:i * P + (j + 1) * HCHUNK],
                                                start=False, stop=(j == chunks_of(i) - 1))
                    last.then_inc(o_made, 1)

                turn(0)
                turn(1)
                key_values(0, 0)
                key_values(0, 1)
                for n in range(U):
                    if n + 2 < U:
                        turn(n + 2)
                    if n + 1 < U:
                        key_values(n + 1, 0)
                    if n >= 1:
                        sum_squares(n - 1)
                    if n + 1 < U:
                        key_values(n + 1, 1)
                    output(n)
                sum_squares(U - 1)


HEAD_DIM = 64
GRID_W = 64
GRID_ROWS = SEQ // GRID_W


def attention(nc, stage, q_dram, k_dram, v_dram, bias_dram, ident_dram, out_dram):
    C, T = q_dram.shape
    NK = k_dram.shape[1]
    heads, ct, kt, qt = C // HEAD_DIM, C // P, NK // P, T // P
    units = [(h, t) for h in range(heads) for t in range(qt)]
    with ExitStack() as ctx:
        sb, ps, sem = opener(nc, ctx, stage)
        q = sb("q", [P, ct, T])
        k = sb("k", [P, ct, NK])
        v = sb("v", [P, ct, NK])
        bias = sb("bias", [P, heads, 2 * GRID_ROWS, GRID_W]) if bias_dram is not None else None
        ident = sb("ident", [P, P])
        v_tok = sb("v_tok", [P, kt, C])
        s = sb("s", [P, 3, NK])
        low = sb("low", [P, len(units)])
        total = sb("total", [P, len(units)])
        inverse = sb("inverse", [P, len(units)])
        p_turned = sb("p_turned", [P, 2, kt, P])
        y_tok = sb("y_tok", [P, qt, C])
        y = sb("y", [P, ct, T])
        bank = ps("bank", [P, 8, 512])

        loaded = sem("loaded")
        v_turn_made = sem("v_turn_made")
        v_turn_ready = sem("v_turn_ready")
        scores_made = sem("scores_made")
        scores_ready = sem("scores_ready")
        low_ready = sem("low_ready")
        p_ready = sem("p_ready")
        p_turn_made = sem("p_turn_made")
        p_turn_ready = sem("p_turn_ready")
        inverse_ready = sem("inverse_ready")
        y_made = sem("y_made")
        y_ready = sem("y_ready")
        out_turned = sem("out_turned")
        out_ready = sem("out_ready")
        stored = sem("stored")
        n_loads = 5 if bias is not None else 4

        with nc.Block() as block:

            @block.sync
            def _(sp):
                for dst, src in ((ident[:], ident_dram), (v[:], v_dram.rearrange("(c p) t -> p c t", p=P)),
                                 (q[:], q_dram.rearrange("(c p) t -> p c t", p=P)),
                                 (k[:], k_dram.rearrange("(c p) t -> p c t", p=P))):
                    sp.dma_start(dst, src).then_inc(loaded, 16)
                if bias is not None:
                    sp.dma_start(bias[:], bias_dram).then_inc(loaded, 16)
                sp.wait_ge(out_ready, ct)
                sp.dma_start(out_dram.rearrange("(c p) t -> p c t", p=P), y[:]).then_inc(stored, 16)
                sp.wait_ge(stored, 16)

            @block.tensor
            def _(pe):
                pe.wait_ge(loaded, 16 * n_loads)
                for j in range(kt):
                    if j >= 2:
                        pe.wait_ge(v_turn_ready, j - 1)
                    for c in range(ct):
                        last = nc.tensor.transpose(bank[:, j % 2, c * P:(c + 1) * P], v[:, c, j * P:(j + 1) * P], ident[:])
                    last.then_inc(v_turn_made, 1)

                def scores(n):
                    h, t = units[n]
                    e = 64 * (h % 2)
                    if n >= 2:
                        pe.wait_ge(scores_ready, n - 1)
                    nc.tensor.matmul(bank[:, 2 + n % 2, 0:NK], q[e:e + 64, h // 2, t * P:(t + 1) * P],
                                     k[e:e + 64, h // 2, :], start=True, stop=True).then_inc(scores_made, 1)

                def turn(n):
                    pe.wait_ge(p_ready, n + 1)
                    if n >= 2:
                        pe.wait_ge(p_turn_ready, n - 1)
                    for j in range(kt):
                        last = nc.tensor.transpose(bank[:, 4 + n % 2, j * P:(j + 1) * P], s[:, n % 3, j * P:(j + 1) * P],
                                                   ident[:])
                    last.then_inc(p_turn_made, 1)

                def values(n):
                    h, t = units[n]
                    pe.wait_ge(p_turn_ready, n + 1)
                    if n >= 2:
                        pe.wait_ge(y_ready, n - 1)
                    for j in range(kt):
                        last = nc.tensor.matmul(bank[:, 6 + n % 2, 0:HEAD_DIM], p_turned[:, n % 2, j],
                                                v_tok[:, j, h * HEAD_DIM:(h + 1) * HEAD_DIM],
                                                start=(j == 0), stop=(j == kt - 1))
                    last.then_inc(y_made, 1)

                scores(0)
                scores(1)
                pe.wait_ge(v_turn_ready, kt)
                turn(0)
                for n in range(len(units)):
                    if n + 2 < len(units):
                        scores(n + 2)
                    if n + 1 < len(units):
                        turn(n + 1)
                    values(n)
                for c in range(ct):
                    pe.wait_ge(y_ready, len(units))
                    if c >= 2:
                        pe.wait_ge(out_ready, c - 1)
                    for t in range(qt):
                        last = nc.tensor.transpose(bank[:, c % 2, t * P:(t + 1) * P], y_tok[:, t, c * P:(c + 1) * P], ident[:])
                    last.then_inc(out_turned, 1)

            @block.vector
            def _(dve):
                dve.wait_ge(loaded, 16 * n_loads)

                def soften(n):
                    h, t = units[n]
                    dve.wait_ge(scores_made, n + 1)
                    if n >= 3:
                        dve.wait_ge(p_turn_made, n - 2)
                    raw = bank[:, 2 + n % 2, 0:NK]
                    if bias is not None:
                        first = GRID_ROWS - 1 - 2 * t
                        nc.vector.scalar_tensor_tensor(
                            s[:, n % 3], raw, HEAD_DIM ** -0.5,
                            bias[:, h, first:first + GRID_ROWS, :].rearrange("p a j -> p (a j)"),
                            ALU.mult, ALU.add).then_inc(scores_ready, 1)
                    else:
                        nc.vector.tensor_scalar(s[:, n % 3], raw, HEAD_DIM ** -0.5, None, ALU.mult).then_inc(
                            scores_ready, 1)
                    dve.wait_ge(scores_ready, n + 1)
                    nc.vector.tensor_reduce(low[:, n:n + 1], s[:, n % 3], X, ALU.max, negate=True).then_inc(low_ready, 1)

                def finish(n):
                    h, t = units[n]
                    dve.wait_ge(p_ready, n + 1)
                    nc.vector.reciprocal(inverse[:, n:n + 1], total[:, n:n + 1]).then_inc(inverse_ready, 1)
                    dve.wait_ge(inverse_ready, n + 1)
                    dve.wait_ge(y_made, n + 1)
                    nc.vector.tensor_scalar(y_tok[:, t, h * HEAD_DIM:(h + 1) * HEAD_DIM], bank[:, 6 + n % 2, 0:HEAD_DIM],
                                            inverse[:, n:n + 1], None, ALU.mult).then_inc(y_ready, 1)

                soften(0)
                soften(1)
                for n in range(len(units)):
                    if n + 2 < len(units):
                        soften(n + 2)
                    finish(n)

            @block.scalar
            def _(act):
                for j in range(kt):
                    act.wait_ge(v_turn_made, j + 1)
                    nc.scalar.copy(v_tok[:, j], bank[:, j % 2, 0:C]).then_inc(v_turn_ready, 1)

                def exponentials(n):
                    act.wait_ge(low_ready, n + 1)
                    nc.scalar.activation(s[:, n % 3], s[:, n % 3], ACT.Exp, bias=low[:, n:n + 1],
                                         accum_out=total[:, n:n + 1]).then_inc(p_ready, 1)

                exponentials(0)
                for n in range(len(units)):
                    if n + 1 < len(units):
                        exponentials(n + 1)
                    act.wait_ge(p_turn_made, n + 1)
                    if n >= 2:
                        act.wait_ge(y_made, n - 1)
                    nc.scalar.copy(p_turned[:, n % 2].rearrange("p j m -> p (j m)"), bank[:, 4 + n % 2, 0:NK]).then_inc(
                        p_turn_ready, 1)
                for c in range(ct):
                    act.wait_ge(out_turned, c + 1)
                    nc.scalar.copy(y[:, c], bank[:, c % 2, 0:T]).then_inc(out_ready, 1)


def window_bias(rpb):
    heads = rpb.shape[0]
    win = 16
    w = np.arange(GRID_W)[:, None]
    j = np.arange(GRID_W)[None, :]
    start = np.clip(w - win // 2, 0, GRID_W - win)
    inside = (j >= start) & (j < start + win)
    offset = np.clip(j - w + win - 1, 0, 2 * win - 2)
    rows = 2 * GRID_ROWS
    out = np.full((2, GRID_W, heads, rows, GRID_W), -1e30, np.float32)
    laid = np.where(inside[None, None], rpb[:, :, offset], np.float32(-1e30))
    laid = laid.transpose(2, 0, 1, 3)
    out[0, :, :, 0:rows - 1] = laid
    out[1, :, :, 1:rows] = laid
    return np.ascontiguousarray(out.reshape(P, heads, rows, GRID_W))


RW_WIDTH = 384
RW_X = RW_WIDTH // P
RCHUNK = 32
RSTEPS = SEQ // RCHUNK
LORA = 64
DECAY_SCALE = float(np.exp(-0.5))
GN_EPS = 64e-5
LEVELS = 5
MU_R, MU_K, MU_V, W0, A0, K_K, K_A, R_K, LN_G, LN_B = 0, 2, 4, 6, 8, 10, 11, 12, 13, 14
RW_COLS = 15


def rwkv7(nc, stage, p_dram, par_dram, mu_l_dram, lora_dram, g2_dram, ident_dram, masks_dram, member_dram,
          eye2_dram, out_dram):
    T = SEQ
    N = RW_X * T
    units = [(d, i, x) for d in range(2) for i in range(T // P) for x in range(RW_X)]
    with ExitStack() as ctx:
        sb, ps, sem = opener(nc, ctx, stage)
        par = sb("par", [P, RW_COLS, RW_X])
        mu_l = sb("mu_l", [P, 2])
        keep_k = sb("keep_k", [P, RW_X])
        lora = sb("lora", [P, 2, RW_WIDTH])
        g2 = sb("g2", [P, RW_WIDTH])
        ident = sb("ident", [P, P])
        blocks = sb("blocks", [P, P])
        masks = sb("masks", [P, 2, 4, P])
        member = sb("member", [P, 4, P])
        eye2 = sb("eye2", [P, HEAD_DIM])
        resets = sb("resets", [P, N])
        raw = sb("raw", [P, 3, RW_X, T + 2])
        raw_l = sb("raw_l", [P, T + 2])
        lat_g = sb("lat_g", [P, T])
        ar = sb("ar", [P, 2, RW_X, 2, T])
        bh = sb("bh", [P, 2, RW_X, T])
        kh = sb("kh", [P, 2, RW_X, T])
        v = sb("v", [P, 2, RW_X, T])
        qt = sb("qt", [P, 2, RW_X, T])
        y_loc = sb("y_loc", [P, 2, RW_X, T])
        bonus = sb("bonus", [P, RW_X, T])
        ends = sb("ends", [P, RSTEPS, 2 * RW_X])
        work = sb("work", [P, 11 * N])
        tmp = [work[:, n * N:(n + 1) * N].rearrange("p (x t) -> p x t", x=RW_X) for n in range(11)]
        dr, dk, dv, r, k, sw, sa, cum, e1, e2, sq = tmp
        e3, norm = dr, dk
        dl, lat = cum[:, 0], sq[:, 0]
        gate, y = e1, e2
        raw_flat = raw[:].rearrange("p j x t -> p (j x t)")
        per_step = RSTEPS * 2 * RW_X * HEAD_DIM
        ht = work[:, 0:per_step].rearrange("p (s n k) -> p s n k", s=RSTEPS, k=HEAD_DIM)
        nn = work[:, per_step:2 * per_step].rearrange("p (s n k) -> p s n k", s=RSTEPS, k=HEAD_DIM)
        states = sb("states", [P, 2, 2 * RW_X, HEAD_DIM])
        tok = sb("tok", [P, 2, 4, P])
        split = raw_flat[:, 0:16 * P].rearrange("p (s a c n) -> p s a c n", s=2, a=2, c=4)
        sm = raw_flat[:, 16 * P:32 * P].rearrange("p (s e a t) -> p s e a t", s=2, e=2, a=4)
        a_first = resets[:, 0:4 * P].rearrange("p (s e n) -> p s e n", s=2, e=2)
        z = resets[:, 4 * P:8 * P].rearrange("p (s e n) -> p s e n", s=2, e=2)
        power = sb("power", [P, 2, 2, 2, P])
        bank = ps("bank", [P, 8, 512])

        loaded = sem("loaded")
        raw_loaded = sem("raw_loaded")
        consts_ready = sem("consts_ready")
        diffed = sem("diffed")
        mixed = sem("mixed")
        tanhed = sem("tanhed")
        lora_made = sem("lora_made")
        sig_ready = sem("sig_ready")
        squared = sem("squared")
        norm_made = sem("norm_made")
        norm_rooted = sem("norm_rooted")
        chain = sem("chain")
        cum_ready = sem("cum_ready")
        cum_used = sem("cum_used")
        exps_ready = sem("exps_ready")
        prepared = sem("prepared")
        bonus_in = sem("bonus_in")
        bonus_made = sem("bonus_made")
        bonus_ready = sem("bonus_ready")
        turn_made = sem("turn_made")
        tok_ready = sem("tok_ready")
        split_ready = sem("split_ready")
        scores_made = sem("scores_made")
        scores_ready = sem("scores_ready")
        first_made = sem("first_made")
        first_ready = sem("first_ready")
        z_started = sem("z_started")
        level_made = sem("level_made")
        z_ready = sem("z_ready")
        power_ready = sem("power_ready")
        ends_made = sem("ends_made")
        ends_read = sem("ends_read")
        parts_read = sem("parts_read")
        step_made = sem("step_made")
        step_added = sem("step_added")
        state_ready = sem("state_ready")
        inter_made = sem("inter_made")
        gate_sig = sem("gate_sig")
        gate_made = sem("gate_made")
        gate_ready = sem("gate_ready")
        tail = sem("tail")
        mean_made = sem("mean_made")
        dev_squared = sem("dev_squared")
        var_made = sem("var_made")
        var_ready = sem("var_ready")
        var_rooted = sem("var_rooted")
        out_ready = sem("out_ready")
        stored = sem("stored")

        def shifted(a, d):
            return a[..., 0:T] if d == 0 else a[..., 2:T + 2]

        def wide(a):
            return a.rearrange("p x t -> p (x t)")

        def steps_of_tile(d, i):
            if d == 0:
                return slice(4 * i, 4 * i + 4)
            last = RSTEPS - 1 - 4 * i
            return slice(last, last - 4 if last >= 4 else None, -1)

        def state_count(s, d):
            return 2 * (s - 1) + d + 1

        def z_bank(n, lv):
            return (4, 7)[(LEVELS * n + lv) % 2]

        with nc.Block() as block:

            @block.sync
            def _(sp):
                for dst, src in ((par, par_dram), (mu_l, mu_l_dram), (lora, lora_dram), (g2, g2_dram),
                                 (ident, ident_dram), (masks, masks_dram), (member, member_dram), (eye2, eye2_dram)):
                    sp.dma_start(dst[:], src).then_inc(loaded, 16)
                sp.wait_ge(consts_ready, 3)
                for j in range(3):
                    sp.dma_start(raw[:, j, :, 1:T + 1],
                                 p_dram[j * RW_WIDTH:(j + 1) * RW_WIDTH, :].rearrange("(x p) t -> p x t", p=P)).then_inc(
                        raw_loaded, 16)
                at = 3 * RW_WIDTH
                sp.dma_start(raw_l[:, 1:T + 1], p_dram[at:at + P, :]).then_inc(raw_loaded, 16)
                sp.dma_start(lat_g[:], p_dram[at + P:at + 2 * P, :]).then_inc(raw_loaded, 16)
                for x in range(RW_X):
                    sp.wait_ge(out_ready, x + 1)
                    sp.dma_start(out_dram[x * P:(x + 1) * P, :], y[:, x]).then_inc(stored, 16)
                sp.wait_ge(stored, 16 * RW_X)

            @block.gpsimd
            def _(pool):
                for d in range(2):
                    pool.wait_ge(raw_loaded, 80)
                    if d == 1:
                        pool.wait_ge(prepared, RW_PREPARED)
                        pool.wait_ge(bonus_in, 1)
                        pool.wait_ge(chain, RW_CHAIN)
                        pool.wait_ge(mixed, 10)
                    nc.gpsimd.tensor_tensor(dl, shifted(raw_l[:], d), raw_l[:, 1:T + 1], ALU.subtract).then_inc(diffed, 1)
                    for j, out in enumerate((dr, dk, dv)):
                        nc.gpsimd.tensor_tensor(out, shifted(raw[:, j], d), raw[:, j, :, 1:T + 1],
                                                ALU.subtract).then_inc(diffed, 1)
                    pool.wait_ge(exps_ready, 3 * (d + 1))
                    pool.wait_ge(mixed, 10 * (d + 1))
                    nc.gpsimd.tensor_tensor(ar[:, d, :, 1, :], r, e1, ALU.mult).then_inc(prepared, 1)
                for n, (d, i, x) in enumerate(units):
                    pool.wait_ge(tok_ready, n + 1)
                    if n >= 2:
                        pool.wait_ge(ends_made, n - 1)
                    for j in range(2):
                        nc.gpsimd.tensor_tensor(split[:, n % 2, j], member[:],
                                                tok[:, n % 2, j].unsqueeze(1).broadcast_to([P, 4, P]),
                                                ALU.mult).then_inc(split_ready, 1)
                pool.wait_ge(parts_read, 2 * len(units))
                nc.gpsimd.tensor_tensor(y_loc[:, 0], y_loc[:, 0], y_loc[:, 1], ALU.add).then_inc(prepared, 1)

            @block.scalar
            def _(act):
                act.wait_ge(raw_loaded, 80)
                nc.scalar.activation(lat_g[:], lat_g[:], ACT.Sigmoid).then_inc(gate_sig, 1)
                act.wait_ge(loaded, 128)
                for d in range(2):
                    act.wait_ge(mixed, 10 * d + 1)
                    nc.scalar.activation(lat[0:LORA], lat[0:LORA], ACT.Tanh).then_inc(tanhed, 1)
                    for x in range(RW_X):
                        act.wait_ge(lora_made, 2 * RW_X * d + x + 1)
                        nc.scalar.activation(sw[:, x], bank[:, x], ACT.Sigmoid, bias=par[:, W0 + d, x:x + 1]).then_inc(
                            sig_ready, 1)
                    for x in range(RW_X):
                        act.wait_ge(lora_made, 2 * RW_X * d + RW_X + x + 1)
                        nc.scalar.activation(sa[:, x], bank[:, 3 + x], ACT.Sigmoid, bias=par[:, A0 + d, x:x + 1]).then_inc(
                            sig_ready, 1)
                    act.wait_ge(mixed, 10 * d + 1 + 2 * RW_X)
                    for x in range(RW_X):
                        nc.scalar.activation(sq[:, x], k[:, x], ACT.Square, scale=par[:, K_K, x:x + 1]).then_inc(squared, 1)
                    for x in range(RW_X):
                        act.wait_ge(norm_made, RW_X * d + x + 1)
                        nc.scalar.activation(norm[:, x], bank[:, x], ACT.Sqrt).then_inc(norm_rooted, 1)
                    act.wait_ge(cum_ready, 2 * d + 1)
                    nc.scalar.activation(e1, cum, ACT.Exp, scale=-DECAY_SCALE).then_inc(exps_ready, 1)
                    nc.scalar.activation(e2, cum, ACT.Exp, scale=DECAY_SCALE).then_inc(exps_ready, 1)
                    act.wait_ge(cum_ready, 2 * d + 2)
                    nc.scalar.activation(e3, sw, ACT.Exp, scale=-DECAY_SCALE).then_inc(exps_ready, 1)

                def front_a(n):
                    act.wait_ge(turn_made, n + 1)
                    if n >= 2:
                        act.wait_ge(ends_made, n - 1)
                    nc.scalar.copy(tok[:, n % 2].rearrange("p a c -> p (a c)"), bank[:, 0]).then_inc(tok_ready, 1)

                def front_b(n):
                    act.wait_ge(first_made, n + 1)
                    if n >= 2:
                        act.wait_ge(level_made, LEVELS * (n - 1))
                    nc.scalar.copy(a_first[:, n % 2], bank[:, 6, 0:2 * P].rearrange("p (e s) -> p e s", e=2)).then_inc(
                        first_ready, 1)

                def level(n, lv):
                    if lv < LEVELS - 1:
                        act.wait_ge(level_made, LEVELS * n + lv + 1)
                        first = 0 if lv < LEVELS - 2 else P
                        nc.scalar.copy(power[:, lv % 2, :, :, :].rearrange("p e a s -> p e (a s)")[:, :, first:],
                                       bank[:, 3].rearrange("p (e n) -> p e n", e=2)[:, :, first:2 * P]).then_inc(
                            power_ready, 1)

                def finish(n):
                    d, i, x = units[n]
                    act.wait_ge(ends_made, n + 1)
                    nc.scalar.copy(nn[:, steps_of_tile(d, i), 3 * d + x, :],
                                   bank[:, 6, 0:4 * HEAD_DIM].rearrange("p (c k) -> p c k", c=4)).then_inc(parts_read, 1)
                    nc.scalar.copy(y_loc[:, d, x, i * P:(i + 1) * P], bank[:, 6, 4 * HEAD_DIM:4 * HEAD_DIM + P]).then_inc(
                        parts_read, 1)

                act.wait_ge(prepared, 2 * RW_PREPARED)
                act.wait_ge(chain, 2 * RW_CHAIN)
                act.wait_ge(bonus_made, 2)
                front_a(0)
                front_b(0)
                for n in range(len(units)):
                    level(n, 0)
                    level(n, 1)
                    if n >= 1:
                        finish(n - 1)
                    level(n, 2)
                    if n + 1 < len(units):
                        front_a(n + 1)
                    level(n, 3)
                    if n + 1 < len(units):
                        front_b(n + 1)
                finish(len(units) - 1)
                act.wait_ge(gate_made, 1)
                nc.scalar.copy(gate, bank[:, 5:8, :]).then_inc(gate_ready, 1)
                for x in range(RW_X):
                    act.wait_ge(tail, RW_X + x + 1)
                    nc.scalar.activation(sq[:, x], y[:, x], ACT.Square).then_inc(dev_squared, 1)
                for x in range(RW_X):
                    act.wait_ge(var_ready, x + 1)
                    nc.scalar.activation(sq[:, x], sq[:, x], ACT.Sqrt).then_inc(var_rooted, 1)

            @block.tensor
            def _(pe):
                pe.wait_ge(loaded, 128)
                pe.wait_ge(consts_ready, 5)
                for d in range(2):
                    pe.wait_ge(tanhed, d + 1)
                    pe.wait_ge(mixed, 10 * d + 1)
                    if d == 1:
                        pe.wait_ge(bonus_ready, 1)
                        pe.wait_ge(sig_ready, 6)
                    for x in range(RW_X):
                        nc.tensor.matmul(bank[:, x], lora[0:LORA, d, x * P:(x + 1) * P], lat[0:LORA], start=True,
                                         stop=True).then_inc(lora_made, 1)
                    for x in range(RW_X):
                        nc.tensor.matmul(bank[:, 3 + x], lora[LORA:, d, x * P:(x + 1) * P], lat[LORA:],
                                         start=True, stop=True).then_inc(lora_made, 1)
                    pe.wait_ge(sig_ready, 6 * d + 3)
                    for x in range(RW_X):
                        pe.wait_ge(squared, RW_X * d + x + 1)
                        nc.tensor.matmul(bank[:, x], blocks[:], sq[:, x], start=True, stop=True).then_inc(norm_made, 1)
                    pe.wait_ge(bonus_in, d + 1)
                    pe.wait_ge(norm_rooted, RW_X * (d + 1))
                    for x in range(RW_X):
                        last = nc.tensor.matmul(bank[:, x], blocks[:], sq[:, x], start=True, stop=True)
                    last.then_inc(bonus_made, 1)
                pe.wait_ge(bonus_ready, 2)
                pe.wait_ge(prepared, 2 * RW_PREPARED)
                pe.wait_ge(chain, 2 * RW_CHAIN)
                pe.wait_ge(sig_ready, 12)

                def heads(e):
                    return slice(64 * e, 64 * e + 64)

                def front_a(n):
                    d, i, x = units[n]
                    at = slice(i * P, (i + 1) * P)
                    if n >= 1:
                        pe.wait_ge(tok_ready, n)
                    for j, a in enumerate((bh[:, d, x, at], kh[:, d, x, at], ar[:, d, x, 0, at], v[:, d, x, at])):
                        last = nc.tensor.transpose(bank[:, 0, j * P:(j + 1) * P], a, ident[:])
                    last.then_inc(turn_made, 1)
                    if n >= 1:
                        pe.wait_ge(scores_ready, n)
                    for e in range(2):
                        for j, a in enumerate((bh, kh)):
                            last = nc.tensor.matmul(bank[:, 1 + e, 2 * j * P:2 * (j + 1) * P], a[heads(e), d, x, at],
                                                    ar[heads(e), d, x, :, at], start=True, stop=True)
                    last.then_inc(scores_made, 1)

                def front_b(n):
                    pe.wait_ge(scores_ready, n + 1)
                    pe.wait_ge(tok_ready, n + 1)
                    if n >= 2:
                        pe.wait_ge(ends_read, 2 * (n - 1))
                        pe.wait_ge(parts_read, 2 * (n - 1))
                    for e in range(2):
                        nc.tensor.transpose(bank[:, 6, e * P:(e + 1) * P], sm[:, n % 2, e, 0], ident[:])
                    for e in range(2):
                        last = nc.tensor.matmul(bank[:, 5, 64 * e:64 * e + 64], sm[:, n % 2, e, 2],
                                                tok[:, n % 2, 3, heads(e)], start=True, stop=True)
                    last.then_inc(first_made, 1)

                def level(n, lv):
                    if lv == 0:
                        pe.wait_ge(first_ready, n + 1)
                        pe.wait_ge(z_started, 2 * (n + 1))
                        if n >= 1:
                            pe.wait_ge(z_ready, LEVELS * n - 1)
                    else:
                        pe.wait_ge(power_ready, (LEVELS - 1) * n + lv)
                        pe.wait_ge(z_ready, LEVELS * n + lv)
                    for e in range(2):
                        a_t = sm[:, n % 2, e, 0] if lv == 0 else power[:, (lv - 1) % 2, e, 1]
                        a = a_first[:, n % 2, e] if lv == 0 else power[:, (lv - 1) % 2, e, 0]
                        if lv < LEVELS - 1:
                            if lv < LEVELS - 2:
                                nc.tensor.matmul(bank[:, 3, 2 * e * P:(2 * e + 1) * P], a_t, a, start=True, stop=True)
                            nc.tensor.matmul(bank[:, 3, (2 * e + 1) * P:(2 * e + 2) * P], a, a_t, start=True, stop=True)
                        last = nc.tensor.matmul(bank[:, z_bank(n, lv), e * P:(e + 1) * P], a_t, z[:, n % 2, e],
                                                start=True, stop=True)
                    last.then_inc(level_made, 1)

                def finish(n, e):
                    s = n % 2
                    pe.wait_ge(z_ready, LEVELS * (n + 1))
                    pe.wait_ge(split_ready, 2 * (n + 1))
                    m = min(n + 2, len(units))
                    pe.wait_ge(first_ready, m)
                    pe.wait_ge(z_started, 2 * m)
                    if n >= 1:
                        pe.wait_ge(ends_read, 2 * n)
                        pe.wait_ge(parts_read, 2 * n)
                    zz, ww, vv = z[:, s, e, 0:64], z[:, s, e, 64:P], tok[:, s, 3, heads(e)]
                    nc.tensor.matmul(bank[heads(e), 5, 0:256], ww, split[:, s, 0, :, heads(e)], start=True, stop=True)
                    nc.tensor.matmul(bank[heads(e), 5, 256:384], ww, sm[:, s, e, 1], start=True, stop=True)
                    for c in range(4):
                        to = bank[heads(e), 6, 64 * c:64 * c + 64]
                        nc.tensor.matmul(to, split[:, s, 0, c, heads(e)], zz, start=True, stop=False)
                        nc.tensor.matmul(to, split[:, s, 1, c, heads(e)], vv, start=False, stop=True)
                    to = bank[heads(e), 6, 256:384]
                    nc.tensor.matmul(to, zz, sm[:, s, e, 1], start=True, stop=False)
                    last = nc.tensor.matmul(to, vv, sm[:, s, e, 3], start=False, stop=True)
                    if e == 1:
                        last.then_inc(ends_made, 1)

                front_a(0)
                front_b(0)
                for n in range(len(units)):
                    level(n, 0)
                    if n >= 1:
                        finish(n - 1, 0)
                    level(n, 1)
                    if n >= 1:
                        finish(n - 1, 1)
                    level(n, 2)
                    if n + 1 < len(units):
                        front_a(n + 1)
                    level(n, 3)
                    if n + 1 < len(units):
                        front_b(n + 1)
                    level(n, 4)
                for e in range(2):
                    finish(len(units) - 1, e)

                pe.wait_ge(ends_read, 2 * len(units))
                pe.wait_ge(parts_read, 2 * len(units))
                pe.wait_ge(gate_sig, 1)
                for x in range(RW_X):
                    last = nc.tensor.matmul(bank[:, 5 + x], g2[:, x * P:(x + 1) * P], lat_g[:], start=True, stop=True)
                last.then_inc(gate_made, 1)
                pe.wait_ge(z_ready, LEVELS * len(units))
                for s in range(1, RSTEPS):
                    for d in range(2):
                        pe.wait_ge(state_ready, state_count(s, d))
                        if s < RSTEPS - 1:
                            for x in range(RW_X):
                                for e in range(2):
                                    last = nc.tensor.matmul(bank[heads(e), d, 64 * x:64 * x + 64],
                                                            ht[heads(e), s, 3 * d + x],
                                                            states[heads(e), s % 2, 3 * d + x], start=True, stop=True)
                            last.then_inc(step_made, 1)
                        c = s if d == 0 else RSTEPS - 1 - s
                        at = slice(c * RCHUNK, (c + 1) * RCHUNK)
                        for x in range(RW_X):
                            for e in range(2):
                                last = nc.tensor.matmul(bank[heads(e), 2 + x, at], states[heads(e), s % 2, 3 * d + x],
                                                        qt[heads(e), d, x, at], start=(s == 1 and d == 0),
                                                        stop=(s == RSTEPS - 1 and d == 1))
                        last.then_inc(inter_made, 1)
                pe.wait_ge(gate_ready, 1)
                for x in range(RW_X):
                    pe.wait_ge(tail, x + 1)
                    nc.tensor.matmul(bank[:, 5 + x], blocks[:], y[:, x], start=True, stop=True).then_inc(mean_made, 1)
                for x in range(RW_X):
                    pe.wait_ge(dev_squared, x + 1)
                    nc.tensor.matmul(bank[:, 5 + x], blocks[:], sq[:, x], start=True, stop=True).then_inc(var_made, 1)

            @block.vector
            def _(dve):
                nc.vector.memset(raw[:], 0.0).then_inc(consts_ready, 1)
                nc.vector.memset(raw_l[:], 0.0).then_inc(consts_ready, 1)
                nc.vector.memset(blocks[:], 0.0).then_inc(consts_ready, 1)
                dve.wait_ge(consts_ready, 3)
                nc.vector.memset(blocks[0:64, 0:64], 1.0).then_inc(consts_ready, 1)
                nc.vector.memset(blocks[64:P, 64:P], 1.0).then_inc(consts_ready, 1)
                nc.vector.memset(resets[:], 1.0).then_inc(consts_ready, 1)
                dve.wait_ge(consts_ready, 6)
                nc.vector.memset(resets[:, 0:N:RCHUNK], 0.0).then_inc(consts_ready, 1)
                dve.wait_ge(loaded, 128)
                nc.vector.tensor_scalar(keep_k[:], par[:, K_A], -1.0, 1.0, ALU.mult, ALU.add).then_inc(consts_ready, 1)
                dve.wait_ge(consts_ready, 8)
                done = [0]

                def step(ins):
                    ins.then_inc(chain, 1)
                    done[0] += 1
                    dve.wait_ge(chain, done[0])

                for d in range(2):
                    dve.wait_ge(diffed, 4 * d + 1)
                    if d == 1:
                        dve.wait_ge(lora_made, 2 * RW_X)
                    nc.vector.scalar_tensor_tensor(lat, dl, mu_l[:, d:d + 1], raw_l[:, 1:T + 1],
                                                   ALU.mult, ALU.add).then_inc(mixed, 1)
                    for j, (diff, out, mu) in enumerate(((dr, r, MU_R), (dk, k, MU_K), (dv, v[:, d], MU_V))):
                        dve.wait_ge(diffed, 4 * d + j + 2)
                        if d == 1 and j == 0:
                            dve.wait_ge(prepared, RW_PREPARED)
                            dve.wait_ge(bonus_in, 1)
                        for x in range(RW_X):
                            nc.vector.scalar_tensor_tensor(out[:, x], diff[:, x], par[:, mu + d, x:x + 1],
                                                           raw[:, j, x, 1:T + 1], ALU.mult, ALU.add).then_inc(mixed, 1)
                    dve.wait_ge(sig_ready, 6 * d + 3)
                    if d == 0:
                        nc.vector.tensor_tensor_scan(wide(cum), resets[:], wide(sw), 0.0, ALU.mult, ALU.add).then_inc(
                            cum_ready, 1)
                    else:
                        nc.vector.tensor_tensor_scan(wide(cum)[:, ::-1], resets[:], wide(sw)[:, ::-1], 0.0,
                                                     ALU.mult, ALU.add).then_inc(cum_ready, 1)
                    dve.wait_ge(cum_ready, 2 * d + 1)
                    nc.vector.tensor_tensor(sw, cum, sw, ALU.subtract).then_inc(cum_ready, 1)
                    for x in range(RW_X):
                        dve.wait_ge(norm_rooted, RW_X * d + x + 1)
                        step(nc.vector.tensor_scalar(norm[:, x], norm[:, x], 1e-12, None, ALU.max))
                        step(nc.vector.reciprocal(norm[:, x], norm[:, x]))
                    dve.wait_ge(mixed, 10 * (d + 1))
                    for x in range(RW_X):
                        nc.vector.scalar_tensor_tensor(norm[:, x], k[:, x], par[:, K_K, x:x + 1], norm[:, x],
                                                       ALU.mult, ALU.mult).then_inc(chain, 1)
                        done[0] += 1
                    dve.wait_ge(chain, done[0])
                    dve.wait_ge(exps_ready, 3 * (d + 1))
                    nc.vector.scalar_tensor_tensor(ar[:, d, :, 0, :], norm, -1.0, e3, ALU.mult, ALU.mult).then_inc(
                        prepared, 1)
                    dve.wait_ge(sig_ready, 6 * (d + 1))
                    step(nc.vector.tensor_tensor(norm, norm, sa, ALU.mult))
                    nc.vector.tensor_tensor(bh[:, d], norm, e2, ALU.mult).then_inc(prepared, 1)
                    for x in range(RW_X):
                        nc.vector.tensor_scalar(sa[:, x], sa[:, x], par[:, K_A, x:x + 1], keep_k[:, x:x + 1],
                                                ALU.mult, ALU.add).then_inc(chain, 1)
                        done[0] += 1
                    dve.wait_ge(chain, done[0])
                    step(nc.vector.tensor_tensor(k, k, sa, ALU.mult))
                    nc.vector.tensor_tensor(kh[:, d], k, e2, ALU.mult).then_inc(prepared, 1)
                    dve.wait_ge(norm_made, RW_X * (d + 1))
                    for x in range(RW_X):
                        ins = nc.vector.scalar_tensor_tensor(sq[:, x], r[:, x], par[:, R_K, x:x + 1], k[:, x],
                                                             ALU.mult, ALU.mult)
                    ins.then_inc(bonus_in, 1)
                    whole = e1[:, :, RCHUNK - 1::RCHUNK] if d == 0 else e1[:, :, T - RCHUNK::-RCHUNK]
                    nc.vector.tensor_copy(ends[:, :, 3 * d:3 * d + 3].rearrange("p s x -> p x s"), whole).then_inc(
                        prepared, 1)
                    dve.wait_ge(bonus_made, d + 1)
                    if d == 0:
                        nc.vector.tensor_tensor(bonus[:], bank[:, 0:3, :], v[:, 0], ALU.mult).then_inc(bonus_ready, 1)
                    else:
                        dve.wait_ge(prepared, 2 * RW_PREPARED)
                        step(nc.vector.tensor_tensor(e1, bank[:, 0:3, :], v[:, 1], ALU.mult))
                        dve.wait_ge(bonus_ready, 1)
                        nc.vector.tensor_tensor(bonus[:], bonus[:], e1, ALU.add).then_inc(bonus_ready, 1)
                    if d == 0:
                        assert done[0] == RW_CHAIN, done[0]

                def front_a(n):
                    d = units[n][0]
                    dve.wait_ge(scores_made, n + 1)
                    if n >= 2:
                        dve.wait_ge(ends_made, n - 1)
                    for e in range(2):
                        ins = nc.vector.tensor_tensor(sm[:, n % 2, e].rearrange("p a t -> p (a t)"), bank[:, 1 + e],
                                                      masks[:, d].rearrange("p a t -> p (a t)"), ALU.mult)
                    ins.then_inc(scores_ready, 1)

                def front_b(n):
                    dve.wait_ge(first_made, n + 1)
                    if n >= 2:
                        dve.wait_ge(ends_made, n - 1)
                    nc.vector.tensor_copy(z[:, n % 2, :, 0:64],
                                          bank[:, 5, 0:P].rearrange("p (e m) -> p e m", e=2)).then_inc(z_started, 1)
                    dve.wait_ge(tok_ready, n + 1)
                    nc.vector.tensor_copy(z[:, n % 2, :, 64:P],
                                          tok[:, n % 2, 2].rearrange("p (e m) -> p e m", e=2)).then_inc(z_started, 1)

                def level(n, lv):
                    dve.wait_ge(level_made, LEVELS * n + lv + 1)
                    if lv == 0:
                        dve.wait_ge(z_started, 2 * (n + 1))
                    else:
                        dve.wait_ge(z_ready, LEVELS * n + lv)
                    nc.vector.tensor_tensor(z[:, n % 2], z[:, n % 2], bank[:, z_bank(n, lv), 0:2 * P].rearrange("p (e m) -> p e m", e=2),
                                            ALU.add).then_inc(z_ready, 1)

                def finish(n):
                    d, i, x = units[n]
                    at = slice(i * P, (i + 1) * P)
                    dve.wait_ge(ends_made, n + 1)
                    nc.vector.tensor_tensor(ht[:, steps_of_tile(d, i), 3 * d + x, :],
                                            bank[:, 5, 0:256].rearrange("p (c k) -> p c k", c=4),
                                            eye2[:].unsqueeze(1).broadcast_to([P, 4, HEAD_DIM]), ALU.add).then_inc(ends_read, 1)
                    nc.vector.tensor_tensor(qt[:, d, x, at], bank[:, 5, 256:384], ar[:, d, x, 1, at], ALU.add).then_inc(
                        ends_read, 1)

                dve.wait_ge(prepared, 2 * RW_PREPARED)
                dve.wait_ge(bonus_ready, 2)
                dve.wait_ge(exps_ready, 6)
                front_a(0)
                front_b(0)
                for n in range(len(units)):
                    level(n, 0)
                    level(n, 1)
                    if n >= 1:
                        finish(n - 1)
                    level(n, 2)
                    if n + 1 < len(units):
                        front_a(n + 1)
                    level(n, 3)
                    if n + 1 < len(units):
                        front_b(n + 1)
                    level(n, 4)
                finish(len(units) - 1)

                def over(a):
                    return a.unsqueeze(2).broadcast_to([P, RW_X, HEAD_DIM])

                of = [slice(RW_X * d, RW_X * d + RW_X) for d in range(2)]
                dve.wait_ge(parts_read, 2 * len(units))
                for d in range(2):
                    nc.vector.tensor_tensor(states[:, 1, of[d]], nn[:, 0, of[d]], over(ends[:, 0, of[d]]), ALU.mult).then_inc(
                        state_ready, 1)
                for s in range(1, RSTEPS - 1):
                    for d in range(2):
                        dve.wait_ge(step_made, state_count(s, d))
                        if s >= 2:
                            dve.wait_ge(inter_made, state_count(s - 1, d))
                        to = states[:, (s + 1) % 2, of[d]]
                        nc.vector.tensor_tensor(to, nn[:, s, of[d]], bank[:, d, 0:RW_X * HEAD_DIM].rearrange(
                            "p (n k) -> p n k", k=HEAD_DIM), ALU.add).then_inc(step_added, 1)
                        dve.wait_ge(step_added, state_count(s, d))
                        nc.vector.tensor_tensor(to, to, over(ends[:, s, of[d]]), ALU.mult).then_inc(state_ready, 1)
                dve.wait_ge(inter_made, 2 * (RSTEPS - 1))
                dve.wait_ge(prepared, 2 * RW_PREPARED + 1)
                for x in range(RW_X):
                    nc.vector.tensor_tensor(y[:, x], y_loc[:, 0, x], bank[:, 2 + x], ALU.add).then_inc(tail, 1)
                for x in range(RW_X):
                    dve.wait_ge(mean_made, x + 1)
                    nc.vector.scalar_tensor_tensor(y[:, x], bank[:, 5 + x], -1.0 / HEAD_DIM, y[:, x], ALU.mult,
                                                   ALU.add).then_inc(tail, 1)
                for x in range(RW_X):
                    dve.wait_ge(var_made, x + 1)
                    nc.vector.tensor_scalar(sq[:, x], bank[:, 5 + x], 1.0 / HEAD_DIM, GN_EPS, ALU.mult, ALU.add).then_inc(
                        tail, 1)
                    dve.wait_ge(tail, 2 * RW_X + x + 1)
                    nc.vector.reciprocal(sq[:, x], sq[:, x]).then_inc(var_ready, 1)
                dve.wait_ge(gate_ready, 1)
                count = 3 * RW_X
                for x in range(RW_X):
                    dve.wait_ge(var_rooted, x + 1)
                    nc.vector.tensor_tensor(y[:, x], y[:, x], sq[:, x], ALU.mult).then_inc(tail, 1)
                for x in range(RW_X):
                    dve.wait_ge(tail, count + x + 1)
                    nc.vector.tensor_scalar(y[:, x], y[:, x], par[:, LN_G, x:x + 1], par[:, LN_B, x:x + 1],
                                            ALU.mult, ALU.add).then_inc(tail, 1)
                for x in range(RW_X):
                    dve.wait_ge(tail, count + RW_X + x + 1)
                    nc.vector.tensor_tensor(y[:, x], y[:, x], bonus[:, x], ALU.add).then_inc(tail, 1)
                for x in range(RW_X):
                    dve.wait_ge(tail, count + 2 * RW_X + x + 1)
                    nc.vector.tensor_tensor(y[:, x], y[:, x], gate[:, x], ALU.mult).then_inc(out_ready, 1)


RW_PREPARED = 5
RW_CHAIN = 2 * RW_X + 3 + 1 + 3 + 1


EXPERTS = 16
CAPACITY = 2 * SEQ // EXPERTS
EXPERT_FF = 2 * D_MODEL


def expert_ffn(nc, stage, z_dram, x_dram, router_dram, gate_dram, up_dram, down_dram, ident_dram, slots_dram,
               gain_dram, out_dram):
    T = SEQ
    TT = T // P
    HALF = 512
    FC = EXPERT_FF // HALF
    FT = HALF // P
    with ExitStack() as ctx:
        sb, ps, sem = opener(nc, ctx, stage)
        z = sb("z", [P, KT, T])
        hot_r = sb("hot", [P, TT, EXPERTS, CAPACITY], F32R)
        hot = hot_r[:].bitcast(F32)
        xe = sb("xe", [P, KT, EXPERTS * CAPACITY])
        router = sb("router", [P, KT, EXPERTS])
        ident = sb("ident", [P, P])
        slots = sb("slots", [P, CAPACITY])
        logits = sb("logits", [P, TT, EXPERTS])
        high = sb("high", [P, TT])
        affinity = sb("affinity", [P, TT, EXPERTS])
        place_tok = sb("place_tok", [P, TT, EXPERTS])
        left = sb("left", [EXPERTS, T])
        best = sb("best", [EXPERTS, 8])
        chosen = sb("chosen", [EXPERTS, T])
        ones = sb("ones", [EXPERTS, T])
        w_in = sb("w_in", [P, 2, 2, KT, HALF])
        w_out = sb("w_out", [P, 2, FT, D_MODEL])
        xs = sb("xs", [P, 2, KT, CAPACITY])
        z_flat = z[:].rearrange("p k t -> p (k t)")
        hot_aff = z_flat.rearrange("p (t e s) -> p t e s", t=TT, e=EXPERTS)
        hot_flat = z_flat
        sg = hot_flat[0:CAPACITY, 0:2 * HALF].rearrange("n (s f) -> n s f", s=2)
        act_t = hot_flat[:, 2 * HALF:3 * HALF].rearrange("p (s j n) -> p s j n", s=2, j=FT)
        ye = hot_flat[:, 3 * HALF:3 * HALF + D_MODEL]
        with nc.sbuf_tensor(f"{stage}_z_tok", [P, 2, TT, D_MODEL], F32R) as z_tok:
            z_high, z_low = z_tok[:, 0], z_tok[:, 1]
        late = sb("late", [P, 2, KT, T])
        acc, scatter = late[:, 0], late[:, 1]
        gain = sb("gain", [P, KT])
        all_ones = sb("all_ones", [P, P])
        sq, scale = xe[:, :, 0:T], xe[:, 0, T:2 * T]
        bank = ps("bank", [P, 8, 512])

        loaded = sem("loaded")
        z_loaded = sem("z_loaded")
        x_loaded = sem("x_loaded")
        logits_made = sem("logits_made")
        route = sem("route")
        exp_ready = sem("exp_ready")
        aff_turned = sem("aff_turned")
        place_turned = sem("place_turned")
        hot_ready = sem("hot_ready")
        z_turned = sem("z_turned")
        z_high_ready = sem("z_high_ready")
        z_tok_ready = sem("z_tok_ready")
        xe_made = sem("xe_made")
        xe_ready = sem("xe_ready")
        weighted = sem("weighted")
        hot_turned = sem("hot_turned")
        scatter_ready = sem("scatter_ready")
        in_loaded = [sem(f"in_loaded{s}") for s in range(2)]
        out_loaded = [sem(f"out_loaded{s}") for s in range(2)]
        in_used = [sem(f"in_used{s}") for s in range(2)]
        out_used = [sem(f"out_used{s}") for s in range(2)]
        xs_ready = [sem(f"xs_ready{s}") for s in range(2)]
        silu_ready = sem("silu_ready")
        act_ready = sem("act_ready")
        act_turned = sem("act_turned")
        act_t_ready = sem("act_t_ready")
        y_made = sem("y_made")
        y_ready = sem("y_ready")
        part_made = sem("part_made")
        part_added = sem("part_added")
        squared = sem("squared")
        summed = sem("summed")
        meaned = sem("meaned")
        inverted = sem("inverted")
        rooted = sem("rooted")
        scaled = sem("scaled")
        stored = sem("stored")

        in_v = [w.rearrange("e (k p) f -> e p k f", p=P) for w in (gate_dram, up_dram)]
        out_v = down_dram.rearrange("e (c p) d -> e p c d", p=P)

        def pairs(eng, body):
            body(0)
            with eng.Fori(1, EXPERTS // 2) as i:
                body(i)

        def wait_reuse(eng, sem, count):
            if not (isinstance(count, int) and count == 0):
                eng.wait_ge(sem, count)

        with nc.Block() as block:

            @block.sync
            def _(sp):
                sp.dma_start(z[:], z_dram.rearrange("(k p) t -> p k t", p=P)).then_inc(z_loaded, 16)
                for dst, src in ((router[:], router_dram.rearrange("(k p) e -> p k e", p=P)), (ident[:], ident_dram),
                                 (slots[:], slots_dram), (gain[:], gain_dram)):
                    sp.dma_start(dst, src).then_inc(loaded, 16)

                def stream(i):
                    for m in range(2 * FC):
                        s, e, c = m % 2, m // FC, m % FC
                        wait_reuse(sp, in_used[s], FC * i + m // 2)
                        for g in range(2):
                            sp.dma_start(w_in[:, s, g], in_v[g][bass.ds(2 * i + e, 1), :, :, c * HALF:(c + 1) * HALF]
                                         .rearrange("e p k f -> p (e k) f")).then_inc(in_loaded[s], 16)
                        wait_reuse(sp, out_used[s], FC * i + m // 2)
                        sp.dma_start(w_out[:, s], out_v[bass.ds(2 * i + e, 1), :, c * FT:(c + 1) * FT, :]
                                     .rearrange("e p c d -> p (e c) d")).then_inc(out_loaded[s], 16)

                pairs(sp, stream)
                for m in range(KT):
                    sp.wait_ge(scaled, m + 1)
                    sp.dma_start(out_dram[m * P:(m + 1) * P, :], acc[:, m]).then_inc(stored, 16)
                sp.wait_ge(stored, 16 * KT)

            @block.gpsimd
            def _(pool):
                pool.wait_ge(xe_ready, 2 * KT)

                def stage_tokens(i):
                    for e in range(2):
                        wait_reuse(pool, in_used[1], (2 * i + e) * (FC // 2))
                        nc.gpsimd.tensor_copy(xs[:, e], xe[:, :, bass.ds((2 * i + e) * CAPACITY, CAPACITY)]).then_inc(
                            xs_ready[e], 1)

                pairs(pool, stage_tokens)

            @block.tensor
            def _(pe):
                pe.wait_ge(z_loaded, 16)
                pe.wait_ge(loaded, 64)
                for n in range(2 * TT):
                    t, h = n // 2, n % 2
                    if n >= 2:
                        pe.wait_ge(z_tok_ready, n - 1)
                    for j in range(4):
                        last = nc.tensor.transpose(bank[:, 2 + n % 2, j * P:(j + 1) * P],
                                                   z[:, 4 * h + j, t * P:(t + 1) * P], ident[:])
                    last.then_inc(z_turned, 1)
                for t in range(TT):
                    for k in range(KT):
                        last = nc.tensor.matmul(bank[:, 0, t * EXPERTS:(t + 1) * EXPERTS], z[:, k, t * P:(t + 1) * P],
                                                router[:, k, :], start=(k == 0), stop=(k == KT - 1))
                last.then_inc(logits_made, 1)
                pe.wait_ge(route, MOE_AFFINITY)
                for t in range(TT):
                    last = nc.tensor.transpose(bank[0:EXPERTS, 1, t * P:(t + 1) * P], affinity[:, t], ident[:])
                last.then_inc(aff_turned, 1)
                pe.wait_ge(route, MOE_PLACES)
                for t in range(TT):
                    last = nc.tensor.transpose(bank[:, 0, t * EXPERTS:(t + 1) * EXPERTS], chosen[:, t * P:(t + 1) * P],
                                               ident[0:EXPERTS, 0:EXPERTS])
                last.then_inc(place_turned, 1)
                pe.wait_ge(hot_ready, TT)
                pe.wait_ge(z_tok_ready, 2 * TT)
                for n in range(2 * KT):
                    h, m = n // KT, n % KT
                    if n >= 2:
                        pe.wait_ge(xe_ready, n - 1)
                    for t in range(TT):
                        for part in (z_low, z_high):
                            last = nc.tensor.matmul(bank[:, 4 + n % 2], part[:, t, m * P:(m + 1) * P],
                                                    hot_r[:, t, 8 * h:8 * h + 8].rearrange("p e s -> p (e s)"),
                                                    start=(t == 0 and part is z_low), stop=(t == TT - 1 and part is z_high))
                    last.then_inc(xe_made, 1)
                for j in range(EXPERTS // 2):
                    pe.wait_ge(weighted, TT)
                    if j >= 2:
                        pe.wait_ge(scatter_ready, j - 1)
                    for t in range(TT):
                        last = nc.tensor.transpose(bank[:, 6 + j % 2, t * P:(t + 1) * P],
                                                   hot_aff[:, t, 2 * j:2 * j + 2].rearrange("p e s -> p (e s)"), ident[:])
                    last.then_inc(hot_turned, 1)
                pe.wait_ge(xe_ready, 2 * KT)
                pe.wait_ge(scatter_ready, EXPERTS // 2)

                def experts(i):
                    def hidden(m):
                        s, e = m % 2, m // FC
                        pe.wait_ge(in_loaded[s], 32 * (FC * i + m // 2 + 1))
                        pe.wait_ge(xs_ready[e], i + 1)
                        if m >= 2:
                            pe.wait_ge(act_ready, 2 * FC * i + m - 1)
                        for k in range(KT):
                            for g in range(2):
                                last = nc.tensor.matmul(bank[64 * g:64 * g + 64, s], xs[:, e, k], w_in[:, s, g, k],
                                                        start=(k == 0), stop=(k == KT - 1))
                        last.then_inc(in_used[s], 1)

                    def output(m):
                        s, e, c = m % 2, m // FC, m % FC
                        pe.wait_ge(act_ready, 2 * FC * i + m + 1)
                        if m >= 2:
                            pe.wait_ge(act_t_ready, 2 * FC * i + m - 1)
                        for j in range(FT):
                            last = nc.tensor.transpose(bank[:, 2 + s, j * P:(j + 1) * P],
                                                       hot_flat[:, s * HALF + j * P:s * HALF + (j + 1) * P], ident[:])
                        last.then_inc(act_turned, 1)
                        pe.wait_ge(act_t_ready, 2 * FC * i + m + 1)
                        pe.wait_ge(out_loaded[s], 16 * (FC * i + m // 2 + 1))
                        if c == 0:
                            wait_reuse(pe, y_ready, 2 * i + e)
                        for j in range(FT):
                            for h in range(2):
                                last = nc.tensor.matmul(bank[64 * e:64 * e + 64, 4 + h], act_t[:, s, j],
                                                        w_out[:, s, j, h * 512:(h + 1) * 512],
                                                        start=(c == 0 and j == 0), stop=(c == FC - 1 and j == FT - 1))
                        last.then_inc(out_used[s], 1)

                    for m in range(2 * FC):
                        hidden(m)
                        if m >= 1:
                            output(m - 1)
                    output(2 * FC - 1)
                    pe.wait_ge(y_ready, 2 * i + 2)
                    for m in range(KT):
                        if m >= 2:
                            pe.wait_ge(part_added, KT * i + m - 1)
                        nc.tensor.matmul(bank[:, 6 + m % 2], ye[:, m * P:(m + 1) * P],
                                         scatter[:, bass.ds(i, 1), :].rearrange("p a t -> p (a t)"),
                                         start=True, stop=True).then_inc(part_made, 1)

                pairs(pe, experts)
                pe.wait_ge(act_ready, EXPERTS * FC)
                for m in range(KT):
                    pe.wait_ge(squared, m + 1)
                    last = nc.tensor.matmul(bank[:, 0], all_ones[:], sq[:, m], start=(m == 0), stop=(m == KT - 1))
                last.then_inc(summed, 1)

            @block.scalar
            def _(act):
                for n in range(2 * TT):
                    act.wait_ge(z_turned, n + 1)
                    nc.scalar.copy(z_high[:, n // 2, 512 * (n % 2):512 * (n % 2) + 512], bank[:, 2 + n % 2]).then_inc(
                        z_high_ready, 1)
                act.wait_ge(route, 3)
                nc.scalar.activation(logits[:], logits[:], ACT.Exp).then_inc(exp_ready, 1)
                for n in range(2 * KT):
                    act.wait_ge(xe_made, n + 1)
                    nc.scalar.copy(xe[:, n % KT, 512 * (n // KT):512 * (n // KT) + 512], bank[:, 4 + n % 2]).then_inc(
                        xe_ready, 1)
                act.wait_ge(xe_ready, 2 * KT)
                for j in range(EXPERTS // 2):
                    act.wait_ge(hot_turned, j + 1)
                    nc.scalar.copy(scatter[:, j], bank[:, 6 + j % 2]).then_inc(scatter_ready, 1)

                act.dma_start(acc, x_dram.rearrange("(m p) t -> p m t", p=P)).then_inc(x_loaded, 16)

                def experts(i):
                    for m in range(2 * FC):
                        s = m % 2
                        act.wait_ge(in_used[s], FC * i + m // 2 + 1)
                        if m >= 2:
                            act.wait_ge(act_turned, 2 * FC * i + m - 1)
                        nc.scalar.activation(sg[:, s], bank[0:CAPACITY, s], ACT.Silu).then_inc(silu_ready, 1)
                        act.wait_ge(act_turned, 2 * FC * i + m + 1)
                        if m >= 2:
                            act.wait_ge(out_used[s], FC * i + m // 2)
                        nc.scalar.copy(act_t[:, s], bank[:, 2 + s].rearrange("p (j n) -> p j n", j=FT)[:, :, 0:CAPACITY]).then_inc(
                            act_t_ready, 1)

                pairs(act, experts)
                act.wait_ge(xs_ready[1], EXPERTS // 2)
                for m in range(KT):
                    act.wait_ge(part_added, KT * (EXPERTS // 2 - 1) + m + 1)
                    nc.scalar.activation(sq[:, m], acc[:, m], ACT.Square).then_inc(squared, 1)
                act.wait_ge(inverted, 1)
                nc.scalar.activation(scale, scale, ACT.Sqrt).then_inc(rooted, 1)

            @block.vector
            def _(dve):
                nc.vector.memset(all_ones[:], 1.0)
                nc.vector.memset(ones[:], 1.0).then_inc(route, 1)
                done = [1]

                def step(ins):
                    ins.then_inc(route, 1)
                    done[0] += 1
                    dve.wait_ge(route, done[0])

                wide = [P, TT, EXPERTS]
                for n in range(2 * TT):
                    dve.wait_ge(z_high_ready, n + 1)
                    cols = slice(512 * (n % 2), 512 * (n % 2) + 512)
                    nc.vector.tensor_tensor(z_low[:, n // 2, cols], bank[:, 2 + n % 2], z_high[:, n // 2, cols].bitcast(F32),
                                            ALU.subtract).then_inc(z_tok_ready, 1)
                dve.wait_ge(logits_made, 1)
                raw = bank[:, 0, 0:TT * EXPERTS].rearrange("p (t e) -> p t e", t=TT)
                step(nc.vector.tensor_reduce(high[:], raw, X, ALU.max))
                step(nc.vector.tensor_tensor(logits[:], raw, high[:].unsqueeze(2).broadcast_to(wide), ALU.subtract))
                dve.wait_ge(exp_ready, 1)
                step(nc.vector.tensor_reduce(high[:], logits[:], X, ALU.add))
                step(nc.vector.reciprocal(high[:], high[:]))
                step(nc.vector.tensor_tensor(affinity[:], logits[:], high[:].unsqueeze(2).broadcast_to(wide), ALU.mult))
                assert done[0] == MOE_AFFINITY, done[0]
                dve.wait_ge(aff_turned, 1)
                step(nc.vector.tensor_copy(left[:], bank[0:EXPERTS, 1]))
                for _ in range(CAPACITY // 8):
                    step(nc.vector.max(best[:], left[:]))
                    step(nc.vector.match_replace(left[:], best[:], left[:], -1.0))
                step(nc.vector.tensor_scalar(chosen[:], left[:], 0.0, None, ALU.is_lt))
                step(nc.vector.tensor_tensor_scan(left[:], ones[:], chosen[:], 0.0, ALU.mult, ALU.add))
                step(nc.vector.tensor_tensor(chosen[:], chosen[:], left[:], ALU.mult))
                assert done[0] == MOE_PLACES, done[0]
                dve.wait_ge(place_turned, 1)
                step(nc.vector.tensor_copy(place_tok[:], raw))
                grid = [P, EXPERTS, CAPACITY]
                for t in range(TT):
                    nc.vector.tensor_tensor(hot_r[:, t], slots[:].unsqueeze(1).broadcast_to(grid),
                                            place_tok[:, t].unsqueeze(2).broadcast_to(grid), ALU.is_equal).then_inc(
                        hot_ready, 1)
                dve.wait_ge(z_turned, 2 * TT)
                dve.wait_ge(hot_ready, TT)
                for t in range(TT):
                    nc.vector.tensor_tensor(hot_aff[:, t], hot[:, t], affinity[:, t].unsqueeze(2).broadcast_to(grid),
                                            ALU.mult).then_inc(weighted, 1)
                dve.wait_ge(x_loaded, 16)

                def experts(i):
                    for e in range(2):
                        for c in range(FC):
                            m = FC * e + c
                            s = m % 2
                            dve.wait_ge(silu_ready, 2 * FC * i + m + 1)
                            nc.vector.tensor_tensor(sg[:, s], sg[:, s], bank[64:64 + CAPACITY, s], ALU.mult).then_inc(
                                act_ready, 1)
                        dve.wait_ge(out_used[1], FC * i + FC // 2 * (e + 1))
                        wait_reuse(dve, part_made, KT * i)
                        nc.vector.tensor_copy(ye[64 * e:64 * e + 64, :].rearrange("p (h d) -> p h d", h=2),
                                              bank[64 * e:64 * e + 64, 4:6, :]).then_inc(y_ready, 1)
                    for m in range(KT):
                        dve.wait_ge(part_made, KT * i + m + 1)
                        wait_reuse(dve, part_added, KT * i)
                        nc.vector.tensor_tensor(acc[:, m], acc[:, m], bank[:, 6 + m % 2], ALU.add).then_inc(part_added, 1)

                pairs(dve, experts)
                dve.wait_ge(xs_ready[1], EXPERTS // 2)
                dve.wait_ge(summed, 1)
                nc.vector.tensor_scalar(scale, bank[:, 0], 1.0 / D_MODEL, EPS, ALU.mult, ALU.add).then_inc(meaned, 1)
                dve.wait_ge(meaned, 1)
                nc.vector.reciprocal(scale, scale).then_inc(inverted, 1)
                dve.wait_ge(rooted, 1)
                dve.wait_ge(loaded, 64)
                for m in range(KT):
                    nc.vector.scalar_tensor_tensor(acc[:, m], acc[:, m], gain[:, m:m + 1], scale, ALU.mult,
                                                   ALU.mult).then_inc(scaled, 1)


MOE_AFFINITY = 6
MOE_PLACES = MOE_AFFINITY + 1 + 2 * (CAPACITY // 8) + 3


D_FF = 2816
N_MEM = 256
NA_WIDTH = 384
MEM_WIDTH = 256


def two_blocks(nc, d, out_dram):
    STAGE_TURN.clear()

    def scratch(name, rows, cols):
        return nc.dram_tensor(name, (rows, cols), F32, kind="Internal").ap()

    p = scratch("p", 5 * D_MODEL + 2 * D_MODEL, LEN)
    ya_raw = scratch("ya_raw", D_MODEL, LEN)
    yb = scratch("yb", D_MODEL, LEN)
    h1 = scratch("h1", D_MODEL, LEN)
    a1 = scratch("a1", D_FF, LEN)
    h2 = scratch("h2", D_MODEL, LEN)
    project(nc, "in", d["h"], d["w_in"], p, gain_dram=d["mix_norm_g"])
    s5(nc, "s5", p[0:D_MODEL], d["ssm_lam"], d["ssm_bc"], d["ssm_d"], d["ident"], ya_raw)
    hgrn2(nc, "hgrn", p[D_MODEL:5 * D_MODEL], d["hgrn_lb"], d["hgrn_norm_g"], d["ident"], d["hgrn_causal"],
          d["hgrn_member"], yb)
    project_chain(nc, "merge", [(ya_raw, d["ssm_w_glu"], "glu", ya_raw, "x"),
                                (None, d["w_ssm_proj"], "gate", p[5 * D_MODEL:6 * D_MODEL], "merged"),
                                (yb, d["w_hgrn_proj"], "gate_add", p[6 * D_MODEL:7 * D_MODEL], "x"),
                                (None, d["w_out"], "add", d["h"], "out")], h1)
    conv_gated_up(nc, "up", h1, d["ffn_norm_g"], d["w_up"], d["conv_w"], d["conv_b"], a1)
    project(nc, "down", a1, d["w_down"], h2, "add", [h1], width=P)

    x = scratch("x", D_MODEL, SEQ)
    widths = [3 * NA_WIDTH, 3 * RW_WIDTH + 2 * P, MEM_WIDTH, D_MODEL, D_MODEL, D_MODEL]
    starts = [sum(widths[:n]) for n in range(len(widths) + 1)]
    p2 = scratch("p2", starts[-1], SEQ)
    p_na, p_rw, q_mem, g_na, g_rw, g_mem = (p2[starts[n]:starts[n + 1]] for n in range(len(widths)))
    kv = scratch("kv", 2 * MEM_WIDTH, N_MEM)
    y_na = scratch("y_na", NA_WIDTH, SEQ)
    y_rw = scratch("y_rw", RW_WIDTH, SEQ)
    y_mem = scratch("y_mem", MEM_WIDTH, SEQ)
    x3 = scratch("x3", D_MODEL, SEQ)
    z3 = scratch("z3", D_MODEL, SEQ)
    rmsnorm(nc, "norm_final", h2[:, N_META:], d["final_norm_g"], x)
    project(nc, "in_2", x, d["w_in_2"], p2, gain_dram=d["norm_mix_g_2"])
    project(nc, "mem_kv", d["mem"], d["w_mem_kv_2"], kv, gain_dram=d["norm_mem_g_2"])
    attention(nc, "na", p_na[0:NA_WIDTH], p_na[NA_WIDTH:2 * NA_WIDTH], p_na[2 * NA_WIDTH:], d["na_bias"],
              d["ident"], y_na)
    attention(nc, "mem", q_mem, kv[0:MEM_WIDTH], kv[MEM_WIDTH:], None, d["ident"], y_mem)
    rwkv7(nc, "rw", p_rw, d["rw_par"], d["rw_mu_l"], d["rw_lora"], d["rw_g2_2"], d["ident"], d["rw_masks"],
          d["rw_member"], d["eye2"], y_rw)
    project_chain(nc, "merge_2", [(y_na, d["w_branch_na_2"], "gate", g_na, "merged"),
                                  (y_rw, d["w_branch_rw_2"], "gate_add", g_rw, "merged"),
                                  (y_mem, d["w_branch_mem_2"], "gate_add", g_mem, "x"),
                                  (None, d["w_out_2"], "add", x, "out")], x3, d["norm_ffn_g_2"], z3)
    expert_ffn(nc, "moe", z3, x3, d["w_router_2"], d["w_exp_gate_2"], d["w_exp_up_2"], d["w_exp_down_2"],
               d["ident"], d["slots"], d["norm_final_g_2"], out_dram)


def by_partition(a):
    return np.ascontiguousarray(a.reshape(-1, P).T)


def by_state(a):
    a = a.reshape(PAIRS, 2, SSM_STATE, *a.shape[2:])
    return np.moveaxis(a, 0, 2).reshape(P, PAIRS, *a.shape[3:])


def laid_out(v):
    d = {}
    d["h"] = np.concatenate([v["meta_tokens"], v["x"][0]], axis=0).T
    d["mem"] = v["mem_2"][0].T
    for name in ("mix_norm_g", "ffn_norm_g", "final_norm_g", "norm_mix_g_2", "norm_mem_g_2", "norm_ffn_g_2",
                 "norm_final_g_2"):
        d[name] = by_partition(v[name].reshape(-1))
    for name in ("w_in", "ssm_w_glu", "w_ssm_proj", "w_hgrn_proj", "w_out", "w_up", "w_down", "w_in_2", "w_mem_kv_2",
                 "w_branch_na_2", "w_branch_rw_2", "w_branch_mem_2", "w_out_2", "w_router_2", "w_exp_gate_2",
                 "w_exp_up_2", "w_exp_down_2", "rw_g2_2"):
        d[name] = v[name][0]
    log_dt = np.broadcast_to(v["ssm_log_dt"][0][:, None], (SSM_GROUPS, SSM_STATE))
    d["ssm_lam"] = np.stack([by_state(a) for a in (v["ssm_lambda_re"][0], v["ssm_lambda_im"][0], log_dt)], 1)
    d["ssm_bc"] = np.stack([by_state(a) for a in (
        v["ssm_b_re"][0], v["ssm_b_im"][0], v["ssm_c_re"][0].transpose(0, 2, 1), v["ssm_c_im"][0].transpose(0, 2, 1))], 1)
    d["ssm_d"] = by_partition(v["ssm_d"][0])
    d["hgrn_lb"] = v["hgrn_lb_logits"].reshape(2, HEADS, P).transpose(2, 0, 1)
    d["hgrn_norm_g"] = v["hgrn_norm_g"][0].reshape(P, 1)
    d["conv_w"] = v["conv_w"][0].reshape(3, 2 * D_FF // P, P).transpose(2, 1, 0)
    d["conv_b"] = by_partition(v["conv_b"][0])
    d["na_bias"] = window_bias(v["na_rpb_2"][0])
    rw = {name: v[f"rw_{name}_2"][0] for name in ("mu_rkv", "mu_w", "mu_a", "w0", "w2", "a0", "a2", "k_k", "k_a", "r_k",
                                                 "ln_g", "ln_b")}
    columns = [rw["mu_rkv"][dd, j] for j in range(3) for dd in range(2)] + [rw["w0"][dd] for dd in range(2)] + [
        rw["a0"][dd] for dd in range(2)] + [rw["k_k"], rw["k_a"], rw["r_k"].reshape(-1), rw["ln_g"], rw["ln_b"]]
    d["rw_par"] = np.stack([c.reshape(RW_X, P) for c in columns]).transpose(2, 0, 1)
    d["rw_mu_l"] = np.concatenate([rw["mu_w"], rw["mu_a"]], 1).T
    d["rw_lora"] = np.concatenate([rw["w2"], rw["a2"]], 1).transpose(1, 0, 2)
    n = np.arange(P)
    f32 = np.float32
    d["ident"] = np.eye(P, dtype=f32)
    d["eye2"] = np.concatenate([np.eye(HEAD_DIM, dtype=f32)] * 2)
    d["slots"] = np.broadcast_to(np.arange(1, CAPACITY + 1, dtype=f32), (P, CAPACITY))
    s, t = n[:, None], n[None, :]
    d["hgrn_causal"] = ((s // HCHUNK == t // HCHUNK) & (s <= t)).astype(f32)
    d["hgrn_member"] = np.broadcast_to((s // HCHUNK == np.arange(P // HCHUNK))[:, :, None],
                                       (P, P // HCHUNK, P)).astype(f32)
    same = s // RCHUNK == t // RCHUNK
    d["rw_masks"] = np.stack([np.stack([same & (s < t), same & (s <= t)] * 2, 1),
                              np.stack([same & (s > t), same & (s >= t)] * 2, 1)], 1).astype(f32)
    d["rw_member"] = np.broadcast_to((s // RCHUNK == np.arange(P // RCHUNK))[:, :, None],
                                     (P, P // RCHUNK, P)).astype(f32)
    return {name: np.ascontiguousarray(a) for name, a in d.items()}


def kernel(**inputs):
    import concourse.bacc as bacc
    from concourse.bass_utils import run_bass_kernel_spmd

    arrays = laid_out({name: np.asarray(a) for name, a in inputs.items()})
    nc = bacc.Bacc("TRN2", target_bir_lowering=False, num_devices=1)
    ins = {name: nc.dram_tensor(f"in_{name}", a.shape, mybir.dt.from_np(a.dtype), kind="ExternalInput").ap()
           for name, a in arrays.items()}
    out = nc.dram_tensor("out", (D_MODEL, SEQ), F32, kind="ExternalOutput").ap()
    two_blocks(nc, ins, out)
    r = run_bass_kernel_spmd(nc, [{f"in_{name}": a for name, a in arrays.items()}], core_ids=[0])
    return np.ascontiguousarray(r.results[0]["out"].T).reshape(1, SEQ, D_MODEL)
```
